# Optimizing a Trainium2 kernel written in Bass

```python
import jax, jax.numpy as jnp
from jax import lax
import numpy as np

D_MODEL = 1024
BATCH = 1
SEQ = 1024
DEPTH = 1
DEC_BATCH = 8
DEC_SEQ = 4
PAST_LEN = 1024
PAGE_SIZE = 128

NSA_HEADS = 8
NSA_GROUPS = 2
NSA_HPG = NSA_HEADS // NSA_GROUPS
HEAD_DIM = 64
CMP_STRIDE = 16
CMP_LEN = 2 * CMP_STRIDE
CMP_HID = HEAD_DIM
SLC_BLOCK = 64
N_SEL = 16
WINDOW = 512
Q_BLOCK = 128
GLA_HEADS = 4
GLA_DK = 64
GLA_DV = 128
GLA_GATE_RANK = 16
GLA_TAU = 16.0
GLA_CHUNK = 64
D_FF = -(-8 * D_MODEL // (3 * 256)) * 256
EPS = 1e-6

NSA_Q = NSA_HEADS * HEAD_DIM
NSA_KV = 2 * NSA_GROUPS * HEAD_DIM
NSA_GATE = 3 * NSA_HEADS
GLA_QK = GLA_HEADS * GLA_DK
GLA_V = GLA_HEADS * GLA_DV
SPLIT_SIZES = (NSA_Q, NSA_KV, NSA_KV, NSA_KV, NSA_GATE, GLA_QK, GLA_QK, GLA_V, GLA_GATE_RANK, GLA_V, 2 * D_MODEL)
SPLIT_POINTS = tuple(int(s) for s in np.cumsum(SPLIT_SIZES)[:-1])
D_IN = sum(SPLIT_SIZES)

kernel_name = 'hybrid_nsa_gla_adaln_decoder_step'

def rmsnorm(x, g):
    xf = x.astype(jnp.float32)
    y = xf * lax.rsqrt(jnp.mean(xf * xf, axis=-1, keepdims=True) + EPS)
    return (y * g.astype(jnp.float32)).astype(x.dtype)

def masked_softmax(s, valid):
    s = jnp.where(valid, s.astype(jnp.float32), -jnp.inf)
    m = jnp.max(s, axis=-1, keepdims=True)
    m = jnp.where(jnp.isfinite(m), m, 0.0)
    e = jnp.exp(s - m)
    d = jnp.sum(e, axis=-1, keepdims=True)
    return e / jnp.where(d > 0, d, 1.0)

def compress(kv, w1, b1, w2, pe):
    B, L = kv.shape[:2]
    n_chunk = L // CMP_STRIDE
    ch = kv[:, :n_chunk * CMP_STRIDE].reshape(B, n_chunk, CMP_STRIDE, NSA_GROUPS, HEAD_DIM)
    w1r = w1.reshape(CMP_LEN, HEAD_DIM, CMP_HID)
    first = jnp.einsum('bnpgd,pdh->bngh', ch + pe[:CMP_STRIDE, None, :], w1r[:CMP_STRIDE])
    second = jnp.einsum('bnpgd,pdh->bngh', ch + pe[CMP_STRIDE:, None, :], w1r[CMP_STRIDE:])
    hid = jax.nn.gelu(first[:, :-1] + second[:, 1:] + b1)
    return jnp.einsum('bngh,hd->bngd', hid, w2)

def overlap_matrix(n_cmp, n_slc):
    n = jnp.arange(n_cmp)[:, None] * CMP_STRIDE
    j = jnp.arange(n_slc)[None, :] * SLC_BLOCK
    return ((n < j + SLC_BLOCK) & (n + CMP_LEN > j)).astype(jnp.float32)

def nsa_core(q, qpos, ck, cv, gather_slc, n_slc, wk, wv, wpos):
    B, T = q.shape[:2]
    n_cmp = ck.shape[1]
    s = jnp.einsum('btghd,bngd->btghn', q, ck)
    cvalid = (jnp.arange(n_cmp) * CMP_STRIDE + CMP_LEN)[None, :] <= qpos[:, None] + 1
    p = masked_softmax(s, cvalid[None, :, None, None, :])
    o_cmp = jnp.einsum('btghn,bngd->btghd', p.astype(cv.dtype), cv)
    imp = jnp.einsum('btgn,nj->btgj', p.sum(axis=3), overlap_matrix(n_cmp, n_slc))
    j = jnp.arange(n_slc)[None, :]
    cur = (qpos // SLC_BLOCK)[:, None]
    forced = ((j == 0) | (j == cur) | (j == cur - 1))[None, :, None, :]
    causal = (j <= cur)[None, :, None, :]
    score = jnp.where(forced, jnp.inf, jnp.where(causal, imp, -jnp.inf))
    _, idx = lax.top_k(score, min(N_SEL, n_slc))
    sk, sv = gather_slc(idx)
    kpos = idx[..., None] * SLC_BLOCK + jnp.arange(SLC_BLOCK)
    svalid = (kpos <= qpos[None, :, None, None, None]).reshape(B, T, NSA_GROUPS, 1, -1)
    s = jnp.einsum('btghd,btgkrd->btghkr', q, sk).reshape(B, T, NSA_GROUPS, NSA_HPG, -1)
    p = masked_softmax(s, svalid)
    o_slc = jnp.einsum('btghm,btgmd->btghd', p.astype(sv.dtype), sv.reshape(B, T, NSA_GROUPS, -1, HEAD_DIM))
    s = jnp.einsum('btghd,bsgd->btghs', q, wk)
    dist = qpos[:, None] - wpos[None, :]
    wvalid = (dist >= 0) & (dist < WINDOW) & (wpos >= 0)[None, :]
    p = masked_softmax(s, wvalid[None, :, None, None, :])
    o_win = jnp.einsum('btghs,bsgd->btghd', p.astype(wv.dtype), wv)
    return o_cmp, o_slc, o_win

def nsa_prompt(q, kv_c, kv_s, kv_w, cmpk, cmpv):
    B, L = q.shape[:2]
    ck = compress(kv_c[:, :, 0], *cmpk)
    cv = compress(kv_c[:, :, 1], *cmpv)
    n_slc = L // SLC_BLOCK
    blocks = kv_s.reshape(B, n_slc, SLC_BLOCK, 2, NSA_GROUPS, HEAD_DIM)
    bi = jnp.arange(B)[:, None, None, None]
    gi = jnp.arange(NSA_GROUPS)[None, None, :, None]

    def gather(idx):
        blk = blocks[bi, idx, :, :, gi, :]
        return blk[..., 0, :], blk[..., 1, :]

    win = jnp.pad(kv_w, ((0, 0), (WINDOW, 0), (0, 0), (0, 0), (0, 0)))

    def one_block(i):
        t0 = i * Q_BLOCK
        qb = lax.dynamic_slice_in_dim(q, t0, Q_BLOCK, axis=1)
        wb = lax.dynamic_slice_in_dim(win, t0, WINDOW + Q_BLOCK, axis=1)
        qpos = t0 + jnp.arange(Q_BLOCK)
        wpos = t0 - WINDOW + jnp.arange(WINDOW + Q_BLOCK)
        return nsa_core(qb, qpos, ck, cv, gather, n_slc, wb[:, :, 0], wb[:, :, 1], wpos)

    outs = lax.map(one_block, jnp.arange(L // Q_BLOCK))
    return tuple(o.swapaxes(0, 1).reshape(q.shape) for o in outs)

def nsa_sample(q, kv_c, kv_s, kv_w, cache_c, cache_s, win_buf, page_table, cmpk, cmpv):
    Bd, S = q.shape[:2]
    P = page_table.shape[1] * PAGE_SIZE
    past_c = cache_c[page_table].reshape(Bd, P, 2, NSA_GROUPS, HEAD_DIM)
    full_c = jnp.concatenate([past_c, kv_c], axis=1)
    ck = compress(full_c[:, :, 0], *cmpk)
    cv = compress(full_c[:, :, 1], *cmpv)
    n_slc = -(-(P + S) // SLC_BLOCK)
    nb_past = P // SLC_BLOCK
    nb_new = n_slc - nb_past
    new_blocks = jnp.pad(kv_s, ((0, 0), (0, nb_new * SLC_BLOCK - S), (0, 0), (0, 0), (0, 0)))
    new_blocks = new_blocks.reshape(Bd, nb_new, SLC_BLOCK, 2, NSA_GROUPS, HEAD_DIM)
    bi = jnp.arange(Bd)[:, None, None, None]
    gi = jnp.arange(NSA_GROUPS)[None, None, :, None]
    r = jnp.arange(SLC_BLOCK)

    def gather(idx):
        start = jnp.minimum(idx, nb_past - 1) * SLC_BLOCK
        phys = page_table[bi, start // PAGE_SIZE]
        past = cache_s[phys[..., None], (start % PAGE_SIZE)[..., None] + r, :, gi[..., None], :]
        new = new_blocks[bi, jnp.clip(idx - nb_past, 0, nb_new - 1), :, :, gi, :]
        blk = jnp.where((idx < nb_past)[..., None, None, None], past, new)
        return blk[..., 0, :], blk[..., 1, :]

    w_buf = win_buf.shape[1]
    wkv = jnp.concatenate([win_buf, kv_w], axis=1)
    wpos = P - w_buf + jnp.arange(w_buf + S)
    qpos = P + jnp.arange(S)
    outs = nsa_core(q, qpos, ck, cv, gather, n_slc, wkv[:, :, 0], wkv[:, :, 1], wpos)
    return outs, wkv[:, S:]

def gla_chunk(s0, q, k, v, lg):
    C = q.shape[1]
    b = jnp.cumsum(lg, axis=1)
    o_inter = jnp.einsum('bthk,bhkv->bthv', q * jnp.exp(b), s0)
    tri = (jnp.arange(C)[:, None] >= jnp.arange(C)[None, :])[None, :, :, None, None]
    dec = jnp.exp(jnp.where(tri, b[:, :, None] - b[:, None, :], -jnp.inf))
    a = jnp.einsum('bthk,btshk,bshk->btsh', q, dec, k)
    o_intra = jnp.einsum('btsh,bshv->bthv', a, v)
    b_last = b[:, -1]
    s_new = jnp.exp(b_last)[..., None] * s0 + jnp.einsum('bshk,bshv->bhkv', k * jnp.exp(b_last[:, None] - b), v)
    return s_new, o_inter + o_intra

def gla_scan(s0, q, k, v, lg):
    B, L = q.shape[:2]
    C = GLA_CHUNK if L % GLA_CHUNK == 0 else L
    n = L // C

    def chunks(a):
        return jnp.moveaxis(a.astype(jnp.float32).reshape((B, n, C) + a.shape[2:]), 1, 0)

    def step(s, inp):
        return gla_chunk(s, *inp)

    s_fin, o = lax.scan(step, s0, (chunks(q), chunks(k), chunks(v), chunks(lg)))
    return s_fin, jnp.moveaxis(o, 0, 1).reshape(B, L, GLA_HEADS, GLA_DV)

def block_forward(x, c, core, w_ada, b_ada, g_pre_mix, g_post_mix, w_in, w_gla_a2, b_gla_a, gla_norm_g,
                  w_nsa_o, w_gla_o, w_out, g_pre_ffn, g_post_ffn, w_ff_gate, w_ff_up, w_ff_down):
    B, L, _ = x.shape
    mod = (c @ w_ada + b_ada)[:, None, :]
    sh1, sc1, ga1, sh2, sc2, ga2 = jnp.split(mod, 6, axis=-1)
    h = rmsnorm(x, g_pre_mix) * (1 + sc1) + sh1
    z = h @ w_in
    q_n, kv_c, kv_s, kv_w, g_n, q_g, k_g, v_g, a_g, r_g, m_g = jnp.split(z, SPLIT_POINTS, axis=-1)
    q_n = (q_n * HEAD_DIM ** -0.5).reshape(B, L, NSA_GROUPS, NSA_HPG, HEAD_DIM)
    kv_c = kv_c.reshape(B, L, 2, NSA_GROUPS, HEAD_DIM)
    kv_s = kv_s.reshape(B, L, 2, NSA_GROUPS, HEAD_DIM)
    kv_w = kv_w.reshape(B, L, 2, NSA_GROUPS, HEAD_DIM)
    q_g = (q_g * GLA_DK ** -0.5).reshape(B, L, GLA_HEADS, GLA_DK)
    k_g = k_g.reshape(B, L, GLA_HEADS, GLA_DK)
    v_g = v_g.reshape(B, L, GLA_HEADS, GLA_DV)
    lg = (jax.nn.log_sigmoid((a_g @ w_gla_a2 + b_gla_a).astype(jnp.float32)) / GLA_TAU).reshape(B, L, GLA_HEADS, GLA_DK)
    o_cmp, o_slc, o_win, o_gla, states = core(q_n, kv_c, kv_s, kv_w, q_g, k_g, v_g, lg)
    gates = jax.nn.sigmoid(g_n).reshape(B, L, 3, NSA_GROUPS, NSA_HPG, 1)
    o_nsa = gates[:, :, 0] * o_cmp + gates[:, :, 1] * o_slc + gates[:, :, 2] * o_win
    y_a = o_nsa.reshape(B, L, NSA_Q) @ w_nsa_o
    o_gla = rmsnorm(o_gla.astype(x.dtype), gla_norm_g) * jax.nn.silu(r_g.reshape(B, L, GLA_HEADS, GLA_DV))
    y_b = o_gla.reshape(B, L, GLA_V) @ w_gla_o
    m_a, m_b = jnp.split(jax.nn.sigmoid(m_g), 2, axis=-1)
    mix = (m_a * y_a + m_b * y_b) @ w_out
    x = x + ga1 * rmsnorm(mix, g_post_mix)
    h = rmsnorm(x, g_pre_ffn) * (1 + sc2) + sh2
    f = (jax.nn.silu(h @ w_ff_gate) * (h @ w_ff_up)) @ w_ff_down
    x = x + ga2 * rmsnorm(f, g_post_ffn)
    return x, states

def setup_inputs(seed: int = 0) -> dict:
    key = jax.random.key(seed)
    keys = list(jax.random.split(key, 48))

    def nrm(shape, scale):
        return jax.random.normal(keys.pop(), shape, jnp.float32) * scale

    def gain(shape):
        return 1.0 + nrm(shape, 0.02)

    D = D_MODEL
    n_pages = PAST_LEN // PAGE_SIZE
    n_used = DEC_BATCH * n_pages
    n_pool = n_used + max(1, n_used // 4)
    page_table = jax.random.permutation(keys.pop(), n_pool)[:n_used].reshape(DEC_BATCH, n_pages).astype(jnp.int32)
    w_buf = min(WINDOW, PAST_LEN)
    cmp_in = CMP_LEN * HEAD_DIM
    return {
        'x_prompt': nrm((BATCH, SEQ, D), 1.0),
        'x_sample': nrm((DEC_BATCH, DEC_SEQ, D), 1.0),
        'cache_cmp_kv': nrm((DEPTH, n_pool, PAGE_SIZE, 2, NSA_GROUPS, HEAD_DIM), 1.0),
        'cache_slc_kv': nrm((DEPTH, n_pool, PAGE_SIZE, 2, NSA_GROUPS, HEAD_DIM), 1.0),
        'state_win_kv': nrm((DEPTH, DEC_BATCH, w_buf, 2, NSA_GROUPS, HEAD_DIM), 1.0),
        'state_gla': nrm((DEPTH, DEC_BATCH, GLA_HEADS, GLA_DK, GLA_DV), 0.5),
        'page_table': page_table,
        'c_prompt': nrm((BATCH, D), 1.0),
        'c_sample': nrm((DEC_BATCH, D), 1.0),
        'w_ada': nrm((DEPTH, D, 6 * D), 0.3 * D ** -0.5),
        'b_ada': nrm((DEPTH, 6 * D), 0.02),
        'g_pre_mix': gain((DEPTH, D)),
        'g_post_mix': gain((DEPTH, D)),
        'w_in': nrm((DEPTH, D, D_IN), D ** -0.5),
        'cmp_w1_k': nrm((DEPTH, cmp_in, CMP_HID), cmp_in ** -0.5),
        'cmp_b1_k': nrm((DEPTH, CMP_HID), 0.02),
        'cmp_w2_k': nrm((DEPTH, CMP_HID, HEAD_DIM), CMP_HID ** -0.5),
        'cmp_pe_k': nrm((DEPTH, CMP_LEN, HEAD_DIM), 0.1),
        'cmp_w1_v': nrm((DEPTH, cmp_in, CMP_HID), cmp_in ** -0.5),
        'cmp_b1_v': nrm((DEPTH, CMP_HID), 0.02),
        'cmp_w2_v': nrm((DEPTH, CMP_HID, HEAD_DIM), CMP_HID ** -0.5),
        'cmp_pe_v': nrm((DEPTH, CMP_LEN, HEAD_DIM), 0.1),
        'w_gla_a2': nrm((DEPTH, GLA_GATE_RANK, GLA_QK), GLA_GATE_RANK ** -0.5),
        'b_gla_a': nrm((DEPTH, GLA_QK), 0.02),
        'gla_norm_g': gain((DEPTH, GLA_DV)),
        'w_nsa_o': nrm((DEPTH, NSA_Q, D), NSA_Q ** -0.5),
        'w_gla_o': nrm((DEPTH, GLA_V, D), GLA_V ** -0.5),
        'w_out': nrm((DEPTH, D, D), D ** -0.5),
        'g_pre_ffn': gain((DEPTH, D)),
        'g_post_ffn': gain((DEPTH, D)),
        'w_ff_gate': nrm((DEPTH, D, D_FF), D ** -0.5),
        'w_ff_up': nrm((DEPTH, D, D_FF), D ** -0.5),
        'w_ff_down': nrm((DEPTH, D_FF, D), D_FF ** -0.5),
    }

def reference(x_prompt, x_sample, cache_cmp_kv, cache_slc_kv, state_win_kv, state_gla, page_table,
              c_prompt, c_sample, w_ada, b_ada, g_pre_mix, g_post_mix, w_in,
              cmp_w1_k, cmp_b1_k, cmp_w2_k, cmp_pe_k, cmp_w1_v, cmp_b1_v, cmp_w2_v, cmp_pe_v,
              w_gla_a2, b_gla_a, gla_norm_g, w_nsa_o, w_gla_o, w_out, g_pre_ffn, g_post_ffn,
              w_ff_gate, w_ff_up, w_ff_down):
    collected = [[] for _ in range(8)]
    yp, ys = x_prompt, x_sample
    for l in range(DEPTH):
        cmpk = (cmp_w1_k[l], cmp_b1_k[l], cmp_w2_k[l], cmp_pe_k[l])
        cmpv = (cmp_w1_v[l], cmp_b1_v[l], cmp_w2_v[l], cmp_pe_v[l])

        def prompt_core(q_n, kv_c, kv_s, kv_w, q_g, k_g, v_g, lg, cmpk=cmpk, cmpv=cmpv):
            o_cmp, o_slc, o_win = nsa_prompt(q_n, kv_c, kv_s, kv_w, cmpk, cmpv)
            s0 = jnp.zeros((q_g.shape[0], GLA_HEADS, GLA_DK, GLA_DV), jnp.float32)
            s_fin, o_gla = gla_scan(s0, q_g, k_g, v_g, lg)
            L = kv_w.shape[1]
            keep = min(WINDOW, L)
            return o_cmp, o_slc, o_win, o_gla, (kv_c, kv_s, kv_w[:, L - keep:], s_fin.astype(state_gla.dtype))

        def sample_core(q_n, kv_c, kv_s, kv_w, q_g, k_g, v_g, lg, l=l, cmpk=cmpk, cmpv=cmpv):
            (o_cmp, o_slc, o_win), win_new = nsa_sample(q_n, kv_c, kv_s, kv_w, cache_cmp_kv[l], cache_slc_kv[l],
                                                        state_win_kv[l], page_table, cmpk, cmpv)
            s_fin, o_gla = gla_scan(state_gla[l].astype(jnp.float32), q_g, k_g, v_g, lg)
            return o_cmp, o_slc, o_win, o_gla, (kv_c, kv_s, win_new, s_fin.astype(state_gla.dtype))

        lw = (w_ada[l], b_ada[l], g_pre_mix[l], g_post_mix[l], w_in[l], w_gla_a2[l], b_gla_a[l], gla_norm_g[l],
              w_nsa_o[l], w_gla_o[l], w_out[l], g_pre_ffn[l], g_post_ffn[l], w_ff_gate[l], w_ff_up[l], w_ff_down[l])
        yp, st_p = block_forward(yp, c_prompt, prompt_core, *lw)
        ys, st_s = block_forward(ys, c_sample, sample_core, *lw)
        for i in range(4):
            collected[2 * i].append(st_p[i])
            collected[2 * i + 1].append(st_s[i])
    cmp_p, cmp_s, slc_p, slc_s, win_p, win_s, gla_p, gla_s = [jnp.stack(c) for c in collected]
    return (yp, ys, cmp_p, cmp_s, slc_p, slc_s, win_p, win_s, gla_p, gla_s)


_drawn_inputs = setup_inputs


def setup_inputs(seed=0):
    import zlib

    import numpy as np

    out = dict(_drawn_inputs(seed))
    spreads = {}
    factors = {'cache_slc_kv': 3.959,
     'g_post_mix': 8.0,
     'cmp_w1_k': 2.68,
     'cmp_b1_k': 24.746,
     'cmp_pe_k': 8.0,
     'cmp_b1_v': 37.751,
     'cmp_pe_v': 4.621,
     'b_gla_a': 5.35,
     'gla_norm_g': 8.0,
     'g_pre_ffn': 20.138,
     'g_post_ffn': 34.065}
    for name, (base, spread) in spreads.items():
        noise = np.random.default_rng([zlib.crc32(name.encode()), seed]).standard_normal(out[name].shape)
        drawn = base * np.exp(spread * noise) if base else spread * noise
        out[name] = __import__('jax').numpy.asarray(drawn.astype(out[name].dtype))
    for name, factor in factors.items():
        out[name] = (out[name] * factor).astype(out[name].dtype)
    return out
```

```python
from contextlib import ExitStack

import numpy as np
import concourse.bacc as bacc
import concourse.bass as bass
from concourse import mybir
from concourse.bass_utils import run_bass_kernel_spmd

F32 = mybir.dt.float32
I32 = mybir.dt.int32
ALU = mybir.AluOpType
ACT = mybir.ActivationFunctionType
X = mybir.AxisListType.X

P = 128
D = 1024
KD = D // P
SEQ = 1024
QT = SEQ // P
NB = 8
DS = 4
ST = NB * DS
T = SEQ + ST
TT = QT + 1
NW = T // 3
NN = 3
PAST = 1024
PAGE = 128
NPAGE = PAST // PAGE
WIN = 512
HD = 64
HP = 4
GD = 2 * HD
GDK = 64
GDV = 128
GH = 4
RANK = 16
CH = 64
DFF = 2816
KF = DFF // P
NCOND = 1 + NB
EPS = 1e-6
NEG = -1e30
CL = 32
CS = 16
NCMP = PAST // CS - 1
SLC = 64
NSLC = PAST // SLC
SLOTS = 6

C_Q = 0
C_KVC = 512
C_KVS = C_KVC + 256
C_KVW = C_KVS + 256
C_GN = C_KVW + 256
C_QG = C_GN + 24
C_KG = C_QG + 256
C_VG = C_KG + 256
C_AG = C_VG + 512
C_RG = C_AG + RANK
C_MG = C_RG + 512

Z_Q, Z_KC, Z_KS, Z_KW, Z_QG, Z_KG, Z_VC, Z_VS, Z_VW, Z_VG, ZU = 0, 4, 5, 6, 7, 9, 11, 12, 13, 14, 18
Z_TAIL = Z_VS
SH1, SC1, GA1, SH2, SC2, GA2 = (8 * i for i in range(6))
V_BADA, V_GPRE, V_GPOST, V_GPRE2, V_GPOST2, V_GNORM, V_B1K, V_B1V, V_N = 0, 48, 56, 64, 72, 80, 81, 82, 83


class Box:
    pass


def z_columns():
    return ([C_KVC, C_KVS, C_KVW] + [C_QG, C_QG + P, C_KG, C_KG + P]
            + [C_KVC + P, C_KVS + P, C_KVW + P] + [C_VG + P * i for i in range(4)])


def allocate(nc, ctx):
    m = Box()
    m.nc = nc

    def sb(name, shape, dt=F32):
        return ctx.enter_context(nc.sbuf_tensor(name, shape, dt))

    def sem(name):
        return nc.alloc_semaphore(name)

    m.sb, m.sem = sb, sem
    m.ps = ctx.enter_context(nc.psum_tensor("ps", [P, 8, 512], F32))
    m.ring = sb("ring", [P, SLOTS, KD, P])
    m.hT = sb("hT", [P, KD, T])
    WORK = 4352
    sizes = [ZU * T, GH * T, TT * GH * GDV, TT * 2 * GD, WORK]
    at = [sum(sizes[:i]) for i in range(6)]
    m.big = sb("big", [P, at[5]])
    m.zT = m.big[:, 0:at[1]].rearrange("p (u t) -> p u t", t=T)
    m.oglaT = m.big[:, at[1]:at[2]].rearrange("p (h t) -> p h t", t=T)
    m.vg = m.big[:, at[2]:at[3]].rearrange("p (i h v) -> p i h v", i=TT, h=GH)
    m.vtm = m.big[:, at[3]:at[4]].rearrange("p (i b c) -> p i b c", i=TT, b=2)
    m.work = m.big[:, at[4]:at[5]]
    m.merged = m.zT[:, ZU - KD:ZU, :]
    m.x2T = m.zT[:, 0:KD, :]
    m.guT = m.big[:, KD * T:(KD + KF) * T].rearrange("p (u t) -> p u t", t=T)
    m.rest = m.big[:, (KD + KF) * T:at[5]]
    m.modT = sb("modT", [P, 48, NCOND])
    m.vecT = sb("vecT", [P, V_N])
    m.peT = sb("peT", [P, 64])
    m.ident = sb("ident", [P, P])
    m.acc = sb("acc", [P, T])
    m.agT = m.acc[0:32, :]
    m.gnT = sb("gnT", [24, ST])
    m.gates = sb("gates", [P, QT, 24])
    m.osT = sb("osT", [P, HP, ST])
    m.pt = sb("page_ids", [1, NB * NPAGE], I32)
    m.w_in = [sem(f"weights_in_slot{i}") for i in range(SLOTS)]
    m.w_used = sem("weight_units_used")
    m.loads = [0] * SLOTS
    m.used = 0
    return m


def w_block(w, col, rows=D, n=P):
    return w.rearrange("(k p) n -> p k n", p=P)[:, :rows // P, col:col + n]


def dyn_block(w, unit):
    return w.rearrange("(k p) n -> p k n", p=P)[:, :, bass.ds(unit * P, P)]


def product(pe, out, w, rhs, first=True, last=True):
    nk = w.shape[1]
    for k in range(nk):
        ins = pe.matmul(out, w[:, k, :], rhs(k), start=first and k == 0, stop=last and k == nk - 1)
    return ins


def stage_prepare(m, I, O):
    nc, ps = m.nc, m.ps
    xs = m.zT[:, 0:9, 0:D]
    rows = m.work[:, 0:P]
    pes = m.work[0:64, P:2 * P]
    cr = m.work[0:NCOND, 1024:2048]
    cT = m.work[:, 2048:2048 + KD * 16].rearrange("p (k c) -> p k c", c=16)
    junk = m.work[:, 2304:2304 + D]
    ss = m.work[:, 3400:3400 + TT]
    ms = m.work[:, 3416:3416 + TT]
    rec = m.work[:, 3432:3432 + TT]
    rstd = m.work[:, 3448:3448 + TT]
    vec_in, c_in, x_in = m.sem("vectors_in"), m.sem("conditions_in"), m.sem("x_in")
    id0, rows_T, rows_out = m.sem("ident_ready"), m.sem("rows_transposed"), m.sem("row_columns_ready")
    mod_mm, mod_step = m.sem("modulation_summed"), m.sem("modulation_steps")
    sq_done, ms_done, sqrt_done, xn_done = (m.sem("squares_done"), m.sem("mean_square_steps"), m.sem("rstd_ready"),
                                            m.sem("x_scaled"))
    xT_done, ev_act, ev_dve = m.sem("x_tiles_transposed"), m.sem("h_written_by_act"), m.sem("h_written_by_dve")
    groups = [(j, h) for j in range(KD) for h in range(2)]

    with nc.Block() as block:
        @block.sync
        def _(sp):
            for r0, a, n in ((V_BADA, I["b_ada"], 48), (V_GPRE, I["g_pre_mix"], 8), (V_GPOST, I["g_post_mix"], 8),
                             (V_GPRE2, I["g_pre_ffn"], 8), (V_GPOST2, I["g_post_ffn"], 8)):
                sp.dma_start(rows[r0:r0 + n, :], a.rearrange("o (a b) -> (o a) b", b=P)).then_inc(vec_in, 16)
            sp.dma_start(rows[V_GNORM:V_GNORM + 1, :], I["gla_norm_g"]).then_inc(vec_in, 16)
            for half in range(2):
                c = slice(half * HD, (half + 1) * HD)
                sp.dma_start(rows[V_B1K:V_B1K + 1, c], I["cmp_b1_k"]).then_inc(vec_in, 16)
                sp.dma_start(rows[V_B1V:V_B1V + 1, c], I["cmp_b1_v"]).then_inc(vec_in, 16)
            for half in range(2):
                c = slice(half * HD, (half + 1) * HD)
                sp.dma_start(pes[0:32, c], I["cmp_pe_k"][0]).then_inc(vec_in, 16)
                sp.dma_start(pes[32:64, c], I["cmp_pe_v"][0]).then_inc(vec_in, 16)
            sp.dma_start(cr[0:1, :], I["c_prompt"]).then_inc(c_in, 16)
            sp.dma_start(cr[1:NCOND, :], I["c_sample"]).then_inc(c_in, 16)
            w_ada = I["w_ada"][0]
            for s in range(SLOTS):
                sp.dma_start(m.ring[:, s], w_block(w_ada, s * P)).then_inc(m.w_in[s], 16)
            with sp.Fori(1, 48 // SLOTS) as it:
                for s in range(SLOTS):
                    sp.wait_ge(m.w_used, it * SLOTS + (s + 1 - SLOTS))
                    sp.dma_start(m.ring[:, s], dyn_block(w_ada, it * SLOTS + s)).then_inc(m.w_in[s], 16)
            for s in range(2):
                sp.wait_ge(m.w_used, 48 - SLOTS + s + 1)
                load_query_unit(sp, m, I, s, s)

        @block.gpsimd
        def _(pool):
            pool.memset(m.ident[:, :], 0.0).then_inc(id0, 1)
            pool.wait_ge(id0, 1)
            pool.affine_select(out=m.ident[:, :], in_=m.ident[:, :], compare_op=ALU.not_equal, fill=1.0, base=0,
                               pattern=[[-1, P]], channel_multiplier=1).then_inc(id0, 1)

        @block.tensor
        def _(pe):
            pe.wait_ge(id0, 2)
            pe.wait_ge(vec_in, 16 * 14)
            pe.transpose(ps[:, 0, 0:V_N], rows[0:V_N, :], m.ident[0:V_N, 0:V_N])
            pe.transpose(ps[:, 0, 128:192], pes, m.ident[0:64, 0:64])
            pe.wait_ge(c_in, 32)
            for k in range(KD):
                ins = pe.transpose(ps[:, 0, 256 + 16 * k:256 + 16 * k + NCOND], cr[:, k * P:(k + 1) * P],
                                   m.ident[0:NCOND, 0:NCOND])
            ins.then_inc(rows_T, 1)
            pe.wait_ge(rows_out, 3)
            with pe.Fori(0, 48 // SLOTS) as it:
                for s in range(SLOTS):
                    pe.wait_ge(m.w_in[s], it * 16 + 16)
                    product(pe, ps[:, 1, bass.ds((it * SLOTS + s) * NCOND, NCOND)], m.ring[:, s],
                            lambda k: cT[:, k, 0:NCOND]).then_inc(m.w_used, 1)
            pe.wait_ge(xn_done, TT)
            for g, (j, h) in enumerate(groups):
                if g >= 4:
                    pe.wait_ge(ev_act if g % 2 == 0 else ev_dve, (g - 4) // 2 + 1)
                for i in range(4):
                    ins = pe.transpose(ps[:, 2 + g % 4, i * P:(i + 1) * P], xs[:, 4 * h + i, j * P:(j + 1) * P],
                                       m.ident[:, :])
                ins.then_inc(xT_done, 1)
            for j in range(KD):
                ins = pe.transpose(ps[:, 6, j * ST:(j + 1) * ST], xs[0:ST, QT, j * P:(j + 1) * P],
                                   m.ident[0:ST, 0:ST])
            ins.then_inc(xT_done, 1)

        @block.scalar
        def _(act):
            act.dma_start(xs[:, 0:QT, :], I["x_prompt"][0].rearrange("(i p) d -> p i d", p=P)).then_inc(x_in, 16)
            act.dma_start(xs[0:ST, QT, :], I["x_sample"].rearrange("b s d -> (b s) d")).then_inc(x_in, 16)
            act.wait_ge(x_in, 32)
            act.wait_ge(ms_done, 1)
            for i in range(TT):
                n = P if i < QT else ST
                if i:
                    act.wait_ge(sq_done, i)
                act.activation(junk[0:n, :], xs[0:n, i, :], ACT.Square, accum_out=ss[0:n, i:i + 1]).then_inc(
                    sq_done, 1)
            act.wait_ge(ms_done, 3)
            act.activation(rstd, rec, ACT.Sqrt).then_inc(sqrt_done, 1)
            act.wait_ge(sqrt_done, 1)
            for i in range(TT):
                n = P if i < QT else ST
                act.activation(xs[0:n, i, :], xs[0:n, i, :], ACT.Copy, scale=rstd[0:n, i:i + 1]).then_inc(xn_done, 1)
            act.wait_ge(mod_step, 5)
            for g, (j, h) in enumerate(groups):
                if g % 2 == 0:
                    act.wait_ge(xT_done, g + 1)
                    act.activation(m.hT[:, j, h * 512:(h + 1) * 512], ps[:, 2 + g % 4, :], ACT.Identity,
                                   bias=m.modT[:, SH1 + j, 0:1], scale=m.modT[:, SC1 + j, 0:1]).then_inc(ev_act, 1)

        @block.vector
        def _(dve):
            dve.memset(ss, 1.0).then_inc(ms_done, 1)
            dve.wait_ge(rows_T, 1)
            dve.tensor_copy(m.vecT[:, :], ps[:, 0, 0:V_N]).then_inc(rows_out, 1)
            dve.tensor_copy(m.peT[:, :], ps[:, 0, 128:192]).then_inc(rows_out, 1)
            dve.tensor_copy(cT[:, :, 0:NCOND],
                            ps[:, 0, 256:384].rearrange("p (k c) -> p k c", c=16)[:, :, 0:NCOND]).then_inc(rows_out, 1)
            dve.wait_ge(sq_done, TT)
            dve.tensor_scalar(ms, ss, 1.0 / D, EPS, ALU.mult, ALU.add).then_inc(ms_done, 1)
            dve.wait_ge(ms_done, 2)
            dve.reciprocal(rec, ms).then_inc(ms_done, 1)
            dve.wait_ge(m.w_used, 48)
            dve.wait_ge(rows_out, 3)

            def col(v, n=8):
                return m.vecT[:, v:v + n].unsqueeze(2).to_broadcast([P, n, NCOND])

            dve.tensor_tensor(m.modT[:, :, :], ps[:, 1, 0:48 * NCOND].rearrange("p (u c) -> p u c", c=NCOND),
                              col(V_BADA, 48), ALU.add).then_inc(mod_step, 1)
            dve.wait_ge(mod_step, 1)
            for sec, g in ((SC1, V_GPRE), (SC2, V_GPRE2)):
                dve.scalar_tensor_tensor(out=m.modT[:, sec:sec + 8, :], in0=m.modT[:, sec:sec + 8, :], scalar=1.0,
                                         in1=col(g), op0=ALU.add, op1=ALU.mult).then_inc(mod_step, 1)
            for sec, g in ((GA1, V_GPOST), (GA2, V_GPOST2)):
                dve.tensor_tensor(m.modT[:, sec:sec + 8, :], m.modT[:, sec:sec + 8, :], col(g), ALU.mult).then_inc(
                    mod_step, 1)
            dve.wait_ge(mod_step, 5)
            for g, (j, h) in enumerate(groups):
                if g % 2 == 1:
                    dve.wait_ge(xT_done, g + 1)
                    dve.tensor_scalar(m.hT[:, j, h * 512:(h + 1) * 512], ps[:, 2 + g % 4, :],
                                      m.modT[:, SC1 + j, 0:1], m.modT[:, SH1 + j, 0:1], ALU.mult, ALU.add).then_inc(
                                          ev_dve, 1)
            dve.wait_ge(xT_done, 17)
            hs = m.hT[:, :, SEQ:T].rearrange("p j (b s) -> p j b s", s=DS)
            pss = ps[:, 6, 0:KD * ST].rearrange("p (j b s) -> p j b s", b=NB, s=DS)
            dve.tensor_tensor(hs, pss, per_batch(m, SC1), ALU.mult).then_inc(mod_step, 1)
            dve.wait_ge(mod_step, 6)
            dve.tensor_tensor(hs, hs, per_batch(m, SH1), ALU.add).then_inc(mod_step, 1)
    m.used += 48
    m.loads = [8] * SLOTS


def per_batch(m, sec):
    return m.modT[:, sec:sec + 8, 1:NCOND].unsqueeze(3).to_broadcast([P, 8, NB, DS])


def load_query_unit(sp, m, I, u, slot):
    for g in range(2):
        sp.dma_start(m.ring[:, slot, :, g * HD:(g + 1) * HD],
                     w_block(I["w_in"][0], C_Q + (4 * g + u) * HD, n=HD)).then_inc(m.w_in[slot], 16)


def stage_project(m, I, O):
    nc, ps = m.nc, m.ps
    sgT = m.work[0:24, 0:T]
    kst = m.work[:, 1088:1088 + 2 * 512].rearrange("p (b c n) -> p b c n", b=2, c=4)
    summed = m.sem("z_tile_summed")
    bank_free = [m.sem(f"z_bank_free{b}") for b in range(6)]
    narrow_pad, narrow_out = m.sem("narrow_columns_padded"), m.sem("narrow_written")
    ones_set = m.sem("gate_ones_set")
    tposed, rows_act, rows_dve = m.sem("z_tiles_transposed"), m.sem("rows_by_act"), m.sem("rows_by_dve")
    rows_out = [m.sem("even_rows_stored"), m.sem("odd_rows_stored")]
    win_copied = m.sem("window_rows_copied")
    w_in = I["w_in"][0]
    u0, l0 = m.used, m.loads
    QU, ZO = 4, ZU - 4
    cols = z_columns()

    def stores(i):
        n = P if i < QT else ST

        def rows(name, half):
            if i < QT:
                a = O[name + "_p"][0, 0].rearrange("t a g d -> t (a g d)")
                first = i * P if name != "win" else i * P - (SEQ - WIN)
                return a[first:first + P, half * GD:(half + 1) * GD]
            a = O[name + "_s"][0].rearrange("b t a g d -> b t (a g d)")
            return a[:, WIN - DS:WIN, half * GD:(half + 1) * GD] if name == "win" else a[:, :, half * GD:(half + 1) * GD]

        out = [(rows("cmp", 0), kst[0:n, i % 2, 0]), (rows("cmp", 1), kst[0:n, i % 2, 3]),
               (rows("slc", 0), kst[0:n, i % 2, 1]), (rows("slc", 1), m.vtm[0:n, i, 0, :])]
        if i >= QT - WIN // P:
            out += [(rows("win", 0), kst[0:n, i % 2, 2]), (rows("win", 1), m.vtm[0:n, i, 1, :])]
        return out

    stored = [16 * sum(len(stores(j)) for j in range(i % 2, i + 1, 2)) for i in range(TT)]

    with nc.Block() as block:
        @block.sync
        def _(sp):
            sp.wait_ge(narrow_pad, 1)
            sp.dma_start(m.ring[:, 2, :, 0:RANK], w_block(w_in, C_AG, n=RANK)).then_inc(m.w_in[2], 16)
            sp.dma_start(m.ring[:, 2, :, 32:56], w_block(w_in, C_GN, n=24)).then_inc(m.w_in[2], 16)
            for u in range(2, QU):
                sp.wait_ge(m.w_used, u0 + u - 1)
                load_query_unit(sp, m, I, u, u % 2)
            for u in range(QU, ZU):
                sp.wait_ge(m.w_used, u0 + u - 1)
                sp.dma_start(m.ring[:, u % 2], w_block(w_in, cols[u - QU])).then_inc(m.w_in[u % 2], 16)
            for i in range(TT):
                sp.wait_ge(rows_act, i + 1)
                sp.wait_ge(rows_dve, 2 * i + 2)
                for to, src in stores(i):
                    sp.dma_start(to, src).then_inc(rows_out[i % 2], 16)
            for i in (TT - 2, TT - 1):
                sp.wait_ge(rows_out[i % 2], stored[i])

        @block.gpsimd
        def _(pool):
            pool.dma_start(O["win_s"][0].rearrange("b t a g d -> b t (a g d)")[:, 0:WIN - DS],
                           I["state_win_kv"][0].rearrange("b t a g d -> b t (a g d)")[:, DS:WIN]).then_inc(
                               win_copied, 16)
            pool.memset(m.ring[:, 2, :, RANK:32], 0.0).then_inc(narrow_pad, 1)
            pool.memset(m.agT[:, :], 1.0).then_inc(ones_set, 1)
            pool.wait_ge(win_copied, 16)

        @block.tensor
        def _(pe):
            def unit(it, s):
                for n in range(NN):
                    pe.wait_ge(bank_free[3 * s + n], it + 1)
                    ins = product(pe, ps[:, 3 * s + n, 0:NW], m.ring[:, s],
                                  lambda k: m.hT[:, k, n * NW:(n + 1) * NW])
                    if n < NN - 1:
                        ins.then_inc(summed, 1)
                return ins

            with pe.Fori(0, QU // 2) as it:
                for s in range(2):
                    pe.wait_ge(m.w_in[s], it * 32 + 16 * (l0[s] + 2))
                    unit(it, s).then_inc(m.w_used, 1)
            with pe.Fori(0, ZO // 2) as it:
                for s in range(2):
                    pe.wait_ge(m.w_in[s], it * 16 + 16 * (l0[s] + QU + 1))
                    unit(it + QU // 2, s).then_inc(m.w_used, 1)
            pe.wait_ge(m.w_in[2], 16 * (l0[2] + 2))
            for n in range(NN):
                pe.wait_ge(bank_free[n], ZU // 2 + 1)
                ins = product(pe, ps[0:56, n, 0:NW], m.ring[:, 2, :, 0:56], lambda k: m.hT[:, k, n * NW:(n + 1) * NW])
                ins.then_inc(m.w_used if n == NN - 1 else summed, 1)
            for b in range(6):
                pe.wait_ge(bank_free[b], ZU // 2 + 1)
            pe.wait_ge(narrow_out, 6)
            for i in range(TT):
                n = P if i < QT else ST
                tok = slice(i * P, i * P + n)
                if i >= 2:
                    pe.wait_ge(rows_act, i - 1)
                    pe.wait_ge(rows_dve, 2 * (i - 1))
                b = 3 * (i % 2)
                for c, t in enumerate((Z_KC, Z_KS, Z_KW, Z_VC)):
                    ins = pe.transpose(ps[0:n, b, c * P:(c + 1) * P], m.zT[:, t, tok], m.ident[:, :])
                ins.then_inc(tposed, 1)
                for c, t in enumerate((Z_VS, Z_VW)):
                    ins = pe.transpose(ps[0:n, b + 1, c * P:(c + 1) * P], m.zT[:, t, tok], m.ident[:, :])
                if i < QT:
                    ins = pe.transpose(ps[0:n, b + 1, 256:280], sgT[:, tok], m.ident[0:24, 0:24])
                ins.then_inc(tposed, 1)
                for h in range(GH):
                    ins = pe.transpose(ps[0:n, b + 2, h * P:(h + 1) * P], m.zT[:, Z_VG + h, tok], m.ident[:, :])
                ins.then_inc(tposed, 1)

        def ready(e, it, s, n):
            if n < NN - 1:
                e.wait_ge(summed, it * 4 + (2 * s + n + 1))
            else:
                e.wait_ge(m.w_used, it * 2 + (u0 + s + 1))

        @block.scalar
        def _(act):
            for b in (0, 2, 4):
                act.sem_inc(bank_free[b], 1)
            with act.Fori(0, ZU // 2) as it:
                for s, n in ((0, 0), (0, 2), (1, 1)):
                    ready(act, it, s, n)
                    act.activation(m.zT[:, bass.ds(it * 2 + s, 1), n * NW:(n + 1) * NW], ps[:, 3 * s + n:3 * s + n + 1, 0:NW],
                                   ACT.Copy).then_inc(bank_free[3 * s + n], 1)
            for n in range(NN):
                ready(act, ZU // 2, 0, n)
                act.activation(sgT[:, n * NW:(n + 1) * NW], ps[32:56, n, 0:NW], ACT.Sigmoid).then_inc(narrow_out, 1)
            for i in range(TT):
                n = P if i < QT else ST
                act.wait_ge(tposed, 3 * i + 1)
                if i >= 2:
                    act.wait_ge(rows_out[i % 2], stored[i - 2])
                act.activation(kst[0:n, i % 2], ps[0:n, 3 * (i % 2)].rearrange("p (c n) -> p c n", c=4),
                               ACT.Copy).then_inc(rows_act, 1)

        @block.vector
        def _(dve):
            for b in (1, 3, 5):
                dve.sem_inc(bank_free[b], 1)
            with dve.Fori(0, ZU // 2) as it:
                for s, n in ((0, 1), (1, 0), (1, 2)):
                    ready(dve, it, s, n)
                    dve.tensor_copy(m.zT[:, bass.ds(it * 2 + s, 1), n * NW:(n + 1) * NW],
                                    ps[:, 3 * s + n:3 * s + n + 1, 0:NW]).then_inc(bank_free[3 * s + n], 1)
            dve.wait_ge(ones_set, 1)
            for n in range(NN):
                ready(dve, ZU // 2, 0, n)
                dve.wait_ge(narrow_out, 3)
                dve.tensor_copy(m.agT[0:RANK, n * NW:(n + 1) * NW], ps[0:RANK, n, 0:NW]).then_inc(narrow_out, 1)
            dve.tensor_copy(m.gnT[:, :], sgT[:, SEQ:T])
            for i in range(TT):
                n = P if i < QT else ST
                b = 3 * (i % 2)
                dve.wait_ge(tposed, 3 * i + 2)
                if i < QT:
                    dve.tensor_copy(m.gates[:, i, :], ps[:, b + 1, 256:280])
                dve.tensor_copy(m.vtm[0:n, i], ps[0:n, b + 1, 0:256].rearrange("p (c n) -> p c n", c=2)).then_inc(
                    rows_dve, 1)
                dve.wait_ge(tposed, 3 * i + 3)
                dve.tensor_copy(m.vg[0:n, i], ps[0:n, b + 2, :].rearrange("p (c n) -> p c n", c=4)).then_inc(
                    rows_dve, 1)
    m.used += ZU + 1
    m.loads = [l0[0] + QU + ZO // 2, l0[1] + QU + ZO // 2, l0[2] + 2] + l0[3:]


def keep(pool, done, ap, pattern, base, mult):
    ins = pool.affine_select(out=ap, in_=ap, compare_op=ALU.is_ge, fill=0.0, base=base, pattern=pattern,
                             channel_multiplier=mult)
    return ins


def stage_gla(m, I, O):
    nc, ps = m.nc, m.ps
    tail = m.zT[:, Z_TAIL:ZU, :].rearrange("p a b -> p (a b)")
    ogf = m.oglaT[:, :, :].rearrange("p a b -> p (a b)")
    W = m.work
    lg = tail[:, 0:2304]
    soft = tail[:, 2304:4608]
    D2 = [tail[:, i * T:(i + 1) * T] for i in range(2)]
    S = tail[:, 0:17 * GDV].rearrange("p (c v) -> p c v", v=GDV)
    E2 = [tail[:, 2176 + i * T:2176 + (i + 1) * T] for i in range(2)]
    kl = tail[:, 4288:4288 + 2048].rearrange("p (i c k) -> p i c k", i=QT, c=2)
    sqb = [tail[:, 4288 + 512 * i:4288 + 512 * i + 512] for i in range(2)]
    S0 = E2[0][:, 0:NB * GDV].rearrange("p (b v) -> p b v", v=GDV)
    B = [ogf[:, p * T:(p + 1) * T] for p in range(2)]
    Qd, Kd = ogf[:, 2 * T:3 * T], ogf[:, 3 * T:4 * T]
    Qo, Ko = W[:, 0:T], W[:, T:2 * T]
    am = W[:, 2112:2112 + 1024].rearrange("p (b x) -> p b x", b=2)
    tri = W[:, 3136:3264]
    M12 = W[:, 3264:3520].rearrange("p (k t) -> p k t", k=2)
    mS, triS, bm = W[0:ST, 3520:3552], W[0:ST, 3552:3584], W[0:ST, 3584:3592]
    wa2 = W[0:RANK + 1, 3592:3848]
    eiB = W[:, 3848:3848 + 288]
    amS = W[0:ST, 4136:4200]
    decay = W[:, 4200:4224]
    ss, ms, rec, rstd = (W[:, 64 * i:64 * i + TT * GH] for i in range(4))
    klB = kl[0:ST].rearrange("p i c k -> p (i c) k")[:, 0:NB, :]
    klS = W[0:ST, 2112:2112 + P]

    a2_in, s0_in, gla_out = m.sem("gate_weights_in"), m.sem("sample_states_in"), m.sem("gla_states_stored")
    cst = m.sem("gla_masks_steps")
    gate_mm, cum_mm = m.sem("gate_products"), m.sem("cumulated")
    soft_step, lg_done, b_done = m.sem("softplus_steps"), m.sem("log_gates_ready"), m.sem("cumulated_copied")
    d_ready, e_ready, m_done, own = (m.sem("decay_exponents"), m.sem("decay_factors"), m.sem("operands_decayed"),
                                     m.sem("gla_vector_steps"))
    kl_T, kl_done, kv_mm, s_done = (m.sem("keys_transposed"), m.sem("keys_copied"), m.sem("state_products"),
                                    m.sem("states_advanced"))
    a_mm, a_done, o_mm, o_done = m.sem("gla_scores"), m.sem("gla_scores_masked"), m.sem("gla_sums"), m.sem("gla_kept")
    smp, smp_pe, zeroed = m.sem("sample_vector_steps"), m.sem("sample_products"), m.sem("halves_zeroed")
    smp_own = m.sem("sample_scores_applied")
    sq, nrm, nrm_own, oT, ow = (m.sem("gla_squares"), m.sem("gla_rstd"), m.sem("gla_norm_steps"), m.sem("gla_transposed"),
                           m.sem("gla_written"))
    scaled = m.sem("gla_scaled")

    with nc.Block() as block:
        @block.sync
        def _(sp):
            sp.dma_start(wa2[0:RANK, :], I["w_gla_a2"][0]).then_inc(a2_in, 16)
            sp.dma_start(wa2[RANK:RANK + 1, :], I["b_gla_a"]).then_inc(a2_in, 16)
            for p in range(2):
                sp.wait_ge(m_done, 6 * p + 6)
                sp.dma_start(S0, I["state_gla"][0].rearrange("b (q h) k v -> q (h k) b v", q=2)[p]).then_inc(s0_in, 16)
                sp.wait_ge(s_done, (p + 1) * 32)
                sp.dma_start(O["gla_p"][0, 0].rearrange("(q h) k v -> q (h k) v", q=2)[p], S[:, 16, :]).then_inc(
                    gla_out, 16)
                sp.wait_ge(smp, p * 8 + 8)
                sp.dma_start(O["gla_s"][0].rearrange("b (q h) k v -> q (h k) b v", q=2)[p], S0).then_inc(gla_out, 16)
            sp.wait_ge(gla_out, 64)

        @block.gpsimd
        def _(pool):
            m1 = M12[:, 0, :]
            m2 = M12[:, 1, :].rearrange("p (c h t) -> p c h t", c=2, h=2)
            n = 0
            for ins in (pool.memset(tri, 1.0 / 16), pool.memset(M12, 0.0), pool.memset(mS, 1.0),
                        pool.memset(triS, 1.0 / 16), pool.memset(bm, 1.0)):
                ins.then_inc(cst, 1)
                n += 1
            pool.wait_ge(cst, n)
            pool.memset(m1, 1.0).then_inc(cst, 1)
            pool.memset(m2[:, :, 1, :], 1.0).then_inc(cst, 1)
            n += 2
            pool.wait_ge(cst, n)
            first = [(tri.rearrange("p (c t) -> p c t", c=2), [[64, 2], [1, 64]], 0, -1),
                     (m1.rearrange("p (c t) -> p c t", c=4), [[32, 4], [1, 32]], 0, -1),
                     (m2[:, :, 1, :], [[-64, 2], [0, 32]], 0, 1),
                     (mS.rearrange("p (c t) -> p c t", c=8), [[4, 8], [1, 4]], 0, -1),
                     (triS.rearrange("p (c t) -> p c t", c=8), [[4, 8], [1, 4]], 0, -1),
                     (bm, [[-4, 8]], 0, 1)]
            second = [(tri.rearrange("p (c t) -> p c t", c=2), [[-64, 2], [0, 64]], 0, 1),
                      (m1.rearrange("p (c t) -> p c t", c=4), [[-32, 4], [0, 32]], 0, 1),
                      (m2[:, :, 1, :], [[64, 2], [0, 32]], 31, -1),
                      (mS.rearrange("p (c t) -> p c t", c=8), [[-4, 8], [0, 4]], 0, 1),
                      (triS.rearrange("p (c t) -> p c t", c=8), [[-4, 8], [0, 4]], 0, 1),
                      (bm, [[4, 8]], 3, -1)]
            for group in (first, second):
                for ap, pattern, base, mult in group:
                    keep(pool, cst, ap, pattern, base, mult).then_inc(cst, 1)
                    n += 1
                pool.wait_ge(cst, n)
            pool.memset(Qo[:, 0:SEQ].rearrange("p (c h t) -> p c h t", h=2, t=32)[:, :, 0, :], 0.0).then_inc(cst, 1)
            pool.memset(Ko[:, 0:SEQ].rearrange("p (c h t) -> p c h t", h=2, t=32)[:, :, 1, :], 0.0).then_inc(cst, 1)
            pool.memset(eiB, 0.0).then_inc(cst, 1)
            for p in range(2):
                pool.wait_ge(lg_done, 2)
                pool.wait_ge(b_done, 4)
                if p:
                    pool.wait_ge(smp, 8)
                pool.memset(kl[0:64, :, 1, :], 0.0).then_inc(zeroed, 1)
                pool.memset(kl[64:128, :, 0, :], 0.0).then_inc(zeroed, 1)

        @block.tensor
        def _(pe):
            pe.wait_ge(a2_in, 32)
            for i in range(TT):
                n = P if i < QT else ST
                ins = pe.matmul(ps[0:n, i // 2, (i % 2) * 256:(i % 2) * 256 + 256], m.agT[0:RANK + 1, i * P:i * P + n],
                                wa2, start=True, stop=True)
            ins.then_inc(gate_mm, 1)
            pe.wait_ge(lg_done, 2)
            pe.wait_ge(cst, 22)
            for p in range(2):
                for i in range(QT):
                    ins = pe.matmul(ps[:, 2 * p + i // 4, (i % 4) * P:(i % 4 + 1) * P],
                                    lg[:, i * 256 + p * P:i * 256 + (p + 1) * P], tri, start=True, stop=True)
                ins = pe.matmul(ps[:, 4, p * ST:(p + 1) * ST], lg[0:ST, QT * 256 + p * P:QT * 256 + (p + 1) * P], triS,
                                start=True, stop=True)
            ins.then_inc(cum_mm, 1)
            for p in range(2):
                q, k = m.zT[:, Z_QG + p, :], m.zT[:, Z_KG + p, :]
                pe.wait_ge(m_done, 6 * p + 6)
                pe.wait_ge(b_done, 4)
                for i in range(QT):
                    ins = pe.transpose(ps[:, i // 4, (i % 4) * P:(i % 4 + 1) * P], k[:, i * P:(i + 1) * P], m.ident[:, :])
                ins.then_inc(kl_T, 1)
                pe.wait_ge(kl_done, 5 * p + 4)
                for j in range(2 * QT):
                    if j >= 4:
                        pe.wait_ge(s_done, 32 * p + 2 * (j - 4) + 2)
                    pe.matmul(ps[:, 4 + j % 4, 0:256], kl[:, j // 2, j % 2, :],
                              m.vg[:, j // 2, 2 * p:2 * p + 2, :].rearrange("p h v -> p (h v)"),
                              start=True, stop=True).then_inc(kv_mm, 1)
                pe.wait_ge(s_done, 32 * p + 32)

                def scores(i):
                    for hh in range(2):
                        r = slice(64 * hh, 64 * hh + 64)
                        tok = slice(i * P, (i + 1) * P)
                        pe.matmul(ps[:, 2 * (i % 2) + hh, 0:P], Kd[r, tok], Qd[r, tok], start=True, stop=True)
                        ins = pe.matmul(ps[:, 2 * (i % 2) + hh, P:2 * P], Ko[r, tok], Qo[r, tok], start=True, stop=True)
                    ins.then_inc(a_mm, 1)

                def sums(i):
                    for hh in range(2):
                        r = slice(64 * hh, 64 * hh + 64)
                        bank = 4 + 2 * (i % 2) + hh
                        v = m.vg[:, i, 2 * p + hh, :]
                        for a in range(2):
                            pe.matmul(ps[:, bank, 0:P], am[:, i % 2, (2 * hh + a) * P:(2 * hh + a + 1) * P], v, start=a == 0, stop=False)
                        for c in range(2):
                            ins = pe.matmul(ps[64 * c:64 * c + 64, bank, 0:P],
                                            q[r, i * P + 64 * c:i * P + 64 * c + 64], S[r, 2 * i + c, :], start=False, stop=True)
                    ins.then_inc(o_mm, 1)

                scores(0)
                for i in range(QT):
                    if i + 1 < QT:
                        if i >= 1:
                            pe.wait_ge(a_done, QT * p + i)
                        scores(i + 1)
                    pe.wait_ge(a_done, QT * p + i + 1)
                    if i >= 2:
                        pe.wait_ge(o_done, QT * p + i - 1)
                    sums(i)
                pe.wait_ge(o_done, QT * p + QT)
                pe.transpose(ps[0:ST, 0, 0:P], k[:, SEQ:T], m.ident[:, :])
                for hh in range(2):
                    r = slice(64 * hh, 64 * hh + 64)
                    ins = pe.matmul(ps[0:ST, 1 + hh, 0:ST], Kd[r, SEQ:T], Qd[r, SEQ:T], start=True, stop=True)
                ins.then_inc(smp_pe, 1)
                pe.wait_ge(smp, 8 * p + 4)
                pe.wait_ge(s0_in, 16 * p + 16)
                for hh in range(2):
                    ins = pe.matmul(ps[0:ST, 6 + hh, 0:P], amS[:, hh * ST:(hh + 1) * ST], m.vg[0:ST, QT, 2 * p + hh, :],
                                    start=True, stop=False)
                ins.then_inc(smp_own, 1)
                pe.wait_ge(smp_own, p + 1)
                for hh in range(2):
                    r = slice(64 * hh, 64 * hh + 64)
                    out = ps[0:ST, 6 + hh, 0:P]
                    for b in range(NB):
                        ins = pe.matmul(out, eiB[r, b * ST:(b + 1) * ST], S0[r, b, :], start=False, stop=b == NB - 1)
                ins.then_inc(smp_pe, 1)
                for b in range(NB):
                    for hh in range(2):
                        ins = pe.matmul(ps[64 * hh:64 * hh + 64, 4 + b // 4, (b % 4) * P:(b % 4 + 1) * P],
                                        klB[:, b, 64 * hh:64 * hh + 64], m.vg[0:ST, QT, 2 * p + hh, :],
                                        start=True, stop=True)
                ins.then_inc(smp_pe, 1)
                pe.wait_ge(smp, 8 * p + 8)
            for i in range(TT):
                n = P if i < QT else ST
                pe.wait_ge(scaled, i + 1)
                if i >= 4:
                    pe.wait_ge(ow, i - 3)
                for h in range(GH):
                    ins = pe.transpose(ps[:, i % 4, h * P:h * P + n], m.vg[0:n, i, h, :], m.ident[0:n, 0:n])
                ins.then_inc(oT, 1)

        @block.scalar
        def _(act):
            act.wait_ge(gate_mm, 1)
            big, small = ps[:, 0:4, :].rearrange("p a b -> p (a b)"), ps[0:ST, 4, 0:256]
            sb_, ss_ = soft[:, 0:2048], soft[0:ST, 2048:2304]
            act.activation(sb_, big, ACT.Abs).then_inc(soft_step, 1)
            act.activation(ss_, small, ACT.Abs).then_inc(soft_step, 1)
            act.wait_ge(soft_step, 2)
            act.activation(sb_, sb_, ACT.Exp, scale=-1.0).then_inc(soft_step, 1)
            act.activation(ss_, ss_, ACT.Exp, scale=-1.0).then_inc(soft_step, 1)
            act.wait_ge(soft_step, 4)
            act.activation(sb_, sb_, ACT.Ln, bias=1.0).then_inc(soft_step, 1)
            act.activation(ss_, ss_, ACT.Ln, bias=1.0).then_inc(soft_step, 1)
            for p in range(2):
                half = lambda a, h: a[:, 0:SEQ].rearrange("p (c h t) -> p c h t", h=2, t=32)[:, :, h, :]
                for dr, md, out, inp, sign in (
                        (3 * p + 1, 6 * p, E2[0], D2[0], 1.0), (3 * p + 1, 6 * p, E2[1], D2[0], -1.0),
                        (3 * p + 2, 6 * p + 1, half(E2[0], 1), half(D2[1], 1), 1.0),
                        (3 * p + 2, 6 * p + 2, half(E2[1], 0), half(D2[1], 0), -1.0),
                        (3 * p + 2, 6 * p + 3, E2[0], B[p], 1.0), (3 * p + 3, 6 * p + 4, E2[1], D2[0], 1.0)):
                    act.wait_ge(d_ready, dr)
                    if md:
                        act.wait_ge(m_done, md)
                    act.activation(out, inp, ACT.Exp, scale=sign).then_inc(e_ready, 1)
                act.activation(decay[:, 0:16], B[p][:, 0:SEQ].rearrange("p (c t) -> p c t", t=CH)[:, :, CH - 1],
                               ACT.Exp).then_inc(e_ready, 1)
                act.activation(decay[:, 16:24], B[p][:, SEQ:T].rearrange("p (c t) -> p c t", t=DS)[:, :, DS - 1],
                               ACT.Exp).then_inc(e_ready, 1)
                act.wait_ge(kl_T, p + 1)
                act.wait_ge(zeroed, 2 * p + 2)
                for c in range(2):
                    for g in range(2):
                        r = slice(64 * c, 64 * c + 64)
                        act.activation(kl[r, 4 * g:4 * g + 4, c, :], ps[r, g, :].rearrange("p (i k) -> p i k", i=4),
                                       ACT.Copy).then_inc(kl_done, 1)
                act.wait_ge(smp, 8 * p + 8)
                act.sem_inc(kl_done, 1)
            for i in range(TT):
                n = P if i < QT else ST
                if i >= 2:
                    act.wait_ge(nrm, i - 1)
                act.wait_ge(smp, 16)
                act.activation(sqb[i % 2][0:n], m.vg[0:n, i].rearrange("p h v -> p (h v)"), ACT.Square).then_inc(sq, 1)
            act.wait_ge(nrm, TT + 2)
            act.activation(rstd, rec, ACT.Sqrt).then_inc(sq, 1)
            act.wait_ge(sq, TT + 1)
            for i in range(TT):
                n = P if i < QT else ST
                act.wait_ge(oT, i + 1)
                act.activation(m.oglaT[:, :, i * P:i * P + n], ps[:, i % 4, :].rearrange("p (h t) -> p h t", h=GH)[:, :, 0:n],
                               ACT.Copy, scale=m.vecT[:, V_GNORM:V_GNORM + 1]).then_inc(ow, 1)

        @block.vector
        def _(dve):
            steps = [0]

            def chain(ins):
                steps[0] += 1
                ins.then_inc(own, 1)
                dve.wait_ge(own, steps[0])

            dve.wait_ge(soft_step, 6)
            dve.scalar_tensor_tensor(out=lg[:, 0:2048], in0=ps[:, 0:4, :].rearrange("p a b -> p (a b)"), scalar=0.0,
                                     in1=soft[:, 0:2048], op0=ALU.min, op1=ALU.subtract).then_inc(lg_done, 1)
            dve.scalar_tensor_tensor(out=lg[0:ST, 2048:2304], in0=ps[0:ST, 4, 0:256], scalar=0.0,
                                     in1=soft[0:ST, 2048:2304], op0=ALU.min, op1=ALU.subtract).then_inc(lg_done, 1)
            dve.wait_ge(cum_mm, 1)
            for p in range(2):
                dve.tensor_copy(B[p][:, 0:SEQ], ps[:, 2 * p:2 * p + 2, :].rearrange("p a b -> p (a b)")).then_inc(b_done, 1)
                dve.tensor_copy(B[p][:, SEQ:T], ps[:, 4, p * ST:(p + 1) * ST]).then_inc(b_done, 1)
            dve.wait_ge(b_done, 4)

            def blocks(a, n, lo=0, hi=SEQ):
                return a[:, lo:hi].rearrange("p (c t) -> p c t", t=n)

            def at(a, n, t, lo=0, hi=SEQ):
                v = blocks(a, n, lo, hi)
                return v[:, :, t:t + 1].to_broadcast([P, v.shape[1], n])

            for p in range(2):
                b, q, k = B[p], m.zT[:, Z_QG + p, :], m.zT[:, Z_KG + p, :]
                if p:
                    dve.wait_ge(e_ready, 8)
                    dve.wait_ge(gla_out, 32)
                dve.tensor_tensor(blocks(D2[0], 32), blocks(b, 32), at(b, 32, 15), ALU.subtract)
                chain(dve.tensor_tensor(blocks(D2[0], DS, SEQ, T), blocks(b, DS, SEQ, T), at(b, DS, 0, SEQ, T),
                                        ALU.subtract))
                dve.tensor_scalar(D2[0], D2[0], -40.0, 40.0, ALU.max, ALU.min).then_inc(d_ready, 1)
                dve.tensor_tensor(blocks(D2[1], CH), blocks(b, CH), at(b, CH, 31), ALU.subtract).then_inc(d_ready, 1)
                dve.wait_ge(e_ready, 8 * p + 1)
                dve.scalar_tensor_tensor(out=Qd, in0=E2[0], scalar=GDK ** -0.5, in1=q, op0=ALU.mult,
                                         op1=ALU.mult).then_inc(m_done, 1)
                dve.wait_ge(e_ready, 8 * p + 2)
                dve.tensor_tensor(Kd, E2[1], k, ALU.mult).then_inc(m_done, 1)
                dve.tensor_tensor(blocks(D2[0], CH), at(b, CH, CH - 1), blocks(b, CH), ALU.subtract)
                chain(dve.tensor_tensor(blocks(D2[0], DS, SEQ, T), at(b, DS, DS - 1, SEQ, T), blocks(b, DS, SEQ, T),
                                        ALU.subtract))
                dve.sem_inc(d_ready, 1)
                half = lambda a, h: a[:, 0:SEQ].rearrange("p (c h t) -> p c h t", h=2, t=32)[:, :, h, :]
                dve.wait_ge(e_ready, 8 * p + 3)
                if p == 0:
                    dve.wait_ge(cst, 22)
                dve.scalar_tensor_tensor(out=half(Qo, 1), in0=half(E2[0], 1), scalar=GDK ** -0.5, in1=half(q, 1),
                                         op0=ALU.mult, op1=ALU.mult).then_inc(m_done, 1)
                dve.wait_ge(e_ready, 8 * p + 4)
                dve.tensor_tensor(half(Ko, 0), half(E2[1], 0), half(k, 0), ALU.mult).then_inc(m_done, 1)
                dve.wait_ge(m_done, 6 * p + 4)
                dve.wait_ge(e_ready, 8 * p + 5)
                dve.scalar_tensor_tensor(out=q, in0=E2[0], scalar=GDK ** -0.5, in1=q, op0=ALU.mult,
                                         op1=ALU.mult).then_inc(m_done, 1)
                dve.wait_ge(e_ready, 8 * p + 6)
                dve.tensor_tensor(k, E2[1], k, ALU.mult).then_inc(m_done, 1)
                dve.wait_ge(e_ready, 8 * p + 8)
                chain(dve.memset(S[:, 0, :], 0.0))
                for j in range(2 * QT):
                    dve.wait_ge(kv_mm, 2 * QT * p + j + 1)
                    for hh in range(2):
                        r = slice(64 * hh, 64 * hh + 64)
                        ins = dve.scalar_tensor_tensor(out=S[r, j + 1, :], in0=S[r, j, :], scalar=decay[r, j:j + 1],
                                                       in1=ps[r, 4 + j % 4, hh * P:(hh + 1) * P], op0=ALU.mult,
                                                       op1=ALU.add)
                        ins.then_inc(s_done, 1)
                    dve.wait_ge(s_done, 32 * p + 2 * j + 2)

                def mask(i):
                    dve.wait_ge(a_mm, QT * p + i + 1)
                    if i >= 2:
                        dve.wait_ge(o_mm, QT * p + i - 1)
                    dve.scalar_tensor_tensor(out=am[:, i % 2].rearrange("p (h x) -> p h x", h=2),
                                             in0=ps[:, 2 * (i % 2):2 * (i % 2) + 2, 0:2 * P], scalar=3e38,
                                             in1=M12.rearrange("p k t -> p (k t)").unsqueeze(1).to_broadcast([P, 2, 2 * P]),
                                             op0=ALU.min, op1=ALU.mult).then_inc(a_done, 1)

                for i in range(QT + 1):
                    if i < QT:
                        mask(i)
                    if i:
                        dve.wait_ge(o_mm, QT * p + i)
                        dve.tensor_copy(m.vg[:, i - 1, 2 * p:2 * p + 2, :],
                                        ps[:, 4 + 2 * ((i - 1) % 2):6 + 2 * ((i - 1) % 2), 0:P]).then_inc(
                                            o_done, 1)
                dve.wait_ge(smp_pe, 3 * p + 1)
                dve.tensor_copy(klS, ps[0:ST, 0, 0:P]).then_inc(smp, 1)
                dve.tensor_tensor(amS.rearrange("p (h t) -> p h t", h=2),
                                  ps[0:ST, 1:3, 0:ST],
                                  mS.unsqueeze(1).to_broadcast([ST, 2, ST]), ALU.mult).then_inc(smp, 1)
                dve.tensor_copy(eiB.rearrange("p (b x) -> p b x", x=ST + DS)[:, :, 0:DS],
                                q[:, SEQ:T].rearrange("p (b s) -> p b s", s=DS)).then_inc(smp, 1)
                dve.wait_ge(smp, 8 * p + 3)
                dve.wait_ge(kv_mm, 2 * QT * (p + 1))
                dve.tensor_tensor(klB, klS.unsqueeze(1).to_broadcast([ST, NB, P]), bm.unsqueeze(2).to_broadcast([ST, NB, P]),
                                  ALU.mult).then_inc(smp, 1)
                dve.wait_ge(smp_pe, 3 * p + 3)
                dve.tensor_copy(m.vg[0:ST, QT, 2 * p:2 * p + 2, :],
                                ps[0:ST, 6:8, 0:P]).then_inc(smp, 1)
                dve.tensor_tensor(S0, S0, decay[:, 16:24].unsqueeze(2).to_broadcast([P, NB, GDV]), ALU.mult).then_inc(smp, 1)
                dve.wait_ge(smp, 8 * p + 6)
                for g in range(2):
                    dve.tensor_tensor(S0[:, 4 * g:4 * g + 4, :], S0[:, 4 * g:4 * g + 4, :],
                                      ps[:, 4 + g, :].rearrange("p (b v) -> p b v", b=4), ALU.add).then_inc(smp, 1)
            chain(dve.memset(ss, 1.0))
            for i in range(TT):
                n = P if i < QT else ST
                dve.wait_ge(sq, i + 1)
                dve.tensor_reduce(ss[0:n, i * GH:(i + 1) * GH], sqb[i % 2][0:n].rearrange("p (h v) -> p h v", h=GH),
                                  X, ALU.add).then_inc(nrm, 1)
            dve.wait_ge(nrm, TT)
            dve.tensor_scalar(ms, ss, 1.0 / GDV, EPS, ALU.mult, ALU.add).then_inc(nrm, 1)
            dve.wait_ge(nrm, TT + 1)
            dve.reciprocal(rec, ms).then_inc(nrm, 1)
            dve.wait_ge(sq, TT + 1)
            for i in range(TT):
                n = P if i < QT else ST
                dve.tensor_tensor(m.vg[0:n, i], m.vg[0:n, i],
                                  rstd[0:n, i * GH:(i + 1) * GH].unsqueeze(2).to_broadcast([n, GH, GDV]),
                                  ALU.mult).then_inc(scaled, 1)


def regions(m):
    z = m.zT[:, :, :].rearrange("p a b -> p (a b)")
    m.tail = z[:, Z_TAIL * T:ZU * T]
    m.vgf = m.vg[:, :, :, :].rearrange("p i h v -> p (i h v)")
    mid = z[:, Z_QG * T:Z_VC * T]
    m.ckT = mid[:, 0:(1 + NB) * 64].rearrange("p (b n) -> p b n", n=64)
    m.cvt = mid[0:64, 576:576 + (1 + NB) * GD].rearrange("p (b n) -> p b n", n=GD)
    m.midw = mid[:, 1728:4224]


def load_page(sp, m, I, cache, batch, j, half, out, done):
    page = sp.value_load(m.pt[0:1, bass.ds(batch * NPAGE + j, 1)], min_val=0, max_val=m.n_pool - 1)
    src = I[cache][0].rearrange("n t a g d -> n t (a g d)")[bass.ds(page, 1), :, half * GD:(half + 1) * GD]
    sp.dma_start(out, src.rearrange("o t c -> t (o c)")).then_inc(done, 16)


def stage_compress(m, I, O):
    nc, ps = m.nc, m.ps
    regions(m)
    W = m.work
    w1 = [m.vgf[:, 0:4096].rearrange("p (t h) -> p t h", h=P), m.tail[:, 0:4096].rearrange("p (t h) -> p t h", h=P)]
    pages = [m.tail[:, 4096 + 1024 * b:5120 + 1024 * b].rearrange("p (j c) -> p j c", c=GD) for b in range(2)]
    kt = W[:, 0:2048].rearrange("p (t b n) -> p t b n", t=CS, b=2)
    w2 = [m.midw[:, P * i:P * (i + 1)] for i in range(2)]
    pb = m.midw[:, 256:258]
    x, u, h = (m.midw[:, 320 + P * i:320 + P * i + 2 * 63].rearrange("p (b n) -> p b n", b=2) for i in range(3))
    w_set, w_ok = m.sem("block_diagonals_zeroed"), m.sem("compress_weights_in")
    pt_in, pages_in = m.sem("page_table_in"), [m.sem(f"pages_in{b}") for b in range(2)]
    page_free = [m.sem(f"page_buffer_free{b}") for b in range(2)]
    kt_done, cmp_mm, bias_mm, bias_done = (m.sem("tokens_laid_out"), m.sem("compress_sums"), m.sem("bias_sums"),
                                           m.sem("bias_ready"))
    g_act, g_dve, out_mm, out_done = (m.sem("gelu_by_act"), m.sem("gelu_by_dve"), m.sem("compressed_products"),
                                      m.sem("compressed_written"))
    NP = NB // 2
    R = 1 + NP

    with nc.Block() as block:
        @block.sync
        def _(sp):
            sp.dma_start(m.pt[:, :], I["page_table"].rearrange("b j -> (b j)").unsqueeze(0)).then_inc(pt_in, 16)
            sp.wait_ge(w_set, 8)
            for kv, (a, b) in enumerate((("cmp_w1_k", "cmp_w2_k"), ("cmp_w1_v", "cmp_w2_v"))):
                for g in range(2):
                    r = slice(64 * g, 64 * g + 64)
                    sp.dma_start(w1[kv][r, :, r], I[a][0].rearrange("(t d) h -> d t h", d=HD)).then_inc(w_ok, 16)
                    sp.dma_start(w2[kv][r, r], I[b][0]).then_inc(w_ok, 16)
            sp.wait_ge(pt_in, 16)
            for kv in range(2):
                with sp.Fori(0, NP) as it:
                    for b in range(2):
                        sp.wait_ge(page_free[b], it + (NP * kv + 1))
                        for j in range(NPAGE):
                            load_page(sp, m, I, "cache_cmp_kv", it * 2 + b, j, kv, pages[b][:, j, :], pages_in[b])

        @block.gpsimd
        def _(pool):
            for kv in range(2):
                pool.memset(w1[kv][0:64, :, 64:128], 0.0).then_inc(w_set, 1)
                pool.memset(w1[kv][64:128, :, 0:64], 0.0).then_inc(w_set, 1)
                pool.memset(w2[kv][0:64, 64:128], 0.0).then_inc(w_set, 1)
                pool.memset(w2[kv][64:128, 0:64], 0.0).then_inc(w_set, 1)

        @block.tensor
        def _(pe):
            def sums(kv, nb):
                for t in range(CL):
                    ins = pe.matmul(ps[:, 4, 0:nb * 63], w1[kv][:, t, :],
                                    kt[:, t % CS, 0:nb, t // CS:t // CS + 63], start=t == 0, stop=t == CL - 1)
                ins.then_inc(cmp_mm, 1)

            def outs(kv, nb, r):
                pe.wait_ge(g_dve, 4 * r + 4)
                if kv == 0:
                    ins = pe.matmul(ps[:, 5, 0:nb * 63], w2[0], h[:, 0:nb, :], start=True, stop=True)
                else:
                    for b in range(nb):
                        ins = pe.matmul(ps[0:63, 5, b * P:(b + 1) * P], h[:, b, :], w2[1], start=True, stop=True)
                ins.then_inc(out_mm, 1)

            pe.wait_ge(w_ok, 128)
            for kv in range(2):
                for t in range(CL):
                    ins = pe.matmul(ps[:, 6, kv:kv + 1], w1[kv][:, t, :], m.peT[:, 32 * kv + t:32 * kv + t + 1],
                                    start=t == 0, stop=t == CL - 1)
            ins.then_inc(bias_mm, 1)
            for b in range(2):
                pe.sem_inc(page_free[b], 1)
            for kv in range(2):
                pe.wait_ge(kt_done, kv * (1 + 4 * NP) + 1)
                sums(kv, 1)
                outs(kv, 1, kv * R)
                with pe.Fori(0, NP) as it:
                    for b in range(2):
                        pe.wait_ge(pages_in[b], it * 128 + 128 * (NP * kv + 1))
                        for j in range(NPAGE):
                            ins = pe.transpose(ps[:, 2 * b + j // 4, (j % 4) * P:(j % 4 + 1) * P], pages[b][:, j, :],
                                               m.ident[:, :])
                        ins.then_inc(page_free[b], 1)
                    pe.wait_ge(kt_done, it * 4 + (kv * (1 + 4 * NP) + 5))
                    sums(kv, 2)
                    outs(kv, 2, it + (kv * R + 1))

        @block.scalar
        def _(act):
            def gelu(r, nb):
                act.wait_ge(cmp_mm, r + 1)
                act.activation(x[:, 0:nb, :], ps[:, 4, 0:nb * 63].rearrange("p (b n) -> p b n", b=nb), ACT.Identity,
                               bias=pb[:, kv:kv + 1]).then_inc(g_act, 1)
                act.wait_ge(g_dve, 4 * r + 3)
                act.activation(u[:, 0:nb, :], u[:, 0:nb, :], ACT.Tanh, scale=0.7978845608028654).then_inc(g_act, 1)

            act.wait_ge(bias_done, 2)
            for kv in range(2):
                gelu(kv * R, 1)
                with act.Fori(0, NP) as it:
                    for b in range(2):
                        act.wait_ge(page_free[b], it + (NP * kv + 2))
                        act.activation(kt[:, :, b, 0:32].rearrange("p t n -> p n t"),
                                       ps[:, 2 * b, :].rearrange("p (n t) -> p n t", t=CS), ACT.Copy).then_inc(kt_done, 1)
                    gelu(it + (kv * R + 1), 2)

        @block.vector
        def _(dve):
            def gelu(r, nb):
                a, b, c = x[:, 0:nb, :], u[:, 0:nb, :], h[:, 0:nb, :]
                dve.wait_ge(g_act, 2 * r + 1)
                dve.tensor_tensor(b, a, a, ALU.mult).then_inc(g_dve, 1)
                dve.wait_ge(g_dve, 4 * r + 1)
                dve.tensor_scalar(b, b, 0.044715, 1.0, ALU.mult, ALU.add).then_inc(g_dve, 1)
                dve.wait_ge(g_dve, 4 * r + 2)
                dve.tensor_tensor(b, b, a, ALU.mult).then_inc(g_dve, 1)
                dve.wait_ge(g_act, 2 * r + 2)
                dve.scalar_tensor_tensor(out=c, in0=b, scalar=1.0, in1=a, op0=ALU.add, op1=ALU.mult).then_inc(g_dve, 1)

            def write(kv, r, first, nb):
                dve.wait_ge(out_mm, r + 1)
                if kv == 0:
                    dve.tensor_scalar(m.ckT[:, bass.ds(first, nb), 0:63],
                                      ps[:, 5, 0:nb * 63].rearrange("p (b n) -> p b n", b=nb), 0.5, None,
                                      ALU.mult).then_inc(out_done, 1)
                else:
                    dve.tensor_scalar(m.cvt[0:63, bass.ds(first, nb), :],
                                      ps[0:63, 5, 0:nb * P].rearrange("p (b n) -> p b n", b=nb), 0.5, None,
                                      ALU.mult).then_inc(out_done, 1)

            dve.wait_ge(bias_mm, 1)
            for kv in range(2):
                dve.tensor_tensor(pb[:, kv:kv + 1], ps[:, 6, kv:kv + 1], m.vecT[:, V_B1K + kv:V_B1K + kv + 1],
                                  ALU.add).then_inc(bias_done, 1)
            for kv in range(2):
                if kv:
                    dve.wait_ge(cmp_mm, R)
                dve.tensor_copy(kt[:, :, 0, :].rearrange("p t n -> p n t"),
                                m.zT[:, Z_KC if kv == 0 else Z_VC, 0:SEQ].rearrange("p (n t) -> p n t", t=CS)).then_inc(
                                    kt_done, 1)
                gelu(kv * R, 1)
                write(kv, kv * R, 0, 1)
                with dve.Fori(0, NP) as it:
                    for b in range(2):
                        dve.wait_ge(page_free[b], it + (NP * kv + 2))
                        dve.tensor_copy(kt[:, :, b, 32:64].rearrange("p t n -> p n t"),
                                        ps[:, 2 * b + 1, :].rearrange("p (n t) -> p n t", t=CS)).then_inc(kt_done, 1)
                    gelu(it + (kv * R + 1), 2)
                    write(kv, it + (kv * R + 1), it * 2 + 1, 2)


def stage_samples(m, I, O):
    nc, ps = m.nc, m.ps
    W, tail = m.work, m.tail
    RB = 2 * HP * DS
    BQ = P // RB
    NQ = NB // BQ
    kpg = [tail[:, 1024 * i:1024 * (i + 1)].rearrange("p (j c) -> p j c", c=GD) for i in range(2)]
    KT = [tail[:, 2048 + 1024 * i:3072 + 1024 * i] for i in range(2)]
    S = tail[:, 4096:5152]
    PT = tail[:, 5152:6304].rearrange("p (j r) -> p j r", r=P)
    V = [None, m.vgf[:, 0:4096].rearrange("p (b j c) -> p b j c", b=BQ, c=GD),
         m.midw[:, 0:2048].rearrange("p (b j c) -> p b j c", b=BQ, c=GD)]
    gateB = m.midw[:, 2048:2432].rearrange("p (k h t) -> p k h t", k=3, h=HP)
    sel = W[0:24, 0:1536].rearrange("p (k h g d) -> p k h g d", k=3, h=HP, g=2)
    Qb = W[:, 1536:1792].rearrange("p (b g h t) -> p b g h t", b=NB, g=2, h=HP)
    Qf = W[:, 1536:1792]
    HS, blk = W[:, 1792:1920], W[:, 1920:2048]
    newm = W[:, 2048:2112].rearrange("p (q t) -> p q t", q=NQ)
    winm = W[:, 2112:2116]
    iota = W[:, 2120:2152]
    ints = W[:, 2152:2156].bitcast(I32)
    intf = W[:, 2176:2304].bitcast(I32)
    tcol, bcol, lo, hi = (W[:, 2156 + i:2157 + i] for i in range(4))
    geq = W[:, 2304:2336]
    on, gt = W[:, 2400:2528], W[:, 2528:2592]
    hp = W[:, 2600:2666]
    imp, t14, drop = W[:, 2670:2684], W[:, 2690:2704], W[:, 2710:2726]
    nmx, den, rden, mn, jd = (W[:, 2730 + i:2731 + i] for i in range(5))
    Pn = W[:, 2740:2804]
    NJ = NSLC - 2

    k_in = [m.sem(f"key_pages_in{i}") for i in range(2)]
    v_in = [None, m.sem("selected_values_in"), m.sem("window_values_in")]
    c_pool, c_own = m.sem("sample_constants"), m.sem("sample_vector_chain")
    gates_mm, kT, kt_act, kt_dve = m.sem("gates_spread"), m.sem("keys_turned"), m.sem("keys_by_act"), m.sem("keys_by_dve")
    const_ok = m.sem("sample_masks_ready")
    k_mm, s_mm, s_ok, ex, r_ok, i_mm = (m.sem("key_tiles_scored"), m.sem("scores_summed"), m.sem("scores_masked"),
                                        m.sem("probabilities_ready"), m.sem("normalised_compressed"),
                                        m.sem("importance_summed"))
    pT, pt_act, pt_dve, pv, on_ok, oT, gated = (m.sem("probabilities_turned"), m.sem("turned_by_act"),
                                                m.sem("turned_by_dve"), m.sem("values_summed"), m.sem("outputs_scaled"),
                                                m.sem("outputs_turned"), m.sem("outputs_gated"))
    seq = [(q, br) for q in range(NQ) for br in range(3)]
    win = I["state_win_kv"][0].rearrange("b (j p) a g d -> p b j (a g d)", p=P)
    KJ = [0, NPAGE, WIN // P]

    def kn(q, br, b):
        return q * 2 * BQ + (br - 1) * BQ + b

    def k_total(n):
        return sum(16 * (NPAGE if (j // BQ) % 2 == 0 else 1) for j in range(n % 2, n + 1, 2))

    with nc.Block() as block:
        @block.sync
        def _(sp):
            for q, br in seq:
                if br == 0:
                    continue
                if q:
                    sp.wait_ge(pv, 3 * (q - 1) + br + 1)
                for b in range(BQ):
                    n = kn(q, br, b)
                    if n >= 2:
                        sp.wait_ge(kT, n - 1)
                    if br == 1:
                        for j in range(NPAGE):
                            load_page(sp, m, I, "cache_slc_kv", BQ * q + b, j, 0, kpg[n % 2][:, j, :], k_in[n % 2])
                            load_page(sp, m, I, "cache_slc_kv", BQ * q + b, j, 1, V[1][:, b, j, :], v_in[1])
                    else:
                        sp.dma_start(kpg[n % 2][:, 0:KJ[2], :], win[:, BQ * q + b, :, 0:GD]).then_inc(k_in[n % 2], 16)
                        sp.dma_start(V[2][:, b], win[:, BQ * q + b, :, GD:2 * GD]).then_inc(v_in[2], 16)

        @block.gpsimd
        def _(pool):
            pool.memset(sel, 0.0).then_inc(c_pool, 1)
            pool.memset(Qf, 0.0).then_inc(c_pool, 1)
            pool.memset(blk, 1.0).then_inc(c_pool, 1)
            pool.iota(iota, [[1, 32]], base=0, channel_multiplier=0, allow_small_or_imprecise_dtypes=True).then_inc(c_pool, 1)
            pool.iota(ints[:, 0:1], [[0, 1]], base=0, channel_multiplier=1).then_inc(c_pool, 1)
            pool.iota(intf, [[1, P]], base=0, channel_multiplier=0).then_inc(c_pool, 1)
            pool.memset(hp, 0.0).then_inc(c_pool, 1)
            pool.memset(drop, 0.0).then_inc(c_pool, 1)
            pool.wait_ge(c_pool, 8)
            pool.affine_select(out=sel, in_=sel, compare_op=ALU.not_equal, fill=1.0, base=0,
                               pattern=[[-8, 3], [-1, HP], [-HP, 2], [0, HD]], channel_multiplier=1).then_inc(c_pool, 1)
            b16 = blk.rearrange("p (c t) -> p c t", t=16)
            keep(pool, None, b16, [[-16, 8], [0, 16]], 0, 1).then_inc(c_pool, 1)
            pool.wait_ge(c_pool, 10)
            keep(pool, None, b16, [[16, 8], [0, 16]], 15, -1).then_inc(c_pool, 1)

        @block.tensor
        def _(pe):
            pe.wait_ge(c_pool, 11)
            for k in range(3):
                for h in range(HP):
                    c = (k * HP + h) * ST
                    ins = pe.matmul(ps[:, 7, c:c + ST], sel[:, k, h].rearrange("p g d -> p (g d)"), m.gnT[:, :],
                                    start=True, stop=True)
            ins.then_inc(gates_mm, 1)
            pe.wait_ge(const_ok, 1)

            def turn_keys(q, br, b):
                n = kn(q, br, b)
                pe.wait_ge(k_in[n % 2], k_total(n))
                for j in range(KJ[br]):
                    ins = pe.transpose(ps[:, 3 + 2 * (n % 2) + j // 4, (j % 4) * P:(j % 4 + 1) * P], kpg[n % 2][:, j, :],
                                       m.ident[:, :])
                ins.then_inc(kT, 1)

            for r, (q, br) in enumerate(seq):
                rows = lambda b: slice(RB * b, RB * b + RB)
                qcols = lambda b: Qf[:, (BQ * q + b) * RB:(BQ * q + b + 1) * RB]
                if br == 0:
                    for b in range(BQ):
                        ins = pe.matmul(ps[rows(b), 0, 0:63], qcols(b), m.ckT[:, 1 + BQ * q + b, 0:63], start=True, stop=True)
                    ins.then_inc(s_mm, 1)
                else:
                    turn_keys(q, br, 0)
                    for b in range(BQ):
                        n = kn(q, br, b)
                        if b + 1 < BQ:
                            turn_keys(q, br, b + 1)
                        pe.wait_ge(kt_act, n + 1)
                        if br == 1:
                            pe.wait_ge(kt_dve, BQ * q + b + 1)
                        for c in range(KJ[br] // 4):
                            ins = pe.matmul(ps[rows(b), c, :], qcols(b), KT[n % 2][:, 512 * c:512 * (c + 1)], start=True,
                                            stop=True)
                        ins.then_inc(k_mm, 1)
                    pe.matmul(ps[:, 2, 0:ST], Qf[:, q * P:(q + 1) * P], m.zT[:, Z_KS + br - 1, SEQ:T], start=True,
                              stop=True).then_inc(s_mm, 1)
                if br == 0:
                    pe.wait_ge(r_ok, q + 1)
                    pe.matmul(ps[:, 1, 0:63], HS, Pn[:, 0:63], start=True, stop=True).then_inc(i_mm, 1)
                pe.wait_ge(ex, r + 1)
                if r:
                    pe.wait_ge(gated, r)
                w = 63 if br == 0 else P
                for j in range(max(KJ[br], 1)):
                    ins = pe.transpose(ps[0:w, 5 + j // 4, (j % 4) * P:(j % 4 + 1) * P], S[:, j * P:j * P + w], m.ident[:, :])
                if br:
                    ins = pe.transpose(ps[0:ST, 7, 0:P], S[:, KJ[br] * P:KJ[br] * P + ST], m.ident[:, :])
                ins.then_inc(pT, 1)
                pe.wait_ge(pt_act, r + 1)
                pe.wait_ge(pt_dve, r + 1)
                if br:
                    pe.wait_ge(v_in[br], (q + 1) * 16 * BQ * (NPAGE if br == 1 else 1))
                for b in range(BQ):
                    out = ps[rows(b), 2, 0:GD]
                    if br == 0:
                        ins = pe.matmul(out, PT[0:63, 0, rows(b)], m.cvt[0:63, 1 + BQ * q + b, :], start=True, stop=True)
                    else:
                        for j in range(KJ[br]):
                            pe.matmul(out, PT[:, j, rows(b)], V[br][:, b, j, :], start=j == 0, stop=False)
                        ins = pe.matmul(out, PT[0:ST, 8, rows(b)], m.vtm[0:ST, QT, br - 1, :], start=False, stop=True)
                ins.then_inc(pv, 1)
                pe.wait_ge(on_ok, r + 1)
                pe.transpose(ps[:, 7, P:2 * P], on, m.ident[:, :]).then_inc(oT, 1)

        @block.scalar
        def _(act):
            for r, (q, br) in enumerate(seq):
                if br:
                    for b in range(BQ):
                        n = kn(q, br, b)
                        act.wait_ge(kT, n + 1)
                        if n >= 2:
                            act.wait_ge(k_mm, n - 1)
                        act.activation(KT[n % 2][:, 0:512], ps[:, 3 + 2 * (n % 2), :], ACT.Copy).then_inc(kt_act, 1)
                act.wait_ge(s_ok, r + 1)
                L = 63 if br == 0 else KJ[br] * P + ST
                act.activation(S[:, 0:L], ps[:, 0, 0:63] if br == 0 else S[:, 0:L], ACT.Exp, bias=nmx,
                               accum_out=den).then_inc(ex, 1)
                act.wait_ge(pT, r + 1)
                if br == 0:
                    act.activation(PT[0:63, 0, :], ps[0:63, 5, 0:P], ACT.Copy).then_inc(pt_act, 1)
                else:
                    act.activation(PT[:, 0:4, :], ps[:, 5, :].rearrange("p (j r) -> p j r", j=4), ACT.Copy).then_inc(pt_act, 1)

        @block.vector
        def _(dve):
            steps = [0]

            def chain(ins):
                steps[0] += 1
                ins.then_inc(c_own, 1)
                dve.wait_ge(c_own, steps[0])

            dve.wait_ge(c_pool, 11)
            for g in range(2):
                for h in range(HP):
                    r = slice(64 * g, 64 * g + 64)
                    dve.tensor_scalar(Qb[r, :, g, h, :], m.zT[r, Z_Q + h, SEQ:T].rearrange("p (b t) -> p b t", t=DS),
                                      HD ** -0.5, None, ALU.mult)
            dve.tensor_scalar(ints[:, 1:2], ints[:, 0:1], 3, None, ALU.bitwise_and)
            dve.tensor_scalar(ints[:, 2:3], ints[:, 0:1], 5, None, ALU.logical_shift_right)
            chain(dve.tensor_scalar(intf, intf, 3, None, ALU.bitwise_and))
            dve.tensor_copy(tcol, ints[:, 1:2])
            dve.tensor_copy(bcol, ints[:, 2:3])
            chain(dve.tensor_copy(HS, intf))
            chain(dve.tensor_scalar(HS, HS, tcol, None, ALU.is_equal))
            chain(dve.tensor_tensor(HS, HS, blk, ALU.mult))
            dve.tensor_scalar(winm, iota[:, 0:4], tcol, NEG, ALU.is_le, ALU.mult)
            for q in range(NQ):
                chain(dve.tensor_scalar(lo, bcol, float(DS), float(DS * BQ * q), ALU.mult, ALU.add))
                chain(dve.tensor_tensor(hi, lo, tcol, ALU.add))
                chain(dve.tensor_scalar(geq, iota, lo, None, ALU.is_ge))
                chain(dve.scalar_tensor_tensor(out=newm[:, q], in0=iota, scalar=hi, in1=geq, op0=ALU.is_le, op1=ALU.mult))
                chain(dve.tensor_scalar(newm[:, q], newm[:, q], -1.0, -NEG, ALU.add, ALU.mult))
            dve.wait_ge(gates_mm, 1)
            dve.tensor_copy(gateB, ps[:, 7, 0:384].rearrange("p (k h t) -> p k h t", k=3, h=HP)).then_inc(const_ok, 1)
            for r, (q, br) in enumerate(seq):
                L = 63 if br == 0 else KJ[br] * P + ST
                if br == 1:
                    for b in range(BQ):
                        n = kn(q, br, b)
                        dve.wait_ge(kT, n + 1)
                        if n >= 2:
                            dve.wait_ge(k_mm, n - 1)
                        dve.tensor_copy(KT[n % 2][:, 512:1024], ps[:, 4 + 2 * (n % 2), :]).then_inc(kt_dve, 1)
                dve.wait_ge(s_mm, r + 1)
                if br == 0:
                    dve.tensor_reduce(nmx, ps[:, 0, 0:63], X, ALU.max, negate=True).then_inc(s_ok, 1)
                else:
                    nk = KJ[br] * P
                    if br == 1:
                        dve.tensor_tensor(S[:, 0:nk].rearrange("p (j t) -> p j t", t=SLC),
                                          ps[:, 0:2, :].rearrange("p a b -> p (a b)").rearrange("p (j t) -> p j t", t=SLC),
                                          drop.unsqueeze(2).to_broadcast([P, NSLC, SLC]), ALU.add)
                    else:
                        dve.tensor_tensor(S[:, 0:4], ps[:, 0, 0:4], winm, ALU.add)
                        dve.tensor_copy(S[:, 4:nk], ps[:, 0, 4:nk])
                    chain(dve.tensor_tensor(S[:, nk:L], ps[:, 2, 0:ST], newm[:, q], ALU.add))
                    dve.tensor_reduce(nmx, S[:, 0:L], X, ALU.max, negate=True).then_inc(s_ok, 1)
                dve.wait_ge(ex, r + 1)
                chain(dve.reciprocal(rden, den))
                if br == 0:
                    dve.tensor_scalar(Pn[:, 0:63], S[:, 0:63], rden, None, ALU.mult).then_inc(r_ok, 1)
                    dve.wait_ge(i_mm, q + 1)
                    chain(dve.tensor_copy(hp[:, 1:64], ps[:, 1, 0:63]))
                    chain(dve.tensor_reduce(imp, hp[:, 4:4 + 4 * NJ].rearrange("p (j n) -> p j n", n=4), X, ALU.add))
                    chain(dve.tensor_tensor(imp, imp, hp[:, 8:8 + 4 * NJ].rearrange("p (j n) -> p j n", n=4)[:, :, 0], ALU.add))
                    chain(dve.tensor_reduce(mn, imp, X, ALU.min))
                    chain(dve.scalar_tensor_tensor(out=t14, in0=imp, scalar=mn, in1=iota[:, 1:1 + NJ], op0=ALU.is_le,
                                                   op1=ALU.mult))
                    chain(dve.tensor_reduce(jd, t14, X, ALU.max))
                    chain(dve.tensor_scalar(drop, iota[:, 0:NSLC], jd, NEG, ALU.is_equal, ALU.mult))
                dve.wait_ge(pT, r + 1)
                if br == 1:
                    dve.tensor_copy(PT[:, 4:8, :], ps[:, 6, :].rearrange("p (j r) -> p j r", j=4))
                if br:
                    dve.tensor_copy(PT[0:ST, 8, :], ps[0:ST, 7, 0:P]).then_inc(pt_dve, 1)
                else:
                    dve.sem_inc(pt_dve, 1)
                dve.wait_ge(pv, r + 1)
                dve.tensor_scalar(on, ps[:, 2, 0:GD], rden, None, ALU.mult).then_inc(on_ok, 1)
                dve.wait_ge(oT, r + 1)
                toks = slice(BQ * DS * q, BQ * DS * (q + 1))
                for g in range(2):
                    gr = slice(64 * g, 64 * g + 64)
                    o = ps[gr, 7, P:2 * P].rearrange("p (b g h t) -> p g h b t", b=BQ, g=2, h=HP)[:, g]
                    gate = gateB[gr, br, :, toks].rearrange("p h (b t) -> p h b t", t=DS)
                    to = m.osT[gr, :, toks].rearrange("p h (b t) -> p h b t", t=DS)
                    if br == 0:
                        ins = dve.tensor_tensor(to, o, gate, ALU.mult)
                    else:
                        part = gt[gr].rearrange("p (h b t) -> p h b t", h=HP, b=BQ)
                        chain(dve.tensor_tensor(part, o, gate, ALU.mult))
                        ins = dve.tensor_tensor(to, to, part, ALU.add)
                ins.then_inc(gated, 1)
                dve.wait_ge(gated, r + 1)


def stage_attention(m, I, O):
    nc, ps = m.nc, m.ps
    W, tail, vgf = m.work, m.tail, m.vgf
    oa = tail[:, 0:4096].rearrange("p (h i g d) -> p h i g d", h=HP, i=QT, g=2)
    Qs = tail[:, 4096:6144].rearrange("p (g t) -> p g t", g=2)
    Pb = [vgf[:, 1024 * i:1024 * (i + 1)] for i in range(2)]
    PT = [vgf[:, 2048 + 512 * i:2560 + 512 * i].rearrange("p (j q) -> p j q", j=4) for i in range(4)]
    cm = vgf[:, 4096:4608].rearrange("p (i n) -> p i n", n=64)
    cvb = W[:, 384:512]
    wc = W[:, 0:256].rearrange("p (k t) -> p k t", k=2)
    mx, den16, fac16 = W[:, 256:272], W[:, 288:304], W[:, 304:320]
    nmx = [W[:, 320 + i:321 + i] for i in range(2)]
    den = [W[:, 324 + i:325 + i] for i in range(4)]
    rden, fac = W[:, 329:330], W[:, 330:331]
    gates = m.gates[:, :, :].rearrange("p i (k g h) -> p i k g h", k=3, g=2)

    items = [(0, 0, 0)] + [(br, qt, g) for qt in range(QT) for g in range(2) for br in (1, 2)]
    N = len(items)
    keys = [None] + [list(range(max(0, qt - 4) if br == 2 else 0, qt + 1)) for br, qt, g in items[1:]]
    npc = [2] + [-(-len(k) // 4) for k in keys[1:]]
    p0 = [sum(npc[:w]) for w in range(N)]
    NPC = sum(npc)

    c_ok, zero_ok = m.sem("attention_masks"), m.sem("query_halves_zeroed")
    qs_ok, cv_ok = m.sem("queries_staged"), m.sem("compressed_values_in_blocks")
    qk, s_ok, ex = m.sem("item_scored"), m.sem("item_max_ready"), m.sem("item_exponentials")
    pT, pt, pv = m.sem("piece_turned"), m.sem("piece_copied"), m.sem("piece_summed")
    o_ok, own, oT = m.sem("item_output_added"), m.sem("attention_vector_chain"), m.sem("attention_turned")
    ow = [m.sem("attention_written_by_dve"), m.sem("attention_written_by_act")]

    def item(e, sem, it, w):
        e.wait_ge(sem, it * N + (w + 2))

    def piece(e, sem, it, p):
        e.wait_ge(sem, it * NPC + (p + 2))

    before = lambda w: w - 2 if w >= 2 else -1

    with nc.Block() as block:
        @block.sync
        def _(sp):
            prefetch_merge(sp, m, I)

        @block.gpsimd
        def _(pool):
            pool.memset(wc, 0.0).then_inc(c_ok, 1)
            pool.memset(cm, 0.0).then_inc(c_ok, 1)
            pool.wait_ge(c_ok, 2)
            pool.memset(Qs[64:128, 0, :], 0.0).then_inc(zero_ok, 1)
            pool.memset(Qs[0:64, 1, :], 0.0).then_inc(zero_ok, 1)
            pool.wait_ge(zero_ok, 2)
            pool.memset(m.ckT[:, 0, 63:64], 0.0).then_inc(zero_ok, 1)
            pool.memset(cvb, 0.0).then_inc(zero_ok, 1)
            for ap, pattern, base, mult in ((wc[:, 0, :], [[1, P]], -1, -1), (wc[:, 1, :], [[-1, P]], 0, 1),
                                            (cm, [[P, QT], [-CS, 64]], 1 - CL, 1)):
                pool.affine_select(out=ap, in_=ap, compare_op=ALU.is_ge, fill=NEG, base=base, pattern=pattern,
                                   channel_multiplier=mult).then_inc(c_ok, 1)

        @block.tensor
        def _(pe):
            pe.wait_ge(zero_ok, 4)
            pe.wait_ge(cv_ok, 2)
            for sem in (qk, pT, pv):
                pe.sem_inc(sem, 1)

            def score(it, w):
                br, qt, g = items[w]
                item(pe, ex, it, before(w))
                if w == 0:
                    pe.wait_ge(qs_ok, it * 2 + 2)
                    item(pe, ex, it, -1)
                    for i in range(QT):
                        for g in range(2):
                            c = 2 * i + g
                            ins = pe.matmul(ps[:, c // 8, (c % 8) * 64:(c % 8 + 1) * 64], Qs[:, g, i * P:(i + 1) * P],
                                            m.ckT[:, 0, :], start=True, stop=True)
                else:
                    lo, n = keys[w][0] * P, len(keys[w]) * P
                    for c in range(0, n, 512):
                        k = min(512, n - c)
                        ins = pe.matmul(ps[:, 2 * (w % 2) + c // 512, 0:k], Qs[:, g, qt * P:(qt + 1) * P],
                                        m.zT[:, Z_KS + br - 1, lo + c:lo + c + k], start=True, stop=True)
                ins.then_inc(qk, 1)

            def turn(it, w, a):
                p = p0[w] + a
                piece(pe, pt, it, before(p))
                if a == 0:
                    item(pe, ex, it, w)
                if w == 0:
                    for j in range(4):
                        ins = pe.transpose(ps[:, 4 + p % 2, j * P:(j + 1) * P], Pb[0][:, (4 * a + j) * P:(4 * a + j + 1) * P],
                                           m.ident[:, :])
                else:
                    for j in range(min(4, len(keys[w]) - 4 * a)):
                        ins = pe.transpose(ps[:, 4 + p % 2, j * P:(j + 1) * P],
                                           Pb[w % 2][:, (4 * a + j) * P:(4 * a + j + 1) * P], m.ident[:, :])
                ins.then_inc(pT, 1)

            def value(it, w, a):
                br, qt, g = items[w]
                p = p0[w] + a
                piece(pe, pt, it, p)
                if a == 0:
                    item(pe, o_ok, it, 0 if w == 1 else before(w))
                if w == 0:
                    for j in range(4):
                        ins = pe.matmul(ps[:, 6 + a, j * P:(j + 1) * P], PT[p % 4][:, j, :], cvb, start=True, stop=True)
                else:
                    n = len(keys[w])
                    for j in range(min(4, n - 4 * a)):
                        kt = 4 * a + j
                        ins = pe.matmul(ps[:, 6 + w % 2, 0:HD], PT[p % 4][:, j, :],
                                        m.vtm[:, keys[w][kt], br - 1, g * HD:(g + 1) * HD], start=kt == 0, stop=kt == n - 1)
                ins.then_inc(pv, 1)

            with pe.Fori(0, HP) as it:
                score(it, 0)
                last = None
                for w in range(N):
                    if w + 1 < N:
                        score(it, w + 1)
                    for a in range(npc[w]):
                        turn(it, w, a)
                        if last is not None:
                            value(it, *last)
                        last = (w, a)
                value(it, *last)
            item(pe, o_ok, HP, -1)
            for n in range(2 * HP):
                h, half = n // 2, n % 2
                if n >= 4:
                    pe.wait_ge(ow[n % 2], (n - 4) // 2 + 1)
                for j in range(4):
                    ins = pe.transpose(ps[:, n % 4, j * P:(j + 1) * P],
                                       oa[:, h, 4 * half + j].rearrange("p g d -> p (g d)"), m.ident[:, :])
                ins.then_inc(oT, 1)

        @block.scalar
        def _(act):
            act.sem_inc(ex, 1)
            act.sem_inc(pt, 1)
            act.wait_ge(zero_ok, 4)
            for g in range(2):
                act.activation(cvb[64 * g:64 * g + 63, HD * g:HD * (g + 1)], m.cvt[0:63, 0, HD * g:HD * (g + 1)],
                               ACT.Copy).then_inc(cv_ok, 1)

            def exps(it, w):
                item(act, s_ok, it, w)
                if w >= 2:
                    piece(act, pT, it, p0[w - 1] - 1)
                else:
                    piece(act, pT, it, -1)
                if w == 2:
                    item(act, o_ok, it, 0)
                if w == 0:
                    v = Pb[0].rearrange("p (c n) -> p c n", n=64)
                    act.activation(v, v, ACT.Exp).then_inc(ex, 1)
                else:
                    n = len(keys[w]) * P
                    act.activation(Pb[w % 2][:, 0:n],
                                   ps[:, 2 * (w % 2):2 * (w % 2) + 2, :].rearrange("p a b -> p (a b)")[:, 0:n], ACT.Exp,
                                   bias=nmx[w % 2], accum_out=den[w % 4]).then_inc(ex, 1)

            def copies(it, w):
                for a in range(npc[w]):
                    p = p0[w] + a
                    piece(act, pT, it, p)
                    piece(act, pv, it, p - 4 if p >= 4 else -1)
                    n = 4 if w == 0 else min(4, len(keys[w]) - 4 * a)
                    act.activation(PT[p % 4][:, 0:n], ps[:, 4 + p % 2, 0:n * P].rearrange("p (j q) -> p j q", j=n),
                                   ACT.Copy).then_inc(pt, 1)

            with act.Fori(0, HP) as it:
                item(act, qk, it, -1)
                for g in range(2):
                    r = slice(64 * g, 64 * g + 64)
                    act.activation(Qs[r, g:g + 1, :], m.zT[r, bass.ds(it, 1), 0:SEQ], ACT.Copy,
                                   scale=HD ** -0.5).then_inc(qs_ok, 1)
                exps(it, 0)
                for w in range(N):
                    if w + 1 < N:
                        exps(it, w + 1)
                    copies(it, w)
            for n in range(1, 2 * HP, 2):
                act.wait_ge(oT, n + 1)
                act.activation(m.zT[:, n // 2, (n % 2) * 512:(n % 2 + 1) * 512], ps[:, n % 4, :], ACT.Copy).then_inc(ow[1], 1)

        @block.vector
        def _(dve):
            dve.sem_inc(s_ok, 1)
            dve.sem_inc(o_ok, 1)
            dve.wait_ge(c_ok, 5)
            per = (N - 1) * 3 + 7
            step = [0]

            def chain(it, ins):
                step[0] += 1
                ins.then_inc(own, 1)
                dve.wait_ge(own, it * per + step[0])

            def maxima(it, w):
                br, qt, g = items[w]
                item(dve, qk, it, w)
                if w == 0:
                    v = Pb[0].rearrange("p (c n) -> p c n", n=64)
                    piece(dve, pT, it, -1)
                    chain(it, dve.tensor_tensor(v.rearrange("p (i g) n -> p i g n", g=2),
                                                ps[:, 0:2, :].rearrange("p a (i g n) -> p (a i) g n", g=2, n=64),
                                                cm.unsqueeze(2).to_broadcast([P, QT, 2, 64]), ALU.add))
                    chain(it, dve.tensor_reduce(mx, v, X, ALU.max))
                    chain(it, dve.scalar_tensor_tensor(out=mx, in0=mx, scalar=NEG / 10, in1=mx, op0=ALU.is_gt, op1=ALU.mult))
                    dve.tensor_tensor(v, v, mx.unsqueeze(2).to_broadcast([P, 16, 64]), ALU.subtract).then_inc(s_ok, 1)
                else:
                    n = len(keys[w])
                    row = ps[:, 2 * (w % 2):2 * (w % 2) + 2, :].rearrange("p a b -> p (a b)")
                    if br == 2 and qt >= 4:
                        edge = ps[:, 2 * (w % 2):2 * (w % 2) + 2, 0:P]
                        chain(it, dve.tensor_tensor(edge, edge, wc, ALU.add))
                    else:
                        edge = row[:, (n - 1) * P:n * P]
                        chain(it, dve.tensor_tensor(edge, edge, wc[:, 1, :], ALU.add))
                    dve.tensor_reduce(nmx[w % 2], row[:, 0:n * P], X, ALU.max, negate=True).then_inc(s_ok, 1)

            def output(it, w):
                br, qt, g = items[w]
                if w == 0:
                    item(dve, ex, it, 0)
                    v = Pb[0].rearrange("p (c n) -> p c n", n=64)
                    chain(it, dve.tensor_reduce(den16, v, X, ALU.add))
                    chain(it, dve.tensor_scalar(den16, den16, 1e-30, None, ALU.max))
                    chain(it, dve.reciprocal(fac16, den16))
                    chain(it, dve.tensor_tensor(fac16.rearrange("p (i g) -> p i g", g=2),
                                                fac16.rearrange("p (i g) -> p i g", g=2),
                                                gates[:, :, 0, :, bass.ds(it, 1)].rearrange("p i g o -> p i (g o)"), ALU.mult))
                    piece(dve, pv, it, p0[0] + npc[0] - 1)
                    dve.tensor_tensor(oa[:, bass.ds(it, 1)].rearrange("p o i g d -> p (o i g) d"),
                                      ps[:, 6:8, :].rearrange("p a (c d) -> p (a c) d", d=HD),
                                      fac16.unsqueeze(2).to_broadcast([P, 16, HD]), ALU.mult).then_inc(o_ok, 1)
                else:
                    piece(dve, pv, it, p0[w] + npc[w] - 1)
                    item(dve, o_ok, it, w - 1)
                    chain(it, dve.reciprocal(rden, den[w % 4]))
                    chain(it, dve.tensor_tensor(fac, rden, gates[:, qt, br, g, bass.ds(it, 1)], ALU.mult))
                    o = oa[:, bass.ds(it, 1), qt, g, :].rearrange("p o d -> p (o d)")
                    dve.scalar_tensor_tensor(out=o, in0=ps[:, 6 + w % 2, 0:HD], scalar=fac, in1=o, op0=ALU.mult,
                                             op1=ALU.add).then_inc(o_ok, 1)

            with dve.Fori(0, HP) as it:
                step[0] = 0
                maxima(it, 0)
                for w in range(N):
                    if w + 1 < N:
                        maxima(it, w + 1)
                    if w:
                        output(it, w - 1)
                output(it, N - 1)
                assert step[0] == per, (step[0], per)
            for n in range(0, 2 * HP, 2):
                dve.wait_ge(oT, n + 1)
                dve.tensor_copy(m.zT[:, n // 2, (n % 2) * 512:(n % 2 + 1) * 512], ps[:, n % 4, :]).then_inc(ow[0], 1)
            dve.tensor_copy(m.zT[:, 0:HP, SEQ:T], m.osT[:, :, :]).then_inc(ow[0], 1)


def prefetch_merge(sp, m, I):
    for u in range(GH):
        sp.dma_start(m.ring[:, u], w_block(I["w_in"][0], C_RG + u * P)).then_inc(m.w_in[u], 16)


def stage_merge(m, I, O):
    nc, ps = m.nc, m.ps
    W = m.work
    gate = [[W[:, NW * (2 * s + c):NW * (2 * s + c + 1)] for c in range(2)] for s in range(2)]
    rt = [W[:, NW * (4 + b):NW * (5 + b)] for b in range(6)]
    u0, l0 = m.used, m.loads
    summed, rbank = m.sem("r_tile_summed"), [m.sem(f"r_bank_free{b}") for b in range(6)]
    r_sig, r_mul, r_ok = m.sem("r_sigmoid"), m.sem("r_silu"), m.sem("gla_gated")
    step_mm, sig, mul, bank, add = (m.sem("merge_step_summed"), m.sem("merge_sigmoids"), m.sem("merge_products"),
                                    m.sem("merge_banks_free"), m.sem("merged_written"))
    w_in, w_n, w_g = I["w_in"][0], I["w_nsa_o"][0], I["w_gla_o"][0]

    def load(sp, j, c, slot):
        inc = m.w_in[slot]
        if c < 2:
            v = w_in[:, C_MG + D * c:C_MG + D * (c + 1)].rearrange("(k p) n -> p k n", p=P)[:, :, bass.ds(j * P, P)]
            sp.dma_start(m.ring[:, slot], v).then_inc(inc, 16)
        else:
            for g in range(2):
                v = w_n.rearrange("(g h d) n -> g d h n", g=2, h=HP)[g][:, :, bass.ds(j * P, P)]
                sp.dma_start(m.ring[64 * g:64 * g + 64, slot, 0:HP, :], v).then_inc(inc, 16)
            v = w_g.rearrange("(k p) n -> p k n", p=P)[:, :, bass.ds(j * P, P)]
            sp.dma_start(m.ring[:, slot, HP:KD, :], v).then_inc(inc, 16)

    with nc.Block() as block:
        @block.sync
        def _(sp):
            for j in range(2):
                for c in range(3):
                    slot = 3 * j + c
                    if slot < GH:
                        sp.wait_ge(m.w_used, u0 + slot + 1)
                    load(sp, j, c, slot)
            with sp.Fori(1, KD // 2) as it:
                for jj in range(2):
                    sp.wait_ge(m.w_used, it * 6 + (u0 + GH + 3 * (jj - 1)))
                    for c in range(3):
                        load(sp, it * 2 + jj, c, 3 * jj + c)
            for s in range(2):
                sp.wait_ge(m.w_used, u0 + GH + 3 * (KD - 2) + s + 1)
                sp.dma_start(m.ring[:, s], w_block(I["w_out"][0], s * P)).then_inc(m.w_in[s], 16)

        @block.tensor
        def _(pe):
            for u in range(GH):
                pe.wait_ge(m.w_in[u], 16 * (l0[u] + 1))
                for n in range(NN):
                    b = 3 * (u % 2) + n
                    if u >= 2:
                        pe.wait_ge(rbank[b], u // 2)
                    ins = product(pe, ps[:, b, 0:NW], m.ring[:, u], lambda k: m.hT[:, k, n * NW:(n + 1) * NW])
                    if n < NN - 1:
                        ins.then_inc(summed, 1)
                ins.then_inc(m.w_used, 1)
            for b in range(6):
                pe.wait_ge(rbank[b], 2)
            pe.wait_ge(r_ok, 4 * NN)
            l1 = [l0[s] + (s < GH) for s in range(SLOTS)]
            with pe.Fori(0, KD // 2) as it:
                for jj in range(2):
                    for c in range(3):
                        k = 3 if c == 2 else 1
                        pe.wait_ge(m.w_in[3 * jj + c], it * (16 * k) + 16 * (l1[3 * jj + c] + k))
                    for n in range(NN):
                        t = 3 * jj + n
                        b = 4 * (t % 2)
                        tok = slice(n * NW, (n + 1) * NW)
                        pe.wait_ge(bank, it * 6 + (t + 1))
                        last = [product(pe, ps[:, b + c, 0:NW], m.ring[:, 3 * jj + c], lambda k: m.hT[:, k, tok])
                                for c in range(2)]
                        product(pe, ps[:, b + 2, 0:NW], m.ring[:, 3 * jj + 2, 0:HP], lambda k: m.zT[:, k, tok])
                        ins = product(pe, ps[:, b + 3, 0:NW], m.ring[:, 3 * jj + 2, HP:KD], lambda k: m.oglaT[:, k, tok])
                        if n == NN - 1:
                            for x in last:
                                x.then_inc(m.w_used, 1)
                            ins.then_inc(m.w_used, 1)
                        else:
                            ins.then_inc(step_mm, 1)

        def ready(e, it, jj, n):
            if n < NN - 1:
                e.wait_ge(step_mm, it * 4 + (2 * jj + n + 1))
            else:
                e.wait_ge(m.w_used, it * 6 + (u0 + GH + 3 * jj + 3))

        def r_ready(e, u, n):
            if n < NN - 1:
                e.wait_ge(summed, 2 * u + n + 1)
            else:
                e.wait_ge(m.w_used, u0 + u + 1)

        @block.scalar
        def _(act):
            for u in range(GH):
                for n in range(NN):
                    b = 3 * (u % 2) + n
                    r_ready(act, u, n)
                    if u >= 2:
                        act.wait_ge(r_ok, 3 * (u - 2) + n + 1)
                    act.activation(rt[b], ps[:, b, 0:NW], ACT.Sigmoid).then_inc(r_sig, 1)
            with act.Fori(0, KD // 2) as it:
                for jj in range(2):
                    for n in range(NN):
                        t = 3 * jj + n
                        ready(act, it, jj, n)
                        act.wait_ge(add, it * 6 + (t + 1))
                        for c in range(2):
                            act.activation(gate[t % 2][c], ps[:, 4 * (t % 2) + c, 0:NW], ACT.Sigmoid).then_inc(sig, 1)

        @block.vector
        def _(dve):
            for u in range(GH):
                for n in range(NN):
                    b = 3 * (u % 2) + n
                    dve.wait_ge(r_sig, 3 * u + n + 1)
                    dve.tensor_tensor(rt[b], rt[b], ps[:, b, 0:NW], ALU.mult).then_inc(rbank[b], 1)
            dve.sem_inc(bank, 2)
            with dve.Fori(0, KD // 2) as it:
                for t in range(6):
                    dve.wait_ge(sig, it * 12 + (2 * t + 2))
                    for c in range(2):
                        ins = dve.tensor_tensor(gate[t % 2][c], gate[t % 2][c], ps[:, 4 * (t % 2) + 2 + c, 0:NW], ALU.mult)
                        if c == 0:
                            ins.then_inc(mul, 1)
                    ins.then_inc(bank, 1)

        @block.gpsimd
        def _(pool):
            for u in range(GH):
                for n in range(NN):
                    b = 3 * (u % 2) + n
                    og = m.oglaT[:, u, n * NW:(n + 1) * NW]
                    pool.wait_ge(rbank[b], u // 2 + 1)
                    pool.tensor_tensor(og, og, rt[b], ALU.mult).then_inc(r_ok, 1)
            pool.sem_inc(add, 2)
            with pool.Fori(0, KD // 2) as it:
                for jj in range(2):
                    for n in range(NN):
                        t = 3 * jj + n
                        pool.wait_ge(mul, it * 6 + (t + 1))
                        pool.wait_ge(bank, it * 6 + (t + 3))
                        out = m.merged[:, bass.ds(it * 2 + jj, 1), n * NW:(n + 1) * NW].rearrange("p o t -> p (o t)")
                        pool.tensor_tensor(out, gate[t % 2][0], gate[t % 2][1], ALU.add).then_inc(add, 1)
    m.used += GH + 3 * KD
    m.loads = [l0[s] + (s < GH) + (3 if s % 3 == 2 else 1) * KD // 2 for s in range(SLOTS)]


def stage_mix(m, I, O):
    nc, ps = m.nc, m.ps
    u0, l0 = m.used, m.loads
    R = m.rest
    rst, ones = R[:, 0:T], R[:, T:T + P]
    sq = [R[:, T + P + NW * b:T + P + NW * (b + 1)] for b in range(4)]
    sq2 = [m.oglaT[:, 0, 512 * i:512 * (i + 1)] for i in range(2)] + [m.oglaT[:, 1, 512 * i:512 * (i + 1)] for i in range(2)]
    sqs = m.oglaT[:, 2, 0:KD * ST].rearrange("p (k t) -> p k t", t=ST)
    tmp = m.oglaT[:, 3, :]
    xr = m.hT[:, :, :].rearrange("p k t -> p (k t)")[:, 0:QT * D].rearrange("p (i d) -> p i d", d=D)
    xs = m.vg[0:ST].rearrange("p i h v -> p (i h v)")[:, 0:D]
    x_in, summed, bank = m.sem("x_rows_in"), m.sem("mix_tile_summed"), [m.sem(f"mix_bank_free{b}") for b in range(6)]
    sq_ok, acc_ok, ss_mm, r_ok = m.sem("mix_squares"), m.sem("squares_added"), m.sem("mean_squares"), m.sem("rstd_steps")
    xT, x2_ok, sq2_ok, acc2 = m.sem("x_turned"), m.sem("residual_ready"), m.sem("residual_squares"), m.sem("residual_added")
    own, n_ok, h_ok, pre = m.sem("mix_vector_chain"), m.sem("h_scaled"), m.sem("h_ready"), m.sem("mix_constants")
    groups = [(h, k) for h in range(2) for k in range(KD)]
    G = len(groups)

    with nc.Block() as block:
        @block.sync
        def _(sp):
            sp.dma_start(xr, I["x_prompt"][0].rearrange("(i p) d -> p i d", p=P)).then_inc(x_in, 16)
            sp.dma_start(xs, I["x_sample"].rearrange("b s d -> (b s) d")).then_inc(x_in, 16)
            with sp.Fori(1, KD // 2) as it:
                for s in range(2):
                    sp.wait_ge(m.w_used, it * 2 + (u0 + s - 1))
                    sp.dma_start(m.ring[:, s], dyn_block(I["w_out"][0], it * 2 + s)).then_inc(m.w_in[s], 16)
            for hh in range(2):
                for c, w in enumerate(("w_ff_gate", "w_ff_up")):
                    sp.dma_start(m.ring[:, 2 + 2 * hh + c], w_block(I[w][0], hh * P)).then_inc(m.w_in[2 + 2 * hh + c], 16)

        @block.gpsimd
        def _(pool):
            pool.memset(ones, 1.0 / D).then_inc(pre, 1)
            pool.memset(m.acc[:, :], 0.0).then_inc(acc_ok, 1)
            pool.wait_ge(acc_ok, 1)
            pool.sem_inc(acc_ok, 1)
            with pool.Fori(0, KD // 2) as it:
                for t in range(6):
                    n = t % 3
                    a = m.acc[:, n * NW:(n + 1) * NW]
                    pool.wait_ge(sq_ok, it * 6 + (t + 1))
                    pool.wait_ge(acc_ok, it * 6 + (t + 2))
                    pool.tensor_tensor(a, a, sq[t % 4], ALU.add).then_inc(acc_ok, 1)
            pool.wait_ge(ss_mm, 1)
            pool.memset(m.acc[:, 0:SEQ], 0.0).then_inc(acc2, 1)
            for g, (h, k) in enumerate(groups):
                a = m.acc[:, 512 * h:512 * (h + 1)]
                pool.wait_ge(sq2_ok, g + 1)
                pool.wait_ge(acc2, g + 1)
                pool.tensor_tensor(a, a, sq2[g % 4], ALU.add).then_inc(acc2, 1)

        @block.tensor
        def _(pe):
            with pe.Fori(0, KD // 2) as it:
                for s in range(2):
                    pe.wait_ge(m.w_in[s], it * 16 + 16 * (l0[s] + 1))
                    for n in range(NN):
                        pe.wait_ge(bank[3 * s + n], it + 1)
                        ins = product(pe, ps[:, 3 * s + n, 0:NW], m.ring[:, s], lambda k: m.merged[:, k, n * NW:(n + 1) * NW])
                        if n < NN - 1:
                            ins.then_inc(summed, 1)
                    ins.then_inc(m.w_used, 1)
            pe.wait_ge(pre, 1)
            pe.wait_ge(acc_ok, 2 + 3 * KD)
            for b in range(3):
                pe.wait_ge(bank[b], KD // 2 + 1)
                ins = pe.matmul(ps[:, b, 0:NW], ones, m.acc[:, b * NW:(b + 1) * NW], start=True, stop=True)
            ins.then_inc(ss_mm, 1)
            pe.wait_ge(x_in, 32)
            for b in range(3, 6):
                pe.wait_ge(bank[b], KD // 2 + 1)
            for g, (h, k) in enumerate(groups):
                if g >= 4:
                    pe.wait_ge(x2_ok, g - 3)
                for i in range(4):
                    ins = pe.transpose(ps[:, 4 + g % 4, i * P:(i + 1) * P], xr[:, 4 * h + i, k * P:(k + 1) * P], m.ident[:, :])
                ins.then_inc(xT, 1)
            for k in range(KD):
                ins = pe.transpose(ps[:, 3, k * ST:(k + 1) * ST], xs[:, k * P:(k + 1) * P], m.ident[0:ST, 0:ST])
            ins.then_inc(xT, 1)
            pe.wait_ge(acc2, G + 1)
            pe.wait_ge(x2_ok, G + 2)
            pe.wait_ge(r_ok, 3)
            for b in range(3):
                ins = pe.matmul(ps[:, b, 0:NW], ones, m.acc[:, b * NW:(b + 1) * NW], start=True, stop=True)
            ins.then_inc(ss_mm, 1)

        @block.scalar
        def _(act):
            with act.Fori(0, KD // 2) as it:
                for t in range(6):
                    s, n = t // 3, t % 3
                    if n < NN - 1:
                        act.wait_ge(summed, it * 4 + (2 * s + n + 1))
                    else:
                        act.wait_ge(m.w_used, it * 2 + (u0 + s + 1))
                    act.wait_ge(acc_ok, it * 6 + (t + 1))
                    act.activation(sq[t % 4], ps[:, t, 0:NW], ACT.Square).then_inc(sq_ok, 1)
            act.wait_ge(r_ok, 2)
            act.activation(rst, rst, ACT.Sqrt).then_inc(r_ok, 1)
            for g, (h, k) in enumerate(groups):
                act.wait_ge(x2_ok, g + 1)
                if g >= 4:
                    act.wait_ge(acc2, g - 2)
                act.activation(sq2[g % 4], m.x2T[:, k, 512 * h:512 * (h + 1)], ACT.Square).then_inc(sq2_ok, 1)
            act.wait_ge(x2_ok, G + 1)
            act.activation(sqs, m.x2T[:, :, SEQ:T], ACT.Square).then_inc(sq2_ok, 1)
            act.wait_ge(r_ok, 5)
            act.activation(rst, rst, ACT.Sqrt).then_inc(r_ok, 1)
            for g, (h, k) in enumerate(groups):
                v = m.hT[:, k, 512 * h:512 * (h + 1)]
                act.wait_ge(n_ok, g + 1)
                act.activation(v, v, ACT.Identity, scale=m.modT[:, SC2 + k, 0:1], bias=m.modT[:, SH2 + k, 0:1]).then_inc(
                    h_ok, 1)

        @block.vector
        def _(dve):
            steps = [0]

            def chain(ins):
                steps[0] += 1
                ins.then_inc(own, 1)
                dve.wait_ge(own, steps[0])

            def rstd():
                for b in range(3):
                    ins = dve.tensor_scalar(rst[:, b * NW:(b + 1) * NW], ps[:, b, 0:NW], EPS, None, ALU.add)
                    if b < 2:
                        ins.then_inc(own, 1)
                        steps[0] += 1
                ins.then_inc(r_ok, 1)

            for b in range(6):
                dve.sem_inc(bank[b], 1)
            with dve.Fori(0, KD // 2) as it:
                for t in range(6):
                    s, n = t // 3, t % 3
                    dve.wait_ge(sq_ok, it * 6 + (t + 1))
                    dve.tensor_copy(m.x2T[:, bass.ds(it * 2 + s, 1), n * NW:(n + 1) * NW], ps[:, t:t + 1, 0:NW]).then_inc(
                        bank[t], 1)
            dve.wait_ge(ss_mm, 1)
            rstd()
            dve.wait_ge(own, steps[0])
            dve.wait_ge(r_ok, 1)
            dve.reciprocal(rst, rst).then_inc(r_ok, 1)
            dve.wait_ge(r_ok, 3)
            for g, (h, k) in enumerate(groups):
                v = m.x2T[:, k, 512 * h:512 * (h + 1)]
                chain(dve.tensor_tensor(v, v, rst[:, 512 * h:512 * (h + 1)], ALU.mult))
                dve.wait_ge(xT, g + 1)
                dve.scalar_tensor_tensor(out=v, in0=v, scalar=m.modT[:, GA1 + k, 0:1], in1=ps[:, 4 + g % 4, :],
                                         op0=ALU.mult, op1=ALU.add).then_inc(x2_ok, 1)
            v = m.x2T[:, :, SEQ:T]
            vb = v.rearrange("p k (b s) -> p k b s", s=DS)
            chain(dve.tensor_tensor(v, v, rst[:, SEQ:T].unsqueeze(1).to_broadcast([P, KD, ST]), ALU.mult))
            chain(dve.tensor_tensor(vb, vb, per_batch(m, GA1), ALU.mult))
            dve.wait_ge(xT, G + 1)
            dve.tensor_tensor(v, v, ps[:, 3, 0:KD * ST].rearrange("p (k t) -> p k t", t=ST), ALU.add).then_inc(x2_ok, 1)
            dve.wait_ge(sq2_ok, G + 1)
            dve.tensor_reduce(m.acc[:, SEQ:T], sqs.rearrange("p k t -> p t k"), X, ALU.add).then_inc(x2_ok, 1)
            dve.wait_ge(ss_mm, 2)
            rstd()
            dve.wait_ge(own, steps[0])
            dve.wait_ge(r_ok, 4)
            dve.reciprocal(rst, rst).then_inc(r_ok, 1)
            dve.wait_ge(r_ok, 6)
            for g, (h, k) in enumerate(groups):
                dve.tensor_tensor(m.hT[:, k, 512 * h:512 * (h + 1)], m.x2T[:, k, 512 * h:512 * (h + 1)],
                                  rst[:, 512 * h:512 * (h + 1)], ALU.mult).then_inc(n_ok, 1)
            hs = m.hT[:, :, SEQ:T]
            hb = hs.rearrange("p k (b s) -> p k b s", s=DS)
            chain(dve.tensor_tensor(hs, v, rst[:, SEQ:T].unsqueeze(1).to_broadcast([P, KD, ST]), ALU.mult))
            chain(dve.tensor_tensor(hb, hb, per_batch(m, SC2), ALU.mult))
            dve.tensor_tensor(hb, hb, per_batch(m, SH2), ALU.add).then_inc(n_ok, 1)
    m.used += KD
    m.loads = [l0[s] + (KD // 2 if s < 2 else 0) for s in range(SLOTS)]


def stage_ffn_up(m, I, O):
    nc, ps = m.nc, m.ps
    u0, l0 = m.used, m.loads
    R = m.rest
    sg = [R[:, NW * b:NW * (b + 1)] for b in range(6)]
    step_mm, sig, mid = m.sem("hidden_summed"), m.sem("hidden_sigmoid"), m.sem("hidden_silu")
    bank = m.sem("hidden_banks_free")
    IT = KF // 2

    with nc.Block() as block:
        @block.sync
        def _(sp):
            with sp.Fori(1, IT) as it:
                for hh in range(2):
                    for c, w in enumerate(("w_ff_gate", "w_ff_up")):
                        slot = 2 + 2 * hh + c
                        sp.wait_ge(m.w_used, it * 4 + (u0 + 2 * hh + c - 3))
                        sp.dma_start(m.ring[:, slot], dyn_block(I[w][0], it * 2 + hh)).then_inc(m.w_in[slot], 16)
            for u in range(2):
                for c in range(3):
                    slot = 3 * u + c
                    if slot >= 2:
                        sp.wait_ge(m.w_used, u0 + 2 * KF - 4 + slot - 2 + 1)
                    load_down(sp, m, I, u, c, slot)

        @block.tensor
        def _(pe):
            with pe.Fori(0, IT) as it:
                for hh in range(2):
                    for c in range(2):
                        pe.wait_ge(m.w_in[2 + 2 * hh + c], it * 16 + 16 * (l0[2 + 2 * hh + c] + 1))
                    for n in range(NN):
                        t = 3 * hh + n
                        pe.wait_ge(bank, it * 6 + (t + 1))
                        last = [product(pe, ps[:, 2 * n + c, 0:NW], m.ring[:, 2 + 2 * hh + c],
                                        lambda k: m.hT[:, k, n * NW:(n + 1) * NW]) for c in range(2)]
                        if n < NN - 1:
                            last[1].then_inc(step_mm, 1)
                        else:
                            for x in last:
                                x.then_inc(m.w_used, 1)

        @block.scalar
        def _(act):
            with act.Fori(0, IT) as it:
                for hh in range(2):
                    for n in range(NN):
                        if n < NN - 1:
                            act.wait_ge(step_mm, it * 4 + (2 * hh + n + 1))
                        else:
                            act.wait_ge(m.w_used, it * 4 + (u0 + 2 * hh + 2))
                        act.activation(sg[3 * hh + n], ps[:, 2 * n, 0:NW], ACT.Sigmoid).then_inc(sig, 1)

        @block.vector
        def _(dve):
            dve.sem_inc(bank, 3)
            with dve.Fori(0, IT) as it:
                for hh in range(2):
                    for n in range(NN):
                        t = 3 * hh + n
                        dve.wait_ge(sig, it * 6 + (t + 1))
                        dve.tensor_tensor(sg[t], sg[t], ps[:, 2 * n, 0:NW], ALU.mult).then_inc(mid, 1)
                        dve.wait_ge(mid, it * 6 + (t + 1))
                        dve.tensor_tensor(m.guT[:, bass.ds(it * 2 + hh, 1), n * NW:(n + 1) * NW],
                                          sg[t].unsqueeze(1), ps[:, 2 * n + 1:2 * n + 2, 0:NW], ALU.mult).then_inc(bank, 1)
    m.used += 2 * KF
    m.loads = [l0[s] + (IT if s >= 2 else 0) for s in range(SLOTS)]


DOWN = [(0, 8), (8, 16), (16, KF)]


def load_down(sp, m, I, u, c, slot):
    a, b = DOWN[c]
    v = I["w_ff_down"][0].rearrange("(k p) n -> p k n", p=P)[:, a:b, bass.ds(u * P, P)]
    sp.dma_start(m.ring[:, slot, 0:b - a, :], v).then_inc(m.w_in[slot], 16)


def stage_ffn_down(m, I, O):
    nc, ps = m.nc, m.ps
    u0, l0 = m.used, m.loads
    R = m.rest
    rst, ones = R[:, 0:T], R[:, T:T + P]
    sq = [R[:, T + P + NW * b:T + P + NW * (b + 1)] for b in range(4)]
    rows = [m.guT[:, 0:2, :].rearrange("p u t -> p (u t)")[:, D * i:D * (i + 1)] for i in range(2)]
    rows += [m.guT[:, 2:4, :].rearrange("p u t -> p (u t)")[:, D * i:D * (i + 1)] for i in range(2)]
    summed, bank = m.sem("f_tile_summed"), [m.sem(f"f_bank_free{b}") for b in range(6)]
    sq_ok, acc_ok, ss_mm, r_ok = m.sem("f_squares"), m.sem("f_squares_added"), m.sem("f_mean_squares"), m.sem("f_rstd_steps")
    own, pre, y_ok, yT, y_row = m.sem("f_vector_chain"), m.sem("f_constants"), m.sem("y_ready"), m.sem("y_turned"), m.sem("y_rows")
    stored = [m.sem(f"y_stored{i}") for i in range(4)]
    groups = [(h, k) for h in range(2) for k in range(KD)]
    G = len(groups)

    with nc.Block() as block:
        @block.sync
        def _(sp):
            with sp.Fori(1, KD // 2) as it:
                for u in range(2):
                    for c in range(3):
                        sp.wait_ge(m.w_used, it * 6 + (u0 + 3 * u + c - 5))
                        load_down(sp, m, I, it * 2 + u, c, 3 * u + c)
            for i in range(TT):
                sp.wait_ge(y_row, 2 * i + 2)
                if i < QT:
                    sp.dma_start(O["y_p"][0, i * P:(i + 1) * P, :], rows[i % 4]).then_inc(stored[i % 4], 16)
                else:
                    sp.dma_start(O["y_s"].rearrange("b s d -> (b s) d"), rows[i % 4][0:ST, :]).then_inc(stored[i % 4], 16)
            for i in range(4):
                sp.wait_ge(stored[i], 16 * len(range(i, TT, 4)))

        @block.gpsimd
        def _(pool):
            pool.memset(ones, 1.0 / D).then_inc(pre, 1)
            pool.memset(m.acc[:, :], 0.0).then_inc(acc_ok, 1)
            pool.wait_ge(acc_ok, 1)
            pool.sem_inc(acc_ok, 1)
            with pool.Fori(0, KD // 2) as it:
                for t in range(6):
                    n = t % 3
                    a = m.acc[:, n * NW:(n + 1) * NW]
                    pool.wait_ge(sq_ok, it * 6 + (t + 1))
                    pool.wait_ge(acc_ok, it * 6 + (t + 2))
                    pool.tensor_tensor(a, a, sq[t % 4], ALU.add).then_inc(acc_ok, 1)

        @block.tensor
        def _(pe):
            with pe.Fori(0, KD // 2) as it:
                for s in range(2):
                    for c, (a, b) in enumerate(DOWN):
                        pe.wait_ge(m.w_in[3 * s + c], it * 16 + 16 * (l0[3 * s + c] + 1))
                        for n in range(NN):
                            if c == 0:
                                pe.wait_ge(bank[3 * s + n], it + 1)
                            ins = product(pe, ps[:, 3 * s + n, 0:NW], m.ring[:, 3 * s + c, 0:b - a],
                                          lambda k: m.guT[:, a + k, n * NW:(n + 1) * NW], first=c == 0, last=c == 2)
                            if c == 2 and n < NN - 1:
                                ins.then_inc(summed, 1)
                        ins.then_inc(m.w_used, 1)
            pe.wait_ge(pre, 1)
            pe.wait_ge(acc_ok, 2 + 3 * KD)
            for b in range(3):
                pe.wait_ge(bank[b], KD // 2 + 1)
                ins = pe.matmul(ps[:, b, 0:NW], ones, m.acc[:, b * NW:(b + 1) * NW], start=True, stop=True)
            ins.then_inc(ss_mm, 1)
            for b in range(3, 6):
                pe.wait_ge(bank[b], KD // 2 + 1)
            pe.wait_ge(r_ok, 3)
            for i in range(TT):
                n = P if i < QT else ST
                pe.wait_ge(y_ok, G // 2 * (i // 4 + 1) if i < QT else G + 1)
                if i >= 4:
                    pe.wait_ge(y_row, 2 * (i - 3))
                for k in range(KD):
                    ins = pe.transpose(ps[0:n, 2 * (i % 4) + k // 4, (k % 4) * P:(k % 4 + 1) * P],
                                       m.x2T[:, k, i * P:i * P + n], m.ident[:, :])
                ins.then_inc(yT, 1)

        @block.scalar
        def _(act):
            with act.Fori(0, KD // 2) as it:
                for t in range(6):
                    s, n = t // 3, t % 3
                    if n < NN - 1:
                        act.wait_ge(summed, it * 4 + (2 * s + n + 1))
                    else:
                        act.wait_ge(m.w_used, it * 6 + (u0 + 3 * s + 3))
                    act.wait_ge(acc_ok, it * 6 + (t + 1))
                    act.activation(sq[t % 4], ps[:, t, 0:NW], ACT.Square).then_inc(sq_ok, 1)
            act.wait_ge(r_ok, 2)
            act.activation(rst, rst, ACT.Sqrt).then_inc(r_ok, 1)
            for i in range(TT):
                n = P if i < QT else ST
                act.wait_ge(yT, i + 1)
                if i >= 4:
                    act.wait_ge(stored[i % 4], 16 * (i // 4))
                for c in range(2):
                    act.activation(rows[i % 4][0:n, 512 * c:512 * (c + 1)], ps[0:n, 2 * (i % 4) + c, :], ACT.Copy).then_inc(
                        y_row, 1)

        @block.vector
        def _(dve):
            steps = [0]

            def chain(ins):
                steps[0] += 1
                ins.then_inc(own, 1)
                dve.wait_ge(own, steps[0])

            for b in range(6):
                dve.sem_inc(bank[b], 1)
            with dve.Fori(0, KD // 2) as it:
                for t in range(6):
                    s, n = t // 3, t % 3
                    dve.wait_ge(sq_ok, it * 6 + (t + 1))
                    dve.tensor_copy(m.hT[:, bass.ds(it * 2 + s, 1), n * NW:(n + 1) * NW], ps[:, t:t + 1, 0:NW]).then_inc(
                        bank[t], 1)
            dve.wait_ge(ss_mm, 1)
            for b in range(3):
                ins = dve.tensor_scalar(rst[:, b * NW:(b + 1) * NW], ps[:, b, 0:NW], EPS, None, ALU.add)
                if b < 2:
                    ins.then_inc(own, 1)
                    steps[0] += 1
            ins.then_inc(r_ok, 1)
            dve.wait_ge(own, steps[0])
            dve.wait_ge(r_ok, 1)
            dve.reciprocal(rst, rst).then_inc(r_ok, 1)
            dve.wait_ge(r_ok, 3)
            for g, (h, k) in enumerate(groups):
                f, v = m.hT[:, k, 512 * h:512 * (h + 1)], m.x2T[:, k, 512 * h:512 * (h + 1)]
                chain(dve.tensor_tensor(f, f, rst[:, 512 * h:512 * (h + 1)], ALU.mult))
                dve.scalar_tensor_tensor(out=v, in0=f, scalar=m.modT[:, GA2 + k, 0:1], in1=v, op0=ALU.mult,
                                         op1=ALU.add).then_inc(y_ok, 1)
            f, v = m.hT[:, :, SEQ:T], m.x2T[:, :, SEQ:T]
            fb = f.rearrange("p k (b s) -> p k b s", s=DS)
            chain(dve.tensor_tensor(f, f, rst[:, SEQ:T].unsqueeze(1).to_broadcast([P, KD, ST]), ALU.mult))
            chain(dve.tensor_tensor(fb, fb, per_batch(m, GA2), ALU.mult))
            dve.tensor_tensor(v, v, f, ALU.add).then_inc(y_ok, 1)


OUTS = [("y_p", (1, SEQ, D)), ("y_s", (NB, DS, D)),
        ("cmp_p", (1, 1, SEQ, 2, 2, HD)), ("cmp_s", (1, NB, DS, 2, 2, HD)),
        ("slc_p", (1, 1, SEQ, 2, 2, HD)), ("slc_s", (1, NB, DS, 2, 2, HD)),
        ("win_p", (1, 1, WIN, 2, 2, HD)), ("win_s", (1, NB, WIN, 2, 2, HD)),
        ("gla_p", (1, 1, GH, GDK, GDV)), ("gla_s", (1, NB, GH, GDK, GDV))]


STAGES = [stage_prepare, stage_project, stage_gla, stage_compress, stage_samples, stage_attention, stage_merge,
          stage_mix, stage_ffn_up, stage_ffn_down]


def build(nc, I, O, probe=None, upto=len(STAGES)):
    with ExitStack() as ctx:
        m = allocate(nc, ctx)
        m.n_pool = I["cache_cmp_kv"].shape[1]
        for stage in STAGES[:upto]:
            with nc.cleanup_on_exit():
                stage(m, I, O)
        if probe is not None:
            probe(m)


def kernel(**inputs):
    nc = bacc.Bacc("TRN2", target_bir_lowering=False, num_devices=1)
    arrays, I, O = {}, {}, {}
    for name, a in inputs.items():
        a = np.ascontiguousarray(a)
        arrays["in_" + name] = a
        I[name] = nc.dram_tensor("in_" + name, a.shape, mybir.dt.from_np(a.dtype), kind="ExternalInput").ap()
    for name, shape in OUTS:
        O[name] = nc.dram_tensor("out_" + name, shape, F32, kind="ExternalOutput").ap()
    build(nc, I, O)
    r = run_bass_kernel_spmd(nc, [arrays], core_ids=[0])
    return tuple(r.results[0]["out_" + name] for name, _ in OUTS)
```

```python
from contextlib import ExitStack

import numpy as np
import concourse.bacc as bacc
import concourse.bass as bass
from concourse import mybir
from concourse.bass_utils import run_bass_kernel_spmd

F32 = mybir.dt.float32
I32 = mybir.dt.int32
ALU = mybir.AluOpType
ACT = mybir.ActivationFunctionType
X = mybir.AxisListType.X

P = 128
D = 1024
KD = D // P
SEQ = 1024
QT = SEQ // P
NB = 8
DS = 4
ST = NB * DS
T = SEQ + ST
TT = QT + 1
NW = T // 3
NN = 3
PAST = 1024
PAGE = 128
NPAGE = PAST // PAGE
WIN = 512
HD = 64
HP = 4
GD = 2 * HD
GDK = 64
GDV = 128
GH = 4
RANK = 16
CH = 64
DFF = 2816
KF = DFF // P
NCOND = 1 + NB
EPS = 1e-6
NEG = -1e30
CL = 32
CS = 16
NCMP = PAST // CS - 1
SLC = 64
NSLC = PAST // SLC
SLOTS = 6

C_Q = 0
C_KVC = 512
C_KVS = C_KVC + 256
C_KVW = C_KVS + 256
C_GN = C_KVW + 256
C_QG = C_GN + 24
C_KG = C_QG + 256
C_VG = C_KG + 256
C_AG = C_VG + 512
C_RG = C_AG + RANK
C_MG = C_RG + 512

Z_Q, Z_KC, Z_KS, Z_KW, Z_QG, Z_KG, Z_VC, Z_VS, Z_VW, Z_VG, ZU = 0, 4, 5, 6, 7, 9, 11, 12, 13, 14, 18
Z_TAIL = Z_VS
SH1, SC1, GA1, SH2, SC2, GA2 = (8 * i for i in range(6))
V_BADA, V_GPRE, V_GPOST, V_GPRE2, V_GPOST2, V_GNORM, V_B1K, V_B1V, V_N = 0, 48, 56, 64, 72, 80, 81, 82, 83


class Box:
    pass


def z_columns():
    return ([C_KVC, C_KVS, C_KVW] + [C_QG, C_QG + P, C_KG, C_KG + P]
            + [C_KVC + P, C_KVS + P, C_KVW + P] + [C_VG + P * i for i in range(4)])


def allocate(nc, ctx):
    m = Box()
    m.nc = nc

    def sb(name, shape, dt=F32):
        return ctx.enter_context(nc.sbuf_tensor(name, shape, dt))

    def sem(name):
        return nc.alloc_semaphore(name)

    m.sb, m.sem = sb, sem
    m.ps = ctx.enter_context(nc.psum_tensor("ps", [P, 8, 512], F32))
    m.ring = sb("ring", [P, SLOTS, KD, P])
    m.hT = sb("hT", [P, KD, T])
    WORK = 4352
    sizes = [ZU * T, GH * T, TT * GH * GDV, TT * 2 * GD, WORK]
    at = [sum(sizes[:i]) for i in range(6)]
    m.big = sb("big", [P, at[5]])
    m.zT = m.big[:, 0:at[1]].rearrange("p (u t) -> p u t", t=T)
    m.oglaT = m.big[:, at[1]:at[2]].rearrange("p (h t) -> p h t", t=T)
    m.vg = m.big[:, at[2]:at[3]].rearrange("p (i h v) -> p i h v", i=TT, h=GH)
    m.vtm = m.big[:, at[3]:at[4]].rearrange("p (i b c) -> p i b c", i=TT, b=2)
    m.work = m.big[:, at[4]:at[5]]
    m.merged = m.zT[:, ZU - KD:ZU, :]
    m.x2T = m.zT[:, 0:KD, :]
    m.guT = m.big[:, KD * T:(KD + KF) * T].rearrange("p (u t) -> p u t", t=T)
    m.rest = m.big[:, (KD + KF) * T:at[5]]
    m.modT = sb("modT", [P, 48, NCOND])
    m.vecT = sb("vecT", [P, V_N])
    m.peT = sb("peT", [P, 64])
    m.ident = sb("ident", [P, P])
    m.acc = sb("acc", [P, T])
    m.agT = m.acc[0:32, :]
    m.gnT = sb("gnT", [24, ST])
    m.gates = sb("gates", [P, QT, 24])
    m.osT = sb("osT", [P, HP, ST])
    m.pt = sb("page_ids", [1, NB * NPAGE], I32)
    m.w2 = sb("compress_w2", [P, 2, P])
    m.cbias = sb("compress_bias", [P, 2])
    m.cT = sb("conditions", [P, KD, NCOND])
    m.ada_rows = m.work[0:NCOND, 3500:3756]
    held = m.ring[:, 4:6].rearrange("p s k n -> p (s k n)")
    m.ckT = held[:, 0:(1 + NB) * 64].rearrange("p (b n) -> p b n", n=64)
    m.cvt = held[0:64, 576:576 + (1 + NB) * GD].rearrange("p (b n) -> p b n", n=GD)
    z = m.zT[:, :, :].rearrange("p a b -> p (a b)")
    m.tail = z[:, Z_TAIL * T:ZU * T]
    m.vgf = m.vg[:, :, :, :].rearrange("p i h v -> p (i h v)")
    m.midw = z[:, Z_QG * T:Z_VC * T]
    m.past = [a.rearrange("p (j c) -> p j c", c=2 * GD) for a in (m.vgf[:, 0:2048], m.vgf[:, 2048:4096],
                                                                 m.midw[:, 0:2048], m.midw[:, 2048:4096])]
    m.past_in = [sem(f"past_in_buffer{b}") for b in range(4)]
    m.w_in = [sem(f"weights_in_slot{i}") for i in range(SLOTS)]
    m.w_used = sem("weight_units_used")
    m.loads = [0] * SLOTS
    m.used = 0
    return m


def w_block(w, col, rows=D, n=P):
    return w.rearrange("(k p) n -> p k n", p=P)[:, :rows // P, col:col + n]


def dyn_block(w, unit):
    return w.rearrange("(k p) n -> p k n", p=P)[:, :, bass.ds(unit * P, P)]


def product(pe, out, w, rhs, first=True, last=True):
    nk = w.shape[1]
    for k in range(nk):
        ins = pe.matmul(out, w[:, k, :], rhs(k), start=first and k == 0, stop=last and k == nk - 1)
    return ins


def load_page(sp, m, I, cache, batch, j, out, done):
    page = sp.value_load(m.pt[0:1, bass.ds(batch * NPAGE + j, 1)], min_val=0, max_val=m.n_pool - 1)
    src = I[cache][0].rearrange("n t a g d -> n t (a g d)")[bass.ds(page, 1)]
    sp.dma_start(out, src.rearrange("o t c -> t (o c)")).then_inc(done, 16)


EARLY = 16
LATER = 48 - EARLY


def load_ada_unit(e, m, I, unit, slot, done):
    e.dma_start(m.ring[:, slot], dyn_block(I["w_ada"][0], unit)).then_inc(done, 16)


def ada_product(pe, m, pair, k0=0):
    for k in range(KD):
        ins = pe.matmul(m.ps[0:NCOND, 7, 0:2 * P], m.cT[:, k, :], m.ring[:, 2 * pair:2 * pair + 2, k, :],
                        start=k == 0, stop=k == KD - 1)
    return ins


def ada_turn(pe, m):
    for c in range(2):
        ins = pe.transpose(m.ps[:, 7, 256 + c * NCOND:256 + (c + 1) * NCOND], m.ada_rows[:, c * P:(c + 1) * P],
                           m.ident[0:NCOND, 0:NCOND])
    return ins


def ada_keep(act, m, unit):
    return act.activation(m.modT[:, bass.ds(unit, 2), :],
                          m.ps[:, 7, 256:256 + 2 * NCOND].rearrange("p (u c) -> p u c", c=NCOND), ACT.Copy)


def ada_rows(act, m):
    return act.activation(m.ada_rows[:, :], m.ps[0:NCOND, 7, 0:2 * P], ACT.Copy)


def modulation(m, dve, a, b, step):
    def col(v, n=8):
        return m.vecT[:, v:v + n].unsqueeze(2).to_broadcast([P, n, NCOND])

    dve.tensor_tensor(m.modT[:, a:b, :], m.modT[:, a:b, :], col(V_BADA + a, b - a), ALU.add).then_inc(step, 1)
    dve.wait_ge(step, 1)
    n = 1
    for sec, g, plus in ((SC1, V_GPRE, 1.0), (GA1, V_GPOST, 0.0), (SC2, V_GPRE2, 1.0), (GA2, V_GPOST2, 0.0)):
        if a <= sec < b:
            v = m.modT[:, sec:sec + 8, :]
            dve.scalar_tensor_tensor(out=v, in0=v, scalar=plus, in1=col(g), op0=ALU.add, op1=ALU.mult).then_inc(step, 1)
            n += 1
    dve.wait_ge(step, n)


def first_layer_in_ring(m):
    return m.ring[:, 0:4].rearrange("p s k n -> p (s k n)").rearrange("p (t h) -> p t h", h=P)


def load_first_layer(sp, w, to, g, done):
    r = slice(64 * g, 64 * g + 64)
    sp.dma_start(to[r, :, r], w[0].rearrange("(t d) h -> d t h", d=HD)).then_inc(done, 16)


def gelu_act(act, sums, x, u, bias, r, cmp_mm, g_act, g_dve):
    act.wait_ge(cmp_mm, r + 1)
    act.activation(x, sums, ACT.Identity, bias=bias).then_inc(g_act, 1)
    act.wait_ge(g_dve, 4 * r + 3 if isinstance(r, int) else r * 4 + 3)
    act.activation(u, u, ACT.Tanh, scale=0.7978845608028654).then_inc(g_act, 1)


def gelu_dve(dve, x, u, h, r, g_act, g_dve):
    dve.wait_ge(g_act, r * 2 + 1)
    dve.tensor_tensor(u, x, x, ALU.mult).then_inc(g_dve, 1)
    dve.wait_ge(g_dve, r * 4 + 1)
    dve.tensor_scalar(u, u, 0.044715, 1.0, ALU.mult, ALU.add).then_inc(g_dve, 1)
    dve.wait_ge(g_dve, r * 4 + 2)
    dve.tensor_tensor(u, u, x, ALU.mult).then_inc(g_dve, 1)
    dve.wait_ge(g_act, r * 2 + 2)
    dve.scalar_tensor_tensor(out=h, in0=u, scalar=1.0, in1=x, op0=ALU.add, op1=ALU.mult).then_inc(g_dve, 1)


def stage_prepare(m, I, O):
    nc, ps = m.nc, m.ps
    xs = m.zT[:, 0:9, 0:D]
    rows = m.work[:, 0:P]
    pes = m.work[0:64, P:2 * P]
    cr = m.work[0:NCOND, 1024:2048]
    junk = m.work[:, 2400:2400 + D]
    ss, ms, rec, rstd = (m.work[:, 3432 + 16 * i:3432 + 16 * i + TT] for i in range(4))
    og = m.oglaT[:, :, :].rearrange("p a b -> p (a b)")
    w1 = [a[:, 0:4096].rearrange("p (t h) -> p t h", h=P) for a in (m.vgf, m.tail)]
    pages = [a.rearrange("p (j c) -> p j c", c=2 * GD) for a in
             (m.tail[:, 4096:6144], m.midw[:, 9 * T - Z_QG * T:9 * T - Z_QG * T + 2048])]
    kt = og[:, 0:2048].rearrange("p (t b n) -> p t b n", t=CS, b=2)
    x, u, h = (og[:, 2048 + P * i:2048 + P * i + 2 * 63].rearrange("p (b n) -> p b n", b=2) for i in range(3))

    vec_in, c_in, x_in = m.sem("vectors_in"), m.sem("conditions_in"), m.sem("x_in")
    id0, rows_T, rows_out = m.sem("ident_ready"), m.sem("rows_transposed"), m.sem("row_columns_ready")
    mod_step, rows_ok, turned_last = m.sem("modulation_steps"), m.sem("modulation_rows"), m.sem("modulation_turned")
    sq_done, ms_done, sqrt_done, xn_done = (m.sem("squares_done"), m.sem("mean_square_steps"), m.sem("rstd_ready"),
                                            [m.sem("even_x_scaled"), m.sem("odd_x_scaled")])
    xT_done, ev_act, ev_dve = m.sem("x_tiles_transposed"), m.sem("h_written_by_act"), m.sem("h_written_by_dve")
    w_set = [m.sem("key_diagonals_zeroed"), m.sem("value_diagonals_zeroed")]
    w_ok = m.sem("compress_weights_in")
    pt_in, pages_in = m.sem("page_table_in"), [m.sem(f"past_pages_in{b}") for b in range(2)]
    turned = [m.sem(f"pages_turned{b}") for b in range(2)]
    kt_done, cmp_mm, bias_mm, bias_done = (m.sem("tokens_laid_out"), m.sem("compress_sums"), m.sem("bias_sums"),
                                           m.sem("bias_ready"))
    g_act, g_dve, out_mm = m.sem("gelu_by_act"), m.sem("gelu_by_dve"), m.sem("compressed_products")
    groups = [(j, h) for h in range(2) for j in range(KD)]
    NP = NB // 2
    hf = m.hT[:, :, :].rearrange("p a b -> p (a b)")
    wp = [hf[:, 4096 * kv:4096 * (kv + 1)].rearrange("p (t h) -> p t h", h=P) for kv in range(2)]
    pos = [m.work[:, 640 + P * kv:640 + P * (kv + 1)] for kv in range(2)]
    one = m.work[:, 900:901]
    pos_mul, pos_sum = m.sem("position_products"), m.sem("position_sums")
    assert 2 * 2 * NP == EARLY

    with nc.Block() as block:
        @block.sync
        def _(sp):
            sp.dma_start(m.pt[:, :], I["page_table"].rearrange("b j -> (b j)").unsqueeze(0)).then_inc(pt_in, 16)
            for r0, a, n in ((V_BADA, I["b_ada"], 48), (V_GPRE, I["g_pre_mix"], 8), (V_GPOST, I["g_post_mix"], 8),
                             (V_GPRE2, I["g_pre_ffn"], 8), (V_GPOST2, I["g_post_ffn"], 8)):
                sp.dma_start(rows[r0:r0 + n, :], a.rearrange("o (a b) -> (o a) b", b=P)).then_inc(vec_in, 16)
            sp.dma_start(rows[V_GNORM:V_GNORM + 1, :], I["gla_norm_g"]).then_inc(vec_in, 16)
            for half in range(2):
                c = slice(half * HD, (half + 1) * HD)
                sp.dma_start(rows[V_B1K:V_B1K + 1, c], I["cmp_b1_k"]).then_inc(vec_in, 16)
                sp.dma_start(rows[V_B1V:V_B1V + 1, c], I["cmp_b1_v"]).then_inc(vec_in, 16)
                sp.dma_start(pes[0:32, c], I["cmp_pe_k"][0]).then_inc(vec_in, 16)
                sp.dma_start(pes[32:64, c], I["cmp_pe_v"][0]).then_inc(vec_in, 16)
            sp.dma_start(cr[0:1, :], I["c_prompt"]).then_inc(c_in, 16)
            sp.dma_start(cr[1:NCOND, :], I["c_sample"]).then_inc(c_in, 16)
            sp.wait_ge(pt_in, 16)

            def pair(it, first):
                for b in range(2):
                    if not first:
                        sp.wait_ge(turned[b], it * 2)
                    for j in range(NPAGE):
                        load_page(sp, m, I, "cache_cmp_kv", it * 2 + b, j, pages[b][:, j, :], pages_in[b])
                for s in range(4):
                    if not first:
                        sp.wait_ge(m.w_used, it * 4 + (s - 3))
                    load_ada_unit(sp, m, I, it * 4 + s, s, m.w_in[s])

            pair(0, True)
            with sp.Fori(1, NP) as it:
                pair(it, False)
            for s in range(2):
                sp.wait_ge(m.w_used, EARLY - 4 + s + 1)
                load_query_unit(sp, m, I, s, s)

        @block.gpsimd
        def _(pool):
            pool.memset(m.ident[:, :], 0.0).then_inc(id0, 1)
            pool.wait_ge(id0, 1)
            pool.affine_select(out=m.ident[:, :], in_=m.ident[:, :], compare_op=ALU.not_equal, fill=1.0, base=0,
                               pattern=[[-1, P]], channel_multiplier=1).then_inc(id0, 1)
            pool.wait_ge(id0, 2)
            for i, w in enumerate((w1[0], m.w2[:, 0:1, :])):
                if i:
                    pool.wait_ge(w_set[0], 2)
                for g in range(2):
                    pool.memset(w[64 * g:64 * g + 64, :, 64 - 64 * g:128 - 64 * g], 0.0).then_inc(w_set[0], 1)
            pool.wait_ge(w_ok, 128)
            pool.wait_ge(rows_out, 3)
            pool.dma_start(xs[:, 0:QT, :], I["x_prompt"][0].rearrange("(i p) d -> p i d", p=P)).then_inc(x_in, 16)
            pool.dma_start(xs[0:ST, QT, :], I["x_sample"].rearrange("b s d -> (b s) d")).then_inc(x_in, 16)
            for kv in range(2):
                if kv:
                    pool.wait_ge(pos_mul, 1)
                pool.tensor_tensor(wp[kv], w1[kv], m.peT[:, 32 * kv:32 * kv + 32].unsqueeze(2).to_broadcast([P, CL, P]),
                                   ALU.mult).then_inc(pos_mul, 1)

        @block.tensor
        def _(pe):
            pe.wait_ge(id0, 2)
            pe.wait_ge(vec_in, 16 * 14)
            pe.transpose(ps[:, 6, 0:V_N], rows[0:V_N, :], m.ident[0:V_N, 0:V_N])
            pe.transpose(ps[:, 6, 128:192], pes, m.ident[0:64, 0:64])
            pe.wait_ge(c_in, 32)
            for k in range(KD):
                ins = pe.transpose(ps[:, 6, 256 + 16 * k:256 + 16 * k + NCOND], cr[:, k * P:(k + 1) * P],
                                   m.ident[0:NCOND, 0:NCOND])
            ins.then_inc(rows_T, 1)
            pe.wait_ge(rows_out, 3)

            def turn(kv, it):
                for b in range(2):
                    if kv == 0:
                        pe.wait_ge(pages_in[b], it * 128 + 128)
                    for j in range(NPAGE):
                        ins = pe.transpose(ps[:, 2 * b + j // 4, (j % 4) * P:(j % 4 + 1) * P],
                                           pages[b][:, j, kv * GD:(kv + 1) * GD], m.ident[:, :])
                    ins.then_inc(turned[b], 1)
                for s in range(2 * kv, 2 * kv + 2):
                    pe.wait_ge(m.w_in[s], it * 16 + 16)
                first = kv == 0 and isinstance(it, int)
                if not first:
                    pe.wait_ge(rows_ok, it * 2 + kv)
                ins = ada_product(pe, m, kv)
                if not first:
                    ins = ada_turn(pe, m)
                ins.then_inc(m.w_used, 2)

            def sums(kv, it):
                pe.wait_ge(kt_done, it * 8 + 4 * (kv + 1))
                for t in range(CL):
                    ins = pe.matmul(ps[:, 4, 0:2 * 63], w1[kv][:, t, :], kt[:, t % CS, :, t // CS:t // CS + 63],
                                    start=t == 0, stop=t == CL - 1)
                ins.then_inc(cmp_mm, 1)

            def outs(kv, it):
                pe.wait_ge(g_dve, it * 8 + 4 * (kv + 1))
                if kv == 0:
                    ins = pe.matmul(ps[:, 5, 0:2 * 63], m.w2[:, 0, :], h, start=True, stop=True)
                else:
                    for b in range(2):
                        ins = pe.matmul(ps[0:63, 5, b * P:(b + 1) * P], h[:, b, :], m.w2[:, 1, :], start=True, stop=True)
                ins.then_inc(out_mm, 1)

            turn(0, 0)
            pe.wait_ge(w_ok, 128)
            sums(0, 0)
            pe.wait_ge(pos_sum, 3)
            for kv in range(2):
                ins = pe.matmul(ps[:, 6, 400 + kv:401 + kv], pos[kv], one, start=True, stop=True)
            ins.then_inc(bias_mm, 1)
            turn(1, 0)
            outs(0, 0)
            sums(1, 0)
            with pe.Fori(1, NP) as it:
                turn(0, it)
                outs(1, it - 1)
                sums(0, it)
                turn(1, it)
                outs(0, it)
                sums(1, it)
            outs(1, NP - 1)
            pe.wait_ge(rows_ok, 2 * NP)
            ada_turn(pe, m).then_inc(turned_last, 1)
            for g, (j, half) in enumerate(groups):
                if g >= 4:
                    pe.wait_ge(ev_act if g % 2 == 0 else ev_dve, (g - 4) // 2 + 1)
                for e in range(2):
                    pe.wait_ge(xn_done[e], 2 * half + 2)
                for i in range(4):
                    ins = pe.transpose(ps[:, g % 4, i * P:(i + 1) * P], xs[:, 4 * half + i, j * P:(j + 1) * P],
                                       m.ident[:, :])
                ins.then_inc(xT_done, 1)
            pe.wait_ge(xn_done[0], 5)
            for j in range(KD):
                ins = pe.transpose(ps[:, 4, j * ST:(j + 1) * ST], xs[0:ST, QT, j * P:(j + 1) * P],
                                   m.ident[0:ST, 0:ST])
            ins.then_inc(xT_done, 1)

        @block.scalar
        def _(act):
            for kv, (wa, wb) in enumerate((("cmp_w1_k", "cmp_w2_k"), ("cmp_w1_v", "cmp_w2_v"))):
                act.wait_ge(w_set[kv], 4)
                for g in range(2):
                    load_first_layer(act, I[wa], w1[kv], g, w_ok)
                    act.dma_start(m.w2[64 * g:64 * g + 64, kv, 64 * g:64 * g + 64], I[wb][0]).then_inc(w_ok, 16)

            def square(i, n):
                act.wait_ge(sq_done, i)
                act.activation(junk[0:n, :].unsqueeze(1), xs[0:n, bass.ds(i, 1), :], ACT.Square,
                               accum_out=ss[0:n, bass.ds(i, 1)]).then_inc(sq_done, 1)

            def round_(kv, it):
                for b in range(2):
                    act.wait_ge(turned[b], it * 2 + (kv + 1))
                    act.activation(kt[:, :, b, 0:32].rearrange("p t n -> p n t"),
                                   ps[:, 2 * b, :].rearrange("p (n t) -> p n t", t=CS), ACT.Copy).then_inc(kt_done, 1)
                act.wait_ge(m.w_used, it * 4 + 2 * (kv + 1))
                if not (kv == 0 and isinstance(it, int) and it == 0):
                    ada_keep(act, m, it * 4 + (2 * kv - 2))
                ada_rows(act, m).then_inc(rows_ok, 1)
                if isinstance(it, int) and it == 0:
                    if kv == 0:
                        act.wait_ge(bias_done, 2)
                    else:
                        act.wait_ge(x_in, 32)
                        act.wait_ge(ms_done, 1)
                        act.activation(junk, xs[:, 0, :], ACT.Square, accum_out=ss[:, 0:1]).then_inc(sq_done, 1)
                        for i in (1, 2):
                            square(i, P)
                else:
                    square(it * 2 + (kv + 1), ST if isinstance(it, int) and 2 * it + kv + 1 == QT else P)
                gelu_act(act, ps[:, 4, 0:2 * 63].rearrange("p (b n) -> p b n", b=2), x, u, m.cbias[:, kv:kv + 1],
                         it * 2 + kv, cmp_mm, g_act, g_dve)

            for kv in range(2):
                round_(kv, 0)
            with act.Fori(1, NP - 1) as it:
                round_(0, it)
                round_(1, it)
            for kv in range(2):
                round_(kv, NP - 1)
            act.wait_ge(turned_last, 1)
            ada_keep(act, m, EARLY - 2).then_inc(turned_last, 1)
            act.wait_ge(ms_done, 3)
            act.activation(rstd, rec, ACT.Sqrt).then_inc(sqrt_done, 1)
            act.wait_ge(sqrt_done, 1)
            for i in range(0, TT, 2):
                n = P if i < QT else ST
                act.activation(xs[0:n, i, :], xs[0:n, i, :], ACT.Copy, scale=rstd[0:n, i:i + 1]).then_inc(xn_done[0], 1)
            act.wait_ge(mod_step, 2)
            for g, (j, half) in enumerate(groups):
                if g % 2 == 0:
                    act.wait_ge(xT_done, g + 1)
                    act.activation(m.hT[:, j, half * 512:(half + 1) * 512], ps[:, g % 4, :], ACT.Identity,
                                   bias=m.modT[:, SH1 + j, 0:1], scale=m.modT[:, SC1 + j, 0:1]).then_inc(ev_act, 1)

        @block.vector
        def _(dve):
            dve.memset(ss, 1.0).then_inc(ms_done, 1)
            dve.memset(one, 1.0).then_inc(pos_sum, 1)
            for w in (w1[1], m.w2[:, 1:2, :]):
                for g in range(2):
                    dve.memset(w[64 * g:64 * g + 64, :, 64 - 64 * g:128 - 64 * g], 0.0).then_inc(w_set[1], 1)
            dve.wait_ge(rows_T, 1)
            dve.tensor_copy(m.vecT[:, :], ps[:, 6, 0:V_N]).then_inc(rows_out, 1)
            dve.tensor_copy(m.peT[:, :], ps[:, 6, 128:192]).then_inc(rows_out, 1)
            dve.tensor_copy(m.cT[:, :, :],
                            ps[:, 6, 256:384].rearrange("p (k c) -> p k c", c=16)[:, :, 0:NCOND]).then_inc(rows_out, 1)
            dve.wait_ge(rows_out, 3)

            def lay_out(kv, it):
                for b in range(2):
                    dve.wait_ge(turned[b], it * 2 + (kv + 1))
                    dve.tensor_copy(kt[:, :, b, 32:64].rearrange("p t n -> p n t"),
                                    ps[:, 2 * b + 1, :].rearrange("p (n t) -> p n t", t=CS)).then_inc(kt_done, 1)

            def write(kv, it):
                dve.wait_ge(out_mm, it * 2 + (kv + 1))
                if kv == 0:
                    dve.tensor_scalar(m.ckT[:, bass.ds(it * 2 + 1, 2), 0:63],
                                      ps[:, 5, 0:2 * 63].rearrange("p (b n) -> p b n", b=2), 0.5, None, ALU.mult)
                else:
                    dve.tensor_scalar(m.cvt[0:63, bass.ds(it * 2 + 1, 2), :],
                                      ps[0:63, 5, 0:2 * P].rearrange("p (b n) -> p b n", b=2), 0.5, None, ALU.mult)

            def bias():
                for kv in range(2):
                    dve.wait_ge(pos_mul, kv + 1)
                    dve.tensor_reduce(pos[kv], wp[kv].rearrange("p t h -> p h t"), X, ALU.add).then_inc(pos_sum, 1)
                dve.wait_ge(bias_mm, 1)
                dve.tensor_tensor(m.cbias[:, :], ps[:, 6, 400:402], m.vecT[:, V_B1K:V_B1K + 2], ALU.add).then_inc(
                    bias_done, 2)

            def pair(it, first):
                lay_out(0, it)
                if first:
                    bias()
                else:
                    write(1, it - 1)
                gelu_dve(dve, x, u, h, it * 2, g_act, g_dve)
                lay_out(1, it)
                write(0, it)
                gelu_dve(dve, x, u, h, it * 2 + 1, g_act, g_dve)

            pair(0, True)
            with dve.Fori(1, NP) as it:
                pair(it, False)
            dve.wait_ge(sq_done, TT)
            dve.tensor_scalar(ms, ss, 1.0 / D, EPS, ALU.mult, ALU.add).then_inc(ms_done, 1)
            dve.wait_ge(ms_done, 2)
            dve.reciprocal(rec, ms).then_inc(ms_done, 1)
            write(1, NP - 1)
            dve.wait_ge(sqrt_done, 1)
            for i in range(1, TT, 2):
                dve.tensor_scalar(xs[:, i, :], xs[:, i, :], rstd[:, i:i + 1], None, ALU.mult).then_inc(xn_done[1], 1)
            dve.wait_ge(turned_last, 2)
            modulation(m, dve, 0, EARLY, mod_step)
            for g, (j, half) in enumerate(groups):
                if g % 2 == 1:
                    dve.wait_ge(xT_done, g + 1)
                    dve.tensor_scalar(m.hT[:, j, half * 512:(half + 1) * 512], ps[:, g % 4, :],
                                      m.modT[:, SC1 + j, 0:1], m.modT[:, SH1 + j, 0:1], ALU.mult, ALU.add).then_inc(
                                          ev_dve, 1)
            dve.wait_ge(xT_done, 17)
            hs = m.hT[:, :, SEQ:T].rearrange("p j (b s) -> p j b s", s=DS)
            pss = ps[:, 4, 0:KD * ST].rearrange("p (j b s) -> p j b s", b=NB, s=DS)
            dve.tensor_tensor(hs, pss, per_batch(m, SC1), ALU.mult).then_inc(mod_step, 1)
            dve.wait_ge(mod_step, 3)
            dve.tensor_tensor(hs, hs, per_batch(m, SH1), ALU.add)
    m.used += EARLY
    m.loads = [EARLY // 4] * 4 + [0] * 2


def per_batch(m, sec):
    return m.modT[:, sec:sec + 8, 1:NCOND].unsqueeze(3).to_broadcast([P, 8, NB, DS])


def load_query_unit(sp, m, I, u, slot):
    for g in range(2):
        sp.dma_start(m.ring[:, slot, :, g * HD:(g + 1) * HD],
                     w_block(I["w_in"][0], C_Q + (4 * g + u) * HD, n=HD)).then_inc(m.w_in[slot], 16)


def stage_project(m, I, O):
    nc, ps = m.nc, m.ps
    sgT = m.work[0:24, 0:T]
    kst = m.work[:, 1088:1088 + 2 * 512].rearrange("p (b c n) -> p b c n", b=2, c=4)
    summed = m.sem("z_tile_summed")
    bank_free = [m.sem(f"z_bank_free{b}") for b in range(6)]
    narrow_pad, narrow_in, narrow_out = m.sem("narrow_columns_padded"), m.sem("narrow_in"), m.sem("narrow_written")
    ones_set = m.sem("gate_ones_set")
    tposed, rows_act, rows_dve = m.sem("z_tiles_transposed"), m.sem("rows_by_act"), m.sem("rows_by_dve")
    rows_out = [m.sem("even_rows_stored"), m.sem("odd_rows_stored")]
    win_copied = m.sem("window_rows_copied")
    w_in = I["w_in"][0]
    narrow = m.work[:, 2400:2400 + KD * 56].rearrange("p (k n) -> p k n", n=56)
    u0, l0 = m.used, m.loads
    QU, ZO = 4, ZU - 4
    cols = z_columns()

    def stores(i):
        n = P if i < QT else ST

        def rows(name, half):
            if i < QT:
                a = O[name + "_p"][0, 0].rearrange("t a g d -> t (a g d)")
                first = i * P if name != "win" else i * P - (SEQ - WIN)
                return a[first:first + P, half * GD:(half + 1) * GD]
            a = O[name + "_s"][0].rearrange("b t a g d -> b t (a g d)")
            return a[:, WIN - DS:WIN, half * GD:(half + 1) * GD] if name == "win" else a[:, :, half * GD:(half + 1) * GD]

        out = [(rows("cmp", 0), kst[0:n, i % 2, 0]), (rows("cmp", 1), kst[0:n, i % 2, 3]),
               (rows("slc", 0), kst[0:n, i % 2, 1]), (rows("slc", 1), m.vtm[0:n, i, 0, :])]
        if i >= QT - WIN // P:
            out += [(rows("win", 0), kst[0:n, i % 2, 2]), (rows("win", 1), m.vtm[0:n, i, 1, :])]
        return out

    stored = [16 * sum(len(stores(j)) for j in range(i % 2, i + 1, 2)) for i in range(TT)]

    with nc.Block() as block:
        @block.sync
        def _(sp):
            sp.wait_ge(narrow_pad, 1)
            sp.dma_start(narrow[:, :, 0:RANK], w_block(w_in, C_AG, n=RANK)).then_inc(narrow_in, 16)
            sp.dma_start(narrow[:, :, 32:56], w_block(w_in, C_GN, n=24)).then_inc(narrow_in, 16)
            for u in range(2, ZU):
                sp.wait_ge(m.w_used, u0 + u - 1)
                if u < QU:
                    load_query_unit(sp, m, I, u, u % 2)
                else:
                    sp.dma_start(m.ring[:, u % 2], w_block(w_in, cols[u - QU])).then_inc(m.w_in[u % 2], 16)
            for i in range(TT):
                sp.wait_ge(rows_act, i + 1)
                sp.wait_ge(rows_dve, 2 * i + 2)
                for to, src in stores(i):
                    sp.dma_start(to, src).then_inc(rows_out[i % 2], 16)
            for i in (TT - 2, TT - 1):
                sp.wait_ge(rows_out[i % 2], stored[i])

        @block.gpsimd
        def _(pool):
            pool.dma_start(O["win_s"][0].rearrange("b t a g d -> b t (a g d)")[:, 0:WIN - DS],
                           I["state_win_kv"][0].rearrange("b t a g d -> b t (a g d)")[:, DS:WIN]).then_inc(
                               win_copied, 16)
            pool.memset(narrow[:, :, RANK:32], 0.0).then_inc(narrow_pad, 1)
            pool.memset(m.agT[:, :], 1.0).then_inc(ones_set, 1)
            pool.wait_ge(win_copied, 16)

        @block.tensor
        def _(pe):
            def unit(it, s):
                for n in range(NN):
                    pe.wait_ge(bank_free[3 * s + n], it + 1)
                    ins = product(pe, ps[:, 3 * s + n, 0:NW], m.ring[:, s],
                                  lambda k: m.hT[:, k, n * NW:(n + 1) * NW])
                    if n < NN - 1:
                        ins.then_inc(summed, 1)
                return ins

            with pe.Fori(0, QU // 2) as it:
                for s in range(2):
                    pe.wait_ge(m.w_in[s], it * 32 + 16 * (l0[s] + 2))
                    unit(it, s).then_inc(m.w_used, 1)
            with pe.Fori(0, ZO // 2) as it:
                for s in range(2):
                    pe.wait_ge(m.w_in[s], it * 16 + 16 * (l0[s] + QU + 1))
                    unit(it + QU // 2, s).then_inc(m.w_used, 1)
            pe.wait_ge(narrow_in, 32)
            for n in range(NN):
                pe.wait_ge(bank_free[n], ZU // 2 + 1)
                ins = product(pe, ps[0:56, n, 0:NW], narrow, lambda k: m.hT[:, k, n * NW:(n + 1) * NW])
                ins.then_inc(m.w_used if n == NN - 1 else summed, 1)
            for b in range(6):
                pe.wait_ge(bank_free[b], ZU // 2 + 1)
            pe.wait_ge(narrow_out, 6)
            for i in range(TT):
                n = P if i < QT else ST
                tok = slice(i * P, i * P + n)
                if i >= 2:
                    pe.wait_ge(rows_act, i - 1)
                    pe.wait_ge(rows_dve, 2 * (i - 1))
                b = 3 * (i % 2)
                for c, t in enumerate((Z_KC, Z_KS, Z_KW, Z_VC)):
                    ins = pe.transpose(ps[0:n, b, c * P:(c + 1) * P], m.zT[:, t, tok], m.ident[:, :])
                ins.then_inc(tposed, 1)
                for c, t in enumerate((Z_VS, Z_VW)):
                    ins = pe.transpose(ps[0:n, b + 1, c * P:(c + 1) * P], m.zT[:, t, tok], m.ident[:, :])
                if i < QT:
                    ins = pe.transpose(ps[0:n, b + 1, 256:280], sgT[:, tok], m.ident[0:24, 0:24])
                ins.then_inc(tposed, 1)
                for h in range(GH):
                    ins = pe.transpose(ps[0:n, b + 2, h * P:(h + 1) * P], m.zT[:, Z_VG + h, tok], m.ident[:, :])
                ins.then_inc(tposed, 1)

        def ready(e, it, s, n):
            if n < NN - 1:
                e.wait_ge(summed, it * 4 + (2 * s + n + 1))
            else:
                e.wait_ge(m.w_used, it * 2 + (u0 + s + 1))

        @block.scalar
        def _(act):
            for b in (0, 2, 4):
                act.sem_inc(bank_free[b], 1)
            with act.Fori(0, ZU // 2) as it:
                for s, n in ((0, 0), (0, 2), (1, 1)):
                    ready(act, it, s, n)
                    act.activation(m.zT[:, bass.ds(it * 2 + s, 1), n * NW:(n + 1) * NW], ps[:, 3 * s + n:3 * s + n + 1, 0:NW],
                                   ACT.Copy).then_inc(bank_free[3 * s + n], 1)
            for n in range(NN):
                ready(act, ZU // 2, 0, n)
                act.activation(sgT[:, n * NW:(n + 1) * NW], ps[32:56, n, 0:NW], ACT.Sigmoid).then_inc(narrow_out, 1)
            for i in range(TT):
                n = P if i < QT else ST
                act.wait_ge(tposed, 3 * i + 1)
                if i >= 2:
                    act.wait_ge(rows_out[i % 2], stored[i - 2])
                act.activation(kst[0:n, i % 2], ps[0:n, 3 * (i % 2)].rearrange("p (c n) -> p c n", c=4),
                               ACT.Copy).then_inc(rows_act, 1)

        @block.vector
        def _(dve):
            for b in (1, 3, 5):
                dve.sem_inc(bank_free[b], 1)
            with dve.Fori(0, ZU // 2) as it:
                for s, n in ((0, 1), (1, 0), (1, 2)):
                    ready(dve, it, s, n)
                    dve.tensor_copy(m.zT[:, bass.ds(it * 2 + s, 1), n * NW:(n + 1) * NW],
                                    ps[:, 3 * s + n:3 * s + n + 1, 0:NW]).then_inc(bank_free[3 * s + n], 1)
            dve.wait_ge(ones_set, 1)
            for n in range(NN):
                ready(dve, ZU // 2, 0, n)
                dve.wait_ge(narrow_out, 3)
                dve.tensor_copy(m.agT[0:RANK, n * NW:(n + 1) * NW], ps[0:RANK, n, 0:NW]).then_inc(narrow_out, 1)
            dve.tensor_copy(m.gnT[:, :], sgT[:, SEQ:T])
            for i in range(TT):
                n = P if i < QT else ST
                b = 3 * (i % 2)
                dve.wait_ge(tposed, 3 * i + 2)
                if i < QT:
                    dve.tensor_copy(m.gates[:, i, :], ps[:, b + 1, 256:280])
                dve.tensor_copy(m.vtm[0:n, i], ps[0:n, b + 1, 0:256].rearrange("p (c n) -> p c n", c=2)).then_inc(
                    rows_dve, 1)
                dve.wait_ge(tposed, 3 * i + 3)
                dve.tensor_copy(m.vg[0:n, i], ps[0:n, b + 2, :].rearrange("p (c n) -> p c n", c=4)).then_inc(
                    rows_dve, 1)
    m.used += ZU + 1
    m.loads = [l0[0] + QU + ZO // 2, l0[1] + QU + ZO // 2] + l0[2:]


def keep(pool, done, ap, pattern, base, mult):
    ins = pool.affine_select(out=ap, in_=ap, compare_op=ALU.is_ge, fill=0.0, base=base, pattern=pattern,
                             channel_multiplier=mult)
    return ins


def stage_gla(m, I, O):
    nc, ps = m.nc, m.ps
    tail = m.zT[:, Z_TAIL:ZU, :].rearrange("p a b -> p (a b)")
    ogf = m.oglaT[:, :, :].rearrange("p a b -> p (a b)")
    W = m.work
    lg = tail[:, 0:2304]
    soft = tail[:, 2304:4608]
    D2 = [tail[:, i * T:(i + 1) * T] for i in range(2)]
    S = tail[:, 0:17 * GDV].rearrange("p (c v) -> p c v", v=GDV)
    E2 = [tail[:, 2176 + i * T:2176 + (i + 1) * T] for i in range(2)]
    kl = tail[:, 4288:4288 + 2048].rearrange("p (i c k) -> p i c k", i=QT, c=2)
    sqb = [tail[:, 4288 + 512 * i:4288 + 512 * i + 512] for i in range(2)]
    S0 = E2[0][:, 0:NB * GDV].rearrange("p (b v) -> p b v", v=GDV)
    B = [ogf[:, p * T:(p + 1) * T] for p in range(2)]
    Qd, Kd = ogf[:, 2 * T:3 * T], ogf[:, 3 * T:4 * T]
    Qo, Ko = W[:, 0:T], W[:, T:2 * T]
    am = W[:, 2112:2112 + 1024].rearrange("p (b x) -> p b x", b=2)
    tri = W[:, 3136:3264]
    M12 = W[:, 3264:3520].rearrange("p (k t) -> p k t", k=2)
    mS, triS, bm = W[0:ST, 3520:3552], W[0:ST, 3552:3584], W[0:ST, 3584:3592]
    wa2 = W[0:RANK + 1, 3592:3848]
    eiB = W[:, 3848:3848 + 288]
    amS = W[0:ST, 4136:4200]
    decay = W[:, 4200:4224]
    ss, ms, rec, rstd = (W[:, 64 * i:64 * i + TT * GH] for i in range(4))
    klB = kl[0:ST].rearrange("p i c k -> p (i c) k")[:, 0:NB, :]
    klS = W[0:ST, 2112:2112 + P]

    a2_in, s0_in, gla_out = m.sem("gate_weights_in"), m.sem("sample_states_in"), m.sem("gla_states_stored")
    cst = m.sem("gla_masks_steps")
    gate_mm, cum_mm = m.sem("gate_products"), m.sem("cumulated")
    soft_step, lg_done, b_done = m.sem("softplus_steps"), m.sem("log_gates_ready"), m.sem("cumulated_copied")
    d_ready, e_ready, m_done, own = (m.sem("decay_exponents"), m.sem("decay_factors"), m.sem("operands_decayed"),
                                     m.sem("gla_vector_steps"))
    kl_T, kl_done, kv_mm, s_done = (m.sem("keys_transposed"), m.sem("keys_copied"), m.sem("state_products"),
                                    m.sem("states_advanced"))
    a_mm, a_done, o_mm, o_done = m.sem("gla_scores"), m.sem("gla_scores_masked"), m.sem("gla_sums"), m.sem("gla_kept")
    smp, smp_pe, zeroed = m.sem("sample_vector_steps"), m.sem("sample_products"), m.sem("halves_zeroed")
    smp_own = m.sem("sample_scores_applied")
    sq, nrm, nrm_own, oT, ow = (m.sem("gla_squares"), m.sem("gla_rstd"), m.sem("gla_norm_steps"), m.sem("gla_transposed"),
                           m.sem("gla_written"))
    scaled = m.sem("gla_scaled")
    w1_zero, w1_in = m.sem("first_layer_zeroed"), m.sem("first_layer_in")
    w1k = first_layer_in_ring(m)

    with nc.Block() as block:
        @block.sync
        def _(sp):
            sp.dma_start(wa2[0:RANK, :], I["w_gla_a2"][0]).then_inc(a2_in, 16)
            sp.dma_start(wa2[RANK:RANK + 1, :], I["b_gla_a"]).then_inc(a2_in, 16)
            sp.wait_ge(w1_zero, 2)
            for g in range(2):
                load_first_layer(sp, I["cmp_w1_k"], w1k, g, w1_in)
            sp.wait_ge(w1_in, 32)
            for p in range(2):
                sp.wait_ge(m_done, 6 * p + 6)
                sp.dma_start(S0, I["state_gla"][0].rearrange("b (q h) k v -> q (h k) b v", q=2)[p]).then_inc(s0_in, 16)
                sp.wait_ge(s_done, (p + 1) * 32)
                sp.dma_start(O["gla_p"][0, 0].rearrange("(q h) k v -> q (h k) v", q=2)[p], S[:, 16, :]).then_inc(
                    gla_out, 16)
                sp.wait_ge(smp, p * 8 + 8)
                sp.dma_start(O["gla_s"][0].rearrange("b (q h) k v -> q (h k) b v", q=2)[p], S0).then_inc(gla_out, 16)
            sp.wait_ge(gla_out, 64)

        @block.gpsimd
        def _(pool):
            for g in range(2):
                pool.memset(w1k[64 * g:64 * g + 64, :, 64 - 64 * g:128 - 64 * g], 0.0).then_inc(w1_zero, 1)
            pool.wait_ge(w1_zero, 2)
            m1 = M12[:, 0, :]
            m2 = M12[:, 1, :].rearrange("p (c h t) -> p c h t", c=2, h=2)
            n = 0
            for ins in (pool.memset(tri, 1.0 / 16), pool.memset(M12, 0.0), pool.memset(mS, 1.0),
                        pool.memset(triS, 1.0 / 16), pool.memset(bm, 1.0)):
                ins.then_inc(cst, 1)
                n += 1
            pool.wait_ge(cst, n)
            pool.memset(m1, 1.0).then_inc(cst, 1)
            pool.memset(m2[:, :, 1, :], 1.0).then_inc(cst, 1)
            n += 2
            pool.wait_ge(cst, n)
            first = [(tri.rearrange("p (c t) -> p c t", c=2), [[64, 2], [1, 64]], 0, -1),
                     (m1.rearrange("p (c t) -> p c t", c=4), [[32, 4], [1, 32]], 0, -1),
                     (m2[:, :, 1, :], [[-64, 2], [0, 32]], 0, 1),
                     (mS.rearrange("p (c t) -> p c t", c=8), [[4, 8], [1, 4]], 0, -1),
                     (triS.rearrange("p (c t) -> p c t", c=8), [[4, 8], [1, 4]], 0, -1),
                     (bm, [[-4, 8]], 0, 1)]
            second = [(tri.rearrange("p (c t) -> p c t", c=2), [[-64, 2], [0, 64]], 0, 1),
                      (m1.rearrange("p (c t) -> p c t", c=4), [[-32, 4], [0, 32]], 0, 1),
                      (m2[:, :, 1, :], [[64, 2], [0, 32]], 31, -1),
                      (mS.rearrange("p (c t) -> p c t", c=8), [[-4, 8], [0, 4]], 0, 1),
                      (triS.rearrange("p (c t) -> p c t", c=8), [[-4, 8], [0, 4]], 0, 1),
                      (bm, [[4, 8]], 3, -1)]
            for group in (first, second):
                for ap, pattern, base, mult in group:
                    keep(pool, cst, ap, pattern, base, mult).then_inc(cst, 1)
                    n += 1
                pool.wait_ge(cst, n)
            pool.memset(Qo[:, 0:SEQ].rearrange("p (c h t) -> p c h t", h=2, t=32)[:, :, 0, :], 0.0).then_inc(cst, 1)
            pool.memset(Ko[:, 0:SEQ].rearrange("p (c h t) -> p c h t", h=2, t=32)[:, :, 1, :], 0.0).then_inc(cst, 1)
            pool.memset(eiB, 0.0).then_inc(cst, 1)
            for p in range(2):
                pool.wait_ge(lg_done, 2)
                pool.wait_ge(b_done, 4)
                if p:
                    pool.wait_ge(smp, 8)
                pool.memset(kl[0:64, :, 1, :], 0.0).then_inc(zeroed, 1)
                pool.memset(kl[64:128, :, 0, :], 0.0).then_inc(zeroed, 1)

        @block.tensor
        def _(pe):
            pe.wait_ge(a2_in, 32)
            for i in range(TT):
                n = P if i < QT else ST
                ins = pe.matmul(ps[0:n, i // 2, (i % 2) * 256:(i % 2) * 256 + 256], m.agT[0:RANK + 1, i * P:i * P + n],
                                wa2, start=True, stop=True)
            ins.then_inc(gate_mm, 1)
            pe.wait_ge(lg_done, 2)
            pe.wait_ge(cst, 22)
            for p in range(2):
                for i in range(QT):
                    ins = pe.matmul(ps[:, 2 * p + i // 4, (i % 4) * P:(i % 4 + 1) * P],
                                    lg[:, i * 256 + p * P:i * 256 + (p + 1) * P], tri, start=True, stop=True)
                ins = pe.matmul(ps[:, 4, p * ST:(p + 1) * ST], lg[0:ST, QT * 256 + p * P:QT * 256 + (p + 1) * P], triS,
                                start=True, stop=True)
            ins.then_inc(cum_mm, 1)
            for p in range(2):
                q, k = m.zT[:, Z_QG + p, :], m.zT[:, Z_KG + p, :]
                pe.wait_ge(m_done, 6 * p + 6)
                pe.wait_ge(b_done, 4)
                for i in range(QT):
                    ins = pe.transpose(ps[:, i // 4, (i % 4) * P:(i % 4 + 1) * P], k[:, i * P:(i + 1) * P], m.ident[:, :])
                ins.then_inc(kl_T, 1)
                pe.wait_ge(kl_done, 5 * p + 4)
                for j in range(2 * QT):
                    if j >= 4:
                        pe.wait_ge(s_done, 32 * p + 2 * (j - 4) + 2)
                    pe.matmul(ps[:, 4 + j % 4, 0:256], kl[:, j // 2, j % 2, :],
                              m.vg[:, j // 2, 2 * p:2 * p + 2, :].rearrange("p h v -> p (h v)"),
                              start=True, stop=True).then_inc(kv_mm, 1)
                pe.wait_ge(s_done, 32 * p + 32)

                def scores(i):
                    for hh in range(2):
                        r = slice(64 * hh, 64 * hh + 64)
                        tok = slice(i * P, (i + 1) * P)
                        pe.matmul(ps[:, 2 * (i % 2) + hh, 0:P], Kd[r, tok], Qd[r, tok], start=True, stop=True)
                        ins = pe.matmul(ps[:, 2 * (i % 2) + hh, P:2 * P], Ko[r, tok], Qo[r, tok], start=True, stop=True)
                    ins.then_inc(a_mm, 1)

                def sums(i):
                    for hh in range(2):
                        r = slice(64 * hh, 64 * hh + 64)
                        bank = 4 + 2 * (i % 2) + hh
                        v = m.vg[:, i, 2 * p + hh, :]
                        for a in range(2):
                            pe.matmul(ps[:, bank, 0:P], am[:, i % 2, (2 * hh + a) * P:(2 * hh + a + 1) * P], v, start=a == 0, stop=False)
                        for c in range(2):
                            ins = pe.matmul(ps[64 * c:64 * c + 64, bank, 0:P],
                                            q[r, i * P + 64 * c:i * P + 64 * c + 64], S[r, 2 * i + c, :], start=False, stop=True)
                    ins.then_inc(o_mm, 1)

                scores(0)
                for i in range(QT):
                    if i + 1 < QT:
                        if i >= 1:
                            pe.wait_ge(a_done, QT * p + i)
                        scores(i + 1)
                    pe.wait_ge(a_done, QT * p + i + 1)
                    if i >= 2:
                        pe.wait_ge(o_done, QT * p + i - 1)
                    sums(i)
                pe.wait_ge(o_done, QT * p + QT)
                pe.transpose(ps[0:ST, 0, 0:P], k[:, SEQ:T], m.ident[:, :])
                for hh in range(2):
                    r = slice(64 * hh, 64 * hh + 64)
                    ins = pe.matmul(ps[0:ST, 1 + hh, 0:ST], Kd[r, SEQ:T], Qd[r, SEQ:T], start=True, stop=True)
                ins.then_inc(smp_pe, 1)
                pe.wait_ge(smp, 8 * p + 4)
                pe.wait_ge(s0_in, 16 * p + 16)
                for hh in range(2):
                    ins = pe.matmul(ps[0:ST, 6 + hh, 0:P], amS[:, hh * ST:(hh + 1) * ST], m.vg[0:ST, QT, 2 * p + hh, :],
                                    start=True, stop=False)
                ins.then_inc(smp_own, 1)
                pe.wait_ge(smp_own, p + 1)
                for hh in range(2):
                    r = slice(64 * hh, 64 * hh + 64)
                    out = ps[0:ST, 6 + hh, 0:P]
                    for b in range(NB):
                        ins = pe.matmul(out, eiB[r, b * ST:(b + 1) * ST], S0[r, b, :], start=False, stop=b == NB - 1)
                ins.then_inc(smp_pe, 1)
                for b in range(NB):
                    for hh in range(2):
                        ins = pe.matmul(ps[64 * hh:64 * hh + 64, 4 + b // 4, (b % 4) * P:(b % 4 + 1) * P],
                                        klB[:, b, 64 * hh:64 * hh + 64], m.vg[0:ST, QT, 2 * p + hh, :],
                                        start=True, stop=True)
                ins.then_inc(smp_pe, 1)
                pe.wait_ge(smp, 8 * p + 8)
            for i in range(TT):
                n = P if i < QT else ST
                pe.wait_ge(scaled, i + 1)
                if i >= 4:
                    pe.wait_ge(ow, i - 3)
                for h in range(GH):
                    ins = pe.transpose(ps[:, i % 4, h * P:h * P + n], m.vg[0:n, i, h, :], m.ident[0:n, 0:n])
                ins.then_inc(oT, 1)

        @block.scalar
        def _(act):
            act.wait_ge(gate_mm, 1)
            big, small = ps[:, 0:4, :].rearrange("p a b -> p (a b)"), ps[0:ST, 4, 0:256]
            sb_, ss_ = soft[:, 0:2048], soft[0:ST, 2048:2304]
            act.activation(sb_, big, ACT.Abs).then_inc(soft_step, 1)
            act.activation(ss_, small, ACT.Abs).then_inc(soft_step, 1)
            act.wait_ge(soft_step, 2)
            act.activation(sb_, sb_, ACT.Exp, scale=-1.0).then_inc(soft_step, 1)
            act.activation(ss_, ss_, ACT.Exp, scale=-1.0).then_inc(soft_step, 1)
            act.wait_ge(soft_step, 4)
            act.activation(sb_, sb_, ACT.Ln, bias=1.0).then_inc(soft_step, 1)
            act.activation(ss_, ss_, ACT.Ln, bias=1.0).then_inc(soft_step, 1)
            for p in range(2):
                half = lambda a, h: a[:, 0:SEQ].rearrange("p (c h t) -> p c h t", h=2, t=32)[:, :, h, :]
                for dr, md, out, inp, sign in (
                        (3 * p + 1, 6 * p, E2[0], D2[0], 1.0), (3 * p + 1, 6 * p, E2[1], D2[0], -1.0),
                        (3 * p + 2, 6 * p + 1, half(E2[0], 1), half(D2[1], 1), 1.0),
                        (3 * p + 2, 6 * p + 2, half(E2[1], 0), half(D2[1], 0), -1.0),
                        (3 * p + 2, 6 * p + 3, E2[0], B[p], 1.0), (3 * p + 3, 6 * p + 4, E2[1], D2[0], 1.0)):
                    act.wait_ge(d_ready, dr)
                    if md:
                        act.wait_ge(m_done, md)
                    act.activation(out, inp, ACT.Exp, scale=sign).then_inc(e_ready, 1)
                act.activation(decay[:, 0:16], B[p][:, 0:SEQ].rearrange("p (c t) -> p c t", t=CH)[:, :, CH - 1],
                               ACT.Exp).then_inc(e_ready, 1)
                act.activation(decay[:, 16:24], B[p][:, SEQ:T].rearrange("p (c t) -> p c t", t=DS)[:, :, DS - 1],
                               ACT.Exp).then_inc(e_ready, 1)
                act.wait_ge(kl_T, p + 1)
                act.wait_ge(zeroed, 2 * p + 2)
                for c in range(2):
                    for g in range(2):
                        r = slice(64 * c, 64 * c + 64)
                        act.activation(kl[r, 4 * g:4 * g + 4, c, :], ps[r, g, :].rearrange("p (i k) -> p i k", i=4),
                                       ACT.Copy).then_inc(kl_done, 1)
                act.wait_ge(smp, 8 * p + 8)
                act.sem_inc(kl_done, 1)
            for i in range(TT):
                n = P if i < QT else ST
                if i >= 2:
                    act.wait_ge(nrm, i - 1)
                act.wait_ge(smp, 16)
                act.activation(sqb[i % 2][0:n], m.vg[0:n, i].rearrange("p h v -> p (h v)"), ACT.Square).then_inc(sq, 1)
            act.wait_ge(nrm, TT + 2)
            act.activation(rstd, rec, ACT.Sqrt).then_inc(sq, 1)
            act.wait_ge(sq, TT + 1)
            for i in range(TT):
                n = P if i < QT else ST
                act.wait_ge(oT, i + 1)
                act.activation(m.oglaT[:, :, i * P:i * P + n], ps[:, i % 4, :].rearrange("p (h t) -> p h t", h=GH)[:, :, 0:n],
                               ACT.Copy, scale=m.vecT[:, V_GNORM:V_GNORM + 1]).then_inc(ow, 1)

        @block.vector
        def _(dve):
            steps = [0]

            def chain(ins):
                steps[0] += 1
                ins.then_inc(own, 1)
                dve.wait_ge(own, steps[0])

            dve.wait_ge(soft_step, 6)
            dve.scalar_tensor_tensor(out=lg[:, 0:2048], in0=ps[:, 0:4, :].rearrange("p a b -> p (a b)"), scalar=0.0,
                                     in1=soft[:, 0:2048], op0=ALU.min, op1=ALU.subtract).then_inc(lg_done, 1)
            dve.scalar_tensor_tensor(out=lg[0:ST, 2048:2304], in0=ps[0:ST, 4, 0:256], scalar=0.0,
                                     in1=soft[0:ST, 2048:2304], op0=ALU.min, op1=ALU.subtract).then_inc(lg_done, 1)
            dve.wait_ge(cum_mm, 1)
            for p in range(2):
                dve.tensor_copy(B[p][:, 0:SEQ], ps[:, 2 * p:2 * p + 2, :].rearrange("p a b -> p (a b)")).then_inc(b_done, 1)
                dve.tensor_copy(B[p][:, SEQ:T], ps[:, 4, p * ST:(p + 1) * ST]).then_inc(b_done, 1)
            dve.wait_ge(b_done, 4)

            def blocks(a, n, lo=0, hi=SEQ):
                return a[:, lo:hi].rearrange("p (c t) -> p c t", t=n)

            def at(a, n, t, lo=0, hi=SEQ):
                v = blocks(a, n, lo, hi)
                return v[:, :, t:t + 1].to_broadcast([P, v.shape[1], n])

            for p in range(2):
                b, q, k = B[p], m.zT[:, Z_QG + p, :], m.zT[:, Z_KG + p, :]
                if p:
                    dve.wait_ge(e_ready, 8)
                    dve.wait_ge(gla_out, 32)
                dve.tensor_tensor(blocks(D2[0], 32), blocks(b, 32), at(b, 32, 15), ALU.subtract)
                chain(dve.tensor_tensor(blocks(D2[0], DS, SEQ, T), blocks(b, DS, SEQ, T), at(b, DS, 0, SEQ, T),
                                        ALU.subtract))
                dve.tensor_scalar(D2[0], D2[0], -40.0, 40.0, ALU.max, ALU.min).then_inc(d_ready, 1)
                dve.tensor_tensor(blocks(D2[1], CH), blocks(b, CH), at(b, CH, 31), ALU.subtract).then_inc(d_ready, 1)
                dve.wait_ge(e_ready, 8 * p + 1)
                dve.scalar_tensor_tensor(out=Qd, in0=E2[0], scalar=GDK ** -0.5, in1=q, op0=ALU.mult,
                                         op1=ALU.mult).then_inc(m_done, 1)
                dve.wait_ge(e_ready, 8 * p + 2)
                dve.tensor_tensor(Kd, E2[1], k, ALU.mult).then_inc(m_done, 1)
                dve.tensor_tensor(blocks(D2[0], CH), at(b, CH, CH - 1), blocks(b, CH), ALU.subtract)
                chain(dve.tensor_tensor(blocks(D2[0], DS, SEQ, T), at(b, DS, DS - 1, SEQ, T), blocks(b, DS, SEQ, T),
                                        ALU.subtract))
                dve.sem_inc(d_ready, 1)
                half = lambda a, h: a[:, 0:SEQ].rearrange("p (c h t) -> p c h t", h=2, t=32)[:, :, h, :]
                dve.wait_ge(e_ready, 8 * p + 3)
                if p == 0:
                    dve.wait_ge(cst, 22)
                dve.scalar_tensor_tensor(out=half(Qo, 1), in0=half(E2[0], 1), scalar=GDK ** -0.5, in1=half(q, 1),
                                         op0=ALU.mult, op1=ALU.mult).then_inc(m_done, 1)
                dve.wait_ge(e_ready, 8 * p + 4)
                dve.tensor_tensor(half(Ko, 0), half(E2[1], 0), half(k, 0), ALU.mult).then_inc(m_done, 1)
                dve.wait_ge(m_done, 6 * p + 4)
                dve.wait_ge(e_ready, 8 * p + 5)
                dve.scalar_tensor_tensor(out=q, in0=E2[0], scalar=GDK ** -0.5, in1=q, op0=ALU.mult,
                                         op1=ALU.mult).then_inc(m_done, 1)
                dve.wait_ge(e_ready, 8 * p + 6)
                dve.tensor_tensor(k, E2[1], k, ALU.mult).then_inc(m_done, 1)
                dve.wait_ge(e_ready, 8 * p + 8)
                chain(dve.memset(S[:, 0, :], 0.0))
                for j in range(2 * QT):
                    dve.wait_ge(kv_mm, 2 * QT * p + j + 1)
                    for hh in range(2):
                        r = slice(64 * hh, 64 * hh + 64)
                        ins = dve.scalar_tensor_tensor(out=S[r, j + 1, :], in0=S[r, j, :], scalar=decay[r, j:j + 1],
                                                       in1=ps[r, 4 + j % 4, hh * P:(hh + 1) * P], op0=ALU.mult,
                                                       op1=ALU.add)
                        ins.then_inc(s_done, 1)
                    dve.wait_ge(s_done, 32 * p + 2 * j + 2)

                def mask(i):
                    dve.wait_ge(a_mm, QT * p + i + 1)
                    if i >= 2:
                        dve.wait_ge(o_mm, QT * p + i - 1)
                    dve.scalar_tensor_tensor(out=am[:, i % 2].rearrange("p (h x) -> p h x", h=2),
                                             in0=ps[:, 2 * (i % 2):2 * (i % 2) + 2, 0:2 * P], scalar=3e38,
                                             in1=M12.rearrange("p k t -> p (k t)").unsqueeze(1).to_broadcast([P, 2, 2 * P]),
                                             op0=ALU.min, op1=ALU.mult).then_inc(a_done, 1)

                for i in range(QT + 1):
                    if i < QT:
                        mask(i)
                    if i:
                        dve.wait_ge(o_mm, QT * p + i)
                        dve.tensor_copy(m.vg[:, i - 1, 2 * p:2 * p + 2, :],
                                        ps[:, 4 + 2 * ((i - 1) % 2):6 + 2 * ((i - 1) % 2), 0:P]).then_inc(
                                            o_done, 1)
                dve.wait_ge(smp_pe, 3 * p + 1)
                dve.tensor_copy(klS, ps[0:ST, 0, 0:P]).then_inc(smp, 1)
                dve.tensor_tensor(amS.rearrange("p (h t) -> p h t", h=2),
                                  ps[0:ST, 1:3, 0:ST],
                                  mS.unsqueeze(1).to_broadcast([ST, 2, ST]), ALU.mult).then_inc(smp, 1)
                dve.tensor_copy(eiB.rearrange("p (b x) -> p b x", x=ST + DS)[:, :, 0:DS],
                                q[:, SEQ:T].rearrange("p (b s) -> p b s", s=DS)).then_inc(smp, 1)
                dve.wait_ge(smp, 8 * p + 3)
                dve.wait_ge(kv_mm, 2 * QT * (p + 1))
                dve.tensor_tensor(klB, klS.unsqueeze(1).to_broadcast([ST, NB, P]), bm.unsqueeze(2).to_broadcast([ST, NB, P]),
                                  ALU.mult).then_inc(smp, 1)
                dve.wait_ge(smp_pe, 3 * p + 3)
                dve.tensor_copy(m.vg[0:ST, QT, 2 * p:2 * p + 2, :],
                                ps[0:ST, 6:8, 0:P]).then_inc(smp, 1)
                dve.tensor_tensor(S0, S0, decay[:, 16:24].unsqueeze(2).to_broadcast([P, NB, GDV]), ALU.mult).then_inc(smp, 1)
                dve.wait_ge(smp, 8 * p + 6)
                for g in range(2):
                    dve.tensor_tensor(S0[:, 4 * g:4 * g + 4, :], S0[:, 4 * g:4 * g + 4, :],
                                      ps[:, 4 + g, :].rearrange("p (b v) -> p b v", b=4), ALU.add).then_inc(smp, 1)
            chain(dve.memset(ss, 1.0))
            for i in range(TT):
                n = P if i < QT else ST
                dve.wait_ge(sq, i + 1)
                dve.tensor_reduce(ss[0:n, i * GH:(i + 1) * GH], sqb[i % 2][0:n].rearrange("p (h v) -> p h v", h=GH),
                                  X, ALU.add).then_inc(nrm, 1)
            dve.wait_ge(nrm, TT)
            dve.tensor_scalar(ms, ss, 1.0 / GDV, EPS, ALU.mult, ALU.add).then_inc(nrm, 1)
            dve.wait_ge(nrm, TT + 1)
            dve.reciprocal(rec, ms).then_inc(nrm, 1)
            dve.wait_ge(sq, TT + 1)
            for i in range(TT):
                n = P if i < QT else ST
                dve.tensor_tensor(m.vg[0:n, i], m.vg[0:n, i],
                                  rstd[0:n, i * GH:(i + 1) * GH].unsqueeze(2).to_broadcast([n, GH, GDV]),
                                  ALU.mult).then_inc(scaled, 1)


def stage_compress(m, I, O):
    nc, ps = m.nc, m.ps
    w1 = [first_layer_in_ring(m), m.tail[:, 0:4096].rearrange("p (t h) -> p t h", h=P)]
    kt = [m.work[:, 1024 * i:1024 * (i + 1)].rearrange("p (t n) -> p t n", t=CS) for i in range(2)]
    x, u, h = ([m.work[:, 2048 + 128 * i + 64 * kv:2048 + 128 * i + 64 * kv + 63] for kv in range(2)] for i in range(3))
    w_set, w_ok = m.sem("prompt_block_diagonal_zeroed"), m.sem("prompt_value_weights_in")
    kt_done, cmp_mm = m.sem("prompt_tokens_laid_out"), m.sem("prompt_compress_sums")
    g_act, g_dve, out_mm = m.sem("prompt_gelu_by_act"), m.sem("prompt_gelu_by_dve"), m.sem("prompt_compressed_products")

    with nc.Block() as block:
        @block.sync
        def _(sp):
            sp.wait_ge(w_set, 2)
            for g in range(2):
                load_first_layer(sp, I["cmp_w1_v"], w1[1], g, w_ok)
            for b in range(4):
                for j in range(NPAGE):
                    load_page(sp, m, I, "cache_slc_kv", b, j, m.past[b][:, j, :], m.past_in[b])

        @block.gpsimd
        def _(pool):
            for g in range(2):
                pool.memset(w1[1][64 * g:64 * g + 64, :, 64 - 64 * g:128 - 64 * g], 0.0).then_inc(w_set, 1)

        @block.tensor
        def _(pe):
            for kv in range(2):
                if kv:
                    pe.wait_ge(w_ok, 32)
                pe.wait_ge(kt_done, 2)
                for t in range(CL):
                    ins = pe.matmul(ps[:, kv, 0:63], w1[kv][:, t, :], kt[kv][:, t % CS, t // CS:t // CS + 63],
                                    start=t == 0, stop=t == CL - 1)
                ins.then_inc(cmp_mm, 1)
            for kv in range(2):
                pe.wait_ge(g_dve, 4 * kv + 4)
                if kv == 0:
                    ins = pe.matmul(ps[:, 2, 0:63], m.w2[:, 0, :], h[0], start=True, stop=True)
                else:
                    ins = pe.matmul(ps[0:63, 3, 0:P], h[1], m.w2[:, 1, :], start=True, stop=True)
                ins.then_inc(out_mm, 1)

        @block.scalar
        def _(act):
            act.activation(kt[1].rearrange("p t n -> p n t"),
                           m.zT[:, Z_VC, 0:SEQ].rearrange("p (n t) -> p n t", t=CS), ACT.Copy).then_inc(kt_done, 1)
            for kv in range(2):
                gelu_act(act, ps[:, kv, 0:63], x[kv], u[kv], m.cbias[:, kv:kv + 1], kv, cmp_mm, g_act, g_dve)

        @block.vector
        def _(dve):
            dve.wait_ge(kt_done, 1)
            dve.tensor_copy(kt[0].rearrange("p t n -> p n t"),
                            m.zT[:, Z_KC, 0:SEQ].rearrange("p (n t) -> p n t", t=CS)).then_inc(kt_done, 1)
            for kv in range(2):
                gelu_dve(dve, x[kv], u[kv], h[kv], kv, g_act, g_dve)
                dve.wait_ge(out_mm, kv + 1)
                if kv == 0:
                    dve.tensor_scalar(m.ckT[:, 0, 0:63], ps[:, 2, 0:63], 0.5, None, ALU.mult)
                else:
                    dve.tensor_scalar(m.cvt[0:63, 0, :], ps[0:63, 3, 0:P], 0.5, None, ALU.mult)


def stage_samples(m, I, O):
    nc, ps = m.nc, m.ps
    W, tail = m.work, m.tail
    RB = 2 * HP * DS
    BQ = P // RB
    NQ = NB // BQ
    kv, kv_in = m.past, m.past_in
    gateB = m.vgf[:, 4096:4480].rearrange("p (k h t) -> p k h t", k=3, h=HP)
    kw = [m.zT[:, Z_KC, 512 * i:512 * (i + 1)].rearrange("p (j c) -> p j c", c=GD) for i in range(2)]
    KT = [tail[:, 1024 * i:1024 + 1024 * i] for i in range(2)]
    S = tail[:, 2048:3104]
    PT = tail[:, 3104:4256].rearrange("p (j r) -> p j r", r=P)
    vw = tail[:, 4256:6304].rearrange("p (b j c) -> p b j c", b=BQ, c=GD)
    sel = W[0:24, 0:1536].rearrange("p (k h g d) -> p k h g d", k=3, h=HP, g=2)
    Qb = W[:, 1536:1792].rearrange("p (b g h t) -> p b g h t", b=NB, g=2, h=HP)
    Qf = W[:, 1536:1792]
    HS, blk = W[:, 1792:1920], W[:, 1920:2048]
    newm = W[:, 2048:2112].rearrange("p (q t) -> p q t", q=NQ)
    winm = W[:, 2112:2116]
    iota = W[:, 2120:2152]
    ints = W[:, 2152:2156].bitcast(I32)
    intf = W[:, 2176:2304].bitcast(I32)
    tcol, bcol, lo, hi = (W[:, 2156 + i:2157 + i] for i in range(4))
    geq = W[:, 2304:2336]
    on, gt = W[:, 2400:2528], W[:, 2528:2592]
    hp = W[:, 2600:2666]
    imp, t14, drop = W[:, 2670:2684], W[:, 2690:2704], W[:, 2710:2726]
    nmx, den, rden, mn, jd = (W[:, 2730 + i:2731 + i] for i in range(5))
    Pn = W[:, 2740:2804]
    NJ = NSLC - 2

    k_in, v_in = [m.sem(f"window_keys_in{i}") for i in range(2)], m.sem("window_values_in")
    c_pool, c_own = m.sem("sample_constants"), m.sem("sample_vector_chain")
    gates_mm, kT, kt_act, kt_dve = m.sem("gates_spread"), m.sem("keys_turned"), m.sem("keys_by_act"), m.sem("keys_by_dve")
    const_ok = m.sem("sample_masks_ready")
    k_mm, s_mm, s_ok, ex, r_ok, i_mm = (m.sem("key_tiles_scored"), m.sem("scores_summed"), m.sem("scores_masked"),
                                        m.sem("probabilities_ready"), m.sem("normalised_compressed"),
                                        m.sem("importance_summed"))
    pT, pt_act, pt_dve, pv, on_ok, oT, gated = (m.sem("probabilities_turned"), m.sem("turned_by_act"),
                                                m.sem("turned_by_dve"), m.sem("values_summed"), m.sem("outputs_scaled"),
                                                m.sem("outputs_turned"), m.sem("outputs_gated"))
    seq = [(q, br) for q in range(NQ) for br in range(3)]
    win = I["state_win_kv"][0].rearrange("b (j p) a g d -> p b j (a g d)", p=P)
    KJ = [0, NPAGE, WIN // P]
    ada_used, mod_step = m.sem("modulation_units_used"), m.sem("rest_of_modulation_steps")
    ada_in = [m.sem(f"modulation_unit_in_slot{s}") for s in range(4)]
    rows_ok, turned_last = m.sem("rest_of_modulation_rows"), m.sem("rest_of_modulation_turned")
    ADA = [[1, 0, 1], [1, 1, 1], [1, 1, 1]]
    NA = LATER // 2
    assert NQ * sum(map(sum, ADA)) == NA

    def kn(q, br, b):
        return q * 2 * BQ + (br - 1) * BQ + b

    with nc.Block() as block:
        @block.sync
        def _(sp):
            for q in range(NQ):
                if q:
                    sp.wait_ge(pv, 3 * (q - 1) + 2)
                    for b in range(BQ):
                        for j in range(NPAGE):
                            load_page(sp, m, I, "cache_slc_kv", BQ * q + b, j, kv[b][:, j, :], kv_in[b])
                for b in range(BQ):
                    n = BQ * q + b
                    if b >= 2:
                        sp.wait_ge(kT, kn(q, 2, b) - 1)
                    if q:
                        sp.wait_ge(pv, 3 * (q - 1) + 3)
                    sp.dma_start(kw[b % 2], win[:, n, :, 0:GD]).then_inc(k_in[b % 2], 16)
                    sp.dma_start(vw[:, b], win[:, n, :, GD:2 * GD]).then_inc(v_in, 16)

        @block.gpsimd
        def _(pool):
            for s in range(4):
                load_ada_unit(pool, m, I, EARLY + s, s, ada_in[s])
            pool.memset(sel, 0.0).then_inc(c_pool, 1)
            pool.memset(Qf, 0.0).then_inc(c_pool, 1)
            pool.memset(blk, 1.0).then_inc(c_pool, 1)
            pool.iota(iota, [[1, 32]], base=0, channel_multiplier=0, allow_small_or_imprecise_dtypes=True).then_inc(c_pool, 1)
            pool.iota(ints[:, 0:1], [[0, 1]], base=0, channel_multiplier=1).then_inc(c_pool, 1)
            pool.iota(intf, [[1, P]], base=0, channel_multiplier=0).then_inc(c_pool, 1)
            pool.memset(hp, 0.0).then_inc(c_pool, 1)
            pool.memset(drop, 0.0).then_inc(c_pool, 1)
            pool.wait_ge(c_pool, 8)
            pool.affine_select(out=sel, in_=sel, compare_op=ALU.not_equal, fill=1.0, base=0,
                               pattern=[[-8, 3], [-1, HP], [-HP, 2], [0, HD]], channel_multiplier=1).then_inc(c_pool, 1)
            b16 = blk.rearrange("p (c t) -> p c t", t=16)
            keep(pool, None, b16, [[-16, 8], [0, 16]], 0, 1).then_inc(c_pool, 1)
            pool.wait_ge(c_pool, 10)
            keep(pool, None, b16, [[16, 8], [0, 16]], 15, -1).then_inc(c_pool, 1)
            with pool.Fori(1, LATER // 4) as it:
                for s in range(4):
                    pool.wait_ge(ada_used, it * 4 + (s - 3))
                    load_ada_unit(pool, m, I, it * 4 + (EARLY + s), s, ada_in[s])

        @block.tensor
        def _(pe):
            pairs = iter(range(NA))

            def ada(n):
                for _ in range(n):
                    j = next(pairs)
                    for c in range(2):
                        pe.wait_ge(ada_in[2 * (j % 2) + c], 16 * (j // 2 + 1))
                    if j:
                        pe.wait_ge(rows_ok, j)
                    ins = ada_product(pe, m, j % 2)
                    if j:
                        ins = ada_turn(pe, m)
                    ins.then_inc(ada_used, 2)

            pe.wait_ge(c_pool, 11)
            for k in range(3):
                for h in range(HP):
                    c = (k * HP + h) * ST
                    ins = pe.matmul(ps[:, 0, c:c + ST], sel[:, k, h].rearrange("p g d -> p (g d)"), m.gnT[:, :],
                                    start=True, stop=True)
            ins.then_inc(gates_mm, 1)
            pe.wait_ge(const_ok, 1)

            def turn_keys(q, br, b):
                n = kn(q, br, b)
                if br == 1:
                    pe.wait_ge(kv_in[b], 16 * NPAGE * (q + 1))
                else:
                    pe.wait_ge(k_in[b % 2], 16 * (2 * q + b // 2 + 1))
                for j in range(KJ[br]):
                    ins = pe.transpose(ps[:, 3 + 2 * (n % 2) + j // 4, (j % 4) * P:(j % 4 + 1) * P],
                                       kv[b][:, j, 0:GD] if br == 1 else kw[b % 2][:, j, :], m.ident[:, :])
                ins.then_inc(kT, 1)

            for r, (q, br) in enumerate(seq):
                rows = lambda b: slice(RB * b, RB * b + RB)
                qcols = lambda b: Qf[:, (BQ * q + b) * RB:(BQ * q + b + 1) * RB]
                if br == 0:
                    for b in range(BQ):
                        ins = pe.matmul(ps[rows(b), 0, 0:63], qcols(b), m.ckT[:, 1 + BQ * q + b, 0:63], start=True, stop=True)
                    ins.then_inc(s_mm, 1)
                else:
                    turn_keys(q, br, 0)
                    for b in range(BQ):
                        n = kn(q, br, b)
                        if b + 1 < BQ:
                            turn_keys(q, br, b + 1)
                        pe.wait_ge(kt_act, n + 1)
                        if br == 1:
                            pe.wait_ge(kt_dve, BQ * q + b + 1)
                        for c in range(KJ[br] // 4):
                            ins = pe.matmul(ps[rows(b), c, :], qcols(b), KT[n % 2][:, 512 * c:512 * (c + 1)], start=True,
                                            stop=True)
                        ins.then_inc(k_mm, 1)
                    if r:
                        pe.wait_ge(gated, r)
                    pe.matmul(ps[:, 2, 0:ST], Qf[:, q * P:(q + 1) * P], m.zT[:, Z_KS + br - 1, SEQ:T], start=True,
                              stop=True).then_inc(s_mm, 1)
                ada(ADA[br][0])
                if br == 0:
                    pe.wait_ge(r_ok, q + 1)
                    pe.matmul(ps[:, 1, 0:63], HS, Pn[:, 0:63], start=True, stop=True).then_inc(i_mm, 1)
                pe.wait_ge(ex, r + 1)
                if r:
                    pe.wait_ge(gated, r)
                w = 63 if br == 0 else P
                for j in range(max(KJ[br], 1)):
                    ins = pe.transpose(ps[0:w, 5 + j // 4, (j % 4) * P:(j % 4 + 1) * P], S[:, j * P:j * P + w], m.ident[:, :])
                if br:
                    ins = pe.transpose(ps[0:ST, 2, P:2 * P], S[:, KJ[br] * P:KJ[br] * P + ST], m.ident[:, :])
                ins.then_inc(pT, 1)
                ada(ADA[br][1])
                pe.wait_ge(pt_act, r + 1)
                pe.wait_ge(pt_dve, r + 1)
                if br == 2:
                    pe.wait_ge(v_in, 16 * BQ * (q + 1))
                for b in range(BQ):
                    out = ps[rows(b), 2, 0:GD]
                    if br == 0:
                        ins = pe.matmul(out, PT[0:63, 0, rows(b)], m.cvt[0:63, 1 + BQ * q + b, :], start=True, stop=True)
                    else:
                        for j in range(KJ[br]):
                            pe.matmul(out, PT[:, j, rows(b)], kv[b][:, j, GD:2 * GD] if br == 1 else vw[:, b, j, :], start=j == 0, stop=False)
                        ins = pe.matmul(out, PT[0:ST, 8, rows(b)], m.vtm[0:ST, QT, br - 1, :], start=False, stop=True)
                ins.then_inc(pv, 1)
                ada(ADA[br][2])
                pe.wait_ge(on_ok, r + 1)
                pe.transpose(ps[:, 2, 2 * P:3 * P], on, m.ident[:, :]).then_inc(oT, 1)
            pe.wait_ge(rows_ok, NA)
            ada_turn(pe, m).then_inc(turned_last, 1)

        @block.scalar
        def _(act):
            pairs = iter(range(NA))

            def ada(n):
                for _ in range(n):
                    j = next(pairs)
                    act.wait_ge(ada_used, 2 * j + 2)
                    if j:
                        ada_keep(act, m, EARLY + 2 * j - 2)
                    ada_rows(act, m).then_inc(rows_ok, 1)

            for r, (q, br) in enumerate(seq):
                if r:
                    ada(ADA[seq[r - 1][1]][2])
                if br:
                    for b in range(BQ):
                        n = kn(q, br, b)
                        act.wait_ge(kT, n + 1)
                        if n >= 2:
                            act.wait_ge(k_mm, n - 1)
                        act.activation(KT[n % 2][:, 0:512], ps[:, 3 + 2 * (n % 2), :], ACT.Copy).then_inc(kt_act, 1)
                act.wait_ge(s_ok, r + 1)
                L = 63 if br == 0 else KJ[br] * P + ST
                act.activation(S[:, 0:L], ps[:, 0, 0:63] if br == 0 else S[:, 0:L], ACT.Exp, bias=nmx,
                               accum_out=den).then_inc(ex, 1)
                ada(ADA[br][0])
                act.wait_ge(pT, r + 1)
                if br == 0:
                    act.activation(PT[0:63, 0, :], ps[0:63, 5, 0:P], ACT.Copy).then_inc(pt_act, 1)
                else:
                    act.activation(PT[:, 0:4, :], ps[:, 5, :].rearrange("p (j r) -> p j r", j=4), ACT.Copy).then_inc(pt_act, 1)
                ada(ADA[br][1])
            ada(ADA[2][2])
            act.wait_ge(turned_last, 1)
            ada_keep(act, m, 48 - 2).then_inc(turned_last, 1)

        @block.vector
        def _(dve):
            steps = [0]

            def chain(ins):
                steps[0] += 1
                ins.then_inc(c_own, 1)
                dve.wait_ge(c_own, steps[0])

            dve.wait_ge(c_pool, 11)
            for g in range(2):
                for h in range(HP):
                    r = slice(64 * g, 64 * g + 64)
                    dve.tensor_scalar(Qb[r, :, g, h, :], m.zT[r, Z_Q + h, SEQ:T].rearrange("p (b t) -> p b t", t=DS),
                                      HD ** -0.5, None, ALU.mult)
            dve.tensor_scalar(ints[:, 1:2], ints[:, 0:1], 3, None, ALU.bitwise_and)
            dve.tensor_scalar(ints[:, 2:3], ints[:, 0:1], 5, None, ALU.logical_shift_right)
            chain(dve.tensor_scalar(intf, intf, 3, None, ALU.bitwise_and))
            dve.tensor_copy(tcol, ints[:, 1:2])
            dve.tensor_copy(bcol, ints[:, 2:3])
            chain(dve.tensor_copy(HS, intf))
            chain(dve.tensor_scalar(HS, HS, tcol, None, ALU.is_equal))
            chain(dve.tensor_tensor(HS, HS, blk, ALU.mult))
            dve.tensor_scalar(winm, iota[:, 0:4], tcol, NEG, ALU.is_le, ALU.mult)
            for q in range(NQ):
                chain(dve.tensor_scalar(lo, bcol, float(DS), float(DS * BQ * q), ALU.mult, ALU.add))
                chain(dve.tensor_tensor(hi, lo, tcol, ALU.add))
                chain(dve.tensor_scalar(geq, iota, lo, None, ALU.is_ge))
                chain(dve.scalar_tensor_tensor(out=newm[:, q], in0=iota, scalar=hi, in1=geq, op0=ALU.is_le, op1=ALU.mult))
                chain(dve.tensor_scalar(newm[:, q], newm[:, q], -1.0, -NEG, ALU.add, ALU.mult))
            dve.wait_ge(gates_mm, 1)
            dve.tensor_copy(gateB, ps[:, 0, 0:384].rearrange("p (k h t) -> p k h t", k=3, h=HP)).then_inc(const_ok, 1)
            for r, (q, br) in enumerate(seq):
                L = 63 if br == 0 else KJ[br] * P + ST
                if br == 1:
                    for b in range(BQ):
                        n = kn(q, br, b)
                        dve.wait_ge(kT, n + 1)
                        if n >= 2:
                            dve.wait_ge(k_mm, n - 1)
                        dve.tensor_copy(KT[n % 2][:, 512:1024], ps[:, 4 + 2 * (n % 2), :]).then_inc(kt_dve, 1)
                dve.wait_ge(s_mm, r + 1)
                if br == 0:
                    dve.tensor_reduce(nmx, ps[:, 0, 0:63], X, ALU.max, negate=True).then_inc(s_ok, 1)
                else:
                    nk = KJ[br] * P
                    if br == 1:
                        dve.tensor_tensor(S[:, 0:nk].rearrange("p (j t) -> p j t", t=SLC),
                                          ps[:, 0:2, :].rearrange("p a b -> p (a b)").rearrange("p (j t) -> p j t", t=SLC),
                                          drop.unsqueeze(2).to_broadcast([P, NSLC, SLC]), ALU.add)
                    else:
                        dve.tensor_tensor(S[:, 0:4], ps[:, 0, 0:4], winm, ALU.add)
                        dve.tensor_copy(S[:, 4:nk], ps[:, 0, 4:nk])
                    chain(dve.tensor_tensor(S[:, nk:L], ps[:, 2, 0:ST], newm[:, q], ALU.add))
                    dve.tensor_reduce(nmx, S[:, 0:L], X, ALU.max, negate=True).then_inc(s_ok, 1)
                dve.wait_ge(ex, r + 1)
                chain(dve.reciprocal(rden, den))
                if br == 0:
                    dve.tensor_scalar(Pn[:, 0:63], S[:, 0:63], rden, None, ALU.mult).then_inc(r_ok, 1)
                    dve.wait_ge(i_mm, q + 1)
                    chain(dve.tensor_copy(hp[:, 1:64], ps[:, 1, 0:63]))
                    chain(dve.tensor_reduce(imp, hp[:, 4:4 + 4 * NJ].rearrange("p (j n) -> p j n", n=4), X, ALU.add))
                    chain(dve.tensor_tensor(imp, imp, hp[:, 8:8 + 4 * NJ].rearrange("p (j n) -> p j n", n=4)[:, :, 0], ALU.add))
                    chain(dve.tensor_reduce(mn, imp, X, ALU.min))
                    chain(dve.scalar_tensor_tensor(out=t14, in0=imp, scalar=mn, in1=iota[:, 1:1 + NJ], op0=ALU.is_le,
                                                   op1=ALU.mult))
                    chain(dve.tensor_reduce(jd, t14, X, ALU.max))
                    chain(dve.tensor_scalar(drop, iota[:, 0:NSLC], jd, NEG, ALU.is_equal, ALU.mult))
                dve.wait_ge(pT, r + 1)
                if br == 1:
                    dve.tensor_copy(PT[:, 4:8, :], ps[:, 6, :].rearrange("p (j r) -> p j r", j=4))
                if br:
                    dve.tensor_copy(PT[0:ST, 8, :], ps[0:ST, 2, P:2 * P]).then_inc(pt_dve, 1)
                else:
                    dve.sem_inc(pt_dve, 1)
                dve.wait_ge(pv, r + 1)
                dve.tensor_scalar(on, ps[:, 2, 0:GD], rden, None, ALU.mult).then_inc(on_ok, 1)
                dve.wait_ge(oT, r + 1)
                toks = slice(BQ * DS * q, BQ * DS * (q + 1))
                for g in range(2):
                    gr = slice(64 * g, 64 * g + 64)
                    o = ps[gr, 2, 2 * P:3 * P].rearrange("p (b g h t) -> p g h b t", b=BQ, g=2, h=HP)[:, g]
                    gate = gateB[gr, br, :, toks].rearrange("p h (b t) -> p h b t", t=DS)
                    to = m.osT[gr, :, toks].rearrange("p h (b t) -> p h b t", t=DS)
                    if br == 0:
                        ins = dve.tensor_tensor(to, o, gate, ALU.mult)
                    else:
                        part = gt[gr].rearrange("p (h b t) -> p h b t", h=HP, b=BQ)
                        chain(dve.tensor_tensor(part, o, gate, ALU.mult))
                        ins = dve.tensor_tensor(to, to, part, ALU.add)
                ins.then_inc(gated, 1)
                dve.wait_ge(gated, r + 1)
            dve.wait_ge(turned_last, 2)
            modulation(m, dve, EARLY, 48, mod_step)


def stage_attention(m, I, O):
    nc, ps = m.nc, m.ps
    W, tail, vgf = m.work, m.tail, m.vgf
    oa = tail[:, 0:4096].rearrange("p (h i g d) -> p h i g d", h=HP, i=QT, g=2)
    Qs = tail[:, 4096:6144].rearrange("p (g t) -> p g t", g=2)
    Pb = [vgf[:, 1024 * i:1024 * (i + 1)] for i in range(2)]
    PT = [vgf[:, 2048 + 512 * i:2560 + 512 * i].rearrange("p (j q) -> p j q", j=4) for i in range(4)]
    cm = vgf[:, 4096:4608].rearrange("p (i n) -> p i n", n=64)
    cvb = W[:, 384:512]
    wc = W[:, 0:256].rearrange("p (k t) -> p k t", k=2)
    mx, den16, fac16 = W[:, 256:272], W[:, 288:304], W[:, 304:320]
    nmx = [W[:, 320 + i:321 + i] for i in range(2)]
    den = [W[:, 324 + i:325 + i] for i in range(4)]
    rden, fac = W[:, 329:330], W[:, 330:331]
    gates = m.gates[:, :, :].rearrange("p i (k g h) -> p i k g h", k=3, g=2)

    items = [(0, 0, 0)] + [(br, qt, g) for qt in range(QT) for g in range(2) for br in (1, 2)]
    N = len(items)
    keys = [None] + [list(range(max(0, qt - 4) if br == 2 else 0, qt + 1)) for br, qt, g in items[1:]]
    npc = [2] + [-(-len(k) // 4) for k in keys[1:]]
    p0 = [sum(npc[:w]) for w in range(N)]
    NPC = sum(npc)

    c_ok, zero_ok = m.sem("attention_masks"), m.sem("query_halves_zeroed")
    qs_ok, cv_ok = m.sem("queries_staged"), m.sem("compressed_values_in_blocks")
    qk, s_ok, ex = m.sem("item_scored"), m.sem("item_max_ready"), m.sem("item_exponentials")
    pT, pt, pv = m.sem("piece_turned"), m.sem("piece_copied"), m.sem("piece_summed")
    o_ok, own, oT = m.sem("item_output_added"), m.sem("attention_vector_chain"), m.sem("attention_turned")
    ow = [m.sem("attention_written_by_dve"), m.sem("attention_written_by_act")]

    def item(e, sem, it, w):
        e.wait_ge(sem, it * N + (w + 2))

    def piece(e, sem, it, p):
        e.wait_ge(sem, it * NPC + (p + 2))

    before = lambda w: w - 2 if w >= 2 else -1

    with nc.Block() as block:
        @block.sync
        def _(sp):
            prefetch_merge(sp, m, I)

        @block.gpsimd
        def _(pool):
            pool.memset(wc, 0.0).then_inc(c_ok, 1)
            pool.memset(cm, 0.0).then_inc(c_ok, 1)
            pool.wait_ge(c_ok, 2)
            pool.memset(Qs[64:128, 0, :], 0.0).then_inc(zero_ok, 1)
            pool.memset(Qs[0:64, 1, :], 0.0).then_inc(zero_ok, 1)
            pool.wait_ge(zero_ok, 2)
            pool.memset(m.ckT[:, 0, 63:64], 0.0).then_inc(zero_ok, 1)
            pool.memset(cvb, 0.0).then_inc(zero_ok, 1)
            for ap, pattern, base, mult in ((wc[:, 0, :], [[1, P]], -1, -1), (wc[:, 1, :], [[-1, P]], 0, 1),
                                            (cm, [[P, QT], [-CS, 64]], 1 - CL, 1)):
                pool.affine_select(out=ap, in_=ap, compare_op=ALU.is_ge, fill=NEG, base=base, pattern=pattern,
                                   channel_multiplier=mult).then_inc(c_ok, 1)

        @block.tensor
        def _(pe):
            pe.wait_ge(zero_ok, 4)
            pe.wait_ge(cv_ok, 2)
            for sem in (qk, pT, pv):
                pe.sem_inc(sem, 1)

            def score(it, w):
                br, qt, g = items[w]
                item(pe, ex, it, before(w))
                if w == 0:
                    pe.wait_ge(qs_ok, it * 2 + 2)
                    item(pe, ex, it, -1)
                    for i in range(QT):
                        for g in range(2):
                            c = 2 * i + g
                            ins = pe.matmul(ps[:, c // 8, (c % 8) * 64:(c % 8 + 1) * 64], Qs[:, g, i * P:(i + 1) * P],
                                            m.ckT[:, 0, :], start=True, stop=True)
                else:
                    lo, n = keys[w][0] * P, len(keys[w]) * P
                    for c in range(0, n, 512):
                        k = min(512, n - c)
                        ins = pe.matmul(ps[:, 2 * (w % 2) + c // 512, 0:k], Qs[:, g, qt * P:(qt + 1) * P],
                                        m.zT[:, Z_KS + br - 1, lo + c:lo + c + k], start=True, stop=True)
                ins.then_inc(qk, 1)

            def turn(it, w, a):
                p = p0[w] + a
                piece(pe, pt, it, before(p))
                if a == 0:
                    item(pe, ex, it, w)
                if w == 0:
                    for j in range(4):
                        ins = pe.transpose(ps[:, 4 + p % 2, j * P:(j + 1) * P], Pb[0][:, (4 * a + j) * P:(4 * a + j + 1) * P],
                                           m.ident[:, :])
                else:
                    for j in range(min(4, len(keys[w]) - 4 * a)):
                        ins = pe.transpose(ps[:, 4 + p % 2, j * P:(j + 1) * P],
                                           Pb[w % 2][:, (4 * a + j) * P:(4 * a + j + 1) * P], m.ident[:, :])
                ins.then_inc(pT, 1)

            def value(it, w, a):
                br, qt, g = items[w]
                p = p0[w] + a
                piece(pe, pt, it, p)
                if a == 0:
                    item(pe, o_ok, it, 0 if w == 1 else before(w))
                if w == 0:
                    for j in range(4):
                        ins = pe.matmul(ps[:, 6 + a, j * P:(j + 1) * P], PT[p % 4][:, j, :], cvb, start=True, stop=True)
                else:
                    n = len(keys[w])
                    for j in range(min(4, n - 4 * a)):
                        kt = 4 * a + j
                        ins = pe.matmul(ps[:, 6 + w % 2, 0:HD], PT[p % 4][:, j, :],
                                        m.vtm[:, keys[w][kt], br - 1, g * HD:(g + 1) * HD], start=kt == 0, stop=kt == n - 1)
                ins.then_inc(pv, 1)

            with pe.Fori(0, HP) as it:
                score(it, 0)
                last = None
                for w in range(N):
                    if w + 1 < N:
                        score(it, w + 1)
                    for a in range(npc[w]):
                        turn(it, w, a)
                        if last is not None:
                            value(it, *last)
                        last = (w, a)
                value(it, *last)
            item(pe, o_ok, HP, -1)
            for n in range(2 * HP):
                h, half = n // 2, n % 2
                if n >= 4:
                    pe.wait_ge(ow[n % 2], (n - 4) // 2 + 1)
                for j in range(4):
                    ins = pe.transpose(ps[:, n % 4, j * P:(j + 1) * P],
                                       oa[:, h, 4 * half + j].rearrange("p g d -> p (g d)"), m.ident[:, :])
                ins.then_inc(oT, 1)

        @block.scalar
        def _(act):
            act.sem_inc(ex, 1)
            act.sem_inc(pt, 1)
            act.wait_ge(zero_ok, 4)
            for g in range(2):
                act.activation(cvb[64 * g:64 * g + 63, HD * g:HD * (g + 1)], m.cvt[0:63, 0, HD * g:HD * (g + 1)],
                               ACT.Copy).then_inc(cv_ok, 1)

            def exps(it, w):
                item(act, s_ok, it, w)
                if w >= 2:
                    piece(act, pT, it, p0[w - 1] - 1)
                else:
                    piece(act, pT, it, -1)
                if w == 2:
                    item(act, o_ok, it, 0)
                if w == 0:
                    v = Pb[0].rearrange("p (c n) -> p c n", n=64)
                    act.activation(v, v, ACT.Exp).then_inc(ex, 1)
                else:
                    n = len(keys[w]) * P
                    act.activation(Pb[w % 2][:, 0:n],
                                   ps[:, 2 * (w % 2):2 * (w % 2) + 2, :].rearrange("p a b -> p (a b)")[:, 0:n], ACT.Exp,
                                   bias=nmx[w % 2], accum_out=den[w % 4]).then_inc(ex, 1)

            def copies(it, w):
                for a in range(npc[w]):
                    p = p0[w] + a
                    piece(act, pT, it, p)
                    piece(act, pv, it, p - 4 if p >= 4 else -1)
                    n = 4 if w == 0 else min(4, len(keys[w]) - 4 * a)
                    act.activation(PT[p % 4][:, 0:n], ps[:, 4 + p % 2, 0:n * P].rearrange("p (j q) -> p j q", j=n),
                                   ACT.Copy).then_inc(pt, 1)

            with act.Fori(0, HP) as it:
                item(act, qk, it, -1)
                for g in range(2):
                    r = slice(64 * g, 64 * g + 64)
                    act.activation(Qs[r, g:g + 1, :], m.zT[r, bass.ds(it, 1), 0:SEQ], ACT.Copy,
                                   scale=HD ** -0.5).then_inc(qs_ok, 1)
                exps(it, 0)
                for w in range(N):
                    copies(it, w)
                    if w + 1 < N:
                        exps(it, w + 1)
            for n in range(1, 2 * HP, 2):
                act.wait_ge(oT, n + 1)
                act.activation(m.zT[:, n // 2, (n % 2) * 512:(n % 2 + 1) * 512], ps[:, n % 4, :], ACT.Copy).then_inc(ow[1], 1)

        @block.vector
        def _(dve):
            dve.sem_inc(s_ok, 1)
            dve.sem_inc(o_ok, 1)
            dve.wait_ge(c_ok, 5)
            per = (N - 1) * 3 + 7
            step = [0]

            def chain(it, ins):
                step[0] += 1
                ins.then_inc(own, 1)
                dve.wait_ge(own, it * per + step[0])

            def maxima(it, w):
                br, qt, g = items[w]
                item(dve, qk, it, w)
                if w == 0:
                    v = Pb[0].rearrange("p (c n) -> p c n", n=64)
                    piece(dve, pT, it, -1)
                    chain(it, dve.tensor_tensor(v.rearrange("p (i g) n -> p i g n", g=2),
                                                ps[:, 0:2, :].rearrange("p a (i g n) -> p (a i) g n", g=2, n=64),
                                                cm.unsqueeze(2).to_broadcast([P, QT, 2, 64]), ALU.add))
                    chain(it, dve.tensor_reduce(mx, v, X, ALU.max))
                    chain(it, dve.scalar_tensor_tensor(out=mx, in0=mx, scalar=NEG / 10, in1=mx, op0=ALU.is_gt, op1=ALU.mult))
                    dve.tensor_tensor(v, v, mx.unsqueeze(2).to_broadcast([P, 16, 64]), ALU.subtract).then_inc(s_ok, 1)
                else:
                    n = len(keys[w])
                    row = ps[:, 2 * (w % 2):2 * (w % 2) + 2, :].rearrange("p a b -> p (a b)")
                    if br == 2 and qt >= 4:
                        edge = ps[:, 2 * (w % 2):2 * (w % 2) + 2, 0:P]
                        chain(it, dve.tensor_tensor(edge, edge, wc, ALU.add))
                    else:
                        edge = row[:, (n - 1) * P:n * P]
                        chain(it, dve.tensor_tensor(edge, edge, wc[:, 1, :], ALU.add))
                    dve.tensor_reduce(nmx[w % 2], row[:, 0:n * P], X, ALU.max, negate=True).then_inc(s_ok, 1)

            def output(it, w):
                br, qt, g = items[w]
                if w == 0:
                    item(dve, ex, it, 0)
                    v = Pb[0].rearrange("p (c n) -> p c n", n=64)
                    chain(it, dve.tensor_reduce(den16, v, X, ALU.add))
                    chain(it, dve.tensor_scalar(den16, den16, 1e-30, None, ALU.max))
                    chain(it, dve.reciprocal(fac16, den16))
                    chain(it, dve.tensor_tensor(fac16.rearrange("p (i g) -> p i g", g=2),
                                                fac16.rearrange("p (i g) -> p i g", g=2),
                                                gates[:, :, 0, :, bass.ds(it, 1)].rearrange("p i g o -> p i (g o)"), ALU.mult))
                    piece(dve, pv, it, p0[0] + npc[0] - 1)
                    dve.tensor_tensor(oa[:, bass.ds(it, 1)].rearrange("p o i g d -> p (o i g) d"),
                                      ps[:, 6:8, :].rearrange("p a (c d) -> p (a c) d", d=HD),
                                      fac16.unsqueeze(2).to_broadcast([P, 16, HD]), ALU.mult).then_inc(o_ok, 1)
                else:
                    piece(dve, pv, it, p0[w] + npc[w] - 1)
                    item(dve, o_ok, it, w - 1)
                    chain(it, dve.reciprocal(rden, den[w % 4]))
                    chain(it, dve.tensor_tensor(fac, rden, gates[:, qt, br, g, bass.ds(it, 1)], ALU.mult))
                    o = oa[:, bass.ds(it, 1), qt, g, :].rearrange("p o d -> p (o d)")
                    dve.scalar_tensor_tensor(out=o, in0=ps[:, 6 + w % 2, 0:HD], scalar=fac, in1=o, op0=ALU.mult,
                                             op1=ALU.add).then_inc(o_ok, 1)

            with dve.Fori(0, HP) as it:
                step[0] = 0
                maxima(it, 0)
                for w in range(N):
                    if w + 1 < N:
                        maxima(it, w + 1)
                    if w:
                        output(it, w - 1)
                output(it, N - 1)
                assert step[0] == per, (step[0], per)
            for n in range(0, 2 * HP, 2):
                dve.wait_ge(oT, n + 1)
                dve.tensor_copy(m.zT[:, n // 2, (n % 2) * 512:(n % 2 + 1) * 512], ps[:, n % 4, :]).then_inc(ow[0], 1)
            dve.tensor_copy(m.zT[:, 0:HP, SEQ:T], m.osT[:, :, :]).then_inc(ow[0], 1)


def prefetch_merge(sp, m, I):
    for u in range(GH):
        sp.dma_start(m.ring[:, u], w_block(I["w_in"][0], C_RG + u * P)).then_inc(m.w_in[u], 16)


def stage_merge(m, I, O):
    nc, ps = m.nc, m.ps
    W = m.work
    gate = [[W[:, NW * (2 * s + c):NW * (2 * s + c + 1)] for c in range(2)] for s in range(2)]
    rt = [W[:, NW * (4 + b):NW * (5 + b)] for b in range(6)]
    u0, l0 = m.used, m.loads
    summed, rbank = m.sem("r_tile_summed"), [m.sem(f"r_bank_free{b}") for b in range(6)]
    r_sig, r_mul, r_ok = m.sem("r_sigmoid"), m.sem("r_silu"), m.sem("gla_gated")
    step_mm, sig, mul, bank, add = (m.sem("merge_step_summed"), m.sem("merge_sigmoids"), m.sem("merge_products"),
                                    m.sem("merge_banks_free"), m.sem("merged_written"))
    w_in, w_n, w_g = I["w_in"][0], I["w_nsa_o"][0], I["w_gla_o"][0]

    def load(sp, j, c, slot):
        inc = m.w_in[slot]
        if c < 2:
            v = w_in[:, C_MG + D * c:C_MG + D * (c + 1)].rearrange("(k p) n -> p k n", p=P)[:, :, bass.ds(j * P, P)]
            sp.dma_start(m.ring[:, slot], v).then_inc(inc, 16)
        else:
            for g in range(2):
                v = w_n.rearrange("(g h d) n -> g d h n", g=2, h=HP)[g][:, :, bass.ds(j * P, P)]
                sp.dma_start(m.ring[64 * g:64 * g + 64, slot, 0:HP, :], v).then_inc(inc, 16)
            v = w_g.rearrange("(k p) n -> p k n", p=P)[:, :, bass.ds(j * P, P)]
            sp.dma_start(m.ring[:, slot, HP:KD, :], v).then_inc(inc, 16)

    with nc.Block() as block:
        @block.sync
        def _(sp):
            for j in range(2):
                for c in range(3):
                    slot = 3 * j + c
                    if slot < GH:
                        sp.wait_ge(m.w_used, u0 + slot + 1)
                    load(sp, j, c, slot)
            with sp.Fori(1, KD // 2) as it:
                for jj in range(2):
                    sp.wait_ge(m.w_used, it * 6 + (u0 + GH + 3 * (jj - 1)))
                    for c in range(3):
                        load(sp, it * 2 + jj, c, 3 * jj + c)
            for s in range(2):
                sp.wait_ge(m.w_used, u0 + GH + 3 * (KD - 2) + s + 1)
                sp.dma_start(m.ring[:, s], w_block(I["w_out"][0], s * P)).then_inc(m.w_in[s], 16)

        @block.tensor
        def _(pe):
            for u in range(GH):
                pe.wait_ge(m.w_in[u], 16 * (l0[u] + 1))
                for n in range(NN):
                    b = 3 * (u % 2) + n
                    if u >= 2:
                        pe.wait_ge(rbank[b], u // 2)
                    ins = product(pe, ps[:, b, 0:NW], m.ring[:, u], lambda k: m.hT[:, k, n * NW:(n + 1) * NW])
                    if n < NN - 1:
                        ins.then_inc(summed, 1)
                ins.then_inc(m.w_used, 1)
            for b in range(6):
                pe.wait_ge(rbank[b], 2)
            pe.wait_ge(r_ok, 4 * NN)
            l1 = [l0[s] + (s < GH) for s in range(SLOTS)]
            with pe.Fori(0, KD // 2) as it:
                for jj in range(2):
                    for c in range(3):
                        k = 3 if c == 2 else 1
                        pe.wait_ge(m.w_in[3 * jj + c], it * (16 * k) + 16 * (l1[3 * jj + c] + k))
                    for n in range(NN):
                        t = 3 * jj + n
                        b = 4 * (t % 2)
                        tok = slice(n * NW, (n + 1) * NW)
                        pe.wait_ge(bank, it * 6 + (t + 1))
                        last = [product(pe, ps[:, b + c, 0:NW], m.ring[:, 3 * jj + c], lambda k: m.hT[:, k, tok])
                                for c in range(2)]
                        product(pe, ps[:, b + 2, 0:NW], m.ring[:, 3 * jj + 2, 0:HP], lambda k: m.zT[:, k, tok])
                        ins = product(pe, ps[:, b + 3, 0:NW], m.ring[:, 3 * jj + 2, HP:KD], lambda k: m.oglaT[:, k, tok])
                        if n == NN - 1:
                            for x in last:
                                x.then_inc(m.w_used, 1)
                            ins.then_inc(m.w_used, 1)
                        else:
                            ins.then_inc(step_mm, 1)

        def ready(e, it, jj, n):
            if n < NN - 1:
                e.wait_ge(step_mm, it * 4 + (2 * jj + n + 1))
            else:
                e.wait_ge(m.w_used, it * 6 + (u0 + GH + 3 * jj + 3))

        def r_ready(e, u, n):
            if n < NN - 1:
                e.wait_ge(summed, 2 * u + n + 1)
            else:
                e.wait_ge(m.w_used, u0 + u + 1)

        @block.scalar
        def _(act):
            for u in range(GH):
                for n in range(NN):
                    b = 3 * (u % 2) + n
                    r_ready(act, u, n)
                    if u >= 2:
                        act.wait_ge(r_ok, 3 * (u - 2) + n + 1)
                    act.activation(rt[b], ps[:, b, 0:NW], ACT.Sigmoid).then_inc(r_sig, 1)
            with act.Fori(0, KD // 2) as it:
                for jj in range(2):
                    for n in range(NN):
                        t = 3 * jj + n
                        ready(act, it, jj, n)
                        act.wait_ge(add, it * 6 + (t + 1))
                        for c in range(2):
                            act.activation(gate[t % 2][c], ps[:, 4 * (t % 2) + c, 0:NW], ACT.Sigmoid).then_inc(sig, 1)

        @block.vector
        def _(dve):
            for u in range(GH):
                for n in range(NN):
                    b = 3 * (u % 2) + n
                    dve.wait_ge(r_sig, 3 * u + n + 1)
                    dve.tensor_tensor(rt[b], rt[b], ps[:, b, 0:NW], ALU.mult).then_inc(rbank[b], 1)
            dve.sem_inc(bank, 2)
            with dve.Fori(0, KD // 2) as it:
                for t in range(6):
                    dve.wait_ge(sig, it * 12 + (2 * t + 2))
                    for c in range(2):
                        ins = dve.tensor_tensor(gate[t % 2][c], gate[t % 2][c], ps[:, 4 * (t % 2) + 2 + c, 0:NW], ALU.mult)
                        if c == 0:
                            ins.then_inc(mul, 1)
                    ins.then_inc(bank, 1)

        @block.gpsimd
        def _(pool):
            for u in range(GH):
                for n in range(NN):
                    b = 3 * (u % 2) + n
                    og = m.oglaT[:, u, n * NW:(n + 1) * NW]
                    pool.wait_ge(rbank[b], u // 2 + 1)
                    pool.tensor_tensor(og, og, rt[b], ALU.mult).then_inc(r_ok, 1)
            pool.sem_inc(add, 2)
            with pool.Fori(0, KD // 2) as it:
                for jj in range(2):
                    for n in range(NN):
                        t = 3 * jj + n
                        pool.wait_ge(mul, it * 6 + (t + 1))
                        pool.wait_ge(bank, it * 6 + (t + 3))
                        out = m.merged[:, bass.ds(it * 2 + jj, 1), n * NW:(n + 1) * NW].rearrange("p o t -> p (o t)")
                        pool.tensor_tensor(out, gate[t % 2][0], gate[t % 2][1], ALU.add).then_inc(add, 1)
    m.used += GH + 3 * KD
    m.loads = [l0[s] + (s < GH) + (3 if s % 3 == 2 else 1) * KD // 2 for s in range(SLOTS)]


def stage_mix(m, I, O):
    nc, ps = m.nc, m.ps
    u0, l0 = m.used, m.loads
    R = m.rest
    rst, ones = R[:, 0:T], R[:, T:T + P]
    sq = [R[:, T + P + NW * b:T + P + NW * (b + 1)] for b in range(4)]
    sq2 = [m.oglaT[:, 0, 512 * i:512 * (i + 1)] for i in range(2)] + [m.oglaT[:, 1, 512 * i:512 * (i + 1)] for i in range(2)]
    sqs = m.oglaT[:, 2, 0:KD * ST].rearrange("p (k t) -> p k t", t=ST)
    tmp = m.oglaT[:, 3, :]
    xr = m.hT[:, :, :].rearrange("p k t -> p (k t)")[:, 0:QT * D].rearrange("p (i d) -> p i d", d=D)
    xs = m.vg[0:ST].rearrange("p i h v -> p (i h v)")[:, 0:D]
    x_in, summed, bank = m.sem("x_rows_in"), m.sem("mix_tile_summed"), [m.sem(f"mix_bank_free{b}") for b in range(6)]
    sq_ok, acc_ok, ss_mm, r_ok = m.sem("mix_squares"), m.sem("squares_added"), m.sem("mean_squares"), m.sem("rstd_steps")
    xT, x2_ok, sq2_ok, acc2 = m.sem("x_turned"), m.sem("residual_ready"), m.sem("residual_squares"), m.sem("residual_added")
    own, n_ok, h_ok, pre = m.sem("mix_vector_chain"), m.sem("h_scaled"), m.sem("h_ready"), m.sem("mix_constants")
    groups = [(h, k) for h in range(2) for k in range(KD)]
    G = len(groups)

    with nc.Block() as block:
        @block.sync
        def _(sp):
            sp.dma_start(xr, I["x_prompt"][0].rearrange("(i p) d -> p i d", p=P)).then_inc(x_in, 16)
            sp.dma_start(xs, I["x_sample"].rearrange("b s d -> (b s) d")).then_inc(x_in, 16)
            with sp.Fori(1, KD // 2) as it:
                for s in range(2):
                    sp.wait_ge(m.w_used, it * 2 + (u0 + s - 1))
                    sp.dma_start(m.ring[:, s], dyn_block(I["w_out"][0], it * 2 + s)).then_inc(m.w_in[s], 16)
            for hh in range(2):
                for c, w in enumerate(("w_ff_gate", "w_ff_up")):
                    sp.dma_start(m.ring[:, 2 + 2 * hh + c], w_block(I[w][0], hh * P)).then_inc(m.w_in[2 + 2 * hh + c], 16)

        @block.gpsimd
        def _(pool):
            pool.memset(ones, 1.0 / D).then_inc(pre, 1)
            pool.memset(m.acc[:, :], 0.0).then_inc(acc_ok, 1)
            pool.wait_ge(acc_ok, 1)
            pool.sem_inc(acc_ok, 1)
            with pool.Fori(0, KD // 2) as it:
                for t in range(6):
                    n = t % 3
                    a = m.acc[:, n * NW:(n + 1) * NW]
                    pool.wait_ge(sq_ok, it * 6 + (t + 1))
                    pool.wait_ge(acc_ok, it * 6 + (t + 2))
                    pool.tensor_tensor(a, a, sq[t % 4], ALU.add).then_inc(acc_ok, 1)
            pool.wait_ge(ss_mm, 1)
            pool.memset(m.acc[:, 0:SEQ], 0.0).then_inc(acc2, 1)
            for g, (h, k) in enumerate(groups):
                a = m.acc[:, 512 * h:512 * (h + 1)]
                pool.wait_ge(sq2_ok, g + 1)
                pool.wait_ge(acc2, g + 1)
                pool.tensor_tensor(a, a, sq2[g % 4], ALU.add).then_inc(acc2, 1)

        @block.tensor
        def _(pe):
            with pe.Fori(0, KD // 2) as it:
                for s in range(2):
                    pe.wait_ge(m.w_in[s], it * 16 + 16 * (l0[s] + 1))
                    for n in range(NN):
                        pe.wait_ge(bank[3 * s + n], it + 1)
                        ins = product(pe, ps[:, 3 * s + n, 0:NW], m.ring[:, s], lambda k: m.merged[:, k, n * NW:(n + 1) * NW])
                        if n < NN - 1:
                            ins.then_inc(summed, 1)
                    ins.then_inc(m.w_used, 1)
            pe.wait_ge(pre, 1)
            pe.wait_ge(acc_ok, 2 + 3 * KD)
            for b in range(3):
                pe.wait_ge(bank[b], KD // 2 + 1)
                ins = pe.matmul(ps[:, b, 0:NW], ones, m.acc[:, b * NW:(b + 1) * NW], start=True, stop=True)
            ins.then_inc(ss_mm, 1)
            pe.wait_ge(x_in, 32)
            for b in range(3, 6):
                pe.wait_ge(bank[b], KD // 2 + 1)
            for g, (h, k) in enumerate(groups):
                if g >= 4:
                    pe.wait_ge(x2_ok, g - 3)
                for i in range(4):
                    ins = pe.transpose(ps[:, 4 + g % 4, i * P:(i + 1) * P], xr[:, 4 * h + i, k * P:(k + 1) * P], m.ident[:, :])
                ins.then_inc(xT, 1)
            for k in range(KD):
                ins = pe.transpose(ps[:, 3, k * ST:(k + 1) * ST], xs[:, k * P:(k + 1) * P], m.ident[0:ST, 0:ST])
            ins.then_inc(xT, 1)
            pe.wait_ge(acc2, G + 1)
            pe.wait_ge(x2_ok, G + 2)
            pe.wait_ge(r_ok, 3)
            for b in range(3):
                ins = pe.matmul(ps[:, b, 0:NW], ones, m.acc[:, b * NW:(b + 1) * NW], start=True, stop=True)
            ins.then_inc(ss_mm, 1)

        @block.scalar
        def _(act):
            with act.Fori(0, KD // 2) as it:
                for t in range(6):
                    s, n = t // 3, t % 3
                    if n < NN - 1:
                        act.wait_ge(summed, it * 4 + (2 * s + n + 1))
                    else:
                        act.wait_ge(m.w_used, it * 2 + (u0 + s + 1))
                    act.wait_ge(acc_ok, it * 6 + (t + 1))
                    act.activation(sq[t % 4], ps[:, t, 0:NW], ACT.Square).then_inc(sq_ok, 1)
            act.wait_ge(r_ok, 2)
            act.activation(rst, rst, ACT.Sqrt).then_inc(r_ok, 1)
            for g, (h, k) in enumerate(groups):
                act.wait_ge(x2_ok, g + 1)
                if g >= 4:
                    act.wait_ge(acc2, g - 2)
                act.activation(sq2[g % 4], m.x2T[:, k, 512 * h:512 * (h + 1)], ACT.Square).then_inc(sq2_ok, 1)
            act.wait_ge(x2_ok, G + 1)
            act.activation(sqs, m.x2T[:, :, SEQ:T], ACT.Square).then_inc(sq2_ok, 1)
            act.wait_ge(r_ok, 5)
            act.activation(rst, rst, ACT.Sqrt).then_inc(r_ok, 1)
            for g, (h, k) in enumerate(groups):
                v = m.hT[:, k, 512 * h:512 * (h + 1)]
                act.wait_ge(n_ok, g + 1)
                act.activation(v, v, ACT.Identity, scale=m.modT[:, SC2 + k, 0:1], bias=m.modT[:, SH2 + k, 0:1]).then_inc(
                    h_ok, 1)

        @block.vector
        def _(dve):
            steps = [0]

            def chain(ins):
                steps[0] += 1
                ins.then_inc(own, 1)
                dve.wait_ge(own, steps[0])

            def rstd():
                for b in range(3):
                    ins = dve.tensor_scalar(rst[:, b * NW:(b + 1) * NW], ps[:, b, 0:NW], EPS, None, ALU.add)
                    if b < 2:
                        ins.then_inc(own, 1)
                        steps[0] += 1
                ins.then_inc(r_ok, 1)

            for b in range(6):
                dve.sem_inc(bank[b], 1)
            with dve.Fori(0, KD // 2) as it:
                for t in range(6):
                    s, n = t // 3, t % 3
                    dve.wait_ge(sq_ok, it * 6 + (t + 1))
                    dve.tensor_copy(m.x2T[:, bass.ds(it * 2 + s, 1), n * NW:(n + 1) * NW], ps[:, t:t + 1, 0:NW]).then_inc(
                        bank[t], 1)
            dve.wait_ge(ss_mm, 1)
            rstd()
            dve.wait_ge(own, steps[0])
            dve.wait_ge(r_ok, 1)
            dve.reciprocal(rst, rst).then_inc(r_ok, 1)
            dve.wait_ge(r_ok, 3)
            for g, (h, k) in enumerate(groups):
                v = m.x2T[:, k, 512 * h:512 * (h + 1)]
                chain(dve.tensor_tensor(v, v, rst[:, 512 * h:512 * (h + 1)], ALU.mult))
                dve.wait_ge(xT, g + 1)
                dve.scalar_tensor_tensor(out=v, in0=v, scalar=m.modT[:, GA1 + k, 0:1], in1=ps[:, 4 + g % 4, :],
                                         op0=ALU.mult, op1=ALU.add).then_inc(x2_ok, 1)
            v = m.x2T[:, :, SEQ:T]
            vb = v.rearrange("p k (b s) -> p k b s", s=DS)
            chain(dve.tensor_tensor(v, v, rst[:, SEQ:T].unsqueeze(1).to_broadcast([P, KD, ST]), ALU.mult))
            chain(dve.tensor_tensor(vb, vb, per_batch(m, GA1), ALU.mult))
            dve.wait_ge(xT, G + 1)
            dve.tensor_tensor(v, v, ps[:, 3, 0:KD * ST].rearrange("p (k t) -> p k t", t=ST), ALU.add).then_inc(x2_ok, 1)
            dve.wait_ge(sq2_ok, G + 1)
            dve.tensor_reduce(m.acc[:, SEQ:T], sqs.rearrange("p k t -> p t k"), X, ALU.add).then_inc(x2_ok, 1)
            dve.wait_ge(ss_mm, 2)
            rstd()
            dve.wait_ge(own, steps[0])
            dve.wait_ge(r_ok, 4)
            dve.reciprocal(rst, rst).then_inc(r_ok, 1)
            dve.wait_ge(r_ok, 6)
            for g, (h, k) in enumerate(groups):
                dve.tensor_tensor(m.hT[:, k, 512 * h:512 * (h + 1)], m.x2T[:, k, 512 * h:512 * (h + 1)],
                                  rst[:, 512 * h:512 * (h + 1)], ALU.mult).then_inc(n_ok, 1)
            hs = m.hT[:, :, SEQ:T]
            hb = hs.rearrange("p k (b s) -> p k b s", s=DS)
            chain(dve.tensor_tensor(hs, v, rst[:, SEQ:T].unsqueeze(1).to_broadcast([P, KD, ST]), ALU.mult))
            chain(dve.tensor_tensor(hb, hb, per_batch(m, SC2), ALU.mult))
            dve.tensor_tensor(hb, hb, per_batch(m, SH2), ALU.add).then_inc(n_ok, 1)
    m.used += KD
    m.loads = [l0[s] + (KD // 2 if s < 2 else 0) for s in range(SLOTS)]


def stage_ffn_up(m, I, O):
    nc, ps = m.nc, m.ps
    u0, l0 = m.used, m.loads
    R = m.rest
    sg = [R[:, NW * b:NW * (b + 1)] for b in range(6)]
    step_mm, sig, mid = m.sem("hidden_summed"), m.sem("hidden_sigmoid"), m.sem("hidden_silu")
    bank = m.sem("hidden_banks_free")
    IT = KF // 2

    with nc.Block() as block:
        @block.sync
        def _(sp):
            with sp.Fori(1, IT) as it:
                for hh in range(2):
                    for c, w in enumerate(("w_ff_gate", "w_ff_up")):
                        slot = 2 + 2 * hh + c
                        sp.wait_ge(m.w_used, it * 4 + (u0 + 2 * hh + c - 3))
                        sp.dma_start(m.ring[:, slot], dyn_block(I[w][0], it * 2 + hh)).then_inc(m.w_in[slot], 16)
            for u in range(2):
                for c in range(3):
                    slot = 3 * u + c
                    if slot >= 2:
                        sp.wait_ge(m.w_used, u0 + 2 * KF - 4 + slot - 2 + 1)
                    load_down(sp, m, I, u, c, slot)

        @block.tensor
        def _(pe):
            with pe.Fori(0, IT) as it:
                for hh in range(2):
                    for c in range(2):
                        pe.wait_ge(m.w_in[2 + 2 * hh + c], it * 16 + 16 * (l0[2 + 2 * hh + c] + 1))
                    for n in range(NN):
                        t = 3 * hh + n
                        pe.wait_ge(bank, it * 6 + (t + 1))
                        last = [product(pe, ps[:, 2 * n + c, 0:NW], m.ring[:, 2 + 2 * hh + c],
                                        lambda k: m.hT[:, k, n * NW:(n + 1) * NW]) for c in range(2)]
                        if n < NN - 1:
                            last[1].then_inc(step_mm, 1)
                        else:
                            for x in last:
                                x.then_inc(m.w_used, 1)

        @block.scalar
        def _(act):
            with act.Fori(0, IT) as it:
                for hh in range(2):
                    for n in range(NN):
                        if n < NN - 1:
                            act.wait_ge(step_mm, it * 4 + (2 * hh + n + 1))
                        else:
                            act.wait_ge(m.w_used, it * 4 + (u0 + 2 * hh + 2))
                        act.activation(sg[3 * hh + n], ps[:, 2 * n, 0:NW], ACT.Sigmoid).then_inc(sig, 1)

        @block.vector
        def _(dve):
            dve.sem_inc(bank, 3)
            with dve.Fori(0, IT) as it:
                for hh in range(2):
                    for n in range(NN):
                        t = 3 * hh + n
                        dve.wait_ge(sig, it * 6 + (t + 1))
                        dve.tensor_tensor(sg[t], sg[t], ps[:, 2 * n, 0:NW], ALU.mult).then_inc(mid, 1)
                        dve.wait_ge(mid, it * 6 + (t + 1))
                        dve.tensor_tensor(m.guT[:, bass.ds(it * 2 + hh, 1), n * NW:(n + 1) * NW],
                                          sg[t].unsqueeze(1), ps[:, 2 * n + 1:2 * n + 2, 0:NW], ALU.mult).then_inc(bank, 1)
    m.used += 2 * KF
    m.loads = [l0[s] + (IT if s >= 2 else 0) for s in range(SLOTS)]


DOWN = [(0, 8), (8, 16), (16, KF)]


def load_down(sp, m, I, u, c, slot):
    a, b = DOWN[c]
    v = I["w_ff_down"][0].rearrange("(k p) n -> p k n", p=P)[:, a:b, bass.ds(u * P, P)]
    sp.dma_start(m.ring[:, slot, 0:b - a, :], v).then_inc(m.w_in[slot], 16)


def stage_ffn_down(m, I, O):
    nc, ps = m.nc, m.ps
    u0, l0 = m.used, m.loads
    R = m.rest
    rst, ones = R[:, 0:T], R[:, T:T + P]
    sq = [R[:, T + P + NW * b:T + P + NW * (b + 1)] for b in range(4)]
    rows = [m.guT[:, 0:2, :].rearrange("p u t -> p (u t)")[:, D * i:D * (i + 1)] for i in range(2)]
    rows += [m.guT[:, 2:4, :].rearrange("p u t -> p (u t)")[:, D * i:D * (i + 1)] for i in range(2)]
    summed, bank = m.sem("f_tile_summed"), [m.sem(f"f_bank_free{b}") for b in range(6)]
    sq_ok, acc_ok, ss_mm, r_ok = m.sem("f_squares"), m.sem("f_squares_added"), m.sem("f_mean_squares"), m.sem("f_rstd_steps")
    own, pre, y_ok, yT, y_row = m.sem("f_vector_chain"), m.sem("f_constants"), m.sem("y_ready"), m.sem("y_turned"), m.sem("y_rows")
    stored = [m.sem(f"y_stored{i}") for i in range(4)]
    groups = [(h, k) for h in range(2) for k in range(KD)]
    G = len(groups)

    with nc.Block() as block:
        @block.sync
        def _(sp):
            with sp.Fori(1, KD // 2) as it:
                for u in range(2):
                    for c in range(3):
                        sp.wait_ge(m.w_used, it * 6 + (u0 + 3 * u + c - 5))
                        load_down(sp, m, I, it * 2 + u, c, 3 * u + c)
            for i in range(TT):
                sp.wait_ge(y_row, 2 * i + 2)
                if i < QT:
                    sp.dma_start(O["y_p"][0, i * P:(i + 1) * P, :], rows[i % 4]).then_inc(stored[i % 4], 16)
                else:
                    sp.dma_start(O["y_s"].rearrange("b s d -> (b s) d"), rows[i % 4][0:ST, :]).then_inc(stored[i % 4], 16)
            for i in range(4):
                sp.wait_ge(stored[i], 16 * len(range(i, TT, 4)))

        @block.gpsimd
        def _(pool):
            pool.memset(ones, 1.0 / D).then_inc(pre, 1)
            pool.memset(m.acc[:, :], 0.0).then_inc(acc_ok, 1)
            pool.wait_ge(acc_ok, 1)
            pool.sem_inc(acc_ok, 1)
            with pool.Fori(0, KD // 2) as it:
                for t in range(6):
                    n = t % 3
                    a = m.acc[:, n * NW:(n + 1) * NW]
                    pool.wait_ge(sq_ok, it * 6 + (t + 1))
                    pool.wait_ge(acc_ok, it * 6 + (t + 2))
                    pool.tensor_tensor(a, a, sq[t % 4], ALU.add).then_inc(acc_ok, 1)

        @block.tensor
        def _(pe):
            with pe.Fori(0, KD // 2) as it:
                for s in range(2):
                    for c, (a, b) in enumerate(DOWN):
                        pe.wait_ge(m.w_in[3 * s + c], it * 16 + 16 * (l0[3 * s + c] + 1))
                        for n in range(NN):
                            if c == 0:
                                pe.wait_ge(bank[3 * s + n], it + 1)
                            ins = product(pe, ps[:, 3 * s + n, 0:NW], m.ring[:, 3 * s + c, 0:b - a],
                                          lambda k: m.guT[:, a + k, n * NW:(n + 1) * NW], first=c == 0, last=c == 2)
                            if c == 2 and n < NN - 1:
                                ins.then_inc(summed, 1)
                        ins.then_inc(m.w_used, 1)
            pe.wait_ge(pre, 1)
            pe.wait_ge(acc_ok, 2 + 3 * KD)
            for b in range(3):
                pe.wait_ge(bank[b], KD // 2 + 1)
                ins = pe.matmul(ps[:, b, 0:NW], ones, m.acc[:, b * NW:(b + 1) * NW], start=True, stop=True)
            ins.then_inc(ss_mm, 1)
            for b in range(3, 6):
                pe.wait_ge(bank[b], KD // 2 + 1)
            pe.wait_ge(r_ok, 3)
            for i in range(TT):
                n = P if i < QT else ST
                pe.wait_ge(y_ok, G // 2 * (i // 4 + 1) if i < QT else G + 1)
                if i >= 4:
                    pe.wait_ge(y_row, 2 * (i - 3))
                for k in range(KD):
                    ins = pe.transpose(ps[0:n, 2 * (i % 4) + k // 4, (k % 4) * P:(k % 4 + 1) * P],
                                       m.x2T[:, k, i * P:i * P + n], m.ident[:, :])
                ins.then_inc(yT, 1)

        @block.scalar
        def _(act):
            with act.Fori(0, KD // 2) as it:
                for t in range(6):
                    s, n = t // 3, t % 3
                    if n < NN - 1:
                        act.wait_ge(summed, it * 4 + (2 * s + n + 1))
                    else:
                        act.wait_ge(m.w_used, it * 6 + (u0 + 3 * s + 3))
                    act.wait_ge(acc_ok, it * 6 + (t + 1))
                    act.activation(sq[t % 4], ps[:, t, 0:NW], ACT.Square).then_inc(sq_ok, 1)
            act.wait_ge(r_ok, 2)
            act.activation(rst, rst, ACT.Sqrt).then_inc(r_ok, 1)
            for i in range(TT):
                n = P if i < QT else ST
                act.wait_ge(yT, i + 1)
                if i >= 4:
                    act.wait_ge(stored[i % 4], 16 * (i // 4))
                for c in range(2):
                    act.activation(rows[i % 4][0:n, 512 * c:512 * (c + 1)], ps[0:n, 2 * (i % 4) + c, :], ACT.Copy).then_inc(
                        y_row, 1)

        @block.vector
        def _(dve):
            steps = [0]

            def chain(ins):
                steps[0] += 1
                ins.then_inc(own, 1)
                dve.wait_ge(own, steps[0])

            for b in range(6):
                dve.sem_inc(bank[b], 1)
            with dve.Fori(0, KD // 2) as it:
                for t in range(6):
                    s, n = t // 3, t % 3
                    dve.wait_ge(sq_ok, it * 6 + (t + 1))
                    dve.tensor_copy(m.hT[:, bass.ds(it * 2 + s, 1), n * NW:(n + 1) * NW], ps[:, t:t + 1, 0:NW]).then_inc(
                        bank[t], 1)
            dve.wait_ge(ss_mm, 1)
            for b in range(3):
                ins = dve.tensor_scalar(rst[:, b * NW:(b + 1) * NW], ps[:, b, 0:NW], EPS, None, ALU.add)
                if b < 2:
                    ins.then_inc(own, 1)
                    steps[0] += 1
            ins.then_inc(r_ok, 1)
            dve.wait_ge(own, steps[0])
            dve.wait_ge(r_ok, 1)
            dve.reciprocal(rst, rst).then_inc(r_ok, 1)
            dve.wait_ge(r_ok, 3)
            for g, (h, k) in enumerate(groups):
                f, v = m.hT[:, k, 512 * h:512 * (h + 1)], m.x2T[:, k, 512 * h:512 * (h + 1)]
                chain(dve.tensor_tensor(f, f, rst[:, 512 * h:512 * (h + 1)], ALU.mult))
                dve.scalar_tensor_tensor(out=v, in0=f, scalar=m.modT[:, GA2 + k, 0:1], in1=v, op0=ALU.mult,
                                         op1=ALU.add).then_inc(y_ok, 1)
            f, v = m.hT[:, :, SEQ:T], m.x2T[:, :, SEQ:T]
            fb = f.rearrange("p k (b s) -> p k b s", s=DS)
            chain(dve.tensor_tensor(f, f, rst[:, SEQ:T].unsqueeze(1).to_broadcast([P, KD, ST]), ALU.mult))
            chain(dve.tensor_tensor(fb, fb, per_batch(m, GA2), ALU.mult))
            dve.tensor_tensor(v, v, f, ALU.add).then_inc(y_ok, 1)


OUTS = [("y_p", (1, SEQ, D)), ("y_s", (NB, DS, D)),
        ("cmp_p", (1, 1, SEQ, 2, 2, HD)), ("cmp_s", (1, NB, DS, 2, 2, HD)),
        ("slc_p", (1, 1, SEQ, 2, 2, HD)), ("slc_s", (1, NB, DS, 2, 2, HD)),
        ("win_p", (1, 1, WIN, 2, 2, HD)), ("win_s", (1, NB, WIN, 2, 2, HD)),
        ("gla_p", (1, 1, GH, GDK, GDV)), ("gla_s", (1, NB, GH, GDK, GDV))]


STAGES = [stage_prepare, stage_project, stage_gla, stage_compress, stage_samples, stage_attention, stage_merge,
          stage_mix, stage_ffn_up, stage_ffn_down]


def build(nc, I, O, probe=None, upto=len(STAGES)):
    with ExitStack() as ctx:
        m = allocate(nc, ctx)
        m.n_pool = I["cache_cmp_kv"].shape[1]
        for stage in STAGES[:upto]:
            with nc.cleanup_on_exit():
                stage(m, I, O)
        if probe is not None:
            probe(m)


def kernel(**inputs):
    nc = bacc.Bacc("TRN2", target_bir_lowering=False, num_devices=1)
    arrays, I, O = {}, {}, {}
    for name, a in inputs.items():
        a = np.ascontiguousarray(a)
        arrays["in_" + name] = a
        I[name] = nc.dram_tensor("in_" + name, a.shape, mybir.dt.from_np(a.dtype), kind="ExternalInput").ap()
    for name, shape in OUTS:
        O[name] = nc.dram_tensor("out_" + name, shape, F32, kind="ExternalOutput").ap()
    build(nc, I, O)
    r = run_bass_kernel_spmd(nc, [arrays], core_ids=[0])
    return tuple(r.results[0]["out_" + name] for name, _ in OUTS)
```

```python
from contextlib import ExitStack

import numpy as np
import concourse.bacc as bacc
import concourse.bass as bass
from concourse import mybir
from concourse.bass_utils import run_bass_kernel_spmd

F32 = mybir.dt.float32
I32 = mybir.dt.int32
ALU = mybir.AluOpType
ACT = mybir.ActivationFunctionType
X = mybir.AxisListType.X

P = 128
D = 1024
KD = D // P
SEQ = 1024
QT = SEQ // P
NB = 8
DS = 4
ST = NB * DS
T = SEQ + ST
TT = QT + 1
NW = T // 3
NN = 3
PAST = 1024
PAGE = 128
NPAGE = PAST // PAGE
WIN = 512
HD = 64
HP = 4
GD = 2 * HD
GDK = 64
GDV = 128
GH = 4
RANK = 16
CH = 64
DFF = 2816
KF = DFF // P
NCOND = 1 + NB
EPS = 1e-6
NEG = -1e30
CL = 32
CS = 16
NCMP = PAST // CS - 1
SLC = 64
NSLC = PAST // SLC
SLOTS = 6

C_Q = 0
C_KVC = 512
C_KVS = C_KVC + 256
C_KVW = C_KVS + 256
C_GN = C_KVW + 256
C_QG = C_GN + 24
C_KG = C_QG + 256
C_VG = C_KG + 256
C_AG = C_VG + 512
C_RG = C_AG + RANK
C_MG = C_RG + 512

Z_Q, Z_KC, Z_KS, Z_KW, Z_QG, Z_KG, Z_VC, Z_VS, Z_VW, Z_VG, ZU = 0, 4, 5, 6, 7, 9, 11, 12, 13, 14, 18
Z_TAIL = Z_VS
SH1, SC1, GA1, SH2, SC2, GA2 = (8 * i for i in range(6))
V_BADA, V_GPRE, V_GPOST, V_GPRE2, V_GPOST2, V_GNORM, V_B1K, V_B1V, V_N = 0, 48, 56, 64, 72, 80, 81, 82, 83


class Box:
    pass


def z_columns():
    return ([C_KVC, C_KVS, C_KVW] + [C_QG, C_QG + P, C_KG, C_KG + P]
            + [C_KVC + P, C_KVS + P, C_KVW + P] + [C_VG + P * i for i in range(4)])


def allocate(nc, ctx):
    m = Box()
    m.nc = nc

    def sb(name, shape, dt=F32):
        return ctx.enter_context(nc.sbuf_tensor(name, shape, dt))

    def sem(name):
        return nc.alloc_semaphore(name)

    m.sb, m.sem = sb, sem
    m.ps = ctx.enter_context(nc.psum_tensor("ps", [P, 8, 512], F32))
    m.ring = sb("ring", [P, SLOTS, KD, P])
    m.hT = sb("hT", [P, KD, T])
    WORK = 4352
    sizes = [ZU * T, GH * T, TT * GH * GDV, TT * 2 * GD, WORK]
    at = [sum(sizes[:i]) for i in range(6)]
    m.big = sb("big", [P, at[5]])
    m.zT = m.big[:, 0:at[1]].rearrange("p (u t) -> p u t", t=T)
    m.oglaT = m.big[:, at[1]:at[2]].rearrange("p (h t) -> p h t", t=T)
    m.vg = m.big[:, at[2]:at[3]].rearrange("p (i h v) -> p i h v", i=TT, h=GH)
    m.vtm = m.big[:, at[3]:at[4]].rearrange("p (i b c) -> p i b c", i=TT, b=2)
    m.work = m.big[:, at[4]:at[5]]
    m.merged = m.zT[:, ZU - KD:ZU, :]
    m.x2T = m.zT[:, 0:KD, :]
    m.guT = m.big[:, KD * T:(KD + KF) * T].rearrange("p (u t) -> p u t", t=T)
    m.rest = m.big[:, (KD + KF) * T:at[5]]
    m.modT = sb("modT", [P, 48, NCOND])
    m.vecT = sb("vecT", [P, V_N])
    m.peT = sb("peT", [P, 64])
    m.ident = sb("ident", [P, P])
    m.acc = sb("acc", [P, T])
    m.agT = m.acc[0:32, :]
    m.gnT = sb("gnT", [24, ST])
    m.gates = sb("gates", [P, QT, 24])
    m.osT = sb("osT", [P, HP, ST])
    m.pt = sb("page_ids", [1, NB * NPAGE], I32)
    m.w2 = sb("compress_w2", [P, 2, P])
    m.cbias = sb("compress_bias", [P, 2])
    m.cT = sb("conditions", [P, KD, NCOND])
    m.ada_rows = m.work[0:NCOND, 3500:3756]
    held = m.ring[:, 4:6].rearrange("p s k n -> p (s k n)")
    m.ckT = held[:, 0:(1 + NB) * 64].rearrange("p (b n) -> p b n", n=64)
    m.cvt = held[0:64, 576:576 + (1 + NB) * GD].rearrange("p (b n) -> p b n", n=GD)
    z = m.zT[:, :, :].rearrange("p a b -> p (a b)")
    m.tail = z[:, Z_TAIL * T:ZU * T]
    m.vgf = m.vg[:, :, :, :].rearrange("p i h v -> p (i h v)")
    m.midw = z[:, Z_QG * T:Z_VC * T]
    m.past = [a.rearrange("p (j c) -> p j c", c=2 * GD) for a in (m.vgf[:, 0:2048], m.vgf[:, 2048:4096],
                                                                 m.midw[:, 0:2048], m.midw[:, 2048:4096])]
    m.narrow = m.work[:, 3880:3880 + KD * 56].rearrange("p (k n) -> p k n", n=56)
    m.narrow_in = sem("narrow_columns_in")
    ogf = m.oglaT[:, :, :].rearrange("p a b -> p (a b)")
    m.B = [ogf[:, p * T:(p + 1) * T] for p in range(2)]
    m.past_in = [sem(f"past_in_buffer{b}") for b in range(4)]
    m.w_in = [sem(f"weights_in_slot{i}") for i in range(SLOTS)]
    m.w_used = sem("weight_units_used")
    m.loads = [0] * SLOTS
    m.used = 0
    return m


def w_block(w, col, rows=D, n=P):
    return w.rearrange("(k p) n -> p k n", p=P)[:, :rows // P, col:col + n]


def dyn_block(w, unit):
    return w.rearrange("(k p) n -> p k n", p=P)[:, :, bass.ds(unit * P, P)]


def product(pe, out, w, rhs, first=True, last=True):
    nk = w.shape[1]
    for k in range(nk):
        ins = pe.matmul(out, w[:, k, :], rhs(k), start=first and k == 0, stop=last and k == nk - 1)
    return ins


def load_page(sp, m, I, cache, batch, j, out, done):
    page = sp.value_load(m.pt[0:1, bass.ds(batch * NPAGE + j, 1)], min_val=0, max_val=m.n_pool - 1)
    src = I[cache][0].rearrange("n t a g d -> n t (a g d)")[bass.ds(page, 1)]
    sp.dma_start(out, src.rearrange("o t c -> t (o c)")).then_inc(done, 16)


EARLY = 16
LATER = 48 - EARLY


def load_ada_unit(e, m, I, unit, slot, done):
    e.dma_start(m.ring[:, slot], dyn_block(I["w_ada"][0], unit)).then_inc(done, 16)


def ada_product(pe, m, pair, k0=0):
    for k in range(KD):
        ins = pe.matmul(m.ps[0:NCOND, 7, 0:2 * P], m.cT[:, k, :], m.ring[:, 2 * pair:2 * pair + 2, k, :],
                        start=k == 0, stop=k == KD - 1)
    return ins


def ada_turn(pe, m):
    for c in range(2):
        ins = pe.transpose(m.ps[:, 7, 256 + c * NCOND:256 + (c + 1) * NCOND], m.ada_rows[:, c * P:(c + 1) * P],
                           m.ident[0:NCOND, 0:NCOND])
    return ins


def ada_keep(act, m, unit):
    return act.activation(m.modT[:, bass.ds(unit, 2), :],
                          m.ps[:, 7, 256:256 + 2 * NCOND].rearrange("p (u c) -> p u c", c=NCOND), ACT.Copy)


def ada_rows(act, m):
    return act.activation(m.ada_rows[:, :], m.ps[0:NCOND, 7, 0:2 * P], ACT.Copy)


def modulation(m, dve, a, b, step):
    def col(v, n=8):
        return m.vecT[:, v:v + n].unsqueeze(2).to_broadcast([P, n, NCOND])

    dve.tensor_tensor(m.modT[:, a:b, :], m.modT[:, a:b, :], col(V_BADA + a, b - a), ALU.add).then_inc(step, 1)
    dve.wait_ge(step, 1)
    n = 1
    for sec, g, plus in ((SC1, V_GPRE, 1.0), (GA1, V_GPOST, 0.0), (SC2, V_GPRE2, 1.0), (GA2, V_GPOST2, 0.0)):
        if a <= sec < b:
            v = m.modT[:, sec:sec + 8, :]
            dve.scalar_tensor_tensor(out=v, in0=v, scalar=plus, in1=col(g), op0=ALU.add, op1=ALU.mult).then_inc(step, 1)
            n += 1
    dve.wait_ge(step, n)


def first_layer_in_ring(m):
    return m.ring[:, 0:4].rearrange("p s k n -> p (s k n)").rearrange("p (t h) -> p t h", h=P)


def load_first_layer(sp, w, to, g, done):
    r = slice(64 * g, 64 * g + 64)
    sp.dma_start(to[r, :, r], w[0].rearrange("(t d) h -> d t h", d=HD)).then_inc(done, 16)


def gelu_act(act, sums, x, u, bias, r, cmp_mm, g_act, g_dve):
    act.wait_ge(cmp_mm, r + 1)
    act.activation(x, sums, ACT.Identity, bias=bias).then_inc(g_act, 1)
    act.wait_ge(g_dve, 4 * r + 3 if isinstance(r, int) else r * 4 + 3)
    act.activation(u, u, ACT.Tanh, scale=0.7978845608028654).then_inc(g_act, 1)


def gelu_dve(dve, x, u, h, r, g_act, g_dve):
    dve.wait_ge(g_act, r * 2 + 1)
    dve.tensor_tensor(u, x, x, ALU.mult).then_inc(g_dve, 1)
    dve.wait_ge(g_dve, r * 4 + 1)
    dve.tensor_scalar(u, u, 0.044715, 1.0, ALU.mult, ALU.add).then_inc(g_dve, 1)
    dve.wait_ge(g_dve, r * 4 + 2)
    dve.tensor_tensor(u, u, x, ALU.mult).then_inc(g_dve, 1)
    dve.wait_ge(g_act, r * 2 + 2)
    dve.scalar_tensor_tensor(out=h, in0=u, scalar=1.0, in1=x, op0=ALU.add, op1=ALU.mult).then_inc(g_dve, 1)


def stage_prepare(m, I, O):
    nc, ps = m.nc, m.ps
    xs = m.zT[:, 0:9, 0:D]
    rows = m.work[:, 0:P]
    pes = m.work[0:64, P:2 * P]
    cr = m.work[0:NCOND, 1024:2048]
    junk = m.work[:, 2400:2400 + D]
    ss, ms, rec, rstd = (m.work[:, 3432 + 16 * i:3432 + 16 * i + TT] for i in range(4))
    og = m.oglaT[:, :, :].rearrange("p a b -> p (a b)")
    w1 = [a[:, 0:4096].rearrange("p (t h) -> p t h", h=P) for a in (m.vgf, m.tail)]
    pages = [a.rearrange("p (j c) -> p j c", c=2 * GD) for a in
             (m.tail[:, 4096:6144], m.midw[:, 9 * T - Z_QG * T:9 * T - Z_QG * T + 2048])]
    kt = og[:, 0:2048].rearrange("p (t b n) -> p t b n", t=CS, b=2)
    x, u, h = (og[:, 2048 + P * i:2048 + P * i + 2 * 63].rearrange("p (b n) -> p b n", b=2) for i in range(3))

    vec_in, c_in, x_in = m.sem("vectors_in"), m.sem("conditions_in"), m.sem("x_in")
    id0, rows_T, rows_out = m.sem("ident_ready"), m.sem("rows_transposed"), m.sem("row_columns_ready")
    mod_step, rows_ok, turned_last = m.sem("modulation_steps"), m.sem("modulation_rows"), m.sem("modulation_turned")
    sq_done, ms_done, sqrt_done, xn_done = (m.sem("squares_done"), m.sem("mean_square_steps"), m.sem("rstd_ready"),
                                            [m.sem("even_x_scaled"), m.sem("odd_x_scaled")])
    xT_done, ev_act, ev_dve = m.sem("x_tiles_transposed"), m.sem("h_written_by_act"), m.sem("h_written_by_dve")
    w_set = [m.sem("key_diagonals_zeroed"), m.sem("value_diagonals_zeroed")]
    w_ok = m.sem("compress_weights_in")
    pt_in, pages_in = m.sem("page_table_in"), [m.sem(f"past_pages_in{b}") for b in range(2)]
    turned = [m.sem(f"pages_turned{b}") for b in range(2)]
    kt_done, cmp_mm, bias_mm, bias_done = (m.sem("tokens_laid_out"), m.sem("compress_sums"), m.sem("bias_sums"),
                                           m.sem("bias_ready"))
    g_act, g_dve, out_mm = m.sem("gelu_by_act"), m.sem("gelu_by_dve"), m.sem("compressed_products")
    groups = [(j, h) for h in range(2) for j in range(KD)]
    NP = NB // 2
    hf = m.hT[:, :, :].rearrange("p a b -> p (a b)")
    wp = [hf[:, 4096 * kv:4096 * (kv + 1)].rearrange("p (t h) -> p t h", h=P) for kv in range(2)]
    pos = [m.work[:, 640 + P * kv:640 + P * (kv + 1)] for kv in range(2)]
    one = m.work[:, 900:901]
    pos_mul, pos_sum = m.sem("position_products"), m.sem("position_sums")
    assert 2 * 2 * NP == EARLY

    def load_past(e, it, b, first):
        if not first:
            e.wait_ge(turned[b], it * 2)
        for j in range(NPAGE):
            load_page(e, m, I, "cache_cmp_kv", it * 2 + b, j, pages[b][:, j, :], pages_in[b])

    with nc.Block() as block:
        @block.sync
        def _(sp):
            sp.dma_start(m.pt[:, :], I["page_table"].rearrange("b j -> (b j)").unsqueeze(0)).then_inc(pt_in, 16)
            for r0, a, n in ((V_BADA, I["b_ada"], 48), (V_GPRE, I["g_pre_mix"], 8), (V_GPOST, I["g_post_mix"], 8),
                             (V_GPRE2, I["g_pre_ffn"], 8), (V_GPOST2, I["g_post_ffn"], 8)):
                sp.dma_start(rows[r0:r0 + n, :], a.rearrange("o (a b) -> (o a) b", b=P)).then_inc(vec_in, 16)
            sp.dma_start(rows[V_GNORM:V_GNORM + 1, :], I["gla_norm_g"]).then_inc(vec_in, 16)
            for half in range(2):
                c = slice(half * HD, (half + 1) * HD)
                sp.dma_start(rows[V_B1K:V_B1K + 1, c], I["cmp_b1_k"]).then_inc(vec_in, 16)
                sp.dma_start(rows[V_B1V:V_B1V + 1, c], I["cmp_b1_v"]).then_inc(vec_in, 16)
                sp.dma_start(pes[0:32, c], I["cmp_pe_k"][0]).then_inc(vec_in, 16)
                sp.dma_start(pes[32:64, c], I["cmp_pe_v"][0]).then_inc(vec_in, 16)
            sp.dma_start(cr[0:1, :], I["c_prompt"]).then_inc(c_in, 16)
            sp.dma_start(cr[1:NCOND, :], I["c_sample"]).then_inc(c_in, 16)
            sp.wait_ge(pt_in, 16)

            def pair(it, first):
                load_past(sp, it, 0, first)
                for s in range(4):
                    if not first:
                        sp.wait_ge(m.w_used, it * 4 + (s - 3))
                    load_ada_unit(sp, m, I, it * 4 + s, s, m.w_in[s])

            pair(0, True)
            with sp.Fori(1, NP) as it:
                pair(it, False)
            sp.wait_ge(id0, 1)
            sp.dma_start(m.narrow[:, :, 0:RANK], w_block(I["w_in"][0], C_AG, n=RANK)).then_inc(m.narrow_in, 16)
            sp.dma_start(m.narrow[:, :, 32:56], w_block(I["w_in"][0], C_GN, n=24)).then_inc(m.narrow_in, 16)
            for s in range(2):
                sp.wait_ge(m.w_used, EARLY - 4 + s + 1)
                load_query_unit(sp, m, I, s, s)

        @block.gpsimd
        def _(pool):
            pool.memset(m.narrow[:, :, RANK:32], 0.0).then_inc(id0, 1)
            pool.wait_ge(id0, 1)
            pool.memset(m.ident[:, :], 0.0).then_inc(id0, 1)
            pool.wait_ge(id0, 2)
            pool.affine_select(out=m.ident[:, :], in_=m.ident[:, :], compare_op=ALU.not_equal, fill=1.0, base=0,
                               pattern=[[-1, P]], channel_multiplier=1).then_inc(id0, 1)
            pool.wait_ge(id0, 3)
            for i, w in enumerate((w1[0], m.w2[:, 0:1, :])):
                if i:
                    pool.wait_ge(w_set[0], 2)
                for g in range(2):
                    pool.memset(w[64 * g:64 * g + 64, :, 64 - 64 * g:128 - 64 * g], 0.0).then_inc(w_set[0], 1)
            pool.wait_ge(pt_in, 16)
            load_past(pool, 0, 1, True)
            pool.wait_ge(w_ok, 128)
            pool.wait_ge(rows_out, 3)
            pool.dma_start(xs[:, 0:QT, :], I["x_prompt"][0].rearrange("(i p) d -> p i d", p=P)).then_inc(x_in, 16)
            pool.dma_start(xs[0:ST, QT, :], I["x_sample"].rearrange("b s d -> (b s) d")).then_inc(x_in, 16)
            for kv in range(2):
                if kv:
                    pool.wait_ge(pos_mul, 1)
                pool.tensor_tensor(wp[kv], w1[kv], m.peT[:, 32 * kv:32 * kv + 32].unsqueeze(2).to_broadcast([P, CL, P]),
                                   ALU.mult).then_inc(pos_mul, 1)
            with pool.Fori(1, NP) as it:
                load_past(pool, it, 1, False)

        @block.tensor
        def _(pe):
            pe.wait_ge(id0, 3)
            pe.wait_ge(vec_in, 16 * 14)
            pe.transpose(ps[:, 6, 0:V_N], rows[0:V_N, :], m.ident[0:V_N, 0:V_N])
            pe.transpose(ps[:, 6, 128:192], pes, m.ident[0:64, 0:64])
            pe.wait_ge(c_in, 32)
            for k in range(KD):
                ins = pe.transpose(ps[:, 6, 256 + 16 * k:256 + 16 * k + NCOND], cr[:, k * P:(k + 1) * P],
                                   m.ident[0:NCOND, 0:NCOND])
            ins.then_inc(rows_T, 1)
            pe.wait_ge(rows_out, 3)

            def turn(kv, it):
                first = kv == 0 and isinstance(it, int)
                if not first:
                    pe.wait_ge(rows_ok, it * 2 + kv)
                for b in range(2):
                    if kv == 0:
                        pe.wait_ge(pages_in[b], it * 128 + 128)
                    for j in range(NPAGE):
                        ins = pe.transpose(ps[:, 2 * b + j // 4, (j % 4) * P:(j % 4 + 1) * P],
                                           pages[b][:, j, kv * GD:(kv + 1) * GD], m.ident[:, :])
                    ins.then_inc(turned[b], 1)
                if not first:
                    ada_turn(pe, m)
                for s in range(2 * kv, 2 * kv + 2):
                    pe.wait_ge(m.w_in[s], it * 16 + 16)
                ada_product(pe, m, kv).then_inc(m.w_used, 2)

            def sums(kv, it):
                pe.wait_ge(kt_done, it * 8 + 4 * (kv + 1))
                for t in range(CL):
                    ins = pe.matmul(ps[:, 4, 0:2 * 63], w1[kv][:, t, :], kt[:, t % CS, :, t // CS:t // CS + 63],
                                    start=t == 0, stop=t == CL - 1)
                ins.then_inc(cmp_mm, 1)

            def outs(kv, it):
                pe.wait_ge(g_dve, it * 8 + 4 * (kv + 1))
                if kv == 0:
                    ins = pe.matmul(ps[:, 5, 0:2 * 63], m.w2[:, 0, :], h, start=True, stop=True)
                else:
                    for b in range(2):
                        ins = pe.matmul(ps[0:63, 5, b * P:(b + 1) * P], h[:, b, :], m.w2[:, 1, :], start=True, stop=True)
                ins.then_inc(out_mm, 1)

            turn(0, 0)
            pe.wait_ge(w_ok, 128)
            sums(0, 0)
            pe.wait_ge(pos_sum, 3)
            for kv in range(2):
                ins = pe.matmul(ps[:, 6, 400 + kv:401 + kv], pos[kv], one, start=True, stop=True)
            ins.then_inc(bias_mm, 1)
            turn(1, 0)
            outs(0, 0)
            sums(1, 0)
            with pe.Fori(1, NP) as it:
                turn(0, it)
                outs(1, it - 1)
                sums(0, it)
                turn(1, it)
                outs(0, it)
                sums(1, it)
            outs(1, NP - 1)
            pe.wait_ge(rows_ok, 2 * NP)
            ada_turn(pe, m).then_inc(turned_last, 1)
            for g, (j, half) in enumerate(groups):
                if g >= 4:
                    pe.wait_ge(ev_act if g % 2 == 0 else ev_dve, (g - 4) // 2 + 1)
                for e in range(2):
                    pe.wait_ge(xn_done[e], 2 * half + 2)
                for i in range(4):
                    ins = pe.transpose(ps[:, g % 4, i * P:(i + 1) * P], xs[:, 4 * half + i, j * P:(j + 1) * P],
                                       m.ident[:, :])
                ins.then_inc(xT_done, 1)
            pe.wait_ge(xn_done[0], 5)
            for j in range(KD):
                ins = pe.transpose(ps[:, 4, j * ST:(j + 1) * ST], xs[0:ST, QT, j * P:(j + 1) * P],
                                   m.ident[0:ST, 0:ST])
            ins.then_inc(xT_done, 1)

        @block.scalar
        def _(act):
            for kv, (wa, wb) in enumerate((("cmp_w1_k", "cmp_w2_k"), ("cmp_w1_v", "cmp_w2_v"))):
                act.wait_ge(w_set[kv], 4)
                for g in range(2):
                    load_first_layer(act, I[wa], w1[kv], g, w_ok)
                    act.dma_start(m.w2[64 * g:64 * g + 64, kv, 64 * g:64 * g + 64], I[wb][0]).then_inc(w_ok, 16)

            def square(i, n):
                act.wait_ge(sq_done, i)
                act.activation(junk[0:n, :].unsqueeze(1), xs[0:n, bass.ds(i, 1), :], ACT.Square,
                               accum_out=ss[0:n, bass.ds(i, 1)]).then_inc(sq_done, 1)

            def round_(kv, it):
                for b in range(2):
                    act.wait_ge(turned[b], it * 2 + (kv + 1))
                    act.activation(kt[:, :, b, 0:32].rearrange("p t n -> p n t"),
                                   ps[:, 2 * b, :].rearrange("p (n t) -> p n t", t=CS), ACT.Copy).then_inc(kt_done, 1)
                act.wait_ge(m.w_used, it * 4 + 2 * (kv + 1))
                if not (kv == 0 and isinstance(it, int) and it == 0):
                    ada_keep(act, m, it * 4 + (2 * kv - 2))
                ada_rows(act, m).then_inc(rows_ok, 1)
                if isinstance(it, int) and it == 0:
                    if kv == 0:
                        act.wait_ge(bias_done, 2)
                    else:
                        act.wait_ge(x_in, 32)
                        act.wait_ge(ms_done, 1)
                        act.activation(junk, xs[:, 0, :], ACT.Square, accum_out=ss[:, 0:1]).then_inc(sq_done, 1)
                        for i in (1, 2):
                            square(i, P)
                else:
                    square(it * 2 + (kv + 1), ST if isinstance(it, int) and 2 * it + kv + 1 == QT else P)
                gelu_act(act, ps[:, 4, 0:2 * 63].rearrange("p (b n) -> p b n", b=2), x, u, m.cbias[:, kv:kv + 1],
                         it * 2 + kv, cmp_mm, g_act, g_dve)

            for kv in range(2):
                round_(kv, 0)
            with act.Fori(1, NP - 1) as it:
                round_(0, it)
                round_(1, it)
            for kv in range(2):
                round_(kv, NP - 1)
            act.wait_ge(turned_last, 1)
            ada_keep(act, m, EARLY - 2).then_inc(turned_last, 1)
            act.wait_ge(ms_done, 3)
            act.activation(rstd, rec, ACT.Sqrt).then_inc(sqrt_done, 1)
            act.wait_ge(sqrt_done, 1)
            for i in range(0, TT, 2):
                n = P if i < QT else ST
                act.activation(xs[0:n, i, :], xs[0:n, i, :], ACT.Copy, scale=rstd[0:n, i:i + 1]).then_inc(xn_done[0], 1)
            act.wait_ge(mod_step, 2)
            for g, (j, half) in enumerate(groups):
                if g % 2 == 0:
                    act.wait_ge(xT_done, g + 1)
                    act.activation(m.hT[:, j, half * 512:(half + 1) * 512], ps[:, g % 4, :], ACT.Identity,
                                   bias=m.modT[:, SH1 + j, 0:1], scale=m.modT[:, SC1 + j, 0:1]).then_inc(ev_act, 1)

        @block.vector
        def _(dve):
            dve.memset(ss, 1.0).then_inc(ms_done, 1)
            dve.memset(one, 1.0).then_inc(pos_sum, 1)
            for w in (w1[1], m.w2[:, 1:2, :]):
                for g in range(2):
                    dve.memset(w[64 * g:64 * g + 64, :, 64 - 64 * g:128 - 64 * g], 0.0).then_inc(w_set[1], 1)
            dve.wait_ge(rows_T, 1)
            dve.tensor_copy(m.vecT[:, :], ps[:, 6, 0:V_N]).then_inc(rows_out, 1)
            dve.tensor_copy(m.peT[:, :], ps[:, 6, 128:192]).then_inc(rows_out, 1)
            dve.tensor_copy(m.cT[:, :, :],
                            ps[:, 6, 256:384].rearrange("p (k c) -> p k c", c=16)[:, :, 0:NCOND]).then_inc(rows_out, 1)
            dve.wait_ge(rows_out, 3)

            def lay_out(kv, it):
                for b in range(2):
                    dve.wait_ge(turned[b], it * 2 + (kv + 1))
                    dve.tensor_copy(kt[:, :, b, 32:64].rearrange("p t n -> p n t"),
                                    ps[:, 2 * b + 1, :].rearrange("p (n t) -> p n t", t=CS)).then_inc(kt_done, 1)

            def write(kv, it):
                dve.wait_ge(out_mm, it * 2 + (kv + 1))
                if kv == 0:
                    dve.tensor_scalar(m.ckT[:, bass.ds(it * 2 + 1, 2), 0:63],
                                      ps[:, 5, 0:2 * 63].rearrange("p (b n) -> p b n", b=2), 0.5, None, ALU.mult)
                else:
                    dve.tensor_scalar(m.cvt[0:63, bass.ds(it * 2 + 1, 2), :],
                                      ps[0:63, 5, 0:2 * P].rearrange("p (b n) -> p b n", b=2), 0.5, None, ALU.mult)

            def bias():
                for kv in range(2):
                    dve.wait_ge(pos_mul, kv + 1)
                    dve.tensor_reduce(pos[kv], wp[kv].rearrange("p t h -> p h t"), X, ALU.add).then_inc(pos_sum, 1)
                dve.wait_ge(bias_mm, 1)
                dve.tensor_tensor(m.cbias[:, :], ps[:, 6, 400:402], m.vecT[:, V_B1K:V_B1K + 2], ALU.add).then_inc(
                    bias_done, 2)

            def pair(it, first):
                lay_out(0, it)
                if first:
                    bias()
                else:
                    write(1, it - 1)
                gelu_dve(dve, x, u, h, it * 2, g_act, g_dve)
                lay_out(1, it)
                write(0, it)
                gelu_dve(dve, x, u, h, it * 2 + 1, g_act, g_dve)

            pair(0, True)
            with dve.Fori(1, NP) as it:
                pair(it, False)
            dve.wait_ge(sq_done, TT)
            dve.tensor_scalar(ms, ss, 1.0 / D, EPS, ALU.mult, ALU.add).then_inc(ms_done, 1)
            dve.wait_ge(ms_done, 2)
            dve.reciprocal(rec, ms).then_inc(ms_done, 1)
            write(1, NP - 1)
            dve.wait_ge(sqrt_done, 1)
            for i in range(1, TT, 2):
                dve.tensor_scalar(xs[:, i, :], xs[:, i, :], rstd[:, i:i + 1], None, ALU.mult).then_inc(xn_done[1], 1)
            dve.wait_ge(turned_last, 2)
            modulation(m, dve, 0, EARLY, mod_step)
            for g, (j, half) in enumerate(groups):
                if g % 2 == 1:
                    dve.wait_ge(xT_done, g + 1)
                    dve.tensor_scalar(m.hT[:, j, half * 512:(half + 1) * 512], ps[:, g % 4, :],
                                      m.modT[:, SC1 + j, 0:1], m.modT[:, SH1 + j, 0:1], ALU.mult, ALU.add).then_inc(
                                          ev_dve, 1)
            dve.wait_ge(xT_done, 17)
            hs = m.hT[:, :, SEQ:T].rearrange("p j (b s) -> p j b s", s=DS)
            pss = ps[:, 4, 0:KD * ST].rearrange("p (j b s) -> p j b s", b=NB, s=DS)
            dve.tensor_tensor(hs, pss, per_batch(m, SC1), ALU.mult).then_inc(mod_step, 1)
            dve.wait_ge(mod_step, 3)
            dve.tensor_tensor(hs, hs, per_batch(m, SH1), ALU.add)
    m.used += EARLY
    m.loads = [EARLY // 4] * 4 + [0] * 2


def per_batch(m, sec):
    return m.modT[:, sec:sec + 8, 1:NCOND].unsqueeze(3).to_broadcast([P, 8, NB, DS])


def load_query_unit(sp, m, I, u, slot):
    for g in range(2):
        sp.dma_start(m.ring[:, slot, :, g * HD:(g + 1) * HD],
                     w_block(I["w_in"][0], C_Q + (4 * g + u) * HD, n=HD)).then_inc(m.w_in[slot], 16)


def stage_project(m, I, O):
    nc, ps = m.nc, m.ps
    NS = 4
    sgT = m.work[0:24, 0:T]
    kst = m.work[:, 1088:1088 + NS * 512].rearrange("p (b c n) -> p b c n", b=NS, c=4)
    summed = m.sem("z_tile_summed")
    bank_free = [m.sem(f"z_bank_free{b}") for b in range(6)]
    narrow_mm, narrow_out = m.sem("narrow_summed"), m.sem("narrow_written")
    a2_in, tri_ok, gate_mm, x_ok = m.sem("gate_weights_in"), m.sem("triangles_ready"), m.sem("gate_products"), m.sem("gates_copied")
    soft_step, lg_ok, cum_mm, b_ok = (m.sem("softplus_steps"), m.sem("log_gates_ready"), m.sem("log_gates_cumulated"),
                                      m.sem("cumulated_copied"))
    lg, soft = m.vgf[:, 0:2304], m.vgf[:, 2304:4608]
    tri, triS, wa2 = m.work[:, 3136:3264], m.work[0:ST, 3264:3296], m.work[0:RANK + 1, 3300:3556]
    ones_set = m.sem("gate_ones_set")
    tposed, rows_act, rows_dve = m.sem("z_tiles_transposed"), m.sem("rows_by_act"), m.sem("rows_by_dve")
    rows_out = [m.sem(f"rows_of_buffer{b}_stored") for b in range(NS)]
    win_copied = m.sem("window_rows_copied")
    w_in = I["w_in"][0]
    u0, l0 = m.used, m.loads
    QU, ZO = 4, ZU - 4
    MID = 5
    cols = z_columns()

    def stores(i):
        n = P if i < QT else ST

        def rows(name, half):
            if i < QT:
                a = O[name + "_p"][0, 0].rearrange("t a g d -> t (a g d)")
                first = i * P if name != "win" else i * P - (SEQ - WIN)
                return a[first:first + P, half * GD:(half + 1) * GD]
            a = O[name + "_s"][0].rearrange("b t a g d -> b t (a g d)")
            return a[:, WIN - DS:WIN, half * GD:(half + 1) * GD] if name == "win" else a[:, :, half * GD:(half + 1) * GD]

        if i < QT:
            both = O["cmp_p"][0, 0].rearrange("t a g d -> t a (g d)")[i * P:(i + 1) * P]
            out = [(both, kst[:, i % NS, 0:4:3])]
        else:
            out = [(rows("cmp", 0), kst[0:n, i % NS, 0]), (rows("cmp", 1), kst[0:n, i % NS, 3])]
        out += [(rows("slc", 0), kst[0:n, i % NS, 1]), (rows("slc", 1), m.vtm[0:n, i, 0, :])]
        if i >= QT - WIN // P:
            out += [(rows("win", 0), kst[0:n, i % NS, 2]), (rows("win", 1), m.vtm[0:n, i, 1, :])]
        return out

    stored = [16 * sum(len(stores(j)) for j in range(i % NS, i + 1, NS)) for i in range(TT)]

    with nc.Block() as block:
        @block.sync
        def _(sp):
            sp.dma_start(wa2[0:RANK, :], I["w_gla_a2"][0]).then_inc(a2_in, 16)
            sp.dma_start(wa2[RANK:RANK + 1, :], I["b_gla_a"]).then_inc(a2_in, 16)
            for u in range(2, ZU):
                sp.wait_ge(m.w_used, u0 + u - 1)
                if u < QU:
                    load_query_unit(sp, m, I, u, u % 2)
                else:
                    sp.dma_start(m.ring[:, u % 2], w_block(w_in, cols[u - QU])).then_inc(m.w_in[u % 2], 16)
            for i in range(TT):
                sp.wait_ge(rows_act, i + 1)
                sp.wait_ge(rows_dve, 2 * i + 2)
                for to, src in stores(i):
                    sp.dma_start(to, src).then_inc(rows_out[i % NS], 16)
            for i in range(TT - NS, TT):
                sp.wait_ge(rows_out[i % NS], stored[i])

        @block.gpsimd
        def _(pool):
            pool.dma_start(O["win_s"][0].rearrange("b t a g d -> b t (a g d)")[:, 0:WIN - DS],
                           I["state_win_kv"][0].rearrange("b t a g d -> b t (a g d)")[:, DS:WIN]).then_inc(
                               win_copied, 16)
            pool.memset(m.agT[:, :], 1.0).then_inc(ones_set, 1)
            pool.wait_ge(ones_set, 1)
            pool.memset(tri, 1.0 / 16).then_inc(tri_ok, 1)
            pool.wait_ge(tri_ok, 1)
            pool.memset(triS, 1.0 / 16).then_inc(tri_ok, 1)
            n = 2
            for ap, lo, hi in ((tri.rearrange("p (c t) -> p c t", c=2), [[64, 2], [1, 64]], [[-64, 2], [0, 64]]),
                               (triS.rearrange("p (c t) -> p c t", c=8), [[4, 8], [1, 4]], [[-4, 8], [0, 4]])):
                for pattern, mult in ((lo, -1), (hi, 1)):
                    pool.wait_ge(tri_ok, n)
                    keep(pool, tri_ok, ap, pattern, 0, mult).then_inc(tri_ok, 1)
                    n += 1
            pool.wait_ge(win_copied, 16)

        @block.tensor
        def _(pe):
            def unit(it, s):
                for n in range(NN):
                    pe.wait_ge(bank_free[3 * s + n], it + 1)
                    ins = product(pe, ps[:, 3 * s + n, 0:NW], m.ring[:, s],
                                  lambda k: m.hT[:, k, n * NW:(n + 1) * NW])
                    if n < NN - 1:
                        ins.then_inc(summed, 1)
                return ins

            pe.wait_ge(m.narrow_in, 32)
            for n in range(NN):
                product(pe, ps[0:56, n, 0:NW], m.narrow, lambda k: m.hT[:, k, n * NW:(n + 1) * NW]).then_inc(narrow_mm, 1)
            pe.wait_ge(narrow_out, 6)
            pe.wait_ge(a2_in, 32)
            for i in range(TT):
                n = P if i < QT else ST
                ins = pe.matmul(ps[0:n, i // 2, (i % 2) * 256:(i % 2) * 256 + 256], m.agT[0:RANK + 1, i * P:i * P + n],
                                wa2, start=True, stop=True)
            ins.then_inc(gate_mm, 1)

            def cumulate(p):
                for i in range(QT):
                    ins = pe.matmul(ps[:, 6 + i // 4, (i % 4) * P:(i % 4 + 1) * P],
                                    lg[:, i * 256 + p * P:i * 256 + (p + 1) * P], tri, start=True, stop=True)
                ins.then_inc(cum_mm, 1)

            with pe.Fori(0, QU // 2) as it:
                for s in range(2):
                    pe.wait_ge(m.w_in[s], it * 32 + 16 * (l0[s] + 2))
                    unit(it, s).then_inc(m.w_used, 1)
            pe.wait_ge(lg_ok, 2)
            pe.wait_ge(tri_ok, 6)
            cumulate(0)
            for part in ((0, MID - QU // 2), (MID - QU // 2, ZO // 2)):
                with pe.Fori(*part) as it:
                    for s in range(2):
                        pe.wait_ge(m.w_in[s], it * 16 + 16 * (l0[s] + QU + 1))
                        unit(it + QU // 2, s).then_inc(m.w_used, 1)
                if part[0] == 0:
                    pe.wait_ge(b_ok, 1)
                    cumulate(1)
            pe.wait_ge(b_ok, 2)
            for p in range(2):
                ins = pe.matmul(ps[:, 6, p * ST:(p + 1) * ST], lg[0:ST, QT * 256 + p * P:QT * 256 + (p + 1) * P], triS,
                                start=True, stop=True)
            ins.then_inc(cum_mm, 1)
            for b in range(6):
                pe.wait_ge(bank_free[b], ZU // 2 + 1)
            for i in range(TT):
                n = P if i < QT else ST
                tok = slice(i * P, i * P + n)
                if i >= 2:
                    pe.wait_ge(rows_act, i - 1)
                    pe.wait_ge(rows_dve, 2 * (i - 1))
                b = 3 * (i % 2)
                for c, t in enumerate((Z_KC, Z_KS, Z_KW, Z_VC)):
                    ins = pe.transpose(ps[0:n, b, c * P:(c + 1) * P], m.zT[:, t, tok], m.ident[:, :])
                ins.then_inc(tposed, 1)
                for c, t in enumerate((Z_VS, Z_VW)):
                    ins = pe.transpose(ps[0:n, b + 1, c * P:(c + 1) * P], m.zT[:, t, tok], m.ident[:, :])
                if i < QT:
                    ins = pe.transpose(ps[0:n, b + 1, 256:280], sgT[:, tok], m.ident[0:24, 0:24])
                ins.then_inc(tposed, 1)
                for h in range(GH):
                    ins = pe.transpose(ps[0:n, b + 2, h * P:(h + 1) * P], m.zT[:, Z_VG + h, tok], m.ident[:, :])
                ins.then_inc(tposed, 1)

        def ready(e, it, s, n):
            if n < NN - 1:
                e.wait_ge(summed, it * 4 + (2 * s + n + 1))
            else:
                e.wait_ge(m.w_used, it * 2 + (u0 + s + 1))

        @block.scalar
        def _(act):
            for n in range(NN):
                act.wait_ge(narrow_mm, n + 1)
                act.activation(sgT[:, n * NW:(n + 1) * NW], ps[32:56, n, 0:NW], ACT.Sigmoid).then_inc(narrow_out, 1)
            act.wait_ge(x_ok, 2)
            for b in (0, 2, 4):
                act.sem_inc(bank_free[b], 1)
            parts = [(lg[:, 0:2048], soft[:, 0:2048]), (lg[0:ST, 2048:2304], soft[0:ST, 2048:2304])]
            for step, f in enumerate((dict(func=ACT.Abs), dict(func=ACT.Exp, scale=-1.0), dict(func=ACT.Ln, bias=1.0))):
                if step:
                    act.wait_ge(soft_step, 2 * step)
                for x, y in parts:
                    act.activation(y, y if step else x, **f).then_inc(soft_step, 1)
            with act.Fori(0, ZU // 2) as it:
                for s, n in ((0, 0), (0, 2), (1, 1)):
                    ready(act, it, s, n)
                    act.activation(m.zT[:, bass.ds(it * 2 + s, 1), n * NW:(n + 1) * NW], ps[:, 3 * s + n:3 * s + n + 1, 0:NW],
                                   ACT.Copy).then_inc(bank_free[3 * s + n], 1)
            for i in range(TT):
                n = P if i < QT else ST
                act.wait_ge(tposed, 3 * i + 1)
                if i >= NS:
                    act.wait_ge(rows_out[i % NS], stored[i - NS])
                act.activation(kst[0:n, i % NS], ps[0:n, 3 * (i % 2)].rearrange("p (c n) -> p c n", c=4),
                               ACT.Copy).then_inc(rows_act, 1)

        @block.vector
        def _(dve):
            dve.wait_ge(ones_set, 1)
            dve.wait_ge(narrow_out, 3)
            for n in range(NN):
                dve.tensor_copy(m.agT[0:RANK, n * NW:(n + 1) * NW], ps[0:RANK, n, 0:NW]).then_inc(narrow_out, 1)
            dve.tensor_copy(m.gnT[:, :], sgT[:, SEQ:T])
            dve.wait_ge(gate_mm, 1)
            dve.tensor_copy(lg[:, 0:2048], ps[:, 0:4, :].rearrange("p a b -> p (a b)")).then_inc(x_ok, 1)
            dve.tensor_copy(lg[0:ST, 2048:2304], ps[0:ST, 4, 0:256]).then_inc(x_ok, 1)
            for b in (1, 3, 5):
                dve.sem_inc(bank_free[b], 1)
            dve.wait_ge(soft_step, 6)
            dve.scalar_tensor_tensor(out=lg[:, 0:2048], in0=lg[:, 0:2048], scalar=0.0, in1=soft[:, 0:2048], op0=ALU.min,
                                     op1=ALU.subtract).then_inc(lg_ok, 1)
            dve.scalar_tensor_tensor(out=lg[0:ST, 2048:2304], in0=lg[0:ST, 2048:2304], scalar=0.0,
                                     in1=soft[0:ST, 2048:2304], op0=ALU.min, op1=ALU.subtract).then_inc(lg_ok, 1)
            for p, part in enumerate(((0, QU // 2), (QU // 2, MID), (MID, ZU // 2))):
                with dve.Fori(*part) as it:
                    for s, n in ((0, 1), (1, 0), (1, 2)):
                        ready(dve, it, s, n)
                        dve.tensor_copy(m.zT[:, bass.ds(it * 2 + s, 1), n * NW:(n + 1) * NW],
                                        ps[:, 3 * s + n:3 * s + n + 1, 0:NW]).then_inc(bank_free[3 * s + n], 1)
                dve.wait_ge(cum_mm, p + 1)
                if p < 2:
                    dve.tensor_copy(m.B[p][:, 0:SEQ], ps[:, 6:8, :].rearrange("p a b -> p (a b)")).then_inc(b_ok, 1)
                else:
                    for q in range(2):
                        dve.tensor_copy(m.B[q][:, SEQ:T], ps[:, 6, q * ST:(q + 1) * ST])
            for i in range(TT):
                n = P if i < QT else ST
                b = 3 * (i % 2)
                dve.wait_ge(tposed, 3 * i + 2)
                if i < QT:
                    dve.tensor_copy(m.gates[:, i, :], ps[:, b + 1, 256:280])
                dve.tensor_copy(m.vtm[0:n, i], ps[0:n, b + 1, 0:256].rearrange("p (c n) -> p c n", c=2)).then_inc(
                    rows_dve, 1)
                dve.wait_ge(tposed, 3 * i + 3)
                dve.tensor_copy(m.vg[0:n, i], ps[0:n, b + 2, :].rearrange("p (c n) -> p c n", c=4)).then_inc(
                    rows_dve, 1)
    m.used += ZU
    m.loads = [l0[0] + QU + ZO // 2, l0[1] + QU + ZO // 2] + l0[2:]


def keep(pool, done, ap, pattern, base, mult):
    ins = pool.affine_select(out=ap, in_=ap, compare_op=ALU.is_ge, fill=0.0, base=base, pattern=pattern,
                             channel_multiplier=mult)
    return ins


def stage_gla(m, I, O):
    nc, ps = m.nc, m.ps
    tail = m.zT[:, Z_TAIL:ZU, :].rearrange("p a b -> p (a b)")
    ogf = m.oglaT[:, :, :].rearrange("p a b -> p (a b)")
    W = m.work
    D2 = [tail[:, i * T:(i + 1) * T] for i in range(2)]
    S = tail[:, 0:17 * GDV].rearrange("p (c v) -> p c v", v=GDV)
    E2 = [tail[:, 2176 + i * T:2176 + (i + 1) * T] for i in range(2)]
    kl = tail[:, 4288:4288 + 2048].rearrange("p (i c k) -> p i c k", i=QT, c=2)
    sqb = [tail[:, 4288 + 512 * i:4288 + 512 * i + 512] for i in range(2)]
    S0 = E2[0][:, 0:NB * GDV].rearrange("p (b v) -> p b v", v=GDV)
    B = m.B
    Qd, Kd = ogf[:, 2 * T:3 * T], ogf[:, 3 * T:4 * T]
    Qo, Ko = W[:, 0:T], W[:, T:2 * T]
    am = W[:, 2112:2112 + 1024].rearrange("p (b x) -> p b x", b=2)
    M12 = W[:, 3264:3520].rearrange("p (k t) -> p k t", k=2)
    mS, bm = W[0:ST, 3520:3552], W[0:ST, 3584:3592]
    eiB = W[:, 3848:3848 + 288]
    amS = W[0:ST, 4136:4200]
    decay = W[:, 4200:4224]
    ss, ms, rec, rstd = (W[:, 64 * i:64 * i + TT * GH] for i in range(4))
    klB = kl[0:ST].rearrange("p i c k -> p (i c) k")[:, 0:NB, :]
    klS = W[0:ST, 2112:2112 + P]

    s0_in, gla_out = m.sem("sample_states_in"), m.sem("gla_states_stored")
    cst = m.sem("gla_masks_steps")
    d_ready, e_ready, m_done, own = (m.sem("decay_exponents"), m.sem("decay_factors"), m.sem("operands_decayed"),
                                     m.sem("gla_vector_steps"))
    kl_T, kl_done, kv_mm, s_done = (m.sem("keys_transposed"), m.sem("keys_copied"), m.sem("state_products"),
                                    m.sem("states_advanced"))
    a_mm, a_done, o_mm, o_done = m.sem("gla_scores"), m.sem("gla_scores_masked"), m.sem("gla_sums"), m.sem("gla_kept")
    smp, smp_pe, zeroed = m.sem("sample_vector_steps"), m.sem("sample_products"), m.sem("halves_zeroed")
    smp_own = m.sem("sample_scores_applied")
    sq, nrm, nrm_own, oT, ow = (m.sem("gla_squares"), m.sem("gla_rstd"), m.sem("gla_norm_steps"), m.sem("gla_transposed"),
                           m.sem("gla_written"))
    scaled = m.sem("gla_scaled")
    w1_zero, w1_in = m.sem("first_layer_zeroed"), m.sem("first_layer_in")
    w1k = first_layer_in_ring(m)

    with nc.Block() as block:
        @block.sync
        def _(sp):
            sp.wait_ge(w1_zero, 2)
            for g in range(2):
                load_first_layer(sp, I["cmp_w1_k"], w1k, g, w1_in)
            sp.wait_ge(w1_in, 32)
            for p in range(2):
                sp.wait_ge(m_done, 6 * p + 6)
                sp.dma_start(S0, I["state_gla"][0].rearrange("b (q h) k v -> q (h k) b v", q=2)[p]).then_inc(s0_in, 16)
                sp.wait_ge(s_done, (p + 1) * 32)
                sp.dma_start(O["gla_p"][0, 0].rearrange("(q h) k v -> q (h k) v", q=2)[p], S[:, 16, :]).then_inc(
                    gla_out, 16)
                sp.wait_ge(smp, p * 8 + 8)
                sp.dma_start(O["gla_s"][0].rearrange("b (q h) k v -> q (h k) b v", q=2)[p], S0).then_inc(gla_out, 16)
            sp.wait_ge(gla_out, 64)

        @block.gpsimd
        def _(pool):
            for g in range(2):
                pool.memset(w1k[64 * g:64 * g + 64, :, 64 - 64 * g:128 - 64 * g], 0.0).then_inc(w1_zero, 1)
            pool.wait_ge(w1_zero, 2)
            m1 = M12[:, 0, :]
            m2 = M12[:, 1, :].rearrange("p (c h t) -> p c h t", c=2, h=2)
            n = 0
            for ins in (pool.memset(M12, 0.0), pool.memset(mS, 1.0), pool.memset(bm, 1.0)):
                ins.then_inc(cst, 1)
                n += 1
            pool.wait_ge(cst, n)
            pool.memset(m1, 1.0).then_inc(cst, 1)
            pool.memset(m2[:, :, 1, :], 1.0).then_inc(cst, 1)
            n += 2
            pool.wait_ge(cst, n)
            first = [(m1.rearrange("p (c t) -> p c t", c=4), [[32, 4], [1, 32]], 0, -1),
                     (m2[:, :, 1, :], [[-64, 2], [0, 32]], 0, 1),
                     (mS.rearrange("p (c t) -> p c t", c=8), [[4, 8], [1, 4]], 0, -1),
                     (bm, [[-4, 8]], 0, 1)]
            second = [(m1.rearrange("p (c t) -> p c t", c=4), [[-32, 4], [0, 32]], 0, 1),
                      (m2[:, :, 1, :], [[64, 2], [0, 32]], 31, -1),
                      (mS.rearrange("p (c t) -> p c t", c=8), [[-4, 8], [0, 4]], 0, 1),
                      (bm, [[4, 8]], 3, -1)]
            for group in (first, second):
                for ap, pattern, base, mult in group:
                    keep(pool, cst, ap, pattern, base, mult).then_inc(cst, 1)
                    n += 1
                pool.wait_ge(cst, n)
            pool.memset(Qo[:, 0:SEQ].rearrange("p (c h t) -> p c h t", h=2, t=32)[:, :, 0, :], 0.0).then_inc(cst, 1)
            pool.memset(Ko[:, 0:SEQ].rearrange("p (c h t) -> p c h t", h=2, t=32)[:, :, 1, :], 0.0).then_inc(cst, 1)
            pool.memset(eiB, 0.0).then_inc(cst, 1)
            pool.wait_ge(cst, 16)
            for p in range(2):
                if p:
                    pool.wait_ge(smp, 8)
                pool.memset(kl[0:64, :, 1, :], 0.0).then_inc(zeroed, 1)
                pool.memset(kl[64:128, :, 0, :], 0.0).then_inc(zeroed, 1)

        @block.tensor
        def _(pe):
            for p in range(2):
                q, k = m.zT[:, Z_QG + p, :], m.zT[:, Z_KG + p, :]
                pe.wait_ge(m_done, 6 * p + 6)
                for i in range(QT):
                    ins = pe.transpose(ps[:, i // 4, (i % 4) * P:(i % 4 + 1) * P], k[:, i * P:(i + 1) * P], m.ident[:, :])
                ins.then_inc(kl_T, 1)
                pe.wait_ge(kl_done, 5 * p + 4)
                for j in range(2 * QT):
                    if j >= 4:
                        pe.wait_ge(s_done, 32 * p + 2 * (j - 4) + 2)
                    pe.matmul(ps[:, 4 + j % 4, 0:256], kl[:, j // 2, j % 2, :],
                              m.vg[:, j // 2, 2 * p:2 * p + 2, :].rearrange("p h v -> p (h v)"),
                              start=True, stop=True).then_inc(kv_mm, 1)
                    pe.matmul(ps[:, 3, 0:P], m.ident[:, :], m.ident[:, :], start=True, stop=True)
                pe.wait_ge(s_done, 32 * p + 32)

                def scores(i):
                    for hh in range(2):
                        r = slice(64 * hh, 64 * hh + 64)
                        tok = slice(i * P, (i + 1) * P)
                        pe.matmul(ps[:, 2 * (i % 2) + hh, 0:P], Kd[r, tok], Qd[r, tok], start=True, stop=True)
                        ins = pe.matmul(ps[:, 2 * (i % 2) + hh, P:2 * P], Ko[r, tok], Qo[r, tok], start=True, stop=True)
                    ins.then_inc(a_mm, 1)

                def sums(i):
                    for hh in range(2):
                        r = slice(64 * hh, 64 * hh + 64)
                        bank = 4 + 2 * (i % 2) + hh
                        v = m.vg[:, i, 2 * p + hh, :]
                        for a in range(2):
                            pe.matmul(ps[:, bank, 0:P], am[:, i % 2, (2 * hh + a) * P:(2 * hh + a + 1) * P], v, start=a == 0, stop=False)
                        for c in range(2):
                            ins = pe.matmul(ps[64 * c:64 * c + 64, bank, 0:P],
                                            q[r, i * P + 64 * c:i * P + 64 * c + 64], S[r, 2 * i + c, :], start=False, stop=True)
                    ins.then_inc(o_mm, 1)

                scores(0)
                for i in range(QT):
                    if i + 1 < QT:
                        if i >= 1:
                            pe.wait_ge(a_done, QT * p + i)
                        scores(i + 1)
                    pe.wait_ge(a_done, QT * p + i + 1)
                    if i >= 2:
                        pe.wait_ge(o_done, QT * p + i - 1)
                    sums(i)
                pe.wait_ge(o_done, QT * p + QT)
                pe.transpose(ps[0:ST, 0, 0:P], k[:, SEQ:T], m.ident[:, :])
                for hh in range(2):
                    r = slice(64 * hh, 64 * hh + 64)
                    ins = pe.matmul(ps[0:ST, 1 + hh, 0:ST], Kd[r, SEQ:T], Qd[r, SEQ:T], start=True, stop=True)
                ins.then_inc(smp_pe, 1)
                pe.wait_ge(smp, 8 * p + 4)
                pe.wait_ge(s0_in, 16 * p + 16)
                for hh in range(2):
                    ins = pe.matmul(ps[0:ST, 6 + hh, 0:P], amS[:, hh * ST:(hh + 1) * ST], m.vg[0:ST, QT, 2 * p + hh, :],
                                    start=True, stop=False)
                ins.then_inc(smp_own, 1)
                pe.wait_ge(smp_own, p + 1)
                for hh in range(2):
                    r = slice(64 * hh, 64 * hh + 64)
                    out = ps[0:ST, 6 + hh, 0:P]
                    for b in range(NB):
                        ins = pe.matmul(out, eiB[r, b * ST:(b + 1) * ST], S0[r, b, :], start=False, stop=b == NB - 1)
                ins.then_inc(smp_pe, 1)
                for b in range(NB):
                    for hh in range(2):
                        ins = pe.matmul(ps[64 * hh:64 * hh + 64, 4 + b // 4, (b % 4) * P:(b % 4 + 1) * P],
                                        klB[:, b, 64 * hh:64 * hh + 64], m.vg[0:ST, QT, 2 * p + hh, :],
                                        start=True, stop=True)
                ins.then_inc(smp_pe, 1)
                pe.wait_ge(smp, 8 * p + 8)
            for i in range(TT):
                n = P if i < QT else ST
                pe.wait_ge(scaled, i + 1)
                if i >= 4:
                    pe.wait_ge(ow, i - 3)
                for h in range(GH):
                    ins = pe.transpose(ps[:, i % 4, h * P:h * P + n], m.vg[0:n, i, h, :], m.ident[0:n, 0:n])
                ins.then_inc(oT, 1)

        @block.scalar
        def _(act):
            for p in range(2):
                half = lambda a, h: a[:, 0:SEQ].rearrange("p (c h t) -> p c h t", h=2, t=32)[:, :, h, :]
                for dr, md, out, inp, sign in (
                        (3 * p + 1, 6 * p, E2[0], D2[0], 1.0), (3 * p + 1, 6 * p, E2[1], D2[0], -1.0),
                        (3 * p + 2, 6 * p + 1, half(E2[0], 1), half(D2[1], 1), 1.0),
                        (3 * p + 2, 6 * p + 2, half(E2[1], 0), half(D2[1], 0), -1.0),
                        (3 * p + 2, 6 * p + 3, E2[0], B[p], 1.0), (3 * p + 3, 6 * p + 4, E2[1], D2[0], 1.0)):
                    act.wait_ge(d_ready, dr)
                    if md:
                        act.wait_ge(m_done, md)
                    act.activation(out, inp, ACT.Exp, scale=sign).then_inc(e_ready, 1)
                act.activation(decay[:, 0:16], B[p][:, 0:SEQ].rearrange("p (c t) -> p c t", t=CH)[:, :, CH - 1],
                               ACT.Exp).then_inc(e_ready, 1)
                act.activation(decay[:, 16:24], B[p][:, SEQ:T].rearrange("p (c t) -> p c t", t=DS)[:, :, DS - 1],
                               ACT.Exp).then_inc(e_ready, 1)
                act.wait_ge(kl_T, p + 1)
                act.wait_ge(zeroed, 2 * p + 2)
                for c in range(2):
                    for g in range(2):
                        r = slice(64 * c, 64 * c + 64)
                        act.activation(kl[r, 4 * g:4 * g + 4, c, :], ps[r, g, :].rearrange("p (i k) -> p i k", i=4),
                                       ACT.Copy).then_inc(kl_done, 1)
                act.wait_ge(smp, 8 * p + 8)
                act.sem_inc(kl_done, 1)
            for i in range(TT):
                n = P if i < QT else ST
                if i >= 2:
                    act.wait_ge(nrm, i - 1)
                act.wait_ge(smp, 16)
                act.activation(sqb[i % 2][0:n], m.vg[0:n, i].rearrange("p h v -> p (h v)"), ACT.Square).then_inc(sq, 1)
            act.wait_ge(nrm, TT + 2)
            act.activation(rstd, rec, ACT.Sqrt).then_inc(sq, 1)
            act.wait_ge(sq, TT + 1)
            for i in range(TT):
                n = P if i < QT else ST
                act.wait_ge(oT, i + 1)
                act.activation(m.oglaT[:, :, i * P:i * P + n], ps[:, i % 4, :].rearrange("p (h t) -> p h t", h=GH)[:, :, 0:n],
                               ACT.Copy, scale=m.vecT[:, V_GNORM:V_GNORM + 1]).then_inc(ow, 1)

        @block.vector
        def _(dve):
            steps = [0]

            def chain(ins):
                steps[0] += 1
                ins.then_inc(own, 1)
                dve.wait_ge(own, steps[0])

            def blocks(a, n, lo=0, hi=SEQ):
                return a[:, lo:hi].rearrange("p (c t) -> p c t", t=n)

            def at(a, n, t, lo=0, hi=SEQ):
                v = blocks(a, n, lo, hi)
                return v[:, :, t:t + 1].to_broadcast([P, v.shape[1], n])

            for p in range(2):
                b, q, k = B[p], m.zT[:, Z_QG + p, :], m.zT[:, Z_KG + p, :]
                if p:
                    dve.wait_ge(e_ready, 8)
                    dve.wait_ge(gla_out, 32)
                dve.tensor_tensor(blocks(D2[0], 32), blocks(b, 32), at(b, 32, 15), ALU.subtract)
                chain(dve.tensor_tensor(blocks(D2[0], DS, SEQ, T), blocks(b, DS, SEQ, T), at(b, DS, 0, SEQ, T),
                                        ALU.subtract))
                dve.tensor_scalar(D2[0], D2[0], -40.0, 40.0, ALU.max, ALU.min).then_inc(d_ready, 1)
                dve.tensor_tensor(blocks(D2[1], CH), blocks(b, CH), at(b, CH, 31), ALU.subtract).then_inc(d_ready, 1)
                dve.wait_ge(e_ready, 8 * p + 1)
                dve.scalar_tensor_tensor(out=Qd, in0=E2[0], scalar=GDK ** -0.5, in1=q, op0=ALU.mult,
                                         op1=ALU.mult).then_inc(m_done, 1)
                dve.wait_ge(e_ready, 8 * p + 2)
                dve.tensor_tensor(Kd, E2[1], k, ALU.mult).then_inc(m_done, 1)
                dve.tensor_tensor(blocks(D2[0], CH), at(b, CH, CH - 1), blocks(b, CH), ALU.subtract)
                chain(dve.tensor_tensor(blocks(D2[0], DS, SEQ, T), at(b, DS, DS - 1, SEQ, T), blocks(b, DS, SEQ, T),
                                        ALU.subtract))
                dve.sem_inc(d_ready, 1)
                half = lambda a, h: a[:, 0:SEQ].rearrange("p (c h t) -> p c h t", h=2, t=32)[:, :, h, :]
                dve.wait_ge(e_ready, 8 * p + 3)
                if p == 0:
                    dve.wait_ge(cst, 16)
                dve.scalar_tensor_tensor(out=half(Qo, 1), in0=half(E2[0], 1), scalar=GDK ** -0.5, in1=half(q, 1),
                                         op0=ALU.mult, op1=ALU.mult).then_inc(m_done, 1)
                dve.wait_ge(e_ready, 8 * p + 4)
                dve.tensor_tensor(half(Ko, 0), half(E2[1], 0), half(k, 0), ALU.mult).then_inc(m_done, 1)
                dve.wait_ge(m_done, 6 * p + 4)
                dve.wait_ge(e_ready, 8 * p + 5)
                dve.scalar_tensor_tensor(out=q, in0=E2[0], scalar=GDK ** -0.5, in1=q, op0=ALU.mult,
                                         op1=ALU.mult).then_inc(m_done, 1)
                dve.wait_ge(e_ready, 8 * p + 6)
                dve.tensor_tensor(k, E2[1], k, ALU.mult).then_inc(m_done, 1)
                dve.wait_ge(e_ready, 8 * p + 8)
                chain(dve.memset(S[:, 0, :], 0.0))
                for j in range(2 * QT):
                    dve.wait_ge(kv_mm, 2 * QT * p + j + 1)
                    for hh in range(2):
                        r = slice(64 * hh, 64 * hh + 64)
                        ins = dve.scalar_tensor_tensor(out=S[r, j + 1, :], in0=S[r, j, :], scalar=decay[r, j:j + 1],
                                                       in1=ps[r, 4 + j % 4, hh * P:(hh + 1) * P], op0=ALU.mult,
                                                       op1=ALU.add)
                        ins.then_inc(s_done, 1)
                    dve.wait_ge(s_done, 32 * p + 2 * j + 2)

                def mask(i):
                    dve.wait_ge(a_mm, QT * p + i + 1)
                    if i >= 2:
                        dve.wait_ge(o_mm, QT * p + i - 1)
                    dve.scalar_tensor_tensor(out=am[:, i % 2].rearrange("p (h x) -> p h x", h=2),
                                             in0=ps[:, 2 * (i % 2):2 * (i % 2) + 2, 0:2 * P], scalar=3e38,
                                             in1=M12.rearrange("p k t -> p (k t)").unsqueeze(1).to_broadcast([P, 2, 2 * P]),
                                             op0=ALU.min, op1=ALU.mult).then_inc(a_done, 1)

                for i in range(QT + 1):
                    if i < QT:
                        mask(i)
                    if i:
                        dve.wait_ge(o_mm, QT * p + i)
                        dve.tensor_copy(m.vg[:, i - 1, 2 * p:2 * p + 2, :],
                                        ps[:, 4 + 2 * ((i - 1) % 2):6 + 2 * ((i - 1) % 2), 0:P]).then_inc(
                                            o_done, 1)
                dve.wait_ge(smp_pe, 3 * p + 1)
                dve.tensor_copy(klS, ps[0:ST, 0, 0:P]).then_inc(smp, 1)
                dve.tensor_tensor(amS.rearrange("p (h t) -> p h t", h=2),
                                  ps[0:ST, 1:3, 0:ST],
                                  mS.unsqueeze(1).to_broadcast([ST, 2, ST]), ALU.mult).then_inc(smp, 1)
                dve.tensor_copy(eiB.rearrange("p (b x) -> p b x", x=ST + DS)[:, :, 0:DS],
                                q[:, SEQ:T].rearrange("p (b s) -> p b s", s=DS)).then_inc(smp, 1)
                dve.wait_ge(smp, 8 * p + 3)
                dve.wait_ge(kv_mm, 2 * QT * (p + 1))
                dve.tensor_tensor(klB, klS.unsqueeze(1).to_broadcast([ST, NB, P]), bm.unsqueeze(2).to_broadcast([ST, NB, P]),
                                  ALU.mult).then_inc(smp, 1)
                dve.wait_ge(smp_pe, 3 * p + 3)
                dve.tensor_copy(m.vg[0:ST, QT, 2 * p:2 * p + 2, :],
                                ps[0:ST, 6:8, 0:P]).then_inc(smp, 1)
                dve.tensor_tensor(S0, S0, decay[:, 16:24].unsqueeze(2).to_broadcast([P, NB, GDV]), ALU.mult).then_inc(smp, 1)
                dve.wait_ge(smp, 8 * p + 6)
                for g in range(2):
                    dve.tensor_tensor(S0[:, 4 * g:4 * g + 4, :], S0[:, 4 * g:4 * g + 4, :],
                                      ps[:, 4 + g, :].rearrange("p (b v) -> p b v", b=4), ALU.add).then_inc(smp, 1)
            chain(dve.memset(ss, 1.0))
            for i in range(TT):
                n = P if i < QT else ST
                dve.wait_ge(sq, i + 1)
                dve.tensor_reduce(ss[0:n, i * GH:(i + 1) * GH], sqb[i % 2][0:n].rearrange("p (h v) -> p h v", h=GH),
                                  X, ALU.add).then_inc(nrm, 1)
            dve.wait_ge(nrm, TT)
            dve.tensor_scalar(ms, ss, 1.0 / GDV, EPS, ALU.mult, ALU.add).then_inc(nrm, 1)
            dve.wait_ge(nrm, TT + 1)
            dve.reciprocal(rec, ms).then_inc(nrm, 1)
            dve.wait_ge(sq, TT + 1)
            for i in range(TT):
                n = P if i < QT else ST
                dve.tensor_tensor(m.vg[0:n, i], m.vg[0:n, i],
                                  rstd[0:n, i * GH:(i + 1) * GH].unsqueeze(2).to_broadcast([n, GH, GDV]),
                                  ALU.mult).then_inc(scaled, 1)


def stage_compress(m, I, O):
    nc, ps = m.nc, m.ps
    w1 = [first_layer_in_ring(m), m.tail[:, 0:4096].rearrange("p (t h) -> p t h", h=P)]
    kt = [m.work[:, 1024 * i:1024 * (i + 1)].rearrange("p (t n) -> p t n", t=CS) for i in range(2)]
    x, u, h = ([m.work[:, 2048 + 128 * i + 64 * kv:2048 + 128 * i + 64 * kv + 63] for kv in range(2)] for i in range(3))
    w_set, w_ok = m.sem("prompt_block_diagonal_zeroed"), m.sem("prompt_value_weights_in")
    kt_done, cmp_mm = m.sem("prompt_tokens_laid_out"), m.sem("prompt_compress_sums")
    g_act, g_dve, out_mm = m.sem("prompt_gelu_by_act"), m.sem("prompt_gelu_by_dve"), m.sem("prompt_compressed_products")

    with nc.Block() as block:
        @block.sync
        def _(sp):
            sp.wait_ge(w_set, 2)
            for g in range(2):
                load_first_layer(sp, I["cmp_w1_v"], w1[1], g, w_ok)
            for b in range(2):
                for j in range(NPAGE):
                    load_page(sp, m, I, "cache_slc_kv", b, j, m.past[b][:, j, :], m.past_in[b])

        @block.gpsimd
        def _(pool):
            for g in range(2):
                pool.memset(w1[1][64 * g:64 * g + 64, :, 64 - 64 * g:128 - 64 * g], 0.0).then_inc(w_set, 1)
            for b in range(2, 4):
                for j in range(NPAGE):
                    load_page(pool, m, I, "cache_slc_kv", b, j, m.past[b][:, j, :], m.past_in[b])

        @block.tensor
        def _(pe):
            for kv in range(2):
                if kv:
                    pe.wait_ge(w_ok, 32)
                pe.wait_ge(kt_done, 2)
                for t in range(CL):
                    ins = pe.matmul(ps[:, kv, 0:63], w1[kv][:, t, :], kt[kv][:, t % CS, t // CS:t // CS + 63],
                                    start=t == 0, stop=t == CL - 1)
                ins.then_inc(cmp_mm, 1)
            for kv in range(2):
                pe.wait_ge(g_dve, 4 * kv + 4)
                if kv == 0:
                    ins = pe.matmul(ps[:, 2, 0:63], m.w2[:, 0, :], h[0], start=True, stop=True)
                else:
                    ins = pe.matmul(ps[0:63, 3, 0:P], h[1], m.w2[:, 1, :], start=True, stop=True)
                ins.then_inc(out_mm, 1)

        @block.scalar
        def _(act):
            act.activation(kt[1].rearrange("p t n -> p n t"),
                           m.zT[:, Z_VC, 0:SEQ].rearrange("p (n t) -> p n t", t=CS), ACT.Copy).then_inc(kt_done, 1)
            for kv in range(2):
                gelu_act(act, ps[:, kv, 0:63], x[kv], u[kv], m.cbias[:, kv:kv + 1], kv, cmp_mm, g_act, g_dve)

        @block.vector
        def _(dve):
            dve.wait_ge(kt_done, 1)
            dve.tensor_copy(kt[0].rearrange("p t n -> p n t"),
                            m.zT[:, Z_KC, 0:SEQ].rearrange("p (n t) -> p n t", t=CS)).then_inc(kt_done, 1)
            for kv in range(2):
                gelu_dve(dve, x[kv], u[kv], h[kv], kv, g_act, g_dve)
                dve.wait_ge(out_mm, kv + 1)
                if kv == 0:
                    dve.tensor_scalar(m.ckT[:, 0, 0:63], ps[:, 2, 0:63], 0.5, None, ALU.mult)
                else:
                    dve.tensor_scalar(m.cvt[0:63, 0, :], ps[0:63, 3, 0:P], 0.5, None, ALU.mult)


def stage_samples(m, I, O):
    nc, ps = m.nc, m.ps
    W, tail = m.work, m.tail
    RB = 2 * HP * DS
    BQ = P // RB
    NQ = NB // BQ
    kv = m.past
    kv_in = [m.past_in, [m.sem(f"past_of_quad1_in_buffer{b}") for b in range(BQ)]]
    assert NQ == 2
    gateB = m.vgf[:, 4096:4480].rearrange("p (k h t) -> p k h t", k=3, h=HP)
    kw = [m.zT[:, Z_KC, 512 * i:512 * (i + 1)].rearrange("p (j c) -> p j c", c=GD) for i in range(2)]
    KT = [tail[:, 1024 * i:1024 + 1024 * i] for i in range(2)]
    S = tail[:, 2048:3104]
    PT = tail[:, 3104:4256].rearrange("p (j r) -> p j r", r=P)
    vw = tail[:, 4256:6304].rearrange("p (b j c) -> p b j c", b=BQ, c=GD)
    sel = W[0:24, 0:1536].rearrange("p (k h g d) -> p k h g d", k=3, h=HP, g=2)
    Qb = W[:, 1536:1792].rearrange("p (b g h t) -> p b g h t", b=NB, g=2, h=HP)
    Qf = W[:, 1536:1792]
    HS, blk = W[:, 1792:1920], W[:, 1920:2048]
    newm = W[:, 2048:2112].rearrange("p (q t) -> p q t", q=NQ)
    winm = W[:, 2112:2116]
    iota = W[:, 2120:2152]
    ints = W[:, 2152:2156].bitcast(I32)
    intf = W[:, 2176:2304].bitcast(I32)
    tcol, bcol, lo, hi = (W[:, 2156 + i:2157 + i] for i in range(4))
    geq = W[:, 2304:2336]
    on, gt = W[:, 2400:2528], W[:, 2528:2592]
    hp = W[:, 2600:2666]
    imp, t14, drop = W[:, 2670:2684], W[:, 2690:2704], W[:, 2710:2726]
    nmx, den, rden, mn, jd = (W[:, 2730 + i:2731 + i] for i in range(5))
    Pn = W[:, 2740:2804]
    NJ = NSLC - 2

    k_in, v_in = [m.sem(f"window_keys_in{i}") for i in range(2)], m.sem("window_values_in")
    c_pool, c_own = m.sem("sample_constants"), m.sem("sample_vector_chain")
    gates_mm, kT, kt_act, kt_dve = m.sem("gates_spread"), m.sem("keys_turned"), m.sem("keys_by_act"), m.sem("keys_by_dve")
    const_ok = m.sem("sample_masks_ready")
    k_mm, s_mm, s_ok, ex, r_ok, i_mm = (m.sem("key_tiles_scored"), m.sem("scores_summed"), m.sem("scores_masked"),
                                        m.sem("probabilities_ready"), m.sem("normalised_compressed"),
                                        m.sem("importance_summed"))
    pT, pt_act, pt_dve, pv, on_ok, oT, gated = (m.sem("probabilities_turned"), m.sem("turned_by_act"),
                                                m.sem("turned_by_dve"), m.sem("values_summed"), m.sem("outputs_scaled"),
                                                m.sem("outputs_turned"), m.sem("outputs_gated"))
    seq = [(q, br) for q in range(NQ) for br in range(3)]
    win = I["state_win_kv"][0].rearrange("b (j p) a g d -> p b j (a g d)", p=P)
    KJ = [0, NPAGE, WIN // P]
    ada_used, mod_step = m.sem("modulation_units_used"), m.sem("rest_of_modulation_steps")
    ada_first = [m.sem(f"first_modulation_unit_in_slot{s}") for s in range(4)]
    ada_in = [m.sem(f"later_modulation_units_in_slot{s}") for s in range(4)]
    rows_ok, turned_last = m.sem("rest_of_modulation_rows"), m.sem("rest_of_modulation_turned")
    ADA = [[1, 0, 1], [1, 1, 1], [1, 1, 1]]
    NA = LATER // 2
    assert NQ * sum(map(sum, ADA)) == NA

    def kn(q, br, b):
        return q * 2 * BQ + (br - 1) * BQ + b

    with nc.Block() as block:
        @block.sync
        def _(sp):
            for s in range(4):
                load_ada_unit(sp, m, I, EARLY + s, s, ada_first[s])
            for q in range(NQ):
                if q:
                    sp.wait_ge(pv, 3 * (q - 1) + 2)
                    for b in range(BQ):
                        for j in range(NPAGE):
                            load_page(sp, m, I, "cache_slc_kv", BQ * q + b, j, kv[b][:, j, :], kv_in[q][b])
                for b in range(BQ):
                    n = BQ * q + b
                    if b >= 2:
                        sp.wait_ge(kT, kn(q, 2, b) - 1)
                    if q:
                        sp.wait_ge(pv, 3 * (q - 1) + 3)
                    sp.dma_start(kw[b % 2], win[:, n, :, 0:GD]).then_inc(k_in[b % 2], 16)
                    sp.dma_start(vw[:, b], win[:, n, :, GD:2 * GD]).then_inc(v_in, 16)

        @block.gpsimd
        def _(pool):
            pool.memset(sel, 0.0).then_inc(c_pool, 1)
            pool.memset(Qf, 0.0).then_inc(c_pool, 1)
            pool.memset(blk, 1.0).then_inc(c_pool, 1)
            pool.iota(iota, [[1, 32]], base=0, channel_multiplier=0, allow_small_or_imprecise_dtypes=True).then_inc(c_pool, 1)
            pool.iota(ints[:, 0:1], [[0, 1]], base=0, channel_multiplier=1).then_inc(c_pool, 1)
            pool.iota(intf, [[1, P]], base=0, channel_multiplier=0).then_inc(c_pool, 1)
            pool.memset(hp, 0.0).then_inc(c_pool, 1)
            pool.memset(drop, 0.0).then_inc(c_pool, 1)
            pool.wait_ge(c_pool, 8)
            pool.affine_select(out=sel, in_=sel, compare_op=ALU.not_equal, fill=1.0, base=0,
                               pattern=[[-8, 3], [-1, HP], [-HP, 2], [0, HD]], channel_multiplier=1).then_inc(c_pool, 1)
            b16 = blk.rearrange("p (c t) -> p c t", t=16)
            keep(pool, None, b16, [[-16, 8], [0, 16]], 0, 1).then_inc(c_pool, 1)
            pool.wait_ge(c_pool, 10)
            keep(pool, None, b16, [[16, 8], [0, 16]], 15, -1).then_inc(c_pool, 1)
            with pool.Fori(1, LATER // 4) as it:
                for s in range(4):
                    pool.wait_ge(ada_used, it * 4 + (s - 3))
                    load_ada_unit(pool, m, I, it * 4 + (EARLY + s), s, ada_in[s])

        @block.tensor
        def _(pe):
            pairs = iter(range(NA))

            def ada(n):
                for _ in range(n):
                    j = next(pairs)
                    if j:
                        pe.wait_ge(rows_ok, j)
                        ada_turn(pe, m)
                    for c in range(2):
                        if j < 2:
                            pe.wait_ge(ada_first[2 * j + c], 16)
                        else:
                            pe.wait_ge(ada_in[2 * (j % 2) + c], 16 * (j // 2))
                    ada_product(pe, m, j % 2).then_inc(ada_used, 2)

            pe.wait_ge(c_pool, 11)
            for k in range(3):
                for h in range(HP):
                    c = (k * HP + h) * ST
                    ins = pe.matmul(ps[:, 0, c:c + ST], sel[:, k, h].rearrange("p g d -> p (g d)"), m.gnT[:, :],
                                    start=True, stop=True)
            ins.then_inc(gates_mm, 1)
            pe.wait_ge(const_ok, 1)

            def turn_keys(q, br, b):
                n = kn(q, br, b)
                if br == 1:
                    pe.wait_ge(kv_in[q][b], 16 * NPAGE)
                else:
                    pe.wait_ge(k_in[b % 2], 16 * (2 * q + b // 2 + 1))
                for j in range(KJ[br]):
                    ins = pe.transpose(ps[:, 3 + 2 * (n % 2) + j // 4, (j % 4) * P:(j % 4 + 1) * P],
                                       kv[b][:, j, 0:GD] if br == 1 else kw[b % 2][:, j, :], m.ident[:, :])
                ins.then_inc(kT, 1)

            for r, (q, br) in enumerate(seq):
                rows = lambda b: slice(RB * b, RB * b + RB)
                qcols = lambda b: Qf[:, (BQ * q + b) * RB:(BQ * q + b + 1) * RB]
                if br == 0:
                    for b in range(BQ):
                        ins = pe.matmul(ps[rows(b), 0, 0:63], qcols(b), m.ckT[:, 1 + BQ * q + b, 0:63], start=True, stop=True)
                    ins.then_inc(s_mm, 1)
                else:
                    turn_keys(q, br, 0)
                    for b in range(BQ):
                        n = kn(q, br, b)
                        if b + 1 < BQ:
                            turn_keys(q, br, b + 1)
                        pe.wait_ge(kt_act, n + 1)
                        if br == 1:
                            pe.wait_ge(kt_dve, BQ * q + b + 1)
                        for c in range(KJ[br] // 4):
                            ins = pe.matmul(ps[rows(b), c, :], qcols(b), KT[n % 2][:, 512 * c:512 * (c + 1)], start=True,
                                            stop=True)
                        ins.then_inc(k_mm, 1)
                    if r:
                        pe.wait_ge(gated, r)
                    pe.matmul(ps[:, 2, 0:ST], Qf[:, q * P:(q + 1) * P], m.zT[:, Z_KS + br - 1, SEQ:T], start=True,
                              stop=True).then_inc(s_mm, 1)
                ada(ADA[br][0])
                if br == 0:
                    pe.wait_ge(r_ok, q + 1)
                    pe.matmul(ps[:, 1, 0:63], HS, Pn[:, 0:63], start=True, stop=True).then_inc(i_mm, 1)
                pe.wait_ge(ex, r + 1)
                if r:
                    pe.wait_ge(gated, r)
                w = 63 if br == 0 else P
                for j in range(max(KJ[br], 1)):
                    ins = pe.transpose(ps[0:w, 5 + j // 4, (j % 4) * P:(j % 4 + 1) * P], S[:, j * P:j * P + w], m.ident[:, :])
                if br:
                    ins = pe.transpose(ps[0:ST, 2, P:2 * P], S[:, KJ[br] * P:KJ[br] * P + ST], m.ident[:, :])
                ins.then_inc(pT, 1)
                ada(ADA[br][1])
                pe.wait_ge(pt_act, r + 1)
                pe.wait_ge(pt_dve, r + 1)
                if br == 2:
                    pe.wait_ge(v_in, 16 * BQ * (q + 1))
                for b in range(BQ):
                    out = ps[rows(b), 2, 0:GD]
                    if br == 0:
                        ins = pe.matmul(out, PT[0:63, 0, rows(b)], m.cvt[0:63, 1 + BQ * q + b, :], start=True, stop=True)
                    else:
                        for j in range(KJ[br]):
                            pe.matmul(out, PT[:, j, rows(b)], kv[b][:, j, GD:2 * GD] if br == 1 else vw[:, b, j, :], start=j == 0, stop=False)
                        ins = pe.matmul(out, PT[0:ST, 8, rows(b)], m.vtm[0:ST, QT, br - 1, :], start=False, stop=True)
                ins.then_inc(pv, 1)
                ada(ADA[br][2])
                pe.wait_ge(on_ok, r + 1)
                pe.transpose(ps[:, 2, 2 * P:3 * P], on, m.ident[:, :]).then_inc(oT, 1)
            pe.wait_ge(rows_ok, NA)
            ada_turn(pe, m).then_inc(turned_last, 1)

        @block.scalar
        def _(act):
            pairs = iter(range(NA))

            def ada(n):
                for _ in range(n):
                    j = next(pairs)
                    act.wait_ge(ada_used, 2 * j + 2)
                    if j:
                        ada_keep(act, m, EARLY + 2 * j - 2)
                    ada_rows(act, m).then_inc(rows_ok, 1)

            for r, (q, br) in enumerate(seq):
                if r:
                    ada(ADA[seq[r - 1][1]][2])
                if br:
                    for b in range(BQ):
                        n = kn(q, br, b)
                        act.wait_ge(kT, n + 1)
                        if n >= 2:
                            act.wait_ge(k_mm, n - 1)
                        act.activation(KT[n % 2][:, 0:512], ps[:, 3 + 2 * (n % 2), :], ACT.Copy).then_inc(kt_act, 1)
                act.wait_ge(s_ok, r + 1)
                L = 63 if br == 0 else KJ[br] * P + ST
                act.activation(S[:, 0:L], ps[:, 0, 0:63] if br == 0 else S[:, 0:L], ACT.Exp, bias=nmx,
                               accum_out=den).then_inc(ex, 1)
                ada(ADA[br][0])
                act.wait_ge(pT, r + 1)
                if br == 0:
                    act.activation(PT[0:63, 0, :], ps[0:63, 5, 0:P], ACT.Copy).then_inc(pt_act, 1)
                else:
                    act.activation(PT[:, 0:4, :], ps[:, 5, :].rearrange("p (j r) -> p j r", j=4), ACT.Copy).then_inc(pt_act, 1)
                ada(ADA[br][1])
            ada(ADA[2][2])
            act.wait_ge(turned_last, 1)
            ada_keep(act, m, 48 - 2).then_inc(turned_last, 1)

        @block.vector
        def _(dve):
            steps = [0]

            def chain(ins):
                steps[0] += 1
                ins.then_inc(c_own, 1)
                dve.wait_ge(c_own, steps[0])

            dve.wait_ge(c_pool, 11)
            for g in range(2):
                for h in range(HP):
                    r = slice(64 * g, 64 * g + 64)
                    dve.tensor_scalar(Qb[r, :, g, h, :], m.zT[r, Z_Q + h, SEQ:T].rearrange("p (b t) -> p b t", t=DS),
                                      HD ** -0.5, None, ALU.mult)
            dve.tensor_scalar(ints[:, 1:2], ints[:, 0:1], 3, None, ALU.bitwise_and)
            dve.tensor_scalar(ints[:, 2:3], ints[:, 0:1], 5, None, ALU.logical_shift_right)
            chain(dve.tensor_scalar(intf, intf, 3, None, ALU.bitwise_and))
            dve.tensor_copy(tcol, ints[:, 1:2])
            dve.tensor_copy(bcol, ints[:, 2:3])
            chain(dve.tensor_copy(HS, intf))
            chain(dve.tensor_scalar(HS, HS, tcol, None, ALU.is_equal))
            chain(dve.tensor_tensor(HS, HS, blk, ALU.mult))
            dve.tensor_scalar(winm, iota[:, 0:4], tcol, NEG, ALU.is_le, ALU.mult)
            for q in range(NQ):
                chain(dve.tensor_scalar(lo, bcol, float(DS), float(DS * BQ * q), ALU.mult, ALU.add))
                chain(dve.tensor_tensor(hi, lo, tcol, ALU.add))
                chain(dve.tensor_scalar(geq, iota, lo, None, ALU.is_ge))
                chain(dve.scalar_tensor_tensor(out=newm[:, q], in0=iota, scalar=hi, in1=geq, op0=ALU.is_le, op1=ALU.mult))
                chain(dve.tensor_scalar(newm[:, q], newm[:, q], -1.0, -NEG, ALU.add, ALU.mult))
            dve.wait_ge(gates_mm, 1)
            dve.tensor_copy(gateB, ps[:, 0, 0:384].rearrange("p (k h t) -> p k h t", k=3, h=HP)).then_inc(const_ok, 1)
            for r, (q, br) in enumerate(seq):
                L = 63 if br == 0 else KJ[br] * P + ST
                if br == 1:
                    for b in range(BQ):
                        n = kn(q, br, b)
                        dve.wait_ge(kT, n + 1)
                        if n >= 2:
                            dve.wait_ge(k_mm, n - 1)
                        dve.tensor_copy(KT[n % 2][:, 512:1024], ps[:, 4 + 2 * (n % 2), :]).then_inc(kt_dve, 1)
                dve.wait_ge(s_mm, r + 1)
                if br == 0:
                    dve.tensor_reduce(nmx, ps[:, 0, 0:63], X, ALU.max, negate=True).then_inc(s_ok, 1)
                else:
                    nk = KJ[br] * P
                    if br == 1:
                        dve.tensor_tensor(S[:, 0:nk].rearrange("p (j t) -> p j t", t=SLC),
                                          ps[:, 0:2, :].rearrange("p a b -> p (a b)").rearrange("p (j t) -> p j t", t=SLC),
                                          drop.unsqueeze(2).to_broadcast([P, NSLC, SLC]), ALU.add)
                    else:
                        dve.tensor_tensor(S[:, 0:4], ps[:, 0, 0:4], winm, ALU.add)
                        dve.tensor_copy(S[:, 4:nk], ps[:, 0, 4:nk])
                    chain(dve.tensor_tensor(S[:, nk:L], ps[:, 2, 0:ST], newm[:, q], ALU.add))
                    dve.tensor_reduce(nmx, S[:, 0:L], X, ALU.max, negate=True).then_inc(s_ok, 1)
                dve.wait_ge(ex, r + 1)
                chain(dve.reciprocal(rden, den))
                if br == 0:
                    dve.tensor_scalar(Pn[:, 0:63], S[:, 0:63], rden, None, ALU.mult).then_inc(r_ok, 1)
                    dve.wait_ge(i_mm, q + 1)
                    chain(dve.tensor_copy(hp[:, 1:64], ps[:, 1, 0:63]))
                    chain(dve.tensor_reduce(imp, hp[:, 4:4 + 4 * NJ].rearrange("p (j n) -> p j n", n=4), X, ALU.add))
                    chain(dve.tensor_tensor(imp, imp, hp[:, 8:8 + 4 * NJ].rearrange("p (j n) -> p j n", n=4)[:, :, 0], ALU.add))
                    chain(dve.tensor_reduce(mn, imp, X, ALU.min))
                    chain(dve.scalar_tensor_tensor(out=t14, in0=imp, scalar=mn, in1=iota[:, 1:1 + NJ], op0=ALU.is_le,
                                                   op1=ALU.mult))
                    chain(dve.tensor_reduce(jd, t14, X, ALU.max))
                    chain(dve.tensor_scalar(drop, iota[:, 0:NSLC], jd, NEG, ALU.is_equal, ALU.mult))
                dve.wait_ge(pT, r + 1)
                if br == 1:
                    dve.tensor_copy(PT[:, 4:8, :], ps[:, 6, :].rearrange("p (j r) -> p j r", j=4))
                if br:
                    dve.tensor_copy(PT[0:ST, 8, :], ps[0:ST, 2, P:2 * P]).then_inc(pt_dve, 1)
                else:
                    dve.sem_inc(pt_dve, 1)
                dve.wait_ge(pv, r + 1)
                dve.tensor_scalar(on, ps[:, 2, 0:GD], rden, None, ALU.mult).then_inc(on_ok, 1)
                dve.wait_ge(oT, r + 1)
                toks = slice(BQ * DS * q, BQ * DS * (q + 1))
                for g in range(2):
                    gr = slice(64 * g, 64 * g + 64)
                    o = ps[gr, 2, 2 * P:3 * P].rearrange("p (b g h t) -> p g h b t", b=BQ, g=2, h=HP)[:, g]
                    gate = gateB[gr, br, :, toks].rearrange("p h (b t) -> p h b t", t=DS)
                    to = m.osT[gr, :, toks].rearrange("p h (b t) -> p h b t", t=DS)
                    if br == 0:
                        ins = dve.tensor_tensor(to, o, gate, ALU.mult)
                    else:
                        part = gt[gr].rearrange("p (h b t) -> p h b t", h=HP, b=BQ)
                        chain(dve.tensor_tensor(part, o, gate, ALU.mult))
                        ins = dve.tensor_tensor(to, to, part, ALU.add)
                ins.then_inc(gated, 1)
                dve.wait_ge(gated, r + 1)
            dve.wait_ge(turned_last, 2)
            modulation(m, dve, EARLY, 48, mod_step)


def stage_attention(m, I, O):
    nc, ps = m.nc, m.ps
    W, tail, vgf = m.work, m.tail, m.vgf
    oa = tail[:, 0:4096].rearrange("p (h i g d) -> p h i g d", h=HP, i=QT, g=2)
    Qs = tail[:, 4096:6144].rearrange("p (g t) -> p g t", g=2)
    Pb = [vgf[:, 1024 * i:1024 * (i + 1)] for i in range(2)]
    PT = [vgf[:, 2048 + 512 * i:2560 + 512 * i].rearrange("p (j q) -> p j q", j=4) for i in range(4)]
    cm = vgf[:, 4096:4608].rearrange("p (i n) -> p i n", n=64)
    cvb = W[:, 384:512]
    wc = W[:, 0:256].rearrange("p (k t) -> p k t", k=2)
    mx, den16, fac16 = W[:, 256:272], W[:, 288:304], W[:, 304:320]
    nmx = [W[:, 320 + i:321 + i] for i in range(2)]
    den = [W[:, 324 + i:325 + i] for i in range(4)]
    rden, fac, scale = W[:, 329:330], W[:, 330:331], W[:, 332:333]
    gates = m.gates[:, :, :].rearrange("p i (k g h) -> p i k g h", k=3, g=2)

    items = [(br, qt, g) for br in (1, 2) for qt in range(QT) for g in range(2)]
    W0 = 32
    items.insert(W0, (0, 0, 0))
    N = len(items)
    keys = [list(range(max(0, qt - 4) if br == 2 else 0, qt + 1)) for br, qt, g in items]
    npc = [2 if br == 0 else -(-len(k) // 4) for k, (br, _, _) in zip(keys, items)]
    P0, o0 = W[:, 1024:2048], W[:, 2048:3072]
    p0 = [sum(npc[:w]) for w in range(N)]
    NPC = sum(npc)

    c_ok, zero_ok = m.sem("attention_masks"), m.sem("query_halves_zeroed")
    qs_ok, cv_ok = m.sem("queries_staged"), m.sem("compressed_values_in_blocks")
    qk, s_ok, ex = m.sem("item_scored"), m.sem("item_max_ready"), m.sem("item_exponentials")
    pT, pt, pv = m.sem("piece_turned"), m.sem("piece_copied"), m.sem("piece_summed")
    o_ok, own, oT = m.sem("item_output_added"), m.sem("attention_vector_chain"), m.sem("attention_turned")
    ow = [m.sem("attention_written_by_dve"), m.sem("attention_written_by_act")]

    def item(e, sem, it, w):
        e.wait_ge(sem, it * N + (w + 2))

    def piece(e, sem, it, p):
        e.wait_ge(sem, it * NPC + (p + 2))

    before = lambda w: w - 2 if w >= 2 else -1

    with nc.Block() as block:
        @block.sync
        def _(sp):
            prefetch_merge(sp, m, I)

        @block.gpsimd
        def _(pool):
            pool.memset(wc, 0.0).then_inc(c_ok, 1)
            pool.memset(cm, 0.0).then_inc(c_ok, 1)
            pool.wait_ge(c_ok, 2)
            pool.memset(Qs[64:128, 0, :], 0.0).then_inc(zero_ok, 1)
            pool.memset(Qs[0:64, 1, :], 0.0).then_inc(zero_ok, 1)
            pool.wait_ge(zero_ok, 2)
            pool.memset(m.ckT[:, 0, 63:64], 0.0).then_inc(zero_ok, 1)
            pool.memset(cvb, 0.0).then_inc(zero_ok, 1)
            for ap, pattern, base, mult in ((wc[:, 0, :], [[1, P]], -1, -1), (wc[:, 1, :], [[-1, P]], 0, 1),
                                            (cm, [[P, QT], [-CS, 64]], 1 - CL, 1)):
                pool.affine_select(out=ap, in_=ap, compare_op=ALU.is_ge, fill=NEG, base=base, pattern=pattern,
                                   channel_multiplier=mult).then_inc(c_ok, 1)
            pool.wait_ge(zero_ok, 4)
            pool.wait_ge(c_ok, 5)
            pool.memset(tail[:, 0:4096], 0.0).then_inc(c_ok, 1)
            pool.wait_ge(c_ok, 6)
            pool.memset(scale, HD ** -0.5).then_inc(c_ok, 1)
            pool.wait_ge(c_ok, 7)
            with pool.Fori(0, HP) as it:
                item(pool, qk, it, -1)
                for g in range(2):
                    r = slice(64 * g, 64 * g + 64)
                    pool.tensor_tensor(Qs[r, g:g + 1, :], m.zT[r, bass.ds(it, 1), 0:SEQ],
                                       scale[r].unsqueeze(2).to_broadcast([HD, 1, SEQ]), ALU.mult).then_inc(qs_ok, 1)

        @block.tensor
        def _(pe):
            pe.wait_ge(zero_ok, 4)
            pe.wait_ge(cv_ok, 2)
            for sem in (qk, pT, pv):
                pe.sem_inc(sem, 1)

            def score(it, w):
                br, qt, g = items[w]
                item(pe, ex, it, before(w))
                if w == 0:
                    pe.wait_ge(qs_ok, it * 2 + 2)
                if w == W0:
                    for i in range(QT):
                        for g in range(2):
                            c = 2 * i + g
                            ins = pe.matmul(ps[:, c // 8, (c % 8) * 64:(c % 8 + 1) * 64], Qs[:, g, i * P:(i + 1) * P],
                                            m.ckT[:, 0, :], start=True, stop=True)
                else:
                    lo, n = keys[w][0] * P, len(keys[w]) * P
                    for c in range(0, n, 512):
                        k = min(512, n - c)
                        ins = pe.matmul(ps[:, 2 * (w % 2) + c // 512, 0:k], Qs[:, g, qt * P:(qt + 1) * P],
                                        m.zT[:, Z_KS + br - 1, lo + c:lo + c + k], start=True, stop=True)
                ins.then_inc(qk, 1)

            def turn(it, w, a):
                p = p0[w] + a
                piece(pe, pt, it, before(p))
                if a == 0:
                    item(pe, ex, it, w)
                if w == W0:
                    for j in range(4):
                        ins = pe.transpose(ps[:, 4 + p % 2, j * P:(j + 1) * P], P0[:, (4 * a + j) * P:(4 * a + j + 1) * P],
                                           m.ident[:, :])
                else:
                    for j in range(min(4, len(keys[w]) - 4 * a)):
                        ins = pe.transpose(ps[:, 4 + p % 2, j * P:(j + 1) * P],
                                           Pb[w % 2][:, (4 * a + j) * P:(4 * a + j + 1) * P], m.ident[:, :])
                ins.then_inc(pT, 1)

            def value(it, w, a):
                br, qt, g = items[w]
                p = p0[w] + a
                piece(pe, pt, it, p)
                if a == 0:
                    item(pe, o_ok, it, w - 1 if w in (W0, W0 + 1) else before(w))
                if w == W0:
                    for j in range(4):
                        ins = pe.matmul(ps[:, 6 + a, j * P:(j + 1) * P], PT[p % 4][:, j, :], cvb, start=True, stop=True)
                else:
                    n = len(keys[w])
                    for j in range(min(4, n - 4 * a)):
                        kt = 4 * a + j
                        ins = pe.matmul(ps[:, 6 + w % 2, 0:HD], PT[p % 4][:, j, :],
                                        m.vtm[:, keys[w][kt], br - 1, g * HD:(g + 1) * HD], start=kt == 0, stop=kt == n - 1)
                ins.then_inc(pv, 1)

            with pe.Fori(0, HP) as it:
                score(it, 0)
                last = None
                for w in range(N):
                    if w + 1 < N:
                        score(it, w + 1)
                    for a in range(npc[w]):
                        turn(it, w, a)
                        if last is not None:
                            value(it, *last)
                        last = (w, a)
                value(it, *last)
            item(pe, o_ok, HP, -1)
            for n in range(2 * HP):
                h, half = n // 2, n % 2
                if n >= 4:
                    pe.wait_ge(ow[n % 2], (n - 4) // 2 + 1)
                for j in range(4):
                    ins = pe.transpose(ps[:, n % 4, j * P:(j + 1) * P],
                                       oa[:, h, 4 * half + j].rearrange("p g d -> p (g d)"), m.ident[:, :])
                ins.then_inc(oT, 1)

        @block.scalar
        def _(act):
            act.sem_inc(ex, 1)
            act.sem_inc(pt, 1)
            act.wait_ge(zero_ok, 4)
            for g in range(2):
                act.activation(cvb[64 * g:64 * g + 63, HD * g:HD * (g + 1)], m.cvt[0:63, 0, HD * g:HD * (g + 1)],
                               ACT.Copy).then_inc(cv_ok, 1)

            def exps(it, w):
                item(act, s_ok, it, w)
                if w >= 2:
                    piece(act, pT, it, p0[w - 1] - 1)
                else:
                    piece(act, pT, it, -1)
                if w == W0:
                    v = P0.rearrange("p (c n) -> p c n", n=64)
                    act.activation(v, v, ACT.Exp).then_inc(ex, 1)
                else:
                    n = len(keys[w]) * P
                    act.activation(Pb[w % 2][:, 0:n],
                                   ps[:, 2 * (w % 2):2 * (w % 2) + 2, :].rearrange("p a b -> p (a b)")[:, 0:n], ACT.Exp,
                                   bias=nmx[w % 2], accum_out=den[w % 4]).then_inc(ex, 1)

            def copies(it, w):
                for a in range(npc[w]):
                    p = p0[w] + a
                    piece(act, pT, it, p)
                    piece(act, pv, it, p - 4 if p >= 4 else -1)
                    n = 4 if w == W0 else min(4, len(keys[w]) - 4 * a)
                    act.activation(PT[p % 4][:, 0:n], ps[:, 4 + p % 2, 0:n * P].rearrange("p (j q) -> p j q", j=n),
                                   ACT.Copy).then_inc(pt, 1)

            with act.Fori(0, HP) as it:
                exps(it, 0)
                for w in range(N):
                    copies(it, w)
                    if w + 1 < N:
                        exps(it, w + 1)
            for n in range(1, 2 * HP, 2):
                act.wait_ge(oT, n + 1)
                act.activation(m.zT[:, n // 2, (n % 2) * 512:(n % 2 + 1) * 512], ps[:, n % 4, :], ACT.Copy).then_inc(ow[1], 1)

        @block.vector
        def _(dve):
            dve.sem_inc(s_ok, 1)
            dve.sem_inc(o_ok, 1)
            dve.wait_ge(c_ok, 6)
            per = (N - 1) * 3 + 8
            step = [0]

            def chain(it, ins):
                step[0] += 1
                ins.then_inc(own, 1)
                dve.wait_ge(own, it * per + step[0])

            def maxima(it, w):
                br, qt, g = items[w]
                item(dve, qk, it, w)
                if w == W0:
                    v = P0.rearrange("p (c n) -> p c n", n=64)
                    piece(dve, pT, it, -1)
                    chain(it, dve.tensor_tensor(v.rearrange("p (i g) n -> p i g n", g=2),
                                                ps[:, 0:2, :].rearrange("p a (i g n) -> p (a i) g n", g=2, n=64),
                                                cm.unsqueeze(2).to_broadcast([P, QT, 2, 64]), ALU.add))
                    chain(it, dve.tensor_reduce(mx, v, X, ALU.max))
                    chain(it, dve.scalar_tensor_tensor(out=mx, in0=mx, scalar=NEG / 10, in1=mx, op0=ALU.is_gt, op1=ALU.mult))
                    dve.tensor_tensor(v, v, mx.unsqueeze(2).to_broadcast([P, 16, 64]), ALU.subtract).then_inc(s_ok, 1)
                else:
                    n = len(keys[w])
                    row = ps[:, 2 * (w % 2):2 * (w % 2) + 2, :].rearrange("p a b -> p (a b)")
                    if br == 2 and qt >= 4:
                        edge = ps[:, 2 * (w % 2):2 * (w % 2) + 2, 0:P]
                        chain(it, dve.tensor_tensor(edge, edge, wc, ALU.add))
                    else:
                        edge = row[:, (n - 1) * P:n * P]
                        chain(it, dve.tensor_tensor(edge, edge, wc[:, 1, :], ALU.add))
                    dve.tensor_reduce(nmx[w % 2], row[:, 0:n * P], X, ALU.max, negate=True).then_inc(s_ok, 1)

            def output(it, w):
                br, qt, g = items[w]
                if w == W0:
                    item(dve, ex, it, W0)
                    v = P0.rearrange("p (c n) -> p c n", n=64)
                    chain(it, dve.tensor_reduce(den16, v, X, ALU.add))
                    chain(it, dve.tensor_scalar(den16, den16, 1e-30, None, ALU.max))
                    chain(it, dve.reciprocal(fac16, den16))
                    chain(it, dve.tensor_tensor(fac16.rearrange("p (i g) -> p i g", g=2),
                                                fac16.rearrange("p (i g) -> p i g", g=2),
                                                gates[:, :, 0, :, bass.ds(it, 1)].rearrange("p i g o -> p i (g o)"), ALU.mult))
                    piece(dve, pv, it, p0[W0] + npc[W0] - 1)
                    chain(it, dve.tensor_tensor(o0.rearrange("p (c d) -> p c d", d=HD),
                                                ps[:, 6:8, :].rearrange("p a (c d) -> p (a c) d", d=HD),
                                                fac16.unsqueeze(2).to_broadcast([P, 16, HD]), ALU.mult))
                    o = oa[:, bass.ds(it, 1)].rearrange("p o i g d -> p (o i g d)")
                    dve.tensor_tensor(o, o, o0, ALU.add).then_inc(o_ok, 1)
                else:
                    piece(dve, pv, it, p0[w] + npc[w] - 1)
                    item(dve, o_ok, it, w - 1)
                    chain(it, dve.reciprocal(rden, den[w % 4]))
                    chain(it, dve.tensor_tensor(fac, rden, gates[:, qt, br, g, bass.ds(it, 1)], ALU.mult))
                    o = oa[:, bass.ds(it, 1), qt, g, :].rearrange("p o d -> p (o d)")
                    dve.scalar_tensor_tensor(out=o, in0=ps[:, 6 + w % 2, 0:HD], scalar=fac, in1=o, op0=ALU.mult,
                                             op1=ALU.add).then_inc(o_ok, 1)

            with dve.Fori(0, HP) as it:
                step[0] = 0
                maxima(it, 0)
                for w in range(N):
                    if w + 1 < N:
                        maxima(it, w + 1)
                    if w:
                        output(it, w - 1)
                output(it, N - 1)
                assert step[0] == per, (step[0], per)
            for n in range(0, 2 * HP, 2):
                dve.wait_ge(oT, n + 1)
                dve.tensor_copy(m.zT[:, n // 2, (n % 2) * 512:(n % 2 + 1) * 512], ps[:, n % 4, :]).then_inc(ow[0], 1)
            dve.tensor_copy(m.zT[:, 0:HP, SEQ:T], m.osT[:, :, :]).then_inc(ow[0], 1)


def prefetch_merge(sp, m, I):
    for u in range(GH):
        sp.dma_start(m.ring[:, u], w_block(I["w_in"][0], C_RG + u * P)).then_inc(m.w_in[u], 16)


def stage_merge(m, I, O):
    nc, ps = m.nc, m.ps
    W = m.work
    gate = [[W[:, NW * (2 * s + c):NW * (2 * s + c + 1)] for c in range(2)] for s in range(2)]
    rt = [W[:, NW * (4 + b):NW * (5 + b)] for b in range(6)]
    u0, l0 = m.used, m.loads
    summed, rbank = m.sem("r_tile_summed"), [m.sem(f"r_bank_free{b}") for b in range(6)]
    r_sig, r_mul, r_ok = m.sem("r_sigmoid"), m.sem("r_silu"), m.sem("gla_gated")
    step_mm, sig, mul, bank, add = (m.sem("merge_step_summed"), m.sem("merge_sigmoids"), m.sem("merge_products"),
                                    m.sem("merge_banks_free"), m.sem("merged_written"))
    w_in, w_n, w_g = I["w_in"][0], I["w_nsa_o"][0], I["w_gla_o"][0]

    def load(sp, j, c, slot):
        inc = m.w_in[slot]
        if c < 2:
            v = w_in[:, C_MG + D * c:C_MG + D * (c + 1)].rearrange("(k p) n -> p k n", p=P)[:, :, bass.ds(j * P, P)]
            sp.dma_start(m.ring[:, slot], v).then_inc(inc, 16)
        else:
            for g in range(2):
                v = w_n.rearrange("(g h d) n -> g d h n", g=2, h=HP)[g][:, :, bass.ds(j * P, P)]
                sp.dma_start(m.ring[64 * g:64 * g + 64, slot, 0:HP, :], v).then_inc(inc, 16)
            v = w_g.rearrange("(k p) n -> p k n", p=P)[:, :, bass.ds(j * P, P)]
            sp.dma_start(m.ring[:, slot, HP:KD, :], v).then_inc(inc, 16)

    with nc.Block() as block:
        @block.sync
        def _(sp):
            for j in range(2):
                for c in range(3):
                    slot = 3 * j + c
                    if slot < GH:
                        sp.wait_ge(m.w_used, u0 + slot + 1)
                    load(sp, j, c, slot)
            with sp.Fori(1, KD // 2) as it:
                for jj in range(2):
                    sp.wait_ge(m.w_used, it * 6 + (u0 + GH + 3 * (jj - 1)))
                    for c in range(3):
                        load(sp, it * 2 + jj, c, 3 * jj + c)
            for s in range(2):
                sp.wait_ge(m.w_used, u0 + GH + 3 * (KD - 2) + s + 1)
                sp.dma_start(m.ring[:, s], w_block(I["w_out"][0], s * P)).then_inc(m.w_in[s], 16)

        @block.tensor
        def _(pe):
            for u in range(GH):
                pe.wait_ge(m.w_in[u], 16 * (l0[u] + 1))
                for n in range(NN):
                    b = 3 * (u % 2) + n
                    if u >= 2:
                        pe.wait_ge(rbank[b], u // 2)
                    ins = product(pe, ps[:, b, 0:NW], m.ring[:, u], lambda k: m.hT[:, k, n * NW:(n + 1) * NW])
                    if n < NN - 1:
                        ins.then_inc(summed, 1)
                ins.then_inc(m.w_used, 1)
            for b in range(6):
                pe.wait_ge(rbank[b], 2)
            pe.wait_ge(r_ok, 4 * NN)
            l1 = [l0[s] + (s < GH) for s in range(SLOTS)]
            with pe.Fori(0, KD // 2) as it:
                for jj in range(2):
                    for c in range(3):
                        k = 3 if c == 2 else 1
                        pe.wait_ge(m.w_in[3 * jj + c], it * (16 * k) + 16 * (l1[3 * jj + c] + k))
                    for n in range(NN):
                        t = 3 * jj + n
                        b = 4 * (t % 2)
                        tok = slice(n * NW, (n + 1) * NW)
                        pe.wait_ge(bank, it * 6 + (t + 1))
                        last = [product(pe, ps[:, b + c, 0:NW], m.ring[:, 3 * jj + c], lambda k: m.hT[:, k, tok])
                                for c in range(2)]
                        product(pe, ps[:, b + 2, 0:NW], m.ring[:, 3 * jj + 2, 0:HP], lambda k: m.zT[:, k, tok])
                        ins = product(pe, ps[:, b + 3, 0:NW], m.ring[:, 3 * jj + 2, HP:KD], lambda k: m.oglaT[:, k, tok])
                        if n == NN - 1:
                            for x in last:
                                x.then_inc(m.w_used, 1)
                            ins.then_inc(m.w_used, 1)
                        else:
                            ins.then_inc(step_mm, 1)

        def ready(e, it, jj, n):
            if n < NN - 1:
                e.wait_ge(step_mm, it * 4 + (2 * jj + n + 1))
            else:
                e.wait_ge(m.w_used, it * 6 + (u0 + GH + 3 * jj + 3))

        def r_ready(e, u, n):
            if n < NN - 1:
                e.wait_ge(summed, 2 * u + n + 1)
            else:
                e.wait_ge(m.w_used, u0 + u + 1)

        @block.scalar
        def _(act):
            for u in range(GH):
                for n in range(NN):
                    b = 3 * (u % 2) + n
                    r_ready(act, u, n)
                    if u >= 2:
                        act.wait_ge(r_ok, 3 * (u - 2) + n + 1)
                    act.activation(rt[b], ps[:, b, 0:NW], ACT.Sigmoid).then_inc(r_sig, 1)
            with act.Fori(0, KD // 2) as it:
                for jj in range(2):
                    for n in range(NN):
                        t = 3 * jj + n
                        ready(act, it, jj, n)
                        act.wait_ge(add, it * 6 + (t + 1))
                        for c in range(2):
                            act.activation(gate[t % 2][c], ps[:, 4 * (t % 2) + c, 0:NW], ACT.Sigmoid).then_inc(sig, 1)

        @block.vector
        def _(dve):
            for u in range(GH):
                for n in range(NN):
                    b = 3 * (u % 2) + n
                    dve.wait_ge(r_sig, 3 * u + n + 1)
                    dve.tensor_tensor(rt[b], rt[b], ps[:, b, 0:NW], ALU.mult).then_inc(rbank[b], 1)
            dve.sem_inc(bank, 2)
            with dve.Fori(0, KD // 2) as it:
                for t in range(6):
                    dve.wait_ge(sig, it * 12 + (2 * t + 2))
                    for c in range(2):
                        ins = dve.tensor_tensor(gate[t % 2][c], gate[t % 2][c], ps[:, 4 * (t % 2) + 2 + c, 0:NW], ALU.mult)
                        if c == 0:
                            ins.then_inc(mul, 1)
                    ins.then_inc(bank, 1)

        @block.gpsimd
        def _(pool):
            for u in range(GH):
                for n in range(NN):
                    b = 3 * (u % 2) + n
                    og = m.oglaT[:, u, n * NW:(n + 1) * NW]
                    pool.wait_ge(rbank[b], u // 2 + 1)
                    pool.tensor_tensor(og, og, rt[b], ALU.mult).then_inc(r_ok, 1)
            pool.sem_inc(add, 2)
            with pool.Fori(0, KD // 2) as it:
                for jj in range(2):
                    for n in range(NN):
                        t = 3 * jj + n
                        pool.wait_ge(mul, it * 6 + (t + 1))
                        pool.wait_ge(bank, it * 6 + (t + 3))
                        out = m.merged[:, bass.ds(it * 2 + jj, 1), n * NW:(n + 1) * NW].rearrange("p o t -> p (o t)")
                        pool.tensor_tensor(out, gate[t % 2][0], gate[t % 2][1], ALU.add).then_inc(add, 1)
    m.used += GH + 3 * KD
    m.loads = [l0[s] + (s < GH) + (3 if s % 3 == 2 else 1) * KD // 2 for s in range(SLOTS)]


def stage_mix(m, I, O):
    nc, ps = m.nc, m.ps
    u0, l0 = m.used, m.loads
    R = m.rest
    rst, ones = R[:, 0:T], R[:, T:T + P]
    sq = [R[:, T + P + NW * b:T + P + NW * (b + 1)] for b in range(4)]
    sq2 = [m.oglaT[:, 0, 512 * i:512 * (i + 1)] for i in range(2)] + [m.oglaT[:, 1, 512 * i:512 * (i + 1)] for i in range(2)]
    sqs = m.oglaT[:, 2, 0:KD * ST].rearrange("p (k t) -> p k t", t=ST)
    tmp = m.oglaT[:, 3, :]
    xr = m.hT[:, :, :].rearrange("p k t -> p (k t)")[:, 0:QT * D].rearrange("p (i d) -> p i d", d=D)
    xs = m.vg[0:ST].rearrange("p i h v -> p (i h v)")[:, 0:D]
    x_in, summed, bank = m.sem("x_rows_in"), m.sem("mix_tile_summed"), [m.sem(f"mix_bank_free{b}") for b in range(6)]
    sq_ok, acc_ok, ss_mm, r_ok = m.sem("mix_squares"), m.sem("squares_added"), m.sem("mean_squares"), m.sem("rstd_steps")
    xT, x2_ok, sq2_ok = m.sem("x_turned"), m.sem("residual_ready"), m.sem("residual_squares")
    own, pre = m.sem("mix_vector_chain"), m.sem("mix_constants")
    n_ok = [m.sem("h_even_tiles_scaled"), m.sem("h_odd_tiles_scaled")]
    scaled, rt_ok, ss2_mm = m.sem("odd_tiles_scaled"), m.sem("roots_ready"), m.sem("residual_squares_summed")
    halves = [slice(0, 512), slice(512, T)]
    LAG = 5
    EARLY_ROOT = 12
    groups = [(h, k) for h in range(2) for k in range(KD)]
    G = len(groups)

    with nc.Block() as block:
        @block.sync
        def _(sp):
            sp.dma_start(xr, I["x_prompt"][0].rearrange("(i p) d -> p i d", p=P)).then_inc(x_in, 16)
            sp.dma_start(xs, I["x_sample"].rearrange("b s d -> (b s) d")).then_inc(x_in, 16)
            with sp.Fori(1, KD // 2) as it:
                for s in range(2):
                    sp.wait_ge(m.w_used, it * 2 + (u0 + s - 1))
                    sp.dma_start(m.ring[:, s], dyn_block(I["w_out"][0], it * 2 + s)).then_inc(m.w_in[s], 16)
            for hh in range(2):
                for c, w in enumerate(("w_ff_gate", "w_ff_up")):
                    sp.dma_start(m.ring[:, 2 + 2 * hh + c], w_block(I[w][0], hh * P)).then_inc(m.w_in[2 + 2 * hh + c], 16)

        @block.gpsimd
        def _(pool):
            pool.memset(ones, 1.0 / D).then_inc(pre, 1)
            pool.memset(m.acc[:, :], 0.0).then_inc(acc_ok, 1)
            pool.wait_ge(acc_ok, 1)
            pool.sem_inc(acc_ok, 1)
            with pool.Fori(0, KD // 2) as it:
                for t in range(6):
                    n = t % 3
                    a = m.acc[:, n * NW:(n + 1) * NW]
                    pool.wait_ge(sq_ok, it * 6 + (t + 1))
                    pool.wait_ge(acc_ok, it * 6 + (t + 2))
                    pool.tensor_tensor(a, a, sq[t % 4], ALU.add).then_inc(acc_ok, 1)
            for g, (h, k) in enumerate(groups):
                if k % 2:
                    pool.wait_ge(rt_ok, h + 1)
                    v = m.x2T[:, k, 512 * h:512 * (h + 1)]
                    pool.tensor_tensor(v, v, rst[:, 512 * h:512 * (h + 1)], ALU.mult).then_inc(scaled, 1)
            for g, (h, k) in enumerate(groups):
                if k % 2:
                    pool.wait_ge(rt_ok, h + 3)
                    pool.wait_ge(x2_ok, g + 1)
                    pool.tensor_tensor(m.hT[:, k, 512 * h:512 * (h + 1)], m.x2T[:, k, 512 * h:512 * (h + 1)],
                                       rst[:, 512 * h:512 * (h + 1)], ALU.mult).then_inc(n_ok[1], 1)

        @block.tensor
        def _(pe):
            with pe.Fori(0, KD // 2) as it:
                for s in range(2):
                    pe.wait_ge(m.w_in[s], it * 16 + 16 * (l0[s] + 1))
                    for n in range(NN):
                        pe.wait_ge(bank[3 * s + n], it + 1)
                        ins = product(pe, ps[:, 3 * s + n, 0:NW], m.ring[:, s], lambda k: m.merged[:, k, n * NW:(n + 1) * NW])
                        if n < NN - 1:
                            ins.then_inc(summed, 1)
                    ins.then_inc(m.w_used, 1)
            pe.wait_ge(pre, 1)
            pe.wait_ge(acc_ok, 2 + 3 * KD)
            for b in range(3):
                pe.wait_ge(bank[b], KD // 2 + 1)
                ins = pe.matmul(ps[:, b, 0:NW], ones, m.acc[:, b * NW:(b + 1) * NW], start=True, stop=True)
            ins.then_inc(ss_mm, 1)
            pe.wait_ge(x_in, 32)
            for b in range(3, 6):
                pe.wait_ge(bank[b], KD // 2 + 1)
            pe.wait_ge(r_ok, 1)
            for i in range(G + LAG):
                if i < G:
                    h, k = groups[i]
                    if i >= 4:
                        pe.wait_ge(x2_ok, i - 3)
                    for j in range(4):
                        ins = pe.transpose(ps[:, 4 + i % 4, j * P:(j + 1) * P], xr[:, 4 * h + j, k * P:(k + 1) * P],
                                           m.ident[:, :])
                    ins.then_inc(xT, 1)
                if i == G - 1:
                    for k in range(KD):
                        ins = pe.transpose(ps[:, 3, k * ST:(k + 1) * ST], xs[:, k * P:(k + 1) * P], m.ident[0:ST, 0:ST])
                    ins.then_inc(xT, 1)
                if i >= LAG:
                    h, k = groups[i - LAG]
                    pe.wait_ge(sq2_ok, i - LAG + 1)
                    pe.matmul(ps[:, h, :], ones, sq2[(i - LAG) % 4], start=k == 0, stop=k == KD - 1).then_inc(
                        ss2_mm, 1)
            pe.wait_ge(sq2_ok, G + 1)
            for k in range(KD):
                ins = pe.matmul(ps[:, 2, 0:ST], ones, sqs[:, k, :], start=k == 0, stop=k == KD - 1)
            ins.then_inc(ss2_mm, 1)

        @block.scalar
        def _(act):
            with act.Fori(0, KD // 2) as it:
                for t in range(6):
                    s, n = t // 3, t % 3
                    if n < NN - 1:
                        act.wait_ge(summed, it * 4 + (2 * s + n + 1))
                    else:
                        act.wait_ge(m.w_used, it * 2 + (u0 + s + 1))
                    act.wait_ge(acc_ok, it * 6 + (t + 1))
                    act.activation(sq[t % 4], ps[:, t, 0:NW], ACT.Square).then_inc(sq_ok, 1)
            def root(n):
                r = rst[:, halves[n % 2]]
                act.wait_ge(r_ok, n + 2)
                act.activation(r, r, ACT.Sqrt).then_inc(rt_ok, 1)

            root(0)
            root(1)
            for g, (h, k) in enumerate(groups):
                act.wait_ge(x2_ok, g + 1)
                if g >= 4:
                    act.wait_ge(ss2_mm, g - 3)
                act.activation(sq2[g % 4], m.x2T[:, k, 512 * h:512 * (h + 1)], ACT.Square).then_inc(sq2_ok, 1)
                if g == EARLY_ROOT:
                    root(2)
            act.wait_ge(x2_ok, G + 1)
            act.activation(sqs, m.x2T[:, :, SEQ:T], ACT.Square).then_inc(sq2_ok, 1)
            for g, (h, k) in enumerate(groups):
                if g == KD:
                    root(3)
                v = m.hT[:, k, 512 * h:512 * (h + 1)]
                act.wait_ge(n_ok[k % 2], g // 2 + 1)
                act.activation(v, v, ACT.Identity, scale=m.modT[:, SC2 + k, 0:1], bias=m.modT[:, SH2 + k, 0:1])

        @block.vector
        def _(dve):
            steps = [0]

            def chain(ins):
                steps[0] += 1
                ins.then_inc(own, 1)
                dve.wait_ge(own, steps[0])

            for b in range(6):
                dve.sem_inc(bank[b], 1)
            with dve.Fori(0, KD // 2) as it:
                for t in range(6):
                    s, n = t // 3, t % 3
                    dve.wait_ge(sq_ok, it * 6 + (t + 1))
                    dve.tensor_copy(m.x2T[:, bass.ds(it * 2 + s, 1), n * NW:(n + 1) * NW], ps[:, t:t + 1, 0:NW]).then_inc(
                        bank[t], 1)
            dve.wait_ge(ss_mm, 1)
            for b in range(3):
                ins = dve.tensor_scalar(rst[:, b * NW:(b + 1) * NW], ps[:, b, 0:NW], EPS, None, ALU.add)
            ins.then_inc(r_ok, 1)
            dve.wait_ge(r_ok, 1)
            for r in halves:
                dve.reciprocal(rst[:, r], rst[:, r]).then_inc(r_ok, 1)

            def inverse(h):
                dve.wait_ge(ss2_mm, (KD, G + 1)[h])
                ins = dve.tensor_scalar(rst[:, 512 * h:512 * (h + 1)], ps[:, h, :], EPS, None, ALU.add)
                if h:
                    ins = dve.tensor_scalar(rst[:, SEQ:T], ps[:, 2, 0:ST], EPS, None, ALU.add)
                chain(ins)
                dve.reciprocal(rst[:, halves[h]], rst[:, halves[h]]).then_inc(r_ok, 1)

            v = m.x2T[:, :, SEQ:T]
            vb = v.rearrange("p k (b s) -> p k b s", s=DS)
            for g, (h, k) in enumerate(groups):
                t = m.x2T[:, k, 512 * h:512 * (h + 1)]
                dve.wait_ge(rt_ok, h + 1)
                if k % 2 == 0:
                    chain(dve.tensor_tensor(t, t, rst[:, 512 * h:512 * (h + 1)], ALU.mult))
                else:
                    dve.wait_ge(scaled, g // 2 + 1)
                dve.wait_ge(xT, g + 1)
                dve.scalar_tensor_tensor(out=t, in0=t, scalar=m.modT[:, GA1 + k, 0:1], in1=ps[:, 4 + g % 4, :],
                                         op0=ALU.mult, op1=ALU.add).then_inc(x2_ok, 1)
                if g == EARLY_ROOT:
                    inverse(0)
            chain(dve.tensor_tensor(v, v, rst[:, SEQ:T].unsqueeze(1).to_broadcast([P, KD, ST]), ALU.mult))
            chain(dve.tensor_tensor(vb, vb, per_batch(m, GA1), ALU.mult))
            dve.wait_ge(xT, G + 1)
            dve.tensor_tensor(v, v, ps[:, 3, 0:KD * ST].rearrange("p (k t) -> p k t", t=ST), ALU.add).then_inc(x2_ok, 1)

            def normalise(h):
                dve.wait_ge(rt_ok, h + 3)
                for k in range(0, KD, 2):
                    dve.tensor_tensor(m.hT[:, k, 512 * h:512 * (h + 1)], m.x2T[:, k, 512 * h:512 * (h + 1)],
                                      rst[:, 512 * h:512 * (h + 1)], ALU.mult).then_inc(n_ok[0], 1)

            normalise(0)
            inverse(1)
            normalise(1)
            hs = m.hT[:, :, SEQ:T]
            hb = hs.rearrange("p k (b s) -> p k b s", s=DS)
            chain(dve.tensor_tensor(hs, v, rst[:, SEQ:T].unsqueeze(1).to_broadcast([P, KD, ST]), ALU.mult))
            chain(dve.tensor_tensor(hb, hb, per_batch(m, SC2), ALU.mult))
            dve.tensor_tensor(hb, hb, per_batch(m, SH2), ALU.add)
    m.used += KD
    m.loads = [l0[s] + (KD // 2 if s < 2 else 0) for s in range(SLOTS)]


def stage_ffn_up(m, I, O):
    nc, ps = m.nc, m.ps
    u0, l0 = m.used, m.loads
    R = m.rest
    sg = [R[:, NW * b:NW * (b + 1)] for b in range(6)]
    step_mm, sig, mid = m.sem("hidden_summed"), m.sem("hidden_sigmoid"), m.sem("hidden_silu")
    bank = m.sem("hidden_banks_free")
    IT = KF // 2

    with nc.Block() as block:
        @block.sync
        def _(sp):
            with sp.Fori(1, IT) as it:
                for hh in range(2):
                    for c, w in enumerate(("w_ff_gate", "w_ff_up")):
                        slot = 2 + 2 * hh + c
                        sp.wait_ge(m.w_used, it * 4 + (u0 + 2 * hh + c - 3))
                        sp.dma_start(m.ring[:, slot], dyn_block(I[w][0], it * 2 + hh)).then_inc(m.w_in[slot], 16)
            for u in range(2):
                for c in range(3):
                    slot = 3 * u + c
                    if slot >= 2:
                        sp.wait_ge(m.w_used, u0 + 2 * KF - 4 + slot - 2 + 1)
                    load_down(sp, m, I, u, c, slot)

        @block.tensor
        def _(pe):
            with pe.Fori(0, IT) as it:
                for hh in range(2):
                    for c in range(2):
                        pe.wait_ge(m.w_in[2 + 2 * hh + c], it * 16 + 16 * (l0[2 + 2 * hh + c] + 1))
                    for n in range(NN):
                        t = 3 * hh + n
                        pe.wait_ge(bank, it * 6 + (t + 1))
                        last = [product(pe, ps[:, 2 * n + c, 0:NW], m.ring[:, 2 + 2 * hh + c],
                                        lambda k: m.hT[:, k, n * NW:(n + 1) * NW]) for c in range(2)]
                        if n < NN - 1:
                            last[1].then_inc(step_mm, 1)
                        else:
                            for x in last:
                                x.then_inc(m.w_used, 1)

        @block.scalar
        def _(act):
            with act.Fori(0, IT) as it:
                for hh in range(2):
                    for n in range(NN):
                        if n < NN - 1:
                            act.wait_ge(step_mm, it * 4 + (2 * hh + n + 1))
                        else:
                            act.wait_ge(m.w_used, it * 4 + (u0 + 2 * hh + 2))
                        act.activation(sg[3 * hh + n], ps[:, 2 * n, 0:NW], ACT.Sigmoid).then_inc(sig, 1)

        @block.vector
        def _(dve):
            dve.sem_inc(bank, 3)
            with dve.Fori(0, IT) as it:
                for hh in range(2):
                    for n in range(NN):
                        t = 3 * hh + n
                        dve.wait_ge(sig, it * 6 + (t + 1))
                        dve.tensor_tensor(sg[t], sg[t], ps[:, 2 * n, 0:NW], ALU.mult).then_inc(mid, 1)
                        dve.wait_ge(mid, it * 6 + (t + 1))
                        dve.tensor_tensor(m.guT[:, bass.ds(it * 2 + hh, 1), n * NW:(n + 1) * NW],
                                          sg[t].unsqueeze(1), ps[:, 2 * n + 1:2 * n + 2, 0:NW], ALU.mult).then_inc(bank, 1)
    m.used += 2 * KF
    m.loads = [l0[s] + (IT if s >= 2 else 0) for s in range(SLOTS)]


DOWN = [(0, 8), (8, 16), (16, KF)]


def load_down(sp, m, I, u, c, slot):
    a, b = DOWN[c]
    v = I["w_ff_down"][0].rearrange("(k p) n -> p k n", p=P)[:, a:b, bass.ds(u * P, P)]
    sp.dma_start(m.ring[:, slot, 0:b - a, :], v).then_inc(m.w_in[slot], 16)


def stage_ffn_down(m, I, O):
    nc, ps = m.nc, m.ps
    u0, l0 = m.used, m.loads
    R = m.rest
    rst, ones = R[:, 0:T], R[:, T:T + P]
    sq = [R[:, T + P + NW * b:T + P + NW * (b + 1)] for b in range(4)]
    rows = [m.guT[:, 0:2, :].rearrange("p u t -> p (u t)")[:, D * i:D * (i + 1)] for i in range(2)]
    rows += [m.guT[:, 2:4, :].rearrange("p u t -> p (u t)")[:, D * i:D * (i + 1)] for i in range(2)]
    summed, bank = m.sem("f_tile_summed"), [m.sem(f"f_bank_free{b}") for b in range(6)]
    sq_ok, acc_ok, ss_mm, r_ok = m.sem("f_squares"), m.sem("f_squares_added"), m.sem("f_mean_squares"), m.sem("f_rstd_steps")
    own, pre, y_ok, yT = m.sem("f_vector_chain"), m.sem("f_constants"), m.sem("y_ready"), m.sem("y_turned")
    y_row = [m.sem("y_left_rows_by_act"), m.sem("y_right_rows_by_act"), m.sem("y_right_rows_by_dve")]
    rt_ok, scaled = m.sem("f_roots_ready"), m.sem("odd_f_tiles_scaled")
    halves = [slice(0, 512), slice(512, T)]
    stored = [m.sem(f"y_stored{i}") for i in range(4)]
    groups = [(h, k) for h in range(2) for k in range(KD)]
    G = len(groups)

    def rows_ready(e, i):
        e.wait_ge(y_row[0], i + 1)
        if i < QT // 2:
            e.wait_ge(y_row[1], i + 1)
        else:
            e.wait_ge(y_row[2], i - QT // 2 + 1)

    with nc.Block() as block:
        @block.sync
        def _(sp):
            with sp.Fori(1, KD // 2) as it:
                for u in range(2):
                    for c in range(3):
                        sp.wait_ge(m.w_used, it * 6 + (u0 + 3 * u + c - 5))
                        load_down(sp, m, I, it * 2 + u, c, 3 * u + c)
            for i in range(TT):
                rows_ready(sp, i)
                if i < QT:
                    sp.dma_start(O["y_p"][0, i * P:(i + 1) * P, :], rows[i % 4]).then_inc(stored[i % 4], 16)
                else:
                    sp.dma_start(O["y_s"].rearrange("b s d -> (b s) d"), rows[i % 4][0:ST, :]).then_inc(stored[i % 4], 16)
            for i in range(4):
                sp.wait_ge(stored[i], 16 * len(range(i, TT, 4)))

        @block.gpsimd
        def _(pool):
            pool.memset(ones, 1.0 / D).then_inc(pre, 1)
            pool.memset(m.acc[:, :], 0.0).then_inc(acc_ok, 1)
            pool.wait_ge(acc_ok, 1)
            pool.sem_inc(acc_ok, 1)
            with pool.Fori(0, KD // 2) as it:
                for t in range(6):
                    n = t % 3
                    a = m.acc[:, n * NW:(n + 1) * NW]
                    pool.wait_ge(sq_ok, it * 6 + (t + 1))
                    pool.wait_ge(acc_ok, it * 6 + (t + 2))
                    pool.tensor_tensor(a, a, sq[t % 4], ALU.add).then_inc(acc_ok, 1)
            for g, (h, k) in enumerate(groups):
                if k % 2:
                    pool.wait_ge(rt_ok, h + 1)
                    f = m.hT[:, k, 512 * h:512 * (h + 1)]
                    pool.tensor_tensor(f, f, rst[:, 512 * h:512 * (h + 1)], ALU.mult).then_inc(scaled, 1)

        @block.tensor
        def _(pe):
            with pe.Fori(0, KD // 2) as it:
                for s in range(2):
                    for c, (a, b) in enumerate(DOWN):
                        pe.wait_ge(m.w_in[3 * s + c], it * 16 + 16 * (l0[3 * s + c] + 1))
                        for n in range(NN):
                            if c == 0:
                                pe.wait_ge(bank[3 * s + n], it + 1)
                            ins = product(pe, ps[:, 3 * s + n, 0:NW], m.ring[:, 3 * s + c, 0:b - a],
                                          lambda k: m.guT[:, a + k, n * NW:(n + 1) * NW], first=c == 0, last=c == 2)
                            if c == 2 and n < NN - 1:
                                ins.then_inc(summed, 1)
                        ins.then_inc(m.w_used, 1)
            pe.wait_ge(pre, 1)
            pe.wait_ge(acc_ok, 2 + 3 * KD)
            for b in range(3):
                pe.wait_ge(bank[b], KD // 2 + 1)
                ins = pe.matmul(ps[:, b, 0:NW], ones, m.acc[:, b * NW:(b + 1) * NW], start=True, stop=True)
            ins.then_inc(ss_mm, 1)
            for b in range(3, 6):
                pe.wait_ge(bank[b], KD // 2 + 1)
            pe.wait_ge(r_ok, 1)
            for i in range(TT):
                n = P if i < QT else ST
                pe.wait_ge(y_ok, G // 2 * (i // 4 + 1) if i < QT else G + 1)
                if i >= 4:
                    rows_ready(pe, i - 4)
                for k in range(KD):
                    ins = pe.transpose(ps[0:n, 2 * (i % 4) + k // 4, (k % 4) * P:(k % 4 + 1) * P],
                                       m.x2T[:, k, i * P:i * P + n], m.ident[:, :])
                ins.then_inc(yT, 1)

        @block.scalar
        def _(act):
            with act.Fori(0, KD // 2) as it:
                for t in range(6):
                    s, n = t // 3, t % 3
                    if n < NN - 1:
                        act.wait_ge(summed, it * 4 + (2 * s + n + 1))
                    else:
                        act.wait_ge(m.w_used, it * 6 + (u0 + 3 * s + 3))
                    act.wait_ge(acc_ok, it * 6 + (t + 1))
                    act.activation(sq[t % 4], ps[:, t, 0:NW], ACT.Square).then_inc(sq_ok, 1)
            for h, r in enumerate(halves):
                act.wait_ge(r_ok, h + 2)
                act.activation(rst[:, r], rst[:, r], ACT.Sqrt).then_inc(rt_ok, 1)
            for i in range(TT):
                n = P if i < QT else ST
                act.wait_ge(yT, i + 1)
                if i >= 4:
                    act.wait_ge(stored[i % 4], 16 * (i // 4))
                for c in range(2 if i < QT // 2 else 1):
                    act.activation(rows[i % 4][0:n, 512 * c:512 * (c + 1)], ps[0:n, 2 * (i % 4) + c, :], ACT.Copy).then_inc(
                        y_row[c], 1)

        @block.vector
        def _(dve):
            steps = [0]

            def chain(ins):
                steps[0] += 1
                ins.then_inc(own, 1)
                dve.wait_ge(own, steps[0])

            for b in range(6):
                dve.sem_inc(bank[b], 1)
            with dve.Fori(0, KD // 2) as it:
                for t in range(6):
                    s, n = t // 3, t % 3
                    dve.wait_ge(sq_ok, it * 6 + (t + 1))
                    dve.tensor_copy(m.hT[:, bass.ds(it * 2 + s, 1), n * NW:(n + 1) * NW], ps[:, t:t + 1, 0:NW]).then_inc(
                        bank[t], 1)
            dve.wait_ge(ss_mm, 1)
            for b in range(3):
                ins = dve.tensor_scalar(rst[:, b * NW:(b + 1) * NW], ps[:, b, 0:NW], EPS, None, ALU.add)
            ins.then_inc(r_ok, 1)
            dve.wait_ge(r_ok, 1)
            for r in halves:
                dve.reciprocal(rst[:, r], rst[:, r]).then_inc(r_ok, 1)
            for g, (h, k) in enumerate(groups):
                f, v = m.hT[:, k, 512 * h:512 * (h + 1)], m.x2T[:, k, 512 * h:512 * (h + 1)]
                dve.wait_ge(rt_ok, h + 1)
                if k % 2 == 0:
                    chain(dve.tensor_tensor(f, f, rst[:, 512 * h:512 * (h + 1)], ALU.mult))
                else:
                    dve.wait_ge(scaled, g // 2 + 1)
                dve.scalar_tensor_tensor(out=v, in0=f, scalar=m.modT[:, GA2 + k, 0:1], in1=v, op0=ALU.mult,
                                         op1=ALU.add).then_inc(y_ok, 1)
            f, v = m.hT[:, :, SEQ:T], m.x2T[:, :, SEQ:T]
            fb = f.rearrange("p k (b s) -> p k b s", s=DS)
            chain(dve.tensor_tensor(f, f, rst[:, SEQ:T].unsqueeze(1).to_broadcast([P, KD, ST]), ALU.mult))
            chain(dve.tensor_tensor(fb, fb, per_batch(m, GA2), ALU.mult))
            dve.tensor_tensor(v, v, f, ALU.add).then_inc(y_ok, 1)
            for i in range(QT // 2, TT):
                n = P if i < QT else ST
                dve.wait_ge(yT, i + 1)
                dve.wait_ge(stored[i % 4], 16 * (i // 4))
                dve.tensor_copy(rows[i % 4][0:n, 512:1024], ps[0:n, 2 * (i % 4) + 1, :]).then_inc(y_row[2], 1)


OUTS = [("y_p", (1, SEQ, D)), ("y_s", (NB, DS, D)),
        ("cmp_p", (1, 1, SEQ, 2, 2, HD)), ("cmp_s", (1, NB, DS, 2, 2, HD)),
        ("slc_p", (1, 1, SEQ, 2, 2, HD)), ("slc_s", (1, NB, DS, 2, 2, HD)),
        ("win_p", (1, 1, WIN, 2, 2, HD)), ("win_s", (1, NB, WIN, 2, 2, HD)),
        ("gla_p", (1, 1, GH, GDK, GDV)), ("gla_s", (1, NB, GH, GDK, GDV))]


STAGES = [stage_prepare, stage_project, stage_gla, stage_compress, stage_samples, stage_attention, stage_merge,
          stage_mix, stage_ffn_up, stage_ffn_down]


def build(nc, I, O, probe=None, upto=len(STAGES)):
    with ExitStack() as ctx:
        m = allocate(nc, ctx)
        m.n_pool = I["cache_cmp_kv"].shape[1]
        for stage in STAGES[:upto]:
            with nc.cleanup_on_exit():
                stage(m, I, O)
        if probe is not None:
            probe(m)


def kernel(**inputs):
    nc = bacc.Bacc("TRN2", target_bir_lowering=False, num_devices=1)
    arrays, I, O = {}, {}, {}
    for name, a in inputs.items():
        a = np.ascontiguousarray(a)
        arrays["in_" + name] = a
        I[name] = nc.dram_tensor("in_" + name, a.shape, mybir.dt.from_np(a.dtype), kind="ExternalInput").ap()
    for name, shape in OUTS:
        O[name] = nc.dram_tensor("out_" + name, shape, F32, kind="ExternalOutput").ap()
    build(nc, I, O)
    r = run_bass_kernel_spmd(nc, [arrays], core_ids=[0])
    return tuple(r.results[0]["out_" + name] for name, _ in OUTS)
```
